# Optimizing a Trainium2 kernel written in Bass

```python
import math, functools
import jax
import jax.numpy as jnp
from jax import lax
import numpy as np

D_MODEL = 1024
BATCH = 1
SEQ = 512
DEPTH = 1
DEC_BATCH = 8
DEC_SEQ = 4
PAST_LEN = 4096
PAGE_SIZE = 128

HEAD_DIM = 64
MIX_WIDTH = D_MODEL
ML_WIDTH = D_MODEL // 4
ML_HEADS = ML_WIDTH // HEAD_DIM
ML_CHUNK = 64
LRU_WIDTH = D_MODEL // 4
LRU_BLOCKS = LRU_WIDTH // HEAD_DIM
LRU_C = 8.0
CONV_W = 4
NSA_WIDTH = MIX_WIDTH - ML_WIDTH - LRU_WIDTH
NSA_HEADS = NSA_WIDTH // HEAD_DIM
NSA_KV_HEADS = 2
NSA_REP = NSA_HEADS // NSA_KV_HEADS
NSA_KV_WIDTH = NSA_KV_HEADS * HEAD_DIM
CMP_BLK = 32
CMP_HID = 2 * HEAD_DIM
SLC_BLK = 64
N_SEL = 16
WINDOW = 512
WIN_QBLK = 128
SEL_QBLK = 128
FORCE_BONUS = 100.0
XA_HEADS = 4
XA_HEAD_DIM = 128
XA_INNER = XA_HEADS * XA_HEAD_DIM
N_MEM = 256
N_GROUPS = 4
EXP_PER_GROUP = 4
N_EXPERTS = N_GROUPS * EXP_PER_GROUP
EXP_FF = 256
TOP_FINE = 2
EPS = 1e-6
NEG = -1e30
IN_NAMES = ('ml_q', 'ml_k', 'ml_v', 'ml_o', 'ml_i', 'ml_f', 'lru_x', 'lru_g', 'nsa_q', 'k_cmp', 'v_cmp', 'k_slc', 'v_slc', 'k_win', 'v_win', 'nsa_gate')
IN_SIZES = (ML_WIDTH, ML_WIDTH, ML_WIDTH, ML_WIDTH, ML_HEADS, ML_HEADS, LRU_WIDTH, LRU_WIDTH, NSA_WIDTH) + (NSA_KV_WIDTH,) * 6 + (3 * NSA_HEADS,)
IN_COLS = 4 * ML_WIDTH + 2 * ML_HEADS + 2 * LRU_WIDTH + NSA_WIDTH + 6 * NSA_KV_WIDTH + 3 * NSA_HEADS
F32 = jnp.float32

kernel_name = 'hymba_mlstm_rglru_nsa_hmoe_step'

def rms_norm(x, g):
    xf = x.astype(F32)
    y = xf * lax.rsqrt(jnp.mean(xf * xf, axis=-1, keepdims=True) + EPS)
    return (y * g.astype(F32)).astype(x.dtype)

def headwise_rms(y, g):
    shp = y.shape
    yh = y.astype(F32).reshape(shp[:-1] + (shp[-1] // HEAD_DIM, HEAD_DIM))
    yh = yh * lax.rsqrt(jnp.mean(yh * yh, axis=-1, keepdims=True) + EPS)
    return yh.reshape(shp) * g.astype(F32)

def masked_softmax(s, mask):
    p = jax.nn.softmax(jnp.where(mask, s, NEG), axis=-1)
    return jnp.where(mask, p, 0.0)

def alibi_slopes():
    h = jnp.arange(1, NSA_HEADS + 1, dtype=F32)
    return (2.0 ** (-8.0 * h / NSA_HEADS)).reshape(NSA_KV_HEADS, NSA_REP)

def split_in(u):
    offs = [int(o) for o in np.cumsum(IN_SIZES)[:-1]]
    return dict(zip(IN_NAMES, jnp.split(u, offs, axis=-1)))

def to_chunks(a, nc, L):
    B = a.shape[0]
    a = a.reshape((B, nc, L) + a.shape[2:])
    return jnp.moveaxis(jnp.swapaxes(a, 2, 3), 1, 0)

def mlstm_chunkwise(q, k, v, i_pre, f_pre, C0, n0, m0):
    B, T, H, D = q.shape
    L = T if T <= ML_CHUNK else math.gcd(T, ML_CHUNK)
    nc = T // L
    xs = (to_chunks(q.astype(F32), nc, L), to_chunks(k.astype(F32) * D ** -0.5, nc, L),
          to_chunks(v.astype(F32), nc, L), to_chunks(jax.nn.log_sigmoid(f_pre.astype(F32)), nc, L),
          to_chunks(i_pre.astype(F32), nc, L))
    causal = jnp.tril(jnp.ones((L, L), dtype=bool))

    def step(carry, chunk):
        C, n, m = carry
        qc, kc, vc, lf, ig = chunk
        b = jnp.cumsum(lf, axis=-1)
        log_d = jnp.where(causal, b[..., :, None] - b[..., None, :] + ig[..., None, :], -jnp.inf)
        inter = b + m[..., None]
        m_t = jnp.maximum(inter, jnp.max(log_d, axis=-1))
        w_carry = jnp.exp(inter - m_t)
        s = jnp.einsum('bhtd,bhsd->bhts', qc, kc) * jnp.exp(log_d - m_t[..., None])
        num = jnp.einsum('bhts,bhse->bhte', s, vc) + w_carry[..., None] * jnp.einsum('bhed,bhtd->bhte', C, qc)
        den = jnp.sum(s, axis=-1) + w_carry * jnp.einsum('bhd,bhtd->bht', n, qc)
        h = num / jnp.maximum(jnp.abs(den), jnp.exp(-m_t))[..., None]
        b_end = b[..., -1]
        log_w = b_end[..., None] - b + ig
        m_new = jnp.maximum(b_end + m, jnp.max(log_w, axis=-1))
        w = jnp.exp(log_w - m_new[..., None])
        decay = jnp.exp(b_end + m - m_new)
        C_new = decay[..., None, None] * C + jnp.einsum('bhs,bhse,bhsd->bhed', w, vc, kc)
        n_new = decay[..., None] * n + jnp.einsum('bhs,bhsd->bhd', w, kc)
        return (C_new, n_new, m_new), h

    (C, n, m), h = lax.scan(step, (C0.astype(F32), n0.astype(F32), m0.astype(F32)), xs)
    h = jnp.swapaxes(jnp.moveaxis(h, 0, 1), 2, 3).reshape(B, T, H * D)
    return h, C, n, m

def mlstm_group(pt, p, C0, n0, m0):
    B, T, _ = pt['ml_q'].shape
    shp = (B, T, ML_HEADS, HEAD_DIM)
    h, C, n, m = mlstm_chunkwise(pt['ml_q'].reshape(shp), pt['ml_k'].reshape(shp), pt['ml_v'].reshape(shp),
                                 pt['ml_i'] + p['ml_i_bias'], pt['ml_f'] + p['ml_f_bias'], C0, n0, m0)
    return jax.nn.sigmoid(pt['ml_o'].astype(F32)) * h, C, n, m

def lru_combine(c1, c2):
    a1, b1 = c1
    a2, b2 = c2
    return a1 * a2, a2 * b1 + b2

def rglru_group(pt, p, conv_buf, h0):
    xb = pt['lru_x'].astype(F32)
    B, T, W = xb.shape
    xe = jnp.concatenate([conv_buf.astype(F32), xb], axis=1)
    xc = p['conv_b'].astype(F32) + xe[:, 0:T] * p['conv_w'][0]
    for j in range(1, CONV_W):
        xc = xc + xe[:, j:j + T] * p['conv_w'][j]
    xh = xc.reshape(B, T, LRU_BLOCKS, HEAD_DIM)
    r = jax.nn.sigmoid(jnp.einsum('btkc,kcd->btkd', xh, p['lru_wa'].astype(F32)).reshape(B, T, W) + p['lru_ba'])
    i = jax.nn.sigmoid(jnp.einsum('btkc,kcd->btkd', xh, p['lru_wx'].astype(F32)).reshape(B, T, W) + p['lru_bx'])
    log_a = -LRU_C * r * jax.nn.softplus(-p['lru_lambda'].astype(F32))
    a = jnp.exp(log_a)
    u = jnp.sqrt(-jnp.expm1(2.0 * log_a)) * (i * xc)
    u = u.at[:, 0].add(a[:, 0] * h0.astype(F32))
    _, h = lax.associative_scan(lru_combine, (a, u), axis=1)
    y = h * jax.nn.gelu(pt['lru_g'].astype(F32))
    return y, xe[:, T:], h[:, -1]

def nsa_split(pt):
    B, T, _ = pt['nsa_q'].shape
    q = pt['nsa_q'].reshape(B, T, NSA_KV_HEADS, NSA_REP, HEAD_DIM)
    kv = [pt[nm].reshape(B, T, NSA_KV_HEADS, HEAD_DIM) for nm in ('k_cmp', 'v_cmp', 'k_slc', 'v_slc', 'k_win', 'v_win')]
    return q, kv

def compress(raw, p, c):
    B, NC = raw.shape[:2]
    z = raw + p['cmp_pos'][c][:, None, :]
    z = jnp.swapaxes(z, 2, 3).reshape(B, NC, NSA_KV_HEADS, CMP_BLK * HEAD_DIM)
    return jax.nn.gelu(z @ p['phi_w1'][c] + p['phi_b1'][c]) @ p['phi_w2'][c]

def cmp_attend(q, kc, vc, qpos, slopes):
    nc = kc.shape[1]
    c_end = jnp.arange(nc) * CMP_BLK + (CMP_BLK - 1)
    dist = qpos[:, None] - c_end[None, :]
    s = jnp.einsum('btgrd,bngd->bgrtn', q, kc).astype(F32) * HEAD_DIM ** -0.5
    s = s - slopes[:, :, None, None] * dist.astype(F32)
    pr = masked_softmax(s, dist >= 0)
    return jnp.einsum('bgrtn,bngd->btgrd', pr, vc.astype(F32)), pr

def select_blocks(p_cmp, qpos, total_len):
    imp = jnp.sum(p_cmp, axis=2)
    nc = imp.shape[-1]
    ratio = SLC_BLK // CMP_BLK
    ns = -(-total_len // SLC_BLK)
    imp = jnp.pad(imp, ((0, 0), (0, 0), (0, 0), (0, ns * ratio - nc)))
    imp = imp.reshape(imp.shape[:3] + (ns, ratio)).sum(-1)
    j = jnp.arange(ns)[None, :]
    cur = (qpos // SLC_BLK)[:, None]
    valid = j <= cur
    forced = (j == 0) | (j == cur) | (j == cur - 1)
    score = jnp.where(valid, imp + FORCE_BONUS * forced.astype(F32), NEG)
    top, idx = lax.top_k(score, min(N_SEL, ns))
    return idx, top > 0.5 * NEG

def sel_attend_item(q, kb, vb, kpos, valid, qpos, slopes):
    G, Q, N, SB, D = kb.shape
    R = q.shape[2]
    s = jnp.einsum('qgrd,gqnkd->gqrnk', q, kb).astype(F32) * D ** -0.5
    dist = qpos[None, :, None, None] - kpos
    mask = (dist >= 0) & valid[..., None]
    s = s - slopes[:, None, :, None, None] * dist.astype(F32)[:, :, None]
    pr = masked_softmax(s.reshape(G, Q, R, N * SB), mask.reshape(G, Q, 1, N * SB))
    return jnp.einsum('gqrm,gqmd->qgrd', pr, vb.reshape(G, Q, N * SB, D).astype(F32))

def band_attend(q, k, v, qpos, kpos, slopes):
    s = jnp.einsum('bcqgrd,bckgd->bcgrqk', q, k).astype(F32) * HEAD_DIM ** -0.5
    dist = qpos[:, :, None] - kpos[:, None, :]
    mask = (dist >= 0) & (dist < WINDOW) & (kpos >= 0)[:, None, :]
    s = s - slopes[None, None, :, :, None, None] * dist.astype(F32)[None, :, None, None]
    pr = masked_softmax(s, mask[None, :, None, None])
    return jnp.einsum('bcgrqk,bckgd->bcqgrd', pr, v.astype(F32))

def nsa_merge(pt, o_cmp, o_slc, o_win):
    B, T, _ = pt['nsa_gate'].shape
    g = jax.nn.sigmoid(pt['nsa_gate'].astype(F32)).reshape(B, T, 3, NSA_KV_HEADS, NSA_REP, 1)
    o = g[:, :, 0] * o_cmp + g[:, :, 1] * o_slc + g[:, :, 2] * o_win
    return o.reshape(B, T, NSA_WIDTH)

def nsa_prompt(pt, p, slopes):
    q, (k_cmp, v_cmp, k_slc, v_slc, k_win, v_win) = nsa_split(pt)
    B, T, G, R, D = q.shape
    qpos = jnp.arange(T)
    nc = T // CMP_BLK
    kc = compress(k_cmp.reshape(B, nc, CMP_BLK, G, D), p, 0)
    vc = compress(v_cmp.reshape(B, nc, CMP_BLK, G, D), p, 1)
    o_cmp, p_cmp = cmp_attend(q, kc, vc, qpos, slopes)
    idx, valid = select_blocks(p_cmp, qpos, T)
    n_sel = idx.shape[-1]
    ns = T // SLC_BLK
    kblk = k_slc.reshape(B, ns, SLC_BLK, G, D).transpose(0, 3, 1, 2, 4)
    vblk = v_slc.reshape(B, ns, SLC_BLK, G, D).transpose(0, 3, 1, 2, 4)
    nq = T // SEL_QBLK

    def by_qblock(a):
        return a.reshape(B, G, nq, SEL_QBLK, n_sel).transpose(0, 2, 1, 3, 4).reshape(B * nq, G, SEL_QBLK, n_sel)

    gi = jnp.arange(G)[:, None, None]
    ar = jnp.arange(SLC_BLK)

    def one_qblock(args):
        item, qi, ii, vi = args
        b = item // nq
        qp = (item % nq) * SEL_QBLK + jnp.arange(SEL_QBLK)
        kpos = ii[..., None] * SLC_BLK + ar
        return sel_attend_item(qi, kblk[b, gi, ii], vblk[b, gi, ii], kpos, vi, qp, slopes)

    o_slc = lax.map(one_qblock, (jnp.arange(B * nq), q.reshape(B * nq, SEL_QBLK, G, R, D),
                                 by_qblock(idx), by_qblock(valid))).reshape(B, T, G, R, D)
    nw = T // WIN_QBLK
    span = WINDOW + WIN_QBLK
    kidx = jnp.arange(nw)[:, None] * WIN_QBLK + jnp.arange(span)[None, :]
    pad = ((0, 0), (WINDOW, 0), (0, 0), (0, 0))
    kw = jnp.pad(k_win, pad)[:, kidx]
    vw = jnp.pad(v_win, pad)[:, kidx]
    o_win = band_attend(q.reshape(B, nw, WIN_QBLK, G, R, D), kw, vw, qpos.reshape(nw, WIN_QBLK),
                        kidx - WINDOW, slopes).reshape(B, T, G, R, D)
    y = nsa_merge(pt, o_cmp, o_slc, o_win)
    kv_rows = jnp.stack([k_cmp, v_cmp, k_slc, v_slc], axis=2)
    win_rows = jnp.stack([k_win, v_win], axis=2)[:, T - min(WINDOW, T):]
    return y, kv_rows, win_rows

def nsa_sample(pt, p, slopes, kv_pool, l, page_table, win_buf):
    q, (k_cmp, v_cmp, k_slc, v_slc, k_win, v_win) = nsa_split(pt)
    B, T, G, R, D = q.shape
    past = page_table.shape[1] * PAGE_SIZE
    total = past + T
    qpos = past + jnp.arange(T)
    raw = kv_pool[l, page_table, :, 0:2].reshape(B, past, 2, G, D)
    raw = jnp.concatenate([raw.astype(k_cmp.dtype), jnp.stack([k_cmp, v_cmp], axis=2)], axis=1)
    nc = total // CMP_BLK
    raw = raw[:, :nc * CMP_BLK].reshape(B, nc, CMP_BLK, 2, G, D)
    kc = compress(raw[:, :, :, 0], p, 0)
    vc = compress(raw[:, :, :, 1], p, 1)
    o_cmp, p_cmp = cmp_attend(q, kc, vc, qpos, slopes)
    idx, valid = select_blocks(p_cmp, qpos, total)
    ns_past = past // SLC_BLK
    ns_new = -(-T // SLC_BLK)
    new_blk = jnp.pad(jnp.stack([k_slc, v_slc], axis=2), ((0, 0), (0, ns_new * SLC_BLK - T), (0, 0), (0, 0), (0, 0)))
    new_blk = new_blk.reshape(B, ns_new, SLC_BLK, 2, G, D).transpose(0, 4, 1, 2, 3, 5)
    bi = jnp.arange(B)[:, None, None, None]
    gi = jnp.arange(G)[None, :, None, None]
    ar = jnp.arange(SLC_BLK)
    start = jnp.minimum(idx, ns_past - 1) * SLC_BLK
    phys = page_table[bi, start // PAGE_SIZE][..., None]
    rows = (start % PAGE_SIZE)[..., None] + ar
    kb_past = kv_pool[l, phys, rows, 2, gi[..., None]]
    vb_past = kv_pool[l, phys, rows, 3, gi[..., None]]
    fresh = new_blk[bi, gi, jnp.clip(idx - ns_past, 0, ns_new - 1)]
    in_past = (idx < ns_past)[..., None, None]
    kb = jnp.where(in_past, kb_past.astype(fresh.dtype), fresh[..., 0, :])
    vb = jnp.where(in_past, vb_past.astype(fresh.dtype), fresh[..., 1, :])
    kpos = idx[..., None] * SLC_BLK + ar
    o_slc = jax.vmap(sel_attend_item, in_axes=(0, 0, 0, 0, 0, None, None))(q, kb, vb, kpos, valid, qpos, slopes)
    wb = win_buf.shape[1]
    kw = jnp.concatenate([win_buf[:, :, 0].astype(k_win.dtype), k_win], axis=1)
    vw = jnp.concatenate([win_buf[:, :, 1].astype(v_win.dtype), v_win], axis=1)
    kpos_w = (past - wb + jnp.arange(wb + T))[None]
    o_win = band_attend(q[:, None], kw[:, None], vw[:, None], qpos[None], kpos_w, slopes)[:, 0]
    y = nsa_merge(pt, o_cmp, o_slc, o_win)
    kv_rows = jnp.stack([k_cmp, v_cmp, k_slc, v_slc], axis=2)
    win_new = jnp.stack([kw, vw], axis=2)[:, T:]
    return y, kv_rows, win_new

def mix_out(ya, yb, yc, p, dtype):
    y = jnp.concatenate([ya.astype(F32), yb.astype(F32), yc.astype(F32)], axis=-1)
    return headwise_rms(y, p['mix_norm']).astype(dtype) @ p['w_out']

def memory_kv(mem, p):
    B, M, _ = mem.shape
    return (rms_norm(mem, p['norm_mem']) @ p['xa_wkv']).reshape(B, M, 2, XA_HEADS, XA_HEAD_DIM)

def cross_attend(xn, mkv, p):
    B, T, _ = xn.shape
    q = (xn @ p['xa_wq']).reshape(B, T, XA_HEADS, XA_HEAD_DIM)
    s = jnp.einsum('bthd,bmhd->bhtm', q, mkv[:, :, 0]).astype(F32) * XA_HEAD_DIM ** -0.5
    a = jax.nn.softmax(s, axis=-1)
    o = jnp.einsum('bhtm,bmhd->bthd', a, mkv[:, :, 1].astype(F32))
    return o.reshape(B, T, XA_INNER).astype(xn.dtype) @ p['xa_wo']

def hier_moe(xn, p):
    shp = xn.shape
    z = xn.reshape(-1, shp[-1])
    pg = jax.nn.softmax((z @ p['router_gw'] + p['router_gb']).astype(F32), axis=-1)
    gw, gsel = lax.top_k(pg, 1)
    gsel_1h = jax.nn.one_hot(gsel[:, 0], N_GROUPS, dtype=F32)
    le = (z @ p['router_ew'] + p['router_eb']).astype(F32).reshape(-1, N_GROUPS, EXP_PER_GROUP)
    le_sel = jnp.einsum('ng,nge->ne', gsel_1h, le)
    tv, ti = lax.top_k(le_sel, TOP_FINE)
    fine = jnp.einsum('nk,nke->ne', jax.nn.softmax(tv, axis=-1), jax.nn.one_hot(ti, EXP_PER_GROUP, dtype=F32))
    comb = ((gw * gsel_1h)[:, :, None] * fine[:, None, :]).reshape(-1, N_EXPERTS)
    hg = jnp.einsum('nd,edf->nef', z, p['exp_w_gate'])
    hu = jnp.einsum('nd,edf->nef', z, p['exp_w_up'])
    h = jax.nn.silu(hg) * hu * comb[:, :, None].astype(z.dtype)
    return jnp.einsum('nef,efd->nd', h, p['exp_w_down']).reshape(shp)

def trunk_layer(x, p, nsa_fn, ml_state, lru_state, mkv):
    h = rms_norm(x, p['norm_mix'])
    pt = split_in(h @ p['w_in'])
    ya, C, n, m = mlstm_group(pt, p, ml_state[0], ml_state[1], ml_state[2])
    yb, conv, h_last = rglru_group(pt, p, lru_state[0], lru_state[1])
    yc, kv_rows, win_rows = nsa_fn(pt)
    x = x + mix_out(ya, yb, yc, p, x.dtype)
    x = x + cross_attend(rms_norm(x, p['norm_xa']), mkv, p)
    x = x + hier_moe(rms_norm(x, p['norm_ffn']), p)
    return x, (kv_rows, win_rows, C, n, m, h_last, conv)

def setup_inputs(seed: int = 0) -> dict:
    key = jax.random.key(seed)
    ks = jax.random.split(key, 64)
    counter = [0]

    def nk():
        counter[0] += 1
        return ks[counter[0] - 1]

    def nrm(shape, scale):
        return scale * jax.random.normal(nk(), shape, F32)

    def gain(shape):
        return 1.0 + nrm(shape, 0.02)

    G, HD = NSA_KV_HEADS, HEAD_DIM
    n_pages = PAST_LEN // PAGE_SIZE
    n_phys = (DEC_BATCH * n_pages * 5) // 4
    wb = min(WINDOW, PAST_LEN)
    page_table = jax.random.permutation(nk(), n_phys)[:DEC_BATCH * n_pages].reshape(DEC_BATCH, n_pages).astype(jnp.int32)
    a_c = jax.random.uniform(nk(), (DEPTH, LRU_WIDTH), F32, 0.9, 0.999)
    a0 = a_c ** (1.0 / LRU_C)
    lru_lambda = jnp.log(a0) - jnp.log1p(-a0)
    return {
        'x_prompt': nrm((BATCH, SEQ, D_MODEL), 1.0),
        'x_sample': nrm((DEC_BATCH, DEC_SEQ, D_MODEL), 1.0),
        'cache_nsa_kv': nrm((DEPTH, n_phys, PAGE_SIZE, 4, G, HD), 1.0),
        'state_nsa_win': nrm((DEPTH, DEC_BATCH, wb, 2, G, HD), 1.0),
        'state_mlstm_C': nrm((DEPTH, DEC_BATCH, ML_HEADS, HD, HD), 1.0),
        'state_mlstm_n': nrm((DEPTH, DEC_BATCH, ML_HEADS, HD), 1.0),
        'state_mlstm_m': nrm((DEPTH, DEC_BATCH, ML_HEADS), 1.0),
        'state_rglru_h': nrm((DEPTH, DEC_BATCH, LRU_WIDTH), 0.5),
        'state_rglru_conv': nrm((DEPTH, DEC_BATCH, CONV_W - 1, LRU_WIDTH), 1.0),
        'cache_mem_kv': nrm((DEPTH, DEC_BATCH, N_MEM, 2, XA_HEADS, XA_HEAD_DIM), 1.0),
        'page_table': page_table,
        'mem_prompt': nrm((BATCH, N_MEM, D_MODEL), 1.0),
        'norm_mix': gain((DEPTH, D_MODEL)),
        'w_in': nrm((DEPTH, D_MODEL, IN_COLS), D_MODEL ** -0.5),
        'ml_i_bias': nrm((DEPTH, ML_HEADS), 0.1),
        'ml_f_bias': 3.0 + 3.0 * jax.random.uniform(nk(), (DEPTH, ML_HEADS), F32),
        'conv_w': nrm((DEPTH, CONV_W, LRU_WIDTH), CONV_W ** -0.5),
        'conv_b': nrm((DEPTH, LRU_WIDTH), 0.02),
        'lru_wa': nrm((DEPTH, LRU_BLOCKS, HD, HD), HD ** -0.5),
        'lru_ba': nrm((DEPTH, LRU_WIDTH), 0.02),
        'lru_wx': nrm((DEPTH, LRU_BLOCKS, HD, HD), HD ** -0.5),
        'lru_bx': nrm((DEPTH, LRU_WIDTH), 0.02),
        'lru_lambda': lru_lambda,
        'phi_w1': nrm((DEPTH, 2, CMP_BLK * HD, CMP_HID), (CMP_BLK * HD) ** -0.5),
        'phi_b1': nrm((DEPTH, 2, CMP_HID), 0.02),
        'phi_w2': nrm((DEPTH, 2, CMP_HID, HD), CMP_HID ** -0.5),
        'cmp_pos': nrm((DEPTH, 2, CMP_BLK, HD), 0.1),
        'mix_norm': gain((DEPTH, MIX_WIDTH)),
        'w_out': nrm((DEPTH, MIX_WIDTH, D_MODEL), MIX_WIDTH ** -0.5),
        'norm_xa': gain((DEPTH, D_MODEL)),
        'norm_mem': gain((DEPTH, D_MODEL)),
        'xa_wq': nrm((DEPTH, D_MODEL, XA_INNER), D_MODEL ** -0.5),
        'xa_wkv': nrm((DEPTH, D_MODEL, 2 * XA_INNER), D_MODEL ** -0.5),
        'xa_wo': nrm((DEPTH, XA_INNER, D_MODEL), XA_INNER ** -0.5),
        'norm_ffn': gain((DEPTH, D_MODEL)),
        'router_gw': nrm((DEPTH, D_MODEL, N_GROUPS), D_MODEL ** -0.5),
        'router_gb': nrm((DEPTH, N_GROUPS), 0.01),
        'router_ew': nrm((DEPTH, D_MODEL, N_EXPERTS), D_MODEL ** -0.5),
        'router_eb': nrm((DEPTH, N_EXPERTS), 0.01),
        'exp_w_gate': nrm((DEPTH, N_EXPERTS, D_MODEL, EXP_FF), D_MODEL ** -0.5),
        'exp_w_up': nrm((DEPTH, N_EXPERTS, D_MODEL, EXP_FF), D_MODEL ** -0.5),
        'exp_w_down': nrm((DEPTH, N_EXPERTS, EXP_FF, D_MODEL), EXP_FF ** -0.5),
        'final_norm': gain((D_MODEL,)),
    }

def reference(x_prompt, x_sample, cache_nsa_kv, state_nsa_win, state_mlstm_C, state_mlstm_n, state_mlstm_m,
              state_rglru_h, state_rglru_conv, cache_mem_kv, page_table, mem_prompt, norm_mix, w_in, ml_i_bias,
              ml_f_bias, conv_w, conv_b, lru_wa, lru_ba, lru_wx, lru_bx, lru_lambda, phi_w1, phi_b1, phi_w2, cmp_pos,
              mix_norm, w_out, norm_xa, norm_mem, xa_wq, xa_wkv, xa_wo, norm_ffn, router_gw, router_gb, router_ew,
              router_eb, exp_w_gate, exp_w_up, exp_w_down, final_norm):
    weights = dict(norm_mix=norm_mix, w_in=w_in, ml_i_bias=ml_i_bias, ml_f_bias=ml_f_bias, conv_w=conv_w,
                   conv_b=conv_b, lru_wa=lru_wa, lru_ba=lru_ba, lru_wx=lru_wx, lru_bx=lru_bx, lru_lambda=lru_lambda,
                   phi_w1=phi_w1, phi_b1=phi_b1, phi_w2=phi_w2, cmp_pos=cmp_pos, mix_norm=mix_norm, w_out=w_out,
                   norm_xa=norm_xa, norm_mem=norm_mem, xa_wq=xa_wq, xa_wkv=xa_wkv, xa_wo=xa_wo, norm_ffn=norm_ffn,
                   router_gw=router_gw, router_gb=router_gb, router_ew=router_ew, router_eb=router_eb,
                   exp_w_gate=exp_w_gate, exp_w_up=exp_w_up, exp_w_down=exp_w_down)
    slopes = alibi_slopes()

    x = x_prompt
    B = x.shape[0]
    outs_p, mem_p = [], []
    for l in range(DEPTH):
        p = {name: w[l] for name, w in weights.items()}
        ml0 = (jnp.zeros((B, ML_HEADS, HEAD_DIM, HEAD_DIM), F32), jnp.zeros((B, ML_HEADS, HEAD_DIM), F32),
               jnp.zeros((B, ML_HEADS), F32))
        lru0 = (jnp.zeros((B, CONV_W - 1, LRU_WIDTH), F32), jnp.zeros((B, LRU_WIDTH), F32))
        mkv = memory_kv(mem_prompt, p)
        x, st = trunk_layer(x, p, functools.partial(nsa_prompt, p=p, slopes=slopes), ml0, lru0, mkv)
        outs_p.append(st)
        mem_p.append(mkv)
    y_prompt = rms_norm(x, final_norm)

    x = x_sample
    outs_s = []
    for l in range(DEPTH):
        p = {name: w[l] for name, w in weights.items()}
        nsa_fn = functools.partial(nsa_sample, p=p, slopes=slopes, kv_pool=cache_nsa_kv, l=l,
                                   page_table=page_table, win_buf=state_nsa_win[l])
        x, st = trunk_layer(x, p, nsa_fn, (state_mlstm_C[l], state_mlstm_n[l], state_mlstm_m[l]),
                            (state_rglru_conv[l], state_rglru_h[l]), cache_mem_kv[l])
        outs_s.append(st)
    y_sample = rms_norm(x, final_norm)

    sp = [jnp.stack(a) for a in zip(*outs_p)]
    ss = [jnp.stack(a) for a in zip(*outs_s)]
    mem_kv_prompt = jnp.stack(mem_p)
    return (y_prompt, y_sample, sp[0], ss[0], sp[1], ss[1], sp[2], ss[2], sp[3], ss[3], sp[4], ss[4],
            sp[5], ss[5], sp[6], ss[6], mem_kv_prompt)


_drawn_inputs = setup_inputs


def setup_inputs(seed=0):
    import zlib

    import numpy as np

    out = dict(_drawn_inputs(seed))
    spreads = {}
    factors = {'ml_i_bias': 8.0,
     'lru_ba': 7.826,
     'lru_bx': 8.0,
     'mix_norm': 2.728,
     'norm_xa': 8.0,
     'norm_mem': 2.777,
     'router_gb': 18.987,
     'router_eb': 60.368,
     'final_norm': 7.512,
     'norm_ffn': 7.957}
    for name, (base, spread) in spreads.items():
        noise = np.random.default_rng([zlib.crc32(name.encode()), seed]).standard_normal(out[name].shape)
        drawn = base * np.exp(spread * noise) if base else spread * noise
        out[name] = jnp.asarray(drawn.astype(out[name].dtype))
    for name, factor in factors.items():
        out[name] = (out[name] * factor).astype(out[name].dtype)
    return out
```

```python
from contextlib import ExitStack

import numpy as np

import concourse.bass as bass
from concourse import mybir

F32 = mybir.dt.float32
I32 = mybir.dt.int32
ALU = mybir.AluOpType
ACT = mybir.ActivationFunctionType
AX = mybir.AxisListType.X

P = 128
D = 1024
KT = D // P
TP = 512
NB, ST = 8, 4
TS = NB * ST
NT = TP + TS
QT = TP // P
HD = 64
MLH = 4
G, REP = 2, 4
PAGE, PAST = 128, 4096
NPB = PAST // PAGE
CT = PAST // 256
NCB = PAST // 32
PCB = TP // 32
NSB = PAST // 64
WIN = 512
XH, XD, NM = 4, 128, 256
NE, FF = 16, 256
HALF = NT // 2
EPS = 1e-6
NEG = -1e30
RING = 4

O_MLQ, O_I, O_F, O_LRU, O_NQ, O_KV, O_GATE = 0, 1024, 1028, 1032, 1544, 2056, 2824
T_Q, T_K, T_V, T_O, T_X, T_GL, T_NQ, T_KC, T_VC, T_KS, T_VS, T_KW, T_VW, T_IF, T_GT = \
    0, 2, 4, 6, 8, 10, 12, 16, 17, 18, 19, 20, 21, 22, 23
NPT = 24
V_MIX, V_XA, V_MEM, V_FFN, V_FIN, V_Y, V_CW, V_CB, V_BA, V_BX, V_LAM, V_PB, V_END = \
    0, 8, 16, 24, 32, 40, 48, 56, 58, 60, 62, 64, 66

CONST = {}
_at = 0
for _name, _n in (("ident", P), ("ones", P), ("headones", P), ("causal", P), ("blocked", P), ("eps", 1),
                  ("pair0", P), ("pair1", P), ("head0", P), ("head1", P), ("head2", P), ("head3", P),
                    ("sblocked", TS), ("inb", NB), ("grp", 32), ("bonus", 65),
                  ("bcmp", NCB), ("bwin", WIN), ("bnew", NB * TS), ("pcmp", QT * 8 * PCB), ("pvalid", QT * PCB),
                   ("vplace", 8)):
    CONST[_name] = (_at, _n)
    _at += _n
NCONST = _at


def shape_constants():
    c = np.zeros((P, NCONST), np.float32)

    def put(name, a):
        o, n = CONST[name]
        a = np.asarray(a, np.float32).reshape(len(a), n)
        c[:len(a), o:o + n] = a

    i = np.arange(P)
    put("ident", np.eye(P))
    put("ones", np.ones((P, P)))
    put("headones", i[:, None] // HD == i[None, :] // HD)
    put("causal", np.where(i[None, :] <= i[:, None], 0, NEG))
    put("blocked", np.where(i[:, None] <= i[None, :], 0, -NEG))
    put("eps", np.full((P, 1), EPS))
    for k in range(2):
        put(f"pair{k}", np.arange(MLH)[:, None] == 2 * k + i[None, :] // HD)
    for h in range(MLH):
        put(f"head{h}", (np.arange(MLH)[:, None] == h) & np.ones((1, P), bool))
    s = np.arange(TS)
    same = s[:, None] // ST == s[None, :] // ST
    put("sblocked", np.where(same & (s[:, None] <= s[None, :]), 0, -NEG))
    put("inb", s[:, None] // ST == np.arange(NB)[None, :])
    row_h, row_t = s // ST, s % ST
    put("grp", (row_h[:, None] // REP == row_h[None, :] // REP) & (row_t[:, None] == row_t[None, :]))
    bonus = np.zeros((32, 65))
    bonus[:, [0, 63, 64]] = 100.0
    put("bonus", bonus)
    slope = 2.0 ** -(row_h + 1.0)
    qpos = PAST + row_t
    put("bcmp", -slope[:, None] * (qpos[:, None] - (np.arange(NCB) * 32 + 31)[None, :]))
    kpos = PAST - WIN + np.arange(WIN)
    dist = qpos[:, None] - kpos[None, :]
    put("bwin", np.where(dist < WIN, -slope[:, None] * dist, NEG))
    new = np.empty((32, NB, TS))
    for b in range(NB):
        back = row_t[:, None] - (s % ST)[None, :]
        new[:, b] = np.where((s // ST == b)[None, :] & (back >= 0), -slope[:, None] * back, NEG)
    put("bnew", new)
    hs = 2.0 ** -(np.arange(8) + 1.0)
    q = np.arange(TP).reshape(QT, P).T
    dist = q[:, :, None] - (np.arange(PCB) * 32 + 31)[None, None, :]
    put("pcmp", np.where(dist >= 0, 0, NEG)[:, :, None, :] - hs[None, None, :, None] * dist[:, :, None, :])
    put("pvalid", dist >= 0)
    col = np.arange(8)
    put("vplace", (i[:, None] // 64 == col[None, :] % 2) & (i[:, None] // 16 % 4 == col[None, :] // 2))
    rel = np.arange(TP)[None, :] - (TP - P) - i[:, None]
    prompt = np.where(rel[:, None, :] <= 0, hs[None, :, None] * rel[:, None, :], NEG).astype(np.float32)
    past = (slope[:, None] * (np.arange(PAST)[None, :] - qpos[:, None])).astype(np.float32)
    return c, prompt, past


class Chain:

    def __init__(self, eng, sem, base=0):
        self.eng, self.sem, self.base, self.n = eng, sem, base, 0

    def step(self, ins):
        self.n += 1
        ins.then_inc(self.sem, 1)
        self.eng.wait_ge(self.sem, self.base + self.n)


class Semaphores:

    def __init__(self, nc):
        self.nc, self.part = nc, []

    def __call__(self, name):
        self.part.append(self.nc.alloc_semaphore(name=name))
        return self.part[-1]

    def keep(self):
        self.part = []

    def end_part(self):
        self.nc.clear_and_free_semaphores(self.part)
        self.part = []
        self.nc.all_engine_barrier()


def build(nc, I, O, K):
    with ExitStack() as ctx:
        sem = Semaphores(nc)

        def sb(name, shape, dt=F32):
            return ctx.enter_context(nc.sbuf_tensor(name, shape, dt))

        bank = [ctx.enter_context(nc.psum_tensor(f"bank{n}", [P, 512], F32)) for n in range(8)]
        gemm_big, gemm_small = bank[0:2], bank[2:4]
        work = bank[4:8]

        cst = sb("cst", [P, NCONST])
        vecT = sb("vecT", [P, V_END])
        xT = sb("xT", [P, KT, NT])
        ring = sb("ring", [P, RING, KT, P])
        yT = sb("yT", [P, KT, NT])
        memtok = sb("memtok", [P, 2, 2 * XH * XD])

        def const(name, rows=P):
            o, n = CONST[name]
            return cst[0:rows, o:o + n]

        ident = const("ident")

        w_loaded = [sem(f"w_loaded{u}") for u in range(RING)]
        w_done = [sem(f"w_done{p}") for p in range(2)]
        out_taken = [sem(f"out_taken{p}") for p in range(2)]

        stage, first, dmas = {}, 0, 0
        for name, n, pieces in (("in", 24, 2), ("mem", 8, 1), ("out", 8, 3), ("xq", 4, 1), ("xo", 8, 1),
                                ("up", 4 * NE, 1), ("down", 32, 1)):
            stage[name] = (first, pieces, dmas)
            first += n
            dmas += 16 * pieces * n // RING

        def slot_free(sp, name, it, u):
            sp.wait_ge(w_done[u % 2], stage[name][0] // 2 + 2 * it + u // 2 - 1)

        def weights_here(pe, name, it, u):
            _, pieces, before = stage[name]
            pe.wait_ge(w_loaded[u], 16 * pieces * it + before + 16 * pieces)

        def halves(par, width=NT):
            if width <= TP:
                return [(gemm_big[par][:, 0:width], 0)]
            return [(gemm_big[par][:, 0:HALF], 0), (gemm_small[par][:, 0:HALF], HALF)]

        def pe_gemm(pe, name, n_tiles, kts, rhs, width=NT, before=None):
            o2 = stage[name][0] // 2
            with pe.Fori(0, n_tiles // RING) as it:
                if before:
                    before(it)
                for u in range(RING):
                    par = u % 2
                    weights_here(pe, name, it, u)
                    pe.wait_ge(out_taken[par], it * 2 + o2 + u // 2)
                    for k in range(kts):
                        r, ends = rhs(k), dict(start=(k == 0), stop=(k == kts - 1))
                        for bank_, at in halves(par, width):
                            mm = pe.matmul(bank_, ring[:, u, k, :], r[:, at:at + bank_.shape[1]], **ends)
                    mm.then_inc(w_done[par], 1)

        def output_here(eng, name, it, u):
            eng.wait_ge(w_done[u % 2], it * 2 + stage[name][0] // 2 + u // 2 + 1)

        def act_copy(act, dst, par, n=NT):
            for bank_, at in halves(par, n):
                last = act.activation(dst[:, at:at + bank_.shape[1]], bank_, ACT.Copy)
            return last

        def dve_copy(dve, dst, par, n=NT):
            for bank_, at in halves(par, n):
                last = dve.tensor_copy(dst[:, at:at + bank_.shape[1]], bank_)
            return last

        def dve_add(dve, dst, par):
            for bank_, at in halves(par):
                last = dve.tensor_tensor(dst[:, at:at + HALF], bank_, dst[:, at:at + HALF], ALU.add)
            return last

        sq_ready, ss_ready = sem("sq_ready"), sem("ss_ready")
        std_ready, rstd_ready, norm_ready = sem("std_ready"), sem("rstd_ready"), sem("norm_ready")
        sums = work[2:4]
        stdt = sb("stdt", [P, NT])

        def norm_act(act, k, x, out, width=NT):
            for t in range(KT):
                act.activation(out[:, t, 0:width], x[:, t, 0:width], ACT.Square).then_inc(sq_ready, 1)
            act.wait_ge(ss_ready, k + 1)
            if k:
                act.wait_ge(norm_ready, KT * k)
            w = min(width, HALF)
            if width > HALF:
                act.activation(stdt[:, HALF:NT], sums[1][:, 0:HALF], ACT.Sqrt, bias=const("eps"), scale=1.0 / D)
            act.activation(stdt[:, 0:w], sums[0][:, 0:w], ACT.Sqrt, bias=const("eps"),
                           scale=1.0 / D).then_inc(std_ready, 1)

        def norm_pe(pe, k, out, width=NT):
            w = min(width, HALF)
            if k:
                pe.wait_ge(std_ready, k)
            for t in range(KT):
                pe.wait_ge(sq_ready, KT * k + t + 1)
                ends = dict(start=(t == 0), stop=(t == KT - 1))
                if width > HALF:
                    pe.matmul(sums[1][:, 0:HALF], const("ones"), out[:, t, HALF:NT], **ends)
                mm = pe.matmul(sums[0][:, 0:w], const("ones"), out[:, t, 0:w], **ends)
            mm.then_inc(ss_ready, 1)

        def norm_dve(dve, k, x, gain, out, width=NT):
            dve.wait_ge(std_ready, k + 1)
            dve.reciprocal(stdt[:, 0:width], stdt[:, 0:width]).then_inc(rstd_ready, 1)
            dve.wait_ge(rstd_ready, k + 1)
            for t in range(KT):
                dve.scalar_tensor_tensor(out=out[:, t, 0:width], in0=x[:, t, 0:width],
                                         scalar=vecT[:, gain + t:gain + t + 1], in1=stdt[:, 0:width],
                                         op0=ALU.mult, op1=ALU.mult).then_inc(norm_ready, 1)

        const_here = sem("const_here")
        out_dma = sem("out_dma")
        stores = [0]

        def store(eng, dst, src, scattered=False):
            stores[0] += 16
            return eng.dma_start(dst, src, allow_slow_non_contiguous=scattered).then_inc(out_dma, 16)

        QB = sb("QB", [P, NB, 32])
        ksn, kwn = sb("ksn", [P, TS]), sb("kwn", [P, TS])
        vnew = sb("vnew", [TS, 2, P])
        gq = sb("gq", [32, NB, 3])
        hb = sb("hb", [P, 2])
        gate_dram = nc.dram_tensor("gate_dram", (TS, 24), F32).ap()

        sem.keep()

        mixed = ctx.enter_context(ExitStack())
        pT = mixed.enter_context(nc.sbuf_tensor("pT", [P, NPT, NT], F32))
        memkv = mixed.enter_context(nc.sbuf_tensor("memkv", [P, 2 * XH, NM], F32))
        tok = mixed.enter_context(nc.sbuf_tensor("tok", [P, QT, 11, P], F32))
        toks = mixed.enter_context(nc.sbuf_tensor("toks", [TS, 11, P], F32))
        TK, TV, TOKKV = 0, 2, 4
        TGATE = 10
        with ExitStack() as c1:
            hT = c1.enter_context(nc.sbuf_tensor("hT", [P, KT, NT], F32))
            xtok = c1.enter_context(nc.sbuf_tensor("xtok", [P, 2, D], F32))
            mT = yT
            hmT = c1.enter_context(nc.sbuf_tensor("hmT", [P, KT, NM], F32))
            vecs = c1.enter_context(nc.sbuf_tensor("vecs", [V_END, P], F32))
            vecs_here = sem("vecs_here")
            x_here = [sem(f"x_here{j}") for j in range(2)]
            turned, turned_out = sem("turned"), sem("turned_out")
            tiles = [(P, xT, P * q) for q in range(QT)] + [(TS, xT, TP)] + [(P, mT, 0), (P, mT, P)]

            block = nc.Block()
            with block:
                @block.sync
                def _(sp):
                    sp.dma_start(cst[:, :], K["const"]).then_inc(const_here, 16)
                    xs = [I["x_prompt"][0, P * q:P * q + P, :] for q in range(QT)]
                    xs += [I["x_sample"].rearrange("b t n -> (b t) n")]
                    xs += [I["mem_prompt"][0, P * q:P * q + P, :] for q in range(2)]
                    for n, src in enumerate(xs):
                        if n >= 2:
                            sp.wait_ge(turned, 2 * n - 2)
                        sp.dma_start(xtok[0:tiles[n][0], n % 2, :], src).then_inc(x_here[n % 2], 16)
                    w = I["w_in"][0].rearrange("(k p) n -> p k n", p=P)
                    for n in range(NPT):
                        u = n % RING
                        if n >= RING:
                            slot_free(sp, "in", n // RING, u)
                        if n < T_X:
                            cols = [(0, 64, O_MLQ + P * n), (64, 64, O_MLQ + P * n + 64)]
                        elif n < T_NQ:
                            cols = [(0, 64, O_LRU + P * (n - T_X)), (64, 64, O_LRU + P * (n - T_X) + 64)]
                        elif n < T_KC:
                            cols = [(64 * g, 64, O_NQ + 256 * g + 64 * (n - T_NQ)) for g in range(G)]
                        elif n < T_IF:
                            cols = [(0, 64, O_KV + P * (n - T_KC)), (64, 64, O_KV + P * (n - T_KC) + 64)]
                        elif n == T_IF:
                            cols = [(0, 4, O_I), (32, 4, O_F)]
                        else:
                            cols = [(0, 12, O_GATE), (12, 12, O_GATE + 12)]
                        for dst, m, src in cols:
                            sp.dma_start(ring[:, u, :, dst:dst + m], w[:, :, src:src + m]).then_inc(w_loaded[u], 16)
                    w = I["xa_wkv"][0].rearrange("(k p) n -> p k n", p=P)
                    for n in range(8):
                        slot_free(sp, "mem", n // RING, n % RING)
                        sp.dma_start(ring[:, n % RING, :, :], w[:, :, P * n:P * n + P]).then_inc(w_loaded[n % RING], 16)

                @block.gpsimd
                def _(pool):
                    rows = [(V_MIX, I["norm_mix"][0]), (V_XA, I["norm_xa"][0]), (V_MEM, I["norm_mem"][0]),
                            (V_FFN, I["norm_ffn"][0]), (V_FIN, I["final_norm"]), (V_CB, I["conv_b"][0]),
                            (V_BA, I["lru_ba"][0]), (V_BX, I["lru_bx"][0]), (V_LAM, I["lru_lambda"][0]),
                            (V_Y, I["mix_norm"][0, 0:512])]
                    for at, v in rows:
                        n = v.shape[0] // P
                        pool.dma_start(vecs[at:at + n, :], v.rearrange("(k p) -> k p", p=P)).then_inc(vecs_here, 16)
                    for g in range(G):
                        pool.dma_start(vecs[V_Y + 4:V_Y + 8, 64 * g:64 * g + 64],
                                       I["mix_norm"][0, 512 + 256 * g:768 + 256 * g]
                                       .rearrange("(r d) -> r d", r=REP)).then_inc(vecs_here, 16)
                    pool.dma_start(vecs[V_CW:V_CW + 8, :], I["conv_w"][0].rearrange("j (k p) -> (j k) p", p=P))\
                        .then_inc(vecs_here, 16)
                    pool.dma_start(vecs[V_PB:V_PB + 2, :], I["phi_b1"][0]).then_inc(vecs_here, 16)

                @block.tensor
                def _(pe):
                    pe.wait_ge(const_here, 16)
                    n = 0
                    for j, (rows, _, _) in enumerate(tiles):
                        pe.wait_ge(x_here[j % 2], 16 * (j // 2 + 1))
                        for half in range(2):
                            if n >= 2:
                                pe.wait_ge(turned_out, n - 1)
                            for i in range(4):
                                k = 4 * half + i
                                mm = pe.transpose(work[n % 2][:, P * i:P * i + rows],
                                                  xtok[0:rows, j % 2, P * k:P * k + P], ident[0:rows, 0:rows])
                            mm.then_inc(turned, 1)
                            n += 1
                    pe.wait_ge(vecs_here, 16 * 14)
                    pe.wait_ge(turned_out, n - 1)
                    pe.transpose(work[n % 2][:, 0:V_END], vecs[:, :], ident[0:V_END, 0:V_END]).then_inc(turned, 1)
                    norm_pe(pe, 0, hT)
                    norm_pe(pe, 1, hmT, NM)
                    pe.wait_ge(norm_ready, KT)
                    pe_gemm(pe, "in", NPT, KT, lambda k: hT[:, k, :])
                    pe.wait_ge(norm_ready, 2 * KT)
                    pe_gemm(pe, "mem", 8, KT, lambda k: hmT[:, k, :], NM)

                @block.scalar
                def _(act):
                    act.wait_ge(const_here, 16)
                    act.wait_ge(turned_out, 15)
                    norm_act(act, 0, xT, hT)
                    norm_act(act, 1, mT, hmT, NM)
                    with act.Fori(0, NPT // RING) as it:
                        for u in (0, 2):
                            output_here(act, "in", it, u)
                            act_copy(act, pT[:, bass.ds(it * RING + u, 1), :].rearrange("p a n -> p (a n)"), 0)\
                                .then_inc(out_taken[0], 1)
                    for n in range(0, 8, 2):
                        output_here(act, "mem", n // RING, n % RING)
                        act_copy(act, memkv[:, n, :], 0, NM).then_inc(out_taken[0], 1)

                @block.vector
                def _(dve):
                    n = 0
                    for rows, dst, at in tiles:
                        for half in range(2):
                            dve.wait_ge(turned, n + 1)
                            dve.tensor_copy(dst[:, 4 * half:4 * half + 4, at:at + rows],
                                            work[n % 2][:, :].rearrange("p (k c) -> p k c", k=4)[:, :, 0:rows])\
                                .then_inc(turned_out, 1)
                            n += 1
                    dve.wait_ge(turned, n + 1)
                    dve.tensor_copy(vecT[:, :], work[n % 2][:, 0:V_END]).then_inc(turned_out, 1)
                    dve.wait_ge(turned_out, n + 1)
                    norm_dve(dve, 0, xT, V_MIX, hT)
                    norm_dve(dve, 1, mT, V_MEM, hmT, NM)
                    with dve.Fori(0, NPT // RING) as it:
                        for u in (1, 3):
                            output_here(dve, "in", it, u)
                            dve_copy(dve, pT[:, bass.ds(it * RING + u, 1), :].rearrange("p a n -> p (a n)"), 1)\
                                .then_inc(out_taken[1], 1)
                    for n in range(1, 8, 2):
                        output_here(dve, "mem", n // RING, n % RING)
                        dve_copy(dve, memkv[:, n, :], 1, NM).then_inc(out_taken[1], 1)

        gate_p = mixed.enter_context(nc.sbuf_tensor("gate_p", [P, QT, 24], F32))
        gate_s = mixed.enter_context(nc.sbuf_tensor("gate_s", [TS, 24], F32))
        lru_state = mixed.enter_context(nc.sbuf_tensor("lru_state", [32, 256], F32))
        lruT = mixed.enter_context(nc.sbuf_tensor("lruT", [P, 2, 32], F32))
        state_here, tok_turned, tok_taken = sem("state_here"), sem("tok_turned"), sem("tok_taken")
        tok_copied = [sem("tok_copied_act"), sem("tok_copied_dve")]
        to_turn = [T_K, T_K + 1, T_V, T_V + 1, T_KC, T_VC, T_KS, T_VS, T_KW, T_VW, T_GT]
        groups = []
        for q in range(QT + 1):
            at, rows = (P * q, P) if q < QT else (TP, TS)
            for j in range(0, len(to_turn), 4):
                part = to_turn[j:j + 4]
                dst = tok[:, q, j:j + len(part), :] if q < QT else toks[:, j:j + len(part), :]
                groups.append(([pT[:, t, at:at + rows] for t in part], rows, dst))
        for q in range(2):
            for j in range(0, 8, 4):
                groups.append(([memkv[:, j + i, P * q:P * q + P] for i in range(4)], P,
                               memtok[:, q, P * j:P * j + 512].rearrange("p (k c) -> p k c", k=4)))

        with nc.Block() as block:
            @block.sync
            def _(sp):
                sp.dma_start(lru_state[0:24, :], I["state_rglru_conv"][0].rearrange("b j w -> (b j) w"))\
                    .then_inc(state_here, 16)
                sp.dma_start(lru_state[24:32, :], I["state_rglru_h"][0]).then_inc(state_here, 16)
                store(sp, O["win_s"][0, :, 0:WIN - ST].rearrange("b t c g d -> b (t c g d)"),
                      I["state_nsa_win"][0, :, ST:WIN].rearrange("b t c g d -> b (t c g d)"))
                n = 0
                for q in range(QT + 1):
                    n += 3
                    sp.wait_ge(tok_copied[0], (n + 1) // 2)
                    sp.wait_ge(tok_copied[1], n // 2)
                    if q < QT:
                        rows = slice(P * q, P * q + P)
                        store(sp, O["kv_p"][0, 0, rows].rearrange("t c g d -> t (c g d)"),
                              tok[:, q, TOKKV:TOKKV + 4, :].rearrange("p c n -> p (c n)"))
                        store(sp, O["win_p"][0, 0, rows].rearrange("t c g d -> t (c g d)"),
                              tok[:, q, TOKKV + 4:TOKKV + 6, :].rearrange("p c n -> p (c n)"))
                    else:
                        store(sp, O["kv_s"][0].rearrange("b t c g d -> (b t) (c g d)"),
                              toks[:, TOKKV:TOKKV + 4, :].rearrange("p c n -> p (c n)"))
                        for b in range(NB):
                            store(sp, O["win_s"][0, b, WIN - ST:WIN].rearrange("t c g d -> t (c g d)"),
                                  toks[ST * b:ST * b + ST, TOKKV + 4:TOKKV + 6, :].rearrange("p c n -> p (c n)"))
                for q in range(2):
                    n += 2
                    sp.wait_ge(tok_copied[0], (n + 1) // 2)
                    sp.wait_ge(tok_copied[1], n // 2)
                    store(sp, O["mem_p"][0, 0, P * q:P * q + P].rearrange("t c h d -> t (c h d)"), memtok[:, q, :])

            @block.tensor
            def _(pe):
                for n, (srcs, rows, _) in enumerate(groups):
                    if n >= 4:
                        pe.wait_ge(tok_copied[n % 2], n // 2 - 1)
                    for i, src in enumerate(srcs):
                        mm = pe.transpose(work[n % 4][0:rows, P * i:P * i + P], src, ident)
                    mm.then_inc(tok_turned, 1)
                pe.wait_ge(state_here, 32)
                pe.wait_ge(tok_copied[0], len(groups) // 2 + len(groups) % 2 - 1)
                pe.wait_ge(tok_copied[1], len(groups) // 2)
                n = len(groups)
                for k in range(2):
                    mm = pe.transpose(work[n % 4][:, 32 * k:32 * k + 32], lru_state[:, P * k:P * k + P],
                                      ident[0:32, 0:32])
                mm.then_inc(tok_turned, 1)

            def copy_out(eng, par):
                for n, (srcs, rows, dst) in enumerate(groups):
                    if n % 2 == par:
                        eng.wait_ge(tok_turned, n + 1)
                        src = work[n % 4][0:rows, 0:P * len(srcs)].rearrange("p (k c) -> p k c", c=P)
                        ins = eng.activation(dst, src, ACT.Copy) if par == 0 else eng.tensor_copy(dst, src)
                        ins.then_inc(tok_copied[par], 1)

            @block.scalar
            def _(act):
                copy_out(act, 0)
                act.wait_ge(tok_copied[0], 8)
                act.wait_ge(tok_copied[1], 7)
                act.activation(gate_p[:, :, :], tok[:, :, TGATE, 0:24], ACT.Sigmoid)
                act.activation(gate_s[:, :], toks[:, TGATE, 0:24], ACT.Sigmoid)

            @block.vector
            def _(dve):
                copy_out(dve, 1)
                dve.wait_ge(tok_turned, len(groups) + 1)
                dve.tensor_copy(lruT[:, :, :],
                                work[len(groups) % 4][:, 0:64].rearrange("p (k c) -> p k c", k=2))

        with ExitStack() as c3:
            def t3(name, shape):
                return c3.enter_context(nc.sbuf_tensor(name, shape, F32))

            XP = TP + 3
            xpad = t3("xpad", [P, 2, XP])
            xsam = t3("xsam", [P, 2, NB, ST + 3])
            xc = t3("xc", [P, 2, NT])
            wab = t3("wab", [P, 2, 2, P])
            gr = t3("gr", [P, 2, NT])
            gi = t3("gi", [P, 2, NT])
            th = t3("th", [P, 2, NT])
            hseq = t3("hseq", [P, 2, NT])
            lam = t3("lam", [P, 8, 2])
            hl = t3("hl", [P, 2, 9])
            cl = t3("cl", [P, 2, 27])
            hlT = t3("hlT", [9, 2, P])
            clT = t3("clT", [27, 2, P])
            w_zero, w_here, chain, lru_mm = sem("lru_zero"), sem("lru_w"), sem("lru_chain"), sem("lru_mm")
            conv_done, gates_done, sp_done = sem("conv_done"), sem("gates_done"), sem("softplus_done")
            u_done, lru_act, last_done, last_turned, last_out = (
                sem("lru_u"), sem("lru_act"), sem("lru_last"), sem("lru_turned"), sem("lru_last_out"))
            lam_in = sem("lam_in")

            with nc.Block() as block:
                @block.sync
                def _(sp):
                    sp.wait_ge(w_zero, 1)
                    for j, name in enumerate(("lru_wa", "lru_wx")):
                        for k in range(4):
                            o = 64 * (k % 2)
                            sp.dma_start(wab[o:o + 64, j, k // 2, o:o + 64], I[name][0, k]).then_inc(w_here, 16)
                    sp.wait_ge(last_out, 2)
                    for k in range(2):
                        cols = slice(P * k, P * k + P)
                        store(sp, O["h_p"][0, :, cols], hlT[0:1, k, :])
                        store(sp, O["h_s"][0, :, cols], hlT[1:9, k, :])
                        store(sp, O["conv_p"][0, 0, :, cols], clT[0:3, k, :])
                        store(sp, O["conv_s"][0, :, :, cols].rearrange("b j w -> (b j) w"), clT[3:27, k, :])

                @block.gpsimd
                def _(pool):
                    pool.memset(wab[:, :, :, :], 0.0).then_inc(w_zero, 1)

                @block.tensor
                def _(pe):
                    pe.wait_ge(w_here, 16 * 8)
                    pe.wait_ge(conv_done, 1)
                    n = 0
                    for k in range(2):
                        for j in range(2):
                            if n >= 2:
                                pe.wait_ge(gates_done, n - 1)
                            pe.matmul(gemm_big[n % 2][:, :], wab[:, j, k, :], xc[:, k, 0:TP], start=True, stop=True)
                            pe.matmul(gemm_small[n % 2][:, 0:TS], wab[:, j, k, :], xc[:, k, TP:NT],
                                      start=True, stop=True).then_inc(lru_mm, 1)
                            n += 1
                    pe.wait_ge(last_done, 1)
                    for k in range(2):
                        pe.transpose(work[0][0:9, P * k:P * k + P], hl[:, k, :], ident)
                    for k in range(2):
                        mm = pe.transpose(work[1][0:27, P * k:P * k + P], cl[:, k, :], ident)
                    mm.then_inc(last_turned, 1)

                @block.scalar
                def _(act):
                    act.wait_ge(lam_in, 1)
                    act.activation(lam[:, 1, :], lam[:, 0, :], ACT.Exp).then_inc(sp_done, 1)
                    n = 0
                    for k in range(2):
                        for j, (dst, bias) in enumerate(((gr, V_BA), (gi, V_BX))):
                            act.wait_ge(lru_mm, n + 1)
                            act.activation(dst[:, k, 0:TP], gemm_big[n % 2][:, :], ACT.Sigmoid,
                                           bias=vecT[:, bias + k:bias + k + 1])
                            act.activation(dst[:, k, TP:NT], gemm_small[n % 2][:, 0:TS], ACT.Sigmoid,
                                           bias=vecT[:, bias + k:bias + k + 1]).then_inc(gates_done, 1)
                            n += 1
                    act.wait_ge(gates_done, 4)
                    act.wait_ge(sp_done, 2)
                    for k in range(2):
                        act.activation(th[:, k, :], gr[:, k, :], ACT.Tanh, scale=lam[:, 6, k:k + 1])
                    ins = act.activation(hseq[:, :, :], pT[:, T_GL:T_GL + 2, :], ACT.Gelu_apprx_tanh)
                    ins.then_inc(lru_act, 1)
                    for k in range(2):
                        ins = act.activation(gr[:, k, :], gr[:, k, :], ACT.Exp, scale=lam[:, 7, k:k + 1])
                    ins.then_inc(lru_act, 1)
                    act.wait_ge(u_done, 1)
                    act.activation(th[:, :, :], th[:, :, :], ACT.Sqrt).then_inc(lru_act, 1)

                @block.vector
                def _(dve):
                    c = Chain(dve, chain)
                    c.step(dve.tensor_scalar(lam[:, 2, :], vecT[:, V_LAM:V_LAM + 2], -1.0, None, ALU.mult))
                    dve.tensor_tensor(lam[:, 0, :], lam[:, 2, :], vecT[:, V_LAM:V_LAM + 2], ALU.min).then_inc(lam_in, 1)
                    c.step(dve.memset(xpad[:, :, 0:3], 0.0))
                    c.step(dve.tensor_copy(xpad[:, :, 3:XP], pT[:, T_X:T_X + 2, 0:TP]))
                    for k in range(2):
                        dve.tensor_copy(xsam[:, k, :, 0:3], lruT[:, k, 0:24].rearrange("p (b j) -> p b j", b=NB))
                        c.step(dve.tensor_copy(xsam[:, k, :, 3:7],
                                               pT[:, T_X + k, TP:NT].rearrange("p (b t) -> p b t", b=NB)))
                    for j in range(4):
                        for k in range(2):
                            tap = vecT[:, V_CW + 2 * j + k:V_CW + 2 * j + k + 1]
                            for dst, src in ((xc[:, k, 0:TP], xpad[:, k, j:j + TP]),
                                             (xc[:, k, TP:NT].rearrange("p (b t) -> p b t", b=NB),
                                              xsam[:, k, :, j:j + ST])):
                                if j == 0:
                                    ins = dve.tensor_scalar(dst, src, tap, vecT[:, V_CB + k:V_CB + k + 1],
                                                            ALU.mult, ALU.add)
                                else:
                                    ins = dve.scalar_tensor_tensor(out=dst, in0=src, scalar=tap, in1=dst,
                                                                   op0=ALU.mult, op1=ALU.add)
                        if j < 3:
                            c.step(ins)
                        else:
                            ins.then_inc(conv_done, 1)
                    dve.wait_ge(conv_done, 1)
                    y, s, s2, acc = lam[:, 1, :], lam[:, 3, :], lam[:, 4, :], lam[:, 5, :]
                    dve.wait_ge(sp_done, 1)
                    c.step(dve.tensor_scalar(s, y, 2.0, None, ALU.add))
                    c.step(dve.reciprocal(s, s))
                    c.step(dve.tensor_tensor(s, s, y, ALU.mult))
                    c.step(dve.tensor_tensor(s2, s, s, ALU.mult))
                    c.step(dve.tensor_scalar(acc, s2, 1.0 / 19, 1.0 / 17, ALU.mult, ALU.add))
                    for m in (15, 13, 11, 9, 7, 5, 3, 1):
                        c.step(dve.tensor_tensor(acc, acc, s2, ALU.mult))
                        c.step(dve.tensor_scalar(acc, acc, 1.0 / m, None, ALU.add))
                    c.step(dve.tensor_tensor(acc, acc, s, ALU.mult))
                    c.step(dve.tensor_scalar(s, lam[:, 2, :], 0.0, 0.5, ALU.max, ALU.mult))
                    c.step(dve.tensor_tensor(acc, acc, s, ALU.add))
                    dve.tensor_scalar(lam[:, 6, :], acc, 16.0, None, ALU.mult)
                    dve.tensor_scalar(lam[:, 7, :], acc, -16.0, None, ALU.mult).then_inc(sp_done, 1)
                    dve.wait_ge(lru_act, 1)
                    c.step(dve.tensor_tensor(gi[:, :, :], gi[:, :, :], xc[:, :, :], ALU.mult))
                    c.step(dve.tensor_scalar(xc[:, :, :], th[:, :, :], 1.0, None, ALU.add))
                    c.step(dve.reciprocal(xc[:, :, :], xc[:, :, :]))
                    dve.scalar_tensor_tensor(out=th[:, :, :], in0=th[:, :, :], scalar=2.0, in1=xc[:, :, :],
                                             op0=ALU.mult, op1=ALU.mult).then_inc(u_done, 1)
                    dve.wait_ge(lru_act, 3)
                    c.step(dve.tensor_tensor(gi[:, :, :], gi[:, :, :], th[:, :, :], ALU.mult))
                    h = xc
                    for k in range(2):
                        c.step(dve.tensor_tensor_scan(h[:, k, 0:TP], gr[:, k, 0:TP], gi[:, k, 0:TP], 0.0,
                                                      ALU.mult, ALU.add))
                    for k in range(2):
                        def step(x, t):
                            return x[:, k, TP:NT].rearrange("p (b t) -> p b t", t=ST)[:, :, t]
                        for t in range(ST):
                            prev = lruT[:, k, 24:32] if t == 0 else step(h, t - 1)
                            c.step(dve.tensor_tensor(step(h, t), step(gr, t), prev, ALU.mult))
                            c.step(dve.tensor_tensor(step(h, t), step(h, t), step(gi, t), ALU.add))
                    c.step(dve.tensor_copy(hl[:, :, 0:1], h[:, :, TP - 1:TP]))
                    for k in range(2):
                        c.step(dve.tensor_copy(hl[:, k, 1:9],
                                               h[:, k, TP:NT].rearrange("p (b t) -> p b t", t=ST)[:, :, ST - 1]))
                        c.step(dve.tensor_copy(cl[:, k, 3:27].rearrange("p (b j) -> p b j", b=NB),
                                               xsam[:, k, :, ST:ST + 3]))
                    dve.tensor_copy(cl[:, :, 0:3], xpad[:, :, TP:TP + 3]).then_inc(last_done, 1)
                    dve.tensor_tensor(yT[:, 2:4, :], h[:, :, :], hseq[:, :, :], ALU.mult)
                    dve.wait_ge(last_turned, 1)
                    dve.tensor_copy(hlT[:, :, :], work[0][0:9, 0:256].rearrange("p (k c) -> p k c", k=2))\
                        .then_inc(last_out, 1)
                    dve.tensor_copy(clT[:, :, :], work[1][0:27, 0:256].rearrange("p (k c) -> p k c", k=2))\
                        .then_inc(last_out, 1)

        with ExitStack() as c4:
            def t4(name, shape):
                return c4.enter_context(nc.sbuf_tensor(name, shape, F32))

            mlb = t4("mlb", [MLH, 2])
            m0 = t4("m0", [MLH, NB])
            lf, bsum, av, mx, wrow, emrow = (
                t4(n, [MLH, NT]) for n in ("lf", "bsum", "av", "mx", "wrow", "emrow"))
            mend = t4("mend", [MLH, 9])
            wcrow = t4("wcrow", [MLH, TS])
            decay = t4("decay", [MLH, NB])
            cols = t4("cols", [P, QT + 1, 2, MLH])
            sg = t4("sg", [P, 2, NT])
            wcb = t4("wcb", [P, 2, TS])
            qw = t4("qw", [HD, MLH, TS])
            nq = t4("nq", [HD, MLH, TS])
            n0 = t4("n0", [NB, 256])
            n0T = t4("n0T", [HD, MLH, NB])
            Cn = t4("Cn", [HD + 1, MLH, NB, HD])
            C0T = t4("C0T", [HD, MLH, NB, HD])
            Cp = t4("Cp", [HD + 1, MLH, HD])
            dg = t4("dg", [P, 2, P])
            idle = ring[:, :, :, :].rearrange("p u k c -> p (u k c)")
            E = idle[:, 0:2 * TP].rearrange("p (j t) -> p j t", j=2)
            W = idle[:, 2 * TP:4 * TP].rearrange("p (j t) -> p j t", j=2)
            vw = idle[:, 4 * TP:4 * TP + QT * MLH * (HD + 1)].rearrange("p (q h d) -> p q h d", q=QT, h=MLH)
            KM = idle[0:TS, 0:2 * TP].rearrange("p (j b d) -> p j b d", j=2, b=NB)
            dgs, Es, Ws = (t4(n, [TS, MLH, TS]) for n in ("dgs", "Es", "Ws"))
            vws = t4("vws", [TS, MLH, HD + 1])
            em = t4("em", [P, NT])
            dd = t4("dd", [P, NT])
            ax, ones4, fx = emrow, dd[0:MLH, :], em[0:MLH, :]
            db = t4("db", [HD + 1, MLH, NB])

            ml_in, ml_chain, ml_act, rows_ready = sem("ml_in"), sem("ml_chain"), sem("ml_act"), sem("ml_rows")
            cols_mm, cols_out = sem("ml_cols_mm"), sem("ml_cols_out")
            c0_mm, c0_out = sem("c0_turned"), sem("c0_out")
            mb_ready, dg_ready, e_ready, s_ready, w_ready, pv_done = (
                sem(f"ml_{n}") for n in ("mb", "dg", "e", "s", "w", "pv"))
            fin_mm, em_out, y_done = sem("ml_fin_mm"), sem("ml_em_out"), sem("ml_y")
            vw_ready, km_ready, cn_mm, cn_out, cp_mm, cp_out = (
                sem(f"ml_{n}") for n in ("vw", "km", "cn_mm", "cn_out", "cp_mm", "cp_out"))
            samp_mm, samp_e, samp_w, qw_ready = (sem(f"ml_{n}") for n in ("samp_mm", "samp_e", "samp_w", "qw"))
            steps = [(h, kt) for h in range(MLH) for kt in range(QT)]

            with nc.Block() as block:
                @block.sync
                def _(sp):
                    sp.dma_start(mlb[:, 0:1], I["ml_i_bias"].rearrange("a h -> h a"),
                                 allow_slow_non_contiguous=True).then_inc(ml_in, 16)
                    sp.dma_start(mlb[:, 1:2], I["ml_f_bias"].rearrange("a h -> h a"),
                                 allow_slow_non_contiguous=True).then_inc(ml_in, 16)
                    sp.dma_start(m0[:, :], I["state_mlstm_m"][0].rearrange("b h -> h b"),
                                 allow_slow_non_contiguous=True).then_inc(ml_in, 16)
                    sp.dma_start(n0[:, :], I["state_mlstm_n"][0].rearrange("b h d -> b (h d)")).then_inc(ml_in, 16)
                    for h in range(MLH):
                        sp.dma_start(Cn[0:HD, h, :, :], I["state_mlstm_C"][0, :, h].rearrange("b e d -> e b d"))\
                            .then_inc(ml_in, 16)
                        sp.dma_start(Cn[HD:HD + 1, h, :, :], I["state_mlstm_n"][0:1, :, h, :]).then_inc(ml_in, 16)
                    sp.wait_ge(rows_ready, 1)
                    store(sp, O["m_p"][0].rearrange("a h -> h a"), mend[:, 0:1], True)
                    store(sp, O["m_s"][0].rearrange("b h -> h b"), mend[:, 1:9], True)
                    sp.wait_ge(cp_out, 1)
                    store(sp, O["C_p"][0, 0].rearrange("h e d -> e h d"), Cp[0:HD, :, :])
                    store(sp, O["n_p"][0, 0:1], Cp[HD:HD + 1, :, :])
                    for h in range(MLH):
                        sp.wait_ge(cn_out, h + 1)
                        store(sp, O["C_s"][0, :, h].rearrange("b e d -> e b d"), Cn[0:HD, h, :, :])
                        store(sp, O["n_s"][0:1, :, h, :], Cn[HD:HD + 1, h, :, :])

                @block.tensor
                def _(pe):
                    pe.wait_ge(ml_in, 16 * 12)
                    for h in range(MLH):
                        if h >= 2:
                            pe.wait_ge(c0_out, h - 1)
                        for b in range(NB):
                            mm = pe.transpose(work[h % 2][0:HD, HD * b:HD * b + HD], Cn[0:HD, h, b, :],
                                              ident[0:HD, 0:HD])
                        mm.then_inc(c0_mm, 1)
                    for h in range(MLH):
                        mm = pe.transpose(work[2][0:HD, NB * h:NB * h + NB], n0[:, HD * h:HD * h + HD],
                                          ident[0:NB, 0:NB])
                    mm.then_inc(c0_mm, 1)
                    pe.wait_ge(rows_ready, 2)
                    for q in range(QT + 1):
                        at, n = (P * q, P) if q < QT else (TP, TS)
                        for j, row in enumerate((av, wrow)):
                            mm = pe.transpose(work[3][0:n, 8 * q + 4 * j:8 * q + 4 * j + 4], row[:, at:at + n],
                                              ident[0:MLH, 0:MLH])
                    mm.then_inc(cols_mm, 1)
                    pe.wait_ge(c0_out, 5)
                    for k in range(2):
                        pe.matmul(work[0][:, TS * k:TS * k + TS], const(f"pair{k}", MLH), wcrow[:, :],
                                  start=True, stop=True)
                    for h in range(MLH):
                        mm = pe.matmul(work[0][0:HD + 1, 64 + NB * h:64 + NB * h + NB],
                                       const(f"head{h}", MLH)[:, 0:HD + 1], decay[:, :], start=True, stop=True)
                    mm.then_inc(cols_mm, 1)
                    for h in range(MLH):
                        k, o = h // 2, HD * (h % 2)
                        s_bank = (work[1], gemm_big[0])[h % 2]
                        pe.matmul(s_bank[0:TS, TS * k:TS * k + TS], pT[o:o + HD, T_K + k, TP:NT],
                                  pT[o:o + HD, T_Q + k, TP:NT], start=True, stop=True)
                    for h in range(MLH):
                        mm = pe.matmul(work[2][0:TS, TS * h:TS * h + TS], const(f"head{h}", MLH)[:, 0:TS],
                                       mx[:, TP:NT], start=True, stop=True)
                    mm.then_inc(samp_mm, 1)
                    pe.wait_ge(cols_out, 2)

                    def scores(n):
                        h, kt = steps[n]
                        k, o = h // 2, HD * (h % 2)
                        if kt == 0:
                            if h:
                                pe.wait_ge(e_ready, QT * h)
                            pe.matmul(work[0][:, 0:TP], const(f"head{h}", MLH), mx[:, 0:TP],
                                      start=True, stop=True).then_inc(mb_ready, 1)
                        if n == 0:
                            pe.wait_ge(samp_w, 1)
                        if n >= 2:
                            pe.wait_ge(w_ready, n - 1)
                        pe.matmul(work[1 + n % 2][:, 0:TP - P * kt], pT[o:o + HD, T_K + k, P * kt:P * kt + P],
                                  pT[o:o + HD, T_Q + k, P * kt:TP], start=True, stop=True).then_inc(s_ready, 1)

                    scores(0)
                    for n, (h, kt) in enumerate(steps):
                        k, o = h // 2, HD * (h % 2)
                        if n + 1 < len(steps):
                            scores(n + 1)
                        if kt == 0 and o == 0 and k:
                            pe.wait_ge(y_done, k)
                        pe.wait_ge(w_ready, n + 1)
                        w = W[:, n % 2, 0:TP - P * kt]
                        ends = dict(start=(kt == 0), stop=(kt == QT - 1))
                        pe.matmul(gemm_big[0][o:o + HD, P * kt:TP], tok[:, kt, TV + k, o:o + HD], w, **ends)
                        pe.matmul(gemm_big[1][o:o + HD, P * kt:TP], const("ones")[:, 0:HD], w, **ends)\
                            .then_inc(pv_done, 1)
                        if kt == QT - 1:
                            num, den = gemm_small[0][o:o + HD, 0:TS], gemm_small[1][o:o + HD, 0:TS]
                            if n == QT - 1:
                                pe.wait_ge(qw_ready, 1)
                            pe.matmul(num, toks[:, TV + k, o:o + HD], Ws[:, h, :], start=True, stop=False)
                            for b in range(NB):
                                pe.matmul(num[:, ST * b:ST * b + ST], C0T[:, h, b, :],
                                          qw[:, h, ST * b:ST * b + ST], start=False, stop=(b == NB - 1))
                            pe.matmul(den, const("ones", TS)[:, 0:HD], Ws[:, h, :], start=True, stop=False)
                            pe.matmul(den, const("ones", HD)[:, 0:HD], nq[:, h, :], start=False, stop=True)
                            if o:
                                if k:
                                    pe.wait_ge(em_out, 1)
                                pe.matmul(work[3][:, :], const(f"pair{k}", MLH), emrow[:, 0:TP],
                                          start=True, stop=True).then_inc(fin_mm, 1)
                                pe.wait_ge(e_ready, n + 1)
                                pe.wait_ge(em_out, k) if k else None
                                pe.wait_ge(dg_ready, n + 1)
                                pe.matmul(work[0][:, 0:TS] if False else gemm_small[0][:, 64:64 + TS],
                                          const(f"pair{k}", MLH), emrow[:, TP:NT],
                                          start=True, stop=True).then_inc(fin_mm, 1)
                    pe.wait_ge(vw_ready, 1)
                    pe.wait_ge(em_out, 2)
                    for h in range(MLH):
                        k, o = h // 2, HD * (h % 2)
                        for kt in range(QT):
                            mm = pe.matmul(work[3][0:HD + 1, HD * h:HD * h + HD], vw[:, kt, h, :],
                                           tok[:, kt, TK + k, o:o + HD], start=(kt == 0), stop=(kt == QT - 1))
                    mm.then_inc(cp_mm, 1)
                    pe.wait_ge(w_ready, len(steps))
                    for h in range(MLH):
                        pe.wait_ge(km_ready, h + 1)
                        if h >= 2:
                            pe.wait_ge(cn_out, h - 1)
                        pe.matmul(work[1 + h % 2][0:HD + 1, :], vws[:, h, :],
                                  KM[:, h % 2, :, :].rearrange("s b d -> s (b d)"),
                                  start=True, stop=True).then_inc(cn_mm, 1)

                @block.scalar
                def _(act):
                    one = const("ones")[:, 0:1]
                    act.activation(sg[:, :, :], pT[:, T_O:T_O + 2, :], ACT.Sigmoid)
                    act.wait_ge(ml_chain, 2)
                    act.activation(lf[:, :], ax[:, :], ACT.Exp, scale=-1.0).then_inc(ml_act, 1)
                    act.wait_ge(ml_act, 1)
                    act.activation(lf[:, :], lf[:, :], ACT.Ln, bias=one[0:MLH]).then_inc(ml_act, 1)
                    act.wait_ge(ml_in, 16 * 12)
                    for h in range(MLH):
                        act.wait_ge(c0_mm, h + 1)
                        act.activation(C0T[:, h, :, :], work[h % 2][0:HD, :].rearrange("p (b e) -> p b e", b=NB),
                                       ACT.Copy).then_inc(c0_out, 1)
                    act.wait_ge(c0_mm, 5)
                    act.activation(n0T[:, :, :], work[2][0:HD, 0:NB * MLH].rearrange("p (h b) -> p h b", h=MLH),
                                   ACT.Copy).then_inc(c0_out, 1)
                    act.wait_ge(rows_ready, 1)
                    act.activation(wrow[:, :], wrow[:, :], ACT.Exp)
                    act.activation(emrow[:, :], emrow[:, :], ACT.Exp, scale=-1.0)
                    act.activation(wcrow[:, :], wcrow[:, :], ACT.Exp)
                    act.activation(decay[:, :], decay[:, :], ACT.Exp).then_inc(rows_ready, 1)
                    act.wait_ge(cols_mm, 1)
                    act.activation(cols[:, 0:QT, :, :],
                                   work[3][:, 0:32].rearrange("p (q j h) -> p q j h", q=QT, j=2), ACT.Copy)
                    act.activation(cols[0:TS, QT, :, :], work[3][0:TS, 32:40].rearrange("p (j h) -> p j h", j=2),
                                   ACT.Copy).then_inc(cols_out, 1)
                    act.wait_ge(cols_mm, 2)
                    act.activation(wcb[:, :, :], work[0][:, 0:64].rearrange("p (k t) -> p k t", k=2), ACT.Copy)
                    act.activation(db[:, :, :], work[0][0:HD + 1, 64:64 + NB * MLH]
                                   .rearrange("p (h b) -> p h b", h=MLH), ACT.Copy).then_inc(cols_out, 1)
                    act.wait_ge(samp_e, 1)
                    for h in range(MLH):
                        ins = act.activation(Es[:, h, :], dgs[:, h, :], ACT.Exp, scale=-1.0,
                                             bias=cols[0:TS, QT, 0, h:h + 1])
                    ins.then_inc(samp_e, 1)
                    for n, (h, kt) in enumerate(steps):
                        act.wait_ge(dg_ready, n + 1)
                        if n >= 2:
                            act.wait_ge(w_ready, n - 1)
                        a = cols[:, kt, 0, h:h + 1]
                        ins = act.activation(E[:, n % 2, 0:P], dg[:, n % 2, :], ACT.Exp, bias=a, scale=-1.0)
                        if kt < QT - 1:
                            ins = act.activation(E[:, n % 2, P:TP - P * kt], work[0][:, P * kt + P:TP], ACT.Exp,
                                                 bias=a, scale=-1.0)
                        ins.then_inc(e_ready, 1)
                        if kt == QT - 1 and h % 2:
                            k = h // 2
                            act.wait_ge(fin_mm, 2 * k + 2)
                            if k:
                                act.wait_ge(y_done, k)
                            act.activation(em[:, 0:TP], work[3][:, :], ACT.Copy)
                            act.activation(em[:, TP:NT], gemm_small[0][:, 64:64 + TS], ACT.Copy).then_inc(em_out, 1)

                @block.vector
                def _(dve):
                    c = Chain(dve, ml_chain)
                    def steps_of(x):
                        return x[:, TP:NT].rearrange("p (b t) -> p b t", b=NB)

                    dve.wait_ge(ml_in, 16 * 12)
                    c.step(dve.tensor_scalar(fx[:, :], pT[32:36, T_IF, :], mlb[:, 1:2], None, ALU.add))
                    c.step(dve.scalar_tensor_tensor(out=ax[:, :], in0=fx[:, :], scalar=-1.0, in1=fx[:, :],
                                                    op0=ALU.mult, op1=ALU.max))
                    c.step(dve.memset(ones4[:, :], 1.0))
                    dve.wait_ge(ml_act, 2)
                    c.step(dve.scalar_tensor_tensor(out=lf[:, :], in0=fx[:, :], scalar=0.0, in1=lf[:, :],
                                                    op0=ALU.min, op1=ALU.subtract))
                    c.step(dve.tensor_tensor_scan(bsum[:, 0:TP], ones4[:, 0:TP], lf[:, 0:TP], 0.0,
                                                  ALU.mult, ALU.add))
                    bs, ls, as_, ms = steps_of(bsum), steps_of(lf), steps_of(av), steps_of(mx)
                    c.step(dve.tensor_copy(bs[:, :, 0], ls[:, :, 0]))
                    for t in range(1, ST):
                        c.step(dve.tensor_tensor(bs[:, :, t], bs[:, :, t - 1], ls[:, :, t], ALU.add))
                    c.step(dve.scalar_tensor_tensor(out=av[:, :], in0=pT[0:MLH, T_IF, :], scalar=mlb[:, 0:1],
                                                    in1=bsum[:, :], op0=ALU.add, op1=ALU.subtract))
                    c.step(dve.tensor_tensor_scan(mx[:, 0:TP], av[:, 0:TP], av[:, 0:TP], 0.0, ALU.max, ALU.max))
                    for t in range(ST):
                        c.step(dve.tensor_tensor(ms[:, :, t], as_[:, :, t], m0[:, :] if t == 0 else ms[:, :, t - 1],
                                                 ALU.max))
                    dve.tensor_scalar(wrow[:, 0:TP], av[:, 0:TP], mx[:, TP - 1:TP], None, ALU.subtract)
                    for t in range(ST):
                        dve.tensor_tensor(steps_of(wrow)[:, :, t], as_[:, :, t], ms[:, :, ST - 1], ALU.subtract)
                        dve.tensor_tensor(wcrow[:, :].rearrange("p (b t) -> p b t", b=NB)[:, :, t], m0[:, :],
                                          ms[:, :, t], ALU.subtract)
                    dve.tensor_tensor(decay[:, :], m0[:, :], ms[:, :, ST - 1], ALU.subtract)
                    c.step(dve.tensor_tensor(emrow[:, :], bsum[:, :], mx[:, :], ALU.add))
                    dve.tensor_copy(mend[:, 0:1], emrow[:, TP - 1:TP])
                    dve.tensor_copy(mend[:, 1:9], steps_of(emrow)[:, :, ST - 1]).then_inc(rows_ready, 1)
                    dve.wait_ge(cols_out, 2)
                    for h in range(MLH):
                        k, o = h // 2, HD * (h % 2)
                        ins = dve.tensor_tensor(qw[:, h, :], pT[o:o + HD, T_Q + k, TP:NT], wcb[o:o + HD, k, :],
                                                ALU.mult)
                    c.step(ins)
                    dve.wait_ge(c0_out, 5)
                    for h in range(MLH):
                        ins = dve.tensor_tensor(nq[:, h, :].rearrange("p (b t) -> p b t", b=NB),
                                                qw[:, h, :].rearrange("p (b t) -> p b t", b=NB),
                                                n0T[:, h, :].unsqueeze(2).to_broadcast([HD, NB, ST]), ALU.mult)
                    ins.then_inc(qw_ready, 1)
                    dve.wait_ge(samp_mm, 1)
                    for h in range(MLH):
                        ins = dve.tensor_tensor(dgs[:, h, :], work[2][0:TS, TS * h:TS * h + TS],
                                                const("sblocked", TS), ALU.add)
                    ins.then_inc(samp_e, 1)
                    dve.wait_ge(samp_e, 2)
                    for h in range(MLH):
                        ins = dve.scalar_tensor_tensor(
                            out=Ws[:, h, :], in0=(work[1], gemm_big[0])[h % 2][0:TS, TS * (h // 2):TS * (h // 2) + TS],
                            scalar=HD ** -0.5, in1=Es[:, h, :], op0=ALU.mult, op1=ALU.mult)
                    ins.then_inc(samp_w, 1)

                    def finish(k):
                        dve.wait_ge(em_out, k + 1)
                        dve.wait_ge(pv_done, 2 * QT * (k + 1))
                        for cols_, big, small in ((slice(0, TP), gemm_big[1], None), (slice(TP, NT), None, gemm_small[1])):
                            den = big[:, :] if big is not None else small[:, 0:TS]
                            c.step(dve.scalar_tensor_tensor(out=dd[:, cols_], in0=den, scalar=-1.0, in1=em[:, cols_],
                                                            op0=ALU.mult, op1=ALU.max))
                            c.step(dve.tensor_tensor(dd[:, cols_], den, dd[:, cols_], ALU.max))
                        c.step(dve.reciprocal(dd[:, :], dd[:, :]))
                        c.step(dve.tensor_tensor(dd[:, :], dd[:, :], sg[:, k, :], ALU.mult))
                        dve.tensor_tensor(yT[:, k, 0:TP], gemm_big[0][:, :], dd[:, 0:TP], ALU.mult)
                        dve.tensor_tensor(yT[:, k, TP:NT], gemm_small[0][:, 0:TS], dd[:, TP:NT], ALU.mult)\
                            .then_inc(y_done, 1)

                    for n, (h, kt) in enumerate(steps):
                        dve.wait_ge(mb_ready, h + 1)
                        if n >= 2:
                            dve.wait_ge(e_ready, n - 1)
                        dve.tensor_tensor(dg[:, n % 2, :], work[0][:, P * kt:P * kt + P], const("blocked"), ALU.add)\
                            .then_inc(dg_ready, 1)
                        dve.wait_ge(e_ready, n + 1)
                        dve.wait_ge(s_ready, n + 1)
                        if n >= 2:
                            dve.wait_ge(pv_done, n - 1)
                        w = TP - P * kt
                        dve.scalar_tensor_tensor(out=W[:, n % 2, 0:w], in0=work[1 + n % 2][:, 0:w],
                                                 scalar=HD ** -0.5, in1=E[:, n % 2, 0:w],
                                                 op0=ALU.mult, op1=ALU.mult).then_inc(w_ready, 1)
                        if kt == QT - 1 and h % 2:
                            finish(h // 2)
                    for h in range(MLH):
                        k, o = h // 2, HD * (h % 2)
                        for kt in range(QT):
                            dve.tensor_scalar(vw[:, kt, h, 0:HD], tok[:, kt, TV + k, o:o + HD],
                                              cols[:, kt, 1, h:h + 1], None, ALU.mult)
                        dve.tensor_scalar(vws[:, h, 0:HD], toks[:, TV + k, o:o + HD], cols[0:TS, QT, 1, h:h + 1],
                                          None, ALU.mult)
                    dve.tensor_copy(vw[:, :, :, HD], cols[:, 0:QT, 1, :])
                    dve.tensor_copy(vws[:, :, HD], cols[0:TS, QT, 1, :]).then_inc(vw_ready, 1)
                    for h in range(MLH):
                        k, o = h // 2, HD * (h % 2)
                        if h >= 2:
                            dve.wait_ge(cn_mm, h - 1)
                        dve.tensor_tensor(KM[:, h % 2, :, :],
                                          toks[:, TK + k, o:o + HD].unsqueeze(1).to_broadcast([TS, NB, HD]),
                                          const("inb", TS).unsqueeze(2).to_broadcast([TS, NB, HD]), ALU.mult)\
                            .then_inc(km_ready, 1)
                        c.step(dve.tensor_tensor(Cn[:, h, :, :], Cn[:, h, :, :],
                                                 db[:, h, :].unsqueeze(2).to_broadcast([HD + 1, NB, HD]), ALU.mult))
                        dve.wait_ge(cn_mm, h + 1)
                        dve.scalar_tensor_tensor(out=Cn[:, h, :, :],
                                                 in0=work[1 + h % 2][0:HD + 1, :].rearrange("p (b d) -> p b d", b=NB),
                                                 scalar=HD ** -0.5, in1=Cn[:, h, :, :], op0=ALU.mult, op1=ALU.add)\
                            .then_inc(cn_out, 1)
                    dve.wait_ge(cp_mm, 1)
                    dve.tensor_scalar(Cp[:, :, :], work[3][0:HD + 1, 0:256].rearrange("p (h d) -> p h d", h=MLH),
                                      HD ** -0.5, None, ALU.mult).then_inc(cp_out, 1)
        sem.end_part()

        def turn_cmp(pe, raw, dst):
            for j in range(4):
                mm = pe.transpose(dst[:, P * j:P * j + P], raw[:, j, :, :].rearrange("p a d -> p (a d)"), ident)
            return mm

        def hidden(pe, w1, ZT, nblk, dst):
            for kv in range(2):
                z = ZT[:, 2 * kv:2 * kv + 2, :].rearrange("p g (n c) -> p g n c", c=16)
                for c in range(16):
                    mm = pe.matmul(dst[:, 2 * nblk * kv:2 * nblk * (kv + 1)], w1[:, kv, c, :],
                                   z[:, :, :, c], start=(c == 0), stop=(c == 15))
            return mm

        def load_phi(sp, w1, w2, sem_):
            sp.dma_start(w1[:, :, :, :], I["phi_w1"][0].rearrange("v (c p) h -> p v c h", p=P)).then_inc(sem_, 16)
            sp.dma_start(w2[:, 0, 0:HD], I["phi_w2"][0, 0]).then_inc(sem_, 16)
            sp.dma_start(w2[:, 1, HD:P], I["phi_w2"][0, 0]).then_inc(sem_, 16)
            sp.dma_start(w2[:, 2, 0:HD], I["phi_w2"][0, 1]).then_inc(sem_, 16)

        kcp = mixed.enter_context(nc.sbuf_tensor("kcp", [P, PCB], F32))
        vexp = mixed.enter_context(nc.sbuf_tensor("vexp", [P, REP, G, HD], F32))
        with ExitStack() as c5:
            def t5(name, shape):
                return c5.enter_context(nc.sbuf_tensor(name, shape, F32))

            w1 = t5("w1p", [P, 2, 16, P])
            w2 = t5("w2p", [P, 3, P])
            raw = t5("rawp", [P, 2, 4, 2, HD])
            ZT = t5("ZTp", [P, 4, 2 * P])
            pos = t5("pos", [32, P])
            posT = t5("posT", [P, 32])
            hid = t5("hid", [P, 2, G, PCB])
            hrep = t5("hrep", [P, G, REP, PCB])
            vrep = t5("vrep", [P, HD])
            gate_dma, qb_zero, scaled = sem("gate_dma"), sem("QB_zero"), sem("q_scaled")
            phi_here, w2_zero, raw_here = sem("phi_here"), sem("w2_zero"), sem("rawp_here")
            z_mm, z_out, pos_mm, hb_ready, h_mm, h_ready, hrep_ready, kv_mm, vrep_ready = (
                sem(f"pcmp_{n}") for n in ("z_mm", "z_out", "pos_mm", "hb", "h_mm", "h", "hrep", "kv_mm", "vrep"))

            with nc.Block() as block:
                @block.sync
                def _(sp):
                    sp.wait_ge(out_dma, stores[0])
                    for j in range(2):
                        for a in range(2):
                            sp.dma_start(raw[:, j, :, a, :],
                                         O["kv_p"][0, 0, 256 * j + a:256 * j + 256:2, 0:2].rearrange(
                                             "p c g d -> p (c g) d")).then_inc(raw_here, 16)
                    sp.dma_start(pos[:, :], I["cmp_pos"][0].rearrange("v (c a) d -> (v c) (a d)", a=2))\
                        .then_inc(raw_here, 16)
                    sp.wait_ge(w2_zero, 1)
                    load_phi(sp, w1, w2, phi_here)

                    sp.dma_start(gate_dram, gate_s[:, :]).then_inc(gate_dma, 16)
                    sp.wait_ge(gate_dma, 16)
                    for h in range(8):
                        for br in range(3):
                            sp.dma_start(gq[ST * h:ST * h + ST, :, br],
                                         gate_dram.rearrange("(b t) c -> c t b", b=NB)[8 * br + h],
                                         allow_slow_non_contiguous=True).then_inc(gate_dma, 16)
                    sp.wait_ge(gate_dma, 16 * 25)

                @block.gpsimd
                def _(pool):
                    pool.memset(QB[:, :, :], 0.0).then_inc(qb_zero, 1)
                    pool.memset(w2[:, :, :], 0.0).then_inc(w2_zero, 1)

                @block.tensor
                def _(pe):
                    pe.wait_ge(raw_here, 80)
                    for j in range(2):
                        turn_cmp(pe, raw[:, j, :, :, :], work[j]).then_inc(z_mm, 1)
                    pe.transpose(work[2][:, 0:32], pos[:, :], ident[0:32, 0:32]).then_inc(z_mm, 1)
                    pe.wait_ge(phi_here, 64)
                    pe.wait_ge(z_out, 3)
                    for kv in range(2):
                        for c in range(16):
                            mm = pe.matmul(work[3][:, kv:kv + 1], w1[:, kv, c, :], posT[:, 16 * kv + c:16 * kv + c + 1],
                                           start=(c == 0), stop=(c == 15))
                    mm.then_inc(pos_mm, 1)
                    hidden(pe, w1, ZT, PCB, work[0]).then_inc(h_mm, 1)
                    pe.wait_ge(h_ready, 1)
                    for g in range(G):
                        mm = pe.matmul(work[1][:, 0:PCB], w2[:, g, :], hid[:, 0, g, :], start=(g == 0), stop=(g == 1))
                    mm.then_inc(kv_mm, 1)
                    pe.wait_ge(hrep_ready, 1)
                    for g in range(G):
                        mm = pe.matmul(work[2][HD * g:HD * g + HD, 0:HD], hrep[:, g, :, :].rearrange("p r n -> p (r n)"),
                                       w2[:, 2, 0:HD], start=True, stop=True)
                    mm.then_inc(kv_mm, 1)

                @block.scalar
                def _(act):
                    act.wait_ge(h_mm, 1)
                    act.wait_ge(hb_ready, 1)
                    for kv in range(2):
                        ins = act.activation(hid[:, kv, :, :].rearrange("p g n -> p (g n)"),
                                             work[0][:, 2 * PCB * kv:2 * PCB * (kv + 1)], ACT.Gelu_apprx_tanh,
                                             bias=hb[:, kv:kv + 1])
                    ins.then_inc(h_ready, 1)

                @block.vector
                def _(dve):
                    for j in range(2):
                        dve.wait_ge(z_mm, j + 1)
                        dve.tensor_copy(ZT[:, :, P * j:P * j + P], work[j][:, :].rearrange("p (k c) -> p k c", k=4))\
                            .then_inc(z_out, 1)
                    dve.wait_ge(z_mm, 3)
                    dve.tensor_copy(posT[:, :], work[2][:, 0:32]).then_inc(z_out, 1)
                    dve.tensor_scalar(pT[:, T_NQ:T_NQ + 4, :], pT[:, T_NQ:T_NQ + 4, :], HD ** -0.5, None, ALU.mult)\
                        .then_inc(scaled, 1)
                    dve.wait_ge(qb_zero, 1)
                    dve.wait_ge(scaled, 1)
                    for g in range(G):
                        rows = slice(HD * g, HD * g + HD)
                        for r in range(REP):
                            at = 16 * g + ST * r
                            dve.tensor_copy(QB[rows, :, at:at + ST],
                                            pT[rows, T_NQ + r, TP:NT].rearrange("p (b t) -> p b t", b=NB))
                    dve.tensor_copy(ksn[:, :], pT[:, T_KS, TP:NT])
                    dve.tensor_copy(kwn[:, :], pT[:, T_KW, TP:NT])
                    dve.tensor_copy(vnew[:, 0, :], toks[:, TOKKV + 3, :])
                    dve.tensor_copy(vnew[:, 1, :], toks[:, TOKKV + 5, :])
                    dve.wait_ge(pos_mm, 1)
                    dve.tensor_tensor(hb[:, :], work[3][:, 0:2], vecT[:, V_PB:V_PB + 2], ALU.add).then_inc(hb_ready, 1)
                    dve.wait_ge(h_ready, 1)
                    dve.tensor_copy(hrep[:, :, :, :], hid[:, 1, :, :].unsqueeze(2).to_broadcast([P, G, REP, PCB]))\
                        .then_inc(hrep_ready, 1)
                    dve.wait_ge(kv_mm, 1)
                    dve.tensor_copy(kcp[:, :], work[1][:, 0:PCB])
                    dve.wait_ge(kv_mm, 2)
                    dve.tensor_copy(vrep[:, :], work[2][:, 0:HD]).then_inc(vrep_ready, 1)
                    dve.wait_ge(vrep_ready, 1)
                    dve.tensor_tensor(vexp[:, :, :, :],
                                      vrep[:, :].unsqueeze(1).to_broadcast([P, 8, HD]).rearrange(
                                          "p (r g) d -> p r g d", r=REP),
                                      const("vplace").rearrange("p (r g) -> p r g", r=REP).unsqueeze(3)
                                      .to_broadcast([P, REP, G, HD]), ALU.mult)

        with ExitStack() as c6:
            def t6(name, shape):
                return c6.enter_context(nc.sbuf_tensor(name, shape, F32))

            tab = t6("tab", [P, 8, TP])
            qz = ring[:, :, :, :].rearrange("p u k c -> p (u k c)").rearrange("p (g r t) -> p g r t", g=G, r=REP)
            qz_zero, qz_ready = sem("qz_zero"), sem("qz_ready")
            sc = t6("sc", [P, QT, G, REP, PCB])
            mxc, smc = t6("mxc", [P, QT * 8]), t6("smc", [P, QT * 8])
            pcT = t6("pcT", [P, TP])
            Pb = t6("Pb", [P, 4, TP])
            PT = t6("PT", [P, 2, TP])
            dgm = t6("dgm", [P, 2, P])
            stat = t6("stat", [P, 4, 4])
            tab_here, cs_mm, nchain, c_exp, pc_mm, pc_out = (
                sem(f"nsa_{n}") for n in ("tab", "cs_mm", "chain", "c_exp", "pc_mm", "pc_out"))
            s_mm, s_max, p_exp, d_ready, pt_mm, pt_out, pv_mm, y_out, pc_ready = (
                sem(f"nsa_{n}") for n in ("s_mm", "s_max", "p_exp", "d", "pt_mm", "pt_out", "pv", "y", "pc"))
            steps6 = [(r, br, qt, g) for r in range(REP) for br in range(2) for qt in range(QT) for g in range(G)]
            PER_R = 2 * QT * G

            with nc.Block() as block:
                @block.sync
                def _(sp):
                    sp.dma_start(tab[:, :, :], K["prompt"]).then_inc(tab_here, 16)

                @block.gpsimd
                def _(pool):
                    pool.memset(qz[HD:P, 0, :, :], 0.0)
                    pool.memset(qz[0:HD, 1, :, :], 0.0).then_inc(qz_zero, 1)

                @block.tensor
                def _(pe):
                    pe.wait_ge(qz_zero, 1)
                    pe.wait_ge(qz_ready, 1)
                    for qt in range(QT):
                        for r in range(REP):
                            for g in range(G):
                                at = PCB * (REP * qt + r)
                                mm = pe.matmul(work[g][:, at:at + PCB],
                                               qz[:, g, r, P * qt:P * qt + P], kcp[:, :], start=True, stop=True)
                                if (qt, r) == (QT - 1, REP - 1):
                                    mm.then_inc(cs_mm, 1)
                    pe.wait_ge(pc_ready, 1)
                    for qt in range(QT):
                        mm = pe.transpose(work[2][:, P * qt:P * qt + P],
                                          sc[:, qt, :, :, :].rearrange("p g r n -> p (g r n)"), ident)
                    mm.then_inc(pc_mm, 1)
                    pe.wait_ge(pc_out, 1)

                    def scores(n):
                        r, br, qt, g = steps6[n]
                        if n >= 4:
                            pe.wait_ge(s_max, n - 3)
                        pe.matmul(work[n % 4][:, 0:P * qt + P], qz[:, g, r, P * qt:P * qt + P],
                                  pT[:, (T_KS, T_KW)[br], 0:P * qt + P],
                                  start=True, stop=True).then_inc(s_mm, 1)

                    def values(n):
                        r, br, qt, g = steps6[n]
                        y = gemm_big[r % 2]
                        if n % PER_R == 0:
                            if r >= 2:
                                pe.wait_ge(y_out, r - 1)
                            pe.matmul(y[:, :], vexp[:, r, :, :].rearrange("p g d -> p (g d)"), pcT[:, :],
                                      start=True, stop=False, skip_group_check=True)
                        pe.wait_ge(pt_out, n + 1)
                        for kt in range(qt + 1):
                            mm = pe.matmul(y[HD * g:HD * g + HD, P * qt:P * qt + P],
                                           tok[:, kt, TOKKV + 3 + 2 * br, HD * g:HD * g + HD],
                                           PT[:, n % 2, P * kt:P * kt + P], start=False,
                                           stop=(n % PER_R == PER_R - 1 and kt == qt), skip_group_check=True)
                        mm.then_inc(pv_mm, 1)

                    scores(0)
                    scores(1)
                    for n, (r, br, qt, g) in enumerate(steps6):
                        if n + 2 < len(steps6):
                            scores(n + 2)
                        pe.wait_ge(d_ready, n + 1)
                        pe.wait_ge(p_exp, n + 1)
                        if n >= 2:
                            pe.wait_ge(pt_out, n - 1)
                        for kt in range(qt + 1):
                            mm = pe.matmul(gemm_small[n % 2][:, P * kt:P * kt + P], Pb[:, n % 4, P * kt:P * kt + P],
                                           dgm[:, n % 2, :], start=True, stop=True)
                        mm.then_inc(pt_mm, 1)
                        if n:
                            values(n - 1)
                    values(len(steps6) - 1)

                @block.scalar
                def _(act):
                    act.wait_ge(c_exp, 1)
                    act.activation(sc[:, :, :, :, :], sc[:, :, :, :, :], ACT.Exp).then_inc(c_exp, 1)
                    for n, (r, br, qt, g) in enumerate(steps6):
                        act.wait_ge(s_max, n + 1)
                        L = P * qt + P
                        act.activation(Pb[:, n % 4, 0:L], Pb[:, n % 4, 0:L], ACT.Exp, bias=stat[:, n % 4, 1:2],
                                       accum_out=stat[:, n % 4, 2:3]).then_inc(p_exp, 1)
                        act.wait_ge(pt_mm, n + 1)
                        if n >= 2:
                            act.wait_ge(pv_mm, n - 1)
                        act.activation(PT[:, n % 2, 0:L], gemm_small[n % 2][:, 0:L], ACT.Copy).then_inc(pt_out, 1)
                        if n % PER_R == 0 and n:
                            act.wait_ge(pv_mm, n)
                            act.activation(yT[:, 4 + r - 1, 0:TP], gemm_big[(r - 1) % 2][:, :], ACT.Copy)\
                                .then_inc(y_out, 1)
                    act.wait_ge(pv_mm, len(steps6))
                    act.activation(yT[:, 7, 0:TP], gemm_big[1][:, :], ACT.Copy).then_inc(y_out, 1)

                @block.vector
                def _(dve):
                    c = Chain(dve, nchain)
                    for g in range(G):
                        rows = slice(HD * g, HD * g + HD)
                        ins = dve.tensor_copy(qz[rows, g, :, :], pT[rows, T_NQ:T_NQ + 4, 0:TP])
                    ins.then_inc(qz_ready, 1)
                    dve.wait_ge(cs_mm, 2)
                    tabc = const("pcmp").rearrange("p (q g r n) -> p q g r n", q=QT, g=G, r=REP)
                    for g in range(G):
                        ins = dve.tensor_tensor(sc[:, :, g, :, :],
                                                work[g][:, 0:256].rearrange("p (q r n) -> p q r n", q=QT, r=REP),
                                                tabc[:, :, g, :, :], ALU.add)
                    c.step(ins)
                    flat = sc[:, :, :, :, :].rearrange("p q g r n -> p (q g r) n")
                    c.step(dve.tensor_reduce(mxc[:, :], flat, AX, ALU.max))
                    dve.tensor_tensor(flat, flat, mxc[:, :].unsqueeze(2).to_broadcast([P, QT * 8, PCB]),
                                      ALU.subtract).then_inc(c_exp, 1)
                    dve.wait_ge(c_exp, 2)
                    c.step(dve.tensor_reduce(smc[:, :], flat, AX, ALU.add))
                    c.step(dve.reciprocal(smc[:, :], smc[:, :]))
                    c.step(dve.tensor_tensor(smc[:, :].rearrange("p (q h) -> p q h", q=QT),
                                             smc[:, :].rearrange("p (q h) -> p q h", q=QT), gate_p[:, :, 0:8], ALU.mult))
                    c.step(dve.tensor_tensor(flat, flat, smc[:, :].unsqueeze(2).to_broadcast([P, QT * 8, PCB]),
                                             ALU.mult))
                    valid = const("pvalid").rearrange("p (q n) -> p q n", q=QT)
                    for qt in range(QT):
                        ins = dve.tensor_tensor(sc[:, qt, :, :, :].rearrange("p g r n -> p (g r) n"),
                                                sc[:, qt, :, :, :].rearrange("p g r n -> p (g r) n"),
                                                valid[:, qt, :].unsqueeze(1).to_broadcast([P, 8, PCB]), ALU.mult)
                    ins.then_inc(pc_ready, 1)
                    dve.wait_ge(pc_mm, 1)
                    dve.tensor_copy(pcT[:, :], work[2][:, :]).then_inc(pc_out, 1)
                    dve.wait_ge(tab_here, 16)

                    def top(n):
                        r, br, qt, g = steps6[n]
                        L = P * qt + P
                        dve.wait_ge(s_mm, n + 1)
                        if n >= 4:
                            dve.wait_ge(pt_mm, n - 3)
                        c.step(dve.tensor_tensor_reduce(Pb[:, n % 4, 0:L], work[n % 4][:, 0:L],
                                                        tab[:, REP * g + r, TP - L:TP], 1.0, -3e38, ALU.add, ALU.max,
                                                        stat[:, n % 4, 0:1]))
                        dve.tensor_scalar(stat[:, n % 4, 1:2], stat[:, n % 4, 0:1], -1.0, None, ALU.mult)\
                            .then_inc(s_max, 1)

                    top(0)
                    for n, (r, br, qt, g) in enumerate(steps6):
                        if n + 1 < len(steps6):
                            top(n + 1)
                        dve.wait_ge(p_exp, n + 1)
                        c.step(dve.reciprocal(stat[:, n % 4, 3:4], stat[:, n % 4, 2:3]))
                        if n >= 2:
                            dve.wait_ge(pt_mm, n - 1)
                        h = 8 * (br + 1) + REP * g + r
                        dve.tensor_scalar(dgm[:, n % 2, :], ident, stat[:, n % 4, 3:4], gate_p[:, qt, h:h + 1],
                                          ALU.mult, ALU.mult).then_inc(d_ready, 1)

        mixed.close()

        with ExitStack() as c7:
            def t7(name, shape, dt=F32):
                return c7.enter_context(nc.sbuf_tensor(name, shape, dt))

            RAW, R = 8, 32
            w1 = t7("w1s", [P, 2, 16, P])
            w2 = t7("w2s", [P, 3, P])
            both = t7("both", [2 * R, PAST])
            ss, past = both[0:R, :], both[R:2 * R, :]
            sw = t7("sw", [R, WIN])
            sn = t7("sn", [R, 2, TS])
            rawc = t7("rawc", [P, RAW, 4, 2, HD])
            kv = t7("kv", [P, CT, 2, 2, P])
            rw = t7("rw", [P, 4, 2, P])
            ZT = t7("ZTs", [P, 4, CT * P])
            hid = t7("hids", [P, 2, G, NCB])
            kc = t7("kcs", [P, NCB])
            vc = t7("vcs", [NCB, P])
            Qb = t7("Qb", [P, R])
            KTb = t7("KTb", [P, 2, 512])
            PTs = t7("PTs", [P, 2, 512])
            pn = t7("pn", [R, NCB])
            sel = t7("sel", [R, 4, 65])
            top8 = t7("top8", [R, 2, 8])
            bnb = stdt[0:R, NB * NPB:NB * NPB + TS + 1]
            st = t7("st", [R, 16])
            Os = t7("Os", [R, P])
            pages = stdt[0:1, 0:NB * NPB].bitcast(I32)

            pg_here, c7_const, s_w2z, s_w2 = sem("pages_here"), sem("past_here"), sem("w2s_zero"), sem("phis_here")
            rawc_here = [sem(f"rawc_here{j}") for j in range(RAW)]
            kv_here = [sem(f"kv_here{j}") for j in range(CT // 2)]
            rw_here = sem("rw_here")
            z_mm, z_out, h_mm, h_ready, kc_mm, kc_out = (
                sem(f"s_{n}") for n in ("z_mm", "z_out", "h_mm", "h", "kc_mm", "kc_out"))
            qb_ready, cs_mm, pn_exp, pn_sub, pn_ready, imp_mm = (
                sem(f"s_{n}") for n in ("qb", "cs_mm", "pn_exp", "pn_sub", "pn", "imp_mm"))
            kt_mm, kt_out, sl_mm, sl_out, new_mm, new_out = (
                sem(f"s_{n}") for n in ("kt_mm", "kt_out", "sl_mm", "sl_out", "new_mm", "new_out"))
            m_ready, e_ready, pt_mm, pt_out, o_mm, o_ready, ot_mm, y_put, chain7 = (
                sem(f"s_{n}") for n in ("m", "e", "pt_mm", "pt_out", "o_mm", "o", "ot_mm", "y", "chain"))
            NKT = CT // 2 + 1
            NPT_ = 10
            CH = 31

            def settled(dve):
                dve.memset(bnb[:, TS:TS + 1], 0.0)

            def settled_pe(pe):
                pe.transpose(work[3][:, 384:512], ident, ident)

            with nc.Block() as block:
                @block.sync
                def _(sp):
                    sp.dma_start(pages[:, :], I["page_table"].rearrange("b n -> (b n)").rearrange("(a n) -> a n", a=1))\
                        .then_inc(pg_here, 16)
                    sp.dma_start(past[:, :], K["past"]).then_inc(c7_const, 16)
                    sp.wait_ge(s_w2z, 1)
                    load_phi(sp, w1, w2, s_w2)
                    sp.wait_ge(pg_here, 16)
                    cache = I["cache_nsa_kv"][0].rearrange("n (p a) c g d -> n p a c (g d)", a=2)
                    cachec = I["cache_nsa_kv"][0].rearrange("n (p a) c g d -> n p a (c g) d", a=2)
                    with sp.Fori(0, NB) as b:
                        for j in range(CT):
                            if j >= RAW:
                                sp.wait_ge(z_mm, b * CT + (j - RAW + 1))
                            elif j == 0:
                                sp.wait_ge(z_mm, b * CT)
                            for half in range(2):
                                page = sp.value_load(pages[0:1, bass.ds(b * NPB + (2 * j + half), 1)],
                                                     min_val=0, max_val=319)
                                for a in range(2):
                                    sp.dma_start(rawc[64 * half:64 * half + 64, j % RAW, :, a, :],
                                                 cachec[bass.ds(page, 1), :, a, 0:4, :].rearrange(
                                                     "n p c d -> p (n c) d")).then_inc(rawc_here[j % RAW], 16)
                        sp.wait_ge(o_mm, b)
                        sp.dma_start(rw[:, :, :, :], I["state_nsa_win"][0, bass.ds(b, 1)].rearrange(
                            "b (c p) v g d -> p (b c) v (g d)", p=P)).then_inc(rw_here, 16)
                        for j in range(CT):
                            for half in range(2):
                                page = sp.value_load(pages[0:1, bass.ds(b * NPB + (2 * j + half), 1)],
                                                     min_val=0, max_val=319)
                                sp.dma_start(kv[64 * half:64 * half + 64, j, :, :, :].rearrange("p a c n -> p a (c n)"),
                                             cache[bass.ds(page, 1), :, :, 2:4, :].rearrange("n p a c m -> p (n a) (c m)"))\
                                    .then_inc(kv_here[j // 2], 16)

                @block.gpsimd
                def _(pool):
                    pool.memset(w2[:, :, :], 0.0).then_inc(s_w2z, 1)

                @block.tensor
                def _(pe):
                    pe.wait_ge(s_w2, 64)
                    with pe.Fori(0, NB) as b:
                        for j in range(CT):
                            pe.wait_ge(rawc_here[j % RAW], b * 128 + 64 * (j // RAW + 1))
                            if j >= 2:
                                pe.wait_ge(z_out, b * CT + (j - 1))
                            else:
                                pe.wait_ge(pt_out, b * NPT_)
                            turn_cmp(pe, rawc[:, j % RAW, :, :, :], work[j % 2]).then_inc(z_mm, 1)
                        pe.wait_ge(z_out, b * CT + CT)
                        hidden(pe, w1, ZT, NCB, work[2]).then_inc(h_mm, 1)
                        pe.wait_ge(qb_ready, b + 1)

                        def keys(n):
                            if n < CT // 2:
                                pe.wait_ge(kv_here[n], b * 64 + 64)
                            else:
                                pe.wait_ge(rw_here, b * 16 + 16)
                            if n >= 2:
                                pe.wait_ge(kt_out, b * NKT + (n - 1))
                            for i in range(4):
                                src = kv[:, 2 * n + i // 2, i % 2, 0, :] if n < CT // 2 else rw[:, i, 0, :]
                                mm = pe.transpose(gemm_small[n % 2][:, P * i:P * i + P], src, ident)
                            mm.then_inc(kt_mm, 1)

                        def scores(n):
                            pe.wait_ge(kt_out, b * NKT + (n + 1))
                            if n >= 2:
                                pe.wait_ge(sl_out, b * NKT + (n - 1))
                            pe.matmul(gemm_big[n % 2][0:R, :], Qb[:, :], KTb[:, n % 2, :],
                                      start=True, stop=True).then_inc(sl_mm, 1)

                        keys(0)
                        keys(1)
                        pe.wait_ge(h_ready, b + 1)
                        for g in range(G):
                            pe.matmul(work[3][:, 0:NCB], w2[:, g, :], hid[:, 0, g, :], start=(g == 0), stop=(g == 1))
                        for g in range(G):
                            mm = pe.matmul(work[3][:, P + HD * g:P + HD * g + HD], hid[:, 1, g, :], w2[:, 2, 0:HD],
                                           start=True, stop=True)
                        mm.then_inc(kc_mm, 1)
                        scores(0)
                        pe.wait_ge(kc_out, b + 1)
                        pe.matmul(work[2][0:R, 0:NCB], Qb[:, :], kc[:, :], start=True, stop=True).then_inc(cs_mm, 1)
                        for n in range(1, NKT):
                            if n + 1 < NKT:
                                keys(n + 1)
                            if n == 4:
                                pe.wait_ge(pn_ready, b + 1)
                            scores(n)
                            if n == 4:
                                pe.matmul(work[2][0:R, P:2 * P], const("grp", R), pn[:, :],
                                          start=True, stop=True).then_inc(imp_mm, 1)
                        pe.wait_ge(sl_out, b * NKT + (NKT - 1))
                        for i, new in enumerate((ksn, kwn)):
                            mm = pe.matmul(gemm_big[1][0:R, P * i:P * i + TS], Qb[:, :], new[:, :],
                                           start=True, stop=True)
                        mm.then_inc(new_mm, 1)

                        groups7 = [[(pn[:, :], vc[:, :], 0, P)] +
                                   [(sn[:, i, :], vnew[:, i, :], 1 + i, TS) for i in range(2)]]
                        groups7 += [[(sw[:, P * i:P * i + P], rw[:, i, 1, :], 2, P) for i in range(4)]]
                        flat = [(ss[:, 256 * j + a:256 * j + 256:2], kv[:, j, a, 1, :], 1, P)
                                for j in range(CT) for a in range(2)]
                        groups7 += [flat[4 * i:4 * i + 4] for i in range(8)]
                        o_bank = [work[3][0:R, 0:P], gemm_small[0][0:R, 0:P], gemm_small[1][0:R, 0:P]]
                        opened = set()

                        def turn(n):
                            for i, (src, _, _, m) in enumerate(groups7[n]):
                                mm = pe.transpose(work[n % 2][0:m, P * i:P * i + R], src, ident[0:R, 0:R])
                            mm.then_inc(pt_mm, 1)

                        def values(n):
                            pe.wait_ge(pt_out, b * NPT_ + (n + 1))
                            for i, (_, val, br, m) in enumerate(groups7[n]):
                                last = (n, i) in ((0, 0), (1, 3), (9, 3))
                                mm = pe.matmul(o_bank[br], PTs[0:m, n % 2, P * i:P * i + R], val,
                                               start=(br not in opened), stop=last)
                                opened.add(br)
                            mm.then_inc(o_mm, 1) if n == NPT_ - 1 else None

                        pe.wait_ge(e_ready, b * 2 + 1)
                        settled_pe(pe)
                        turn(0)
                        for n in range(1, NPT_):
                            turn(n)
                            if n == 1:
                                pe.wait_ge(e_ready, b * 2 + 2)
                            values(n - 1)
                        values(NPT_ - 1)
                        pe.wait_ge(o_ready, b + 1)
                        settled_pe(pe)
                        pe.transpose(work[3][:, 256:256 + R], Os[:, :], ident[0:R, 0:R]).then_inc(ot_mm, 1)

                @block.scalar
                def _(act):
                    with act.Fori(0, NB) as b:
                        for j in range(0, CT, 2):
                            act.wait_ge(z_mm, b * CT + (j + 1))
                            act.wait_ge(h_mm, b)
                            if j:
                                act.wait_ge(z_out, b * CT + j)
                            act.activation(ZT[:, :, P * j:P * j + P], work[0][:, :].rearrange("p (k c) -> p k c", k=4),
                                           ACT.Copy).then_inc(z_out, 1)
                        act.wait_ge(h_mm, b + 1)
                        for kv_ in range(2):
                            ins = act.activation(hid[:, kv_, :, :].rearrange("p g n -> p (g n)"),
                                                 work[2][:, 256 * kv_:256 * kv_ + 256], ACT.Gelu_apprx_tanh,
                                                 bias=hb[:, kv_:kv_ + 1])
                        ins.then_inc(h_ready, 1)
                        act.wait_ge(kc_mm, b + 1)
                        act.activation(kc[:, :], work[3][:, 0:NCB], ACT.Copy)
                        act.activation(vc[:, :], work[3][:, P:2 * P], ACT.Copy).then_inc(kc_out, 1)
                        def keys_out(n):
                            act.wait_ge(kt_mm, b * NKT + (n + 1))
                            if n >= 2:
                                act.wait_ge(sl_mm, b * NKT + (n - 1))
                            if n < CT // 2:
                                dst = KTb[:, n % 2, :].rearrange("q (j p a) -> q j a p", j=2, a=2)
                                src = gemm_small[n % 2][:, :].rearrange("q (j a p) -> q j a p", j=2, a=2)
                            else:
                                dst, src = KTb[:, n % 2, :], gemm_small[n % 2][:, :]
                            act.activation(dst, src, ACT.Copy).then_inc(kt_out, 1)

                        keys_out(0)
                        keys_out(1)
                        act.wait_ge(pn_sub, b + 1)
                        act.activation(pn[:, :], pn[:, :], ACT.Exp, bias=st[:, 1:2], accum_out=st[:, 2:3])\
                            .then_inc(pn_exp, 1)
                        for n in range(2, NKT):
                            keys_out(n)
                        act.wait_ge(m_ready, b * 2 + 1)
                        act.activation(sw[:, :], sw[:, :], ACT.Exp, bias=st[:, 7:8], accum_out=st[:, 8:9])
                        act.activation(sn[:, 1, :], sn[:, 1, :], ACT.Exp, bias=st[:, 7:8], accum_out=st[:, 9:10])
                        act.wait_ge(m_ready, b * 2 + 2)
                        act.activation(sn[:, 0, :], sn[:, 0, :], ACT.Exp, bias=st[:, 4:5], accum_out=st[:, 6:7])\
                            .then_inc(e_ready, 1)
                        act.activation(ss[:, :], ss[:, :], ACT.Exp, bias=st[:, 4:5], accum_out=st[:, 5:6])\
                            .then_inc(e_ready, 1)

                @block.vector
                def _(dve):
                    with dve.Fori(0, NB) as b:
                        c = Chain(dve, chain7, b * CH)
                        for j in range(1, CT, 2):
                            dve.wait_ge(z_mm, b * CT + (j + 1))
                            dve.wait_ge(h_mm, b)
                            dve.wait_ge(z_out, b * CT + j)
                            dve.tensor_copy(ZT[:, :, P * j:P * j + P], work[1][:, :].rearrange("p (k c) -> p k c", k=4))\
                                .then_inc(z_out, 1)
                        dve.tensor_copy(Qb[:, :], QB[:, bass.ds(b, 1), :].rearrange("p a q -> p (a q)"))\
                            .then_inc(qb_ready, 1)
                        dve.wait_ge(cs_mm, b + 1)
                        settled(dve)
                        c.step(dve.tensor_tensor_reduce(pn[:, :], work[2][0:R, 0:NCB], const("bcmp", R), 1.0, -3e38,
                                                        ALU.add, ALU.max, st[:, 0:1]))
                        dve.tensor_scalar(st[:, 1:2], st[:, 0:1], -1.0, None, ALU.mult).then_inc(pn_sub, 1)

                        def scores_out(n):
                            dve.wait_ge(sl_mm, b * NKT + (n + 1))
                            if n < CT // 2:
                                dst, table = ss[:, 512 * n:512 * n + 512], past[:, 512 * n:512 * n + 512]
                            else:
                                dst, table = sw[:, :], const("bwin", R)
                            dve.tensor_tensor(dst, gemm_big[n % 2][0:R, :], table, ALU.add).then_inc(sl_out, 1)

                        dve.wait_ge(c7_const, 16)
                        scores_out(0)
                        dve.wait_ge(pn_exp, b + 1)
                        c.step(dve.reciprocal(st[:, 3:4], st[:, 2:3]))
                        dve.tensor_scalar(pn[:, :], pn[:, :], st[:, 3:4], None, ALU.mult).then_inc(pn_ready, 1)
                        for n in range(1, 5):
                            scores_out(n)
                        dve.wait_ge(imp_mm, b + 1)
                        two = work[2][0:R, P:2 * P].rearrange("p (n a) -> p n a", a=2)
                        c.step(dve.tensor_copy(sel[:, 3, 0:64], two[:, :, 1]))
                        c.step(dve.tensor_tensor(sel[:, 0, 0:64], two[:, :, 0], sel[:, 3, 0:64], ALU.add))
                        c.step(dve.memset(sel[:, 0, 64:65], 0.0))
                        c.step(dve.tensor_tensor(sel[:, 0, :], sel[:, 0, :], const("bonus", R), ALU.add))
                        for i in range(2):
                            settled(dve)
                            c.step(dve.max(top8[:, i, :], sel[:, i, :]))
                            settled(dve)
                            c.step(dve.match_replace(sel[:, i + 1, :], top8[:, i, :], sel[:, i, :], -3e38))
                        c.step(dve.tensor_scalar(sel[:, 3, :], sel[:, 2, :], -1e38, NEG, ALU.is_gt, ALU.mult))
                        for n in range(5, NKT):
                            scores_out(n)
                        c.step(dve.tensor_copy(bnb[:, 0:TS], cst[0:R, bass.ds(b * TS + CONST["bnew"][0], TS)]))
                        dve.wait_ge(new_mm, b + 1)
                        settled(dve)
                        for i in range(2):
                            ins = dve.tensor_tensor_reduce(
                                sn[:, i, :], gemm_big[1][0:R, P * i:P * i + TS],
                                bnb[:, 0:TS], 1.0, -3e38, ALU.add, ALU.max,
                                st[:, 10 + i:11 + i])
                        c.step(ins)
                        c.step(dve.tensor_reduce(st[:, 12:13], sw[:, :], AX, ALU.max))
                        c.step(dve.tensor_tensor(st[:, 12:13], st[:, 12:13], st[:, 11:12], ALU.max))
                        dve.tensor_scalar(st[:, 7:8], st[:, 12:13], -1.0, None, ALU.mult).then_inc(m_ready, 1)
                        settled(dve)
                        c.step(dve.tensor_tensor_reduce(
                            ss[:, :].rearrange("p (n k) -> p n k", k=64), ss[:, :].rearrange("p (n k) -> p n k", k=64),
                            sel[:, 3, 0:64].unsqueeze(2).to_broadcast([R, 64, 64]), 1.0, -3e38, ALU.add, ALU.max,
                            st[:, 13:14]))
                        c.step(dve.tensor_tensor(st[:, 13:14], st[:, 13:14], st[:, 10:11], ALU.max))
                        dve.tensor_scalar(st[:, 4:5], st[:, 13:14], -1.0, None, ALU.mult).then_inc(m_ready, 1)
                        for n in range(NPT_):
                            dve.wait_ge(pt_mm, b * NPT_ + (n + 1))
                            k, m = (3, TS) if n == 0 else (4, P)
                            src = work[n % 2][:, :].rearrange("p (k c) -> p k c", k=4)
                            dst = PTs[:, n % 2, :].rearrange("p (k c) -> p k c", k=4)
                            if n == 0:
                                dve.tensor_copy(dst[:, 0, 0:R], src[:, 0, 0:R])
                                dve.tensor_copy(dst[0:TS, 1:3, 0:R], src[0:TS, 1:3, 0:R]).then_inc(pt_out, 1)
                            else:
                                dve.tensor_copy(dst[:, :, 0:R], src[:, :, 0:R]).then_inc(pt_out, 1)
                        c.step(dve.tensor_tensor(st[:, 5:6], st[:, 5:6], st[:, 6:7], ALU.add))
                        c.step(dve.tensor_tensor(st[:, 8:9], st[:, 8:9], st[:, 9:10], ALU.add))
                        dve.reciprocal(st[:, 5:6], st[:, 5:6])
                        c.step(dve.reciprocal(st[:, 8:9], st[:, 8:9]))
                        gates = gq[:, bass.ds(b, 1), :].rearrange("p a c -> p (a c)")
                        c.step(dve.tensor_copy(st[:, 13:16], gates))
                        dve.tensor_tensor(st[:, 5:6], st[:, 5:6], st[:, 14:15], ALU.mult)
                        c.step(dve.tensor_tensor(st[:, 8:9], st[:, 8:9], st[:, 15:16], ALU.mult))
                        dve.wait_ge(o_mm, b + 1)
                        c.step(dve.tensor_scalar(Os[:, :], work[3][0:R, 0:P], st[:, 13:14], None, ALU.mult))
                        c.step(dve.scalar_tensor_tensor(out=Os[:, :], in0=gemm_small[0][0:R, 0:P], scalar=st[:, 5:6],
                                                        in1=Os[:, :], op0=ALU.mult, op1=ALU.add))
                        dve.scalar_tensor_tensor(out=Os[:, :], in0=gemm_small[1][0:R, 0:P], scalar=st[:, 8:9],
                                                 in1=Os[:, :], op0=ALU.mult, op1=ALU.add).then_inc(o_ready, 1)
                        dve.wait_ge(ot_mm, b + 1)
                        for g in range(G):
                            rows = slice(HD * g, HD * g + HD)
                            dve.tensor_copy(
                                yT[rows, 4:8, bass.ds(b * ST + TP, ST)],
                                work[3][rows, 256 + 16 * g:272 + 16 * g].rearrange("p (r t) -> p r t", r=REP))
                        assert c.n <= CH
                        while c.n < CH:
                            c.step(dve.tensor_copy(st[:, 0:1], st[:, 1:2]))
        sem.end_part()

        def tile_of(x, it, u):
            return x[:, bass.ds(it * RING + u, 1), :].rearrange("p a n -> p (a n)")

        with ExitStack() as c8:
            nT = c8.enter_context(nc.sbuf_tensor("nT", [P, KT, NT], F32))
            cross = c8.enter_context(ExitStack())
            qx = cross.enter_context(nc.sbuf_tensor("qx", [P, XH, NT], F32))
            ox = cross.enter_context(nc.sbuf_tensor("ox", [P, XH, NT], F32))
            hstd = cross.enter_context(nc.sbuf_tensor("hstd", [P, 2, NT], F32))
            hsq, hss, hsd, hinv, y_norm = (sem(f"head_{n}") for n in ("sq", "sum", "std", "inv", "norm"))

            with nc.Block() as block:
                @block.sync
                def _(sp):
                    w = I["w_out"][0]
                    for n in range(8):
                        u, cols_ = n % RING, slice(P * n, P * n + P)
                        slot_free(sp, "out", n // RING, u)
                        sp.dma_start(ring[:, u, 0:4, :], w[0:512, cols_].rearrange("(k p) n -> p k n", p=P))\
                            .then_inc(w_loaded[u], 16)
                        for g in range(G):
                            sp.dma_start(ring[HD * g:HD * g + HD, u, 4:8, :],
                                         w[512 + 256 * g:768 + 256 * g, cols_].rearrange("(r d) n -> d r n", r=REP))\
                                .then_inc(w_loaded[u], 16)
                    w = I["xa_wq"][0].rearrange("(k p) n -> p k n", p=P)
                    for n in range(4):
                        slot_free(sp, "xq", 0, n)
                        sp.dma_start(ring[:, n, :, :], w[:, :, P * n:P * n + P]).then_inc(w_loaded[n], 16)

                @block.tensor
                def _(pe):
                    for k in range(KT):
                        pe.wait_ge(hsq, k + 1)
                        if k >= 2:
                            pe.wait_ge(hsd, k - 1)
                        for i in range(2):
                            mm = pe.matmul(work[2 * (k % 2) + i][:, 0:HALF], const("headones"),
                                           nT[:, k, HALF * i:HALF * i + HALF], start=True, stop=True)
                        mm.then_inc(hss, 1)
                    pe.wait_ge(y_norm, KT)
                    pe_gemm(pe, "out", 8, KT, lambda k: nT[:, k, :])
                    norm_pe(pe, 2, yT)
                    pe.wait_ge(norm_ready, 3 * KT)
                    pe_gemm(pe, "xq", 4, KT, lambda k: yT[:, k, :])

                @block.scalar
                def _(act):
                    for k in range(KT):
                        act.activation(nT[:, k, :], yT[:, k, :], ACT.Square).then_inc(hsq, 1)
                    for k in range(KT):
                        act.wait_ge(hss, k + 1)
                        if k >= 2:
                            act.wait_ge(y_norm, k - 1)
                        for i in range(2):
                            ins = act.activation(hstd[:, k % 2, HALF * i:HALF * i + HALF],
                                                 work[2 * (k % 2) + i][:, 0:HALF], ACT.Sqrt,
                                                 bias=const("eps"), scale=1.0 / HD)
                        ins.then_inc(hsd, 1)
                    act.wait_ge(out_taken[1], stage["xq"][0] // 2)
                    act.wait_ge(out_taken[0], stage["xq"][0] // 2)
                    norm_act(act, 2, xT, yT)
                    for n in (0, 2):
                        output_here(act, "xq", 0, n)
                        act_copy(act, qx[:, n, :], 0).then_inc(out_taken[0], 1)

                @block.vector
                def _(dve):
                    for k in range(KT):
                        dve.wait_ge(hsd, k + 1)
                        dve.reciprocal(hstd[:, k % 2, :], hstd[:, k % 2, :]).then_inc(hinv, 1)
                        dve.wait_ge(hinv, k + 1)
                        dve.scalar_tensor_tensor(out=nT[:, k, :], in0=yT[:, k, :], scalar=vecT[:, V_Y + k:V_Y + k + 1],
                                                 in1=hstd[:, k % 2, :], op0=ALU.mult, op1=ALU.mult).then_inc(y_norm, 1)
                    with dve.Fori(0, 2) as it:
                        for u in range(RING):
                            output_here(dve, "out", it, u)
                            dve_add(dve, tile_of(xT, it, u), u % 2).then_inc(out_taken[u % 2], 1)
                    norm_dve(dve, 2, xT, V_XA, yT)
                    for n in (1, 3):
                        output_here(dve, "xq", 0, n)
                        dve_copy(dve, qx[:, n, :], 1).then_inc(out_taken[1], 1)

            with ExitStack() as c9:
                def t9(name, shape):
                    return c9.enter_context(nc.sbuf_tensor(name, shape, F32))

                XS = XD ** -0.5
                KTx = t9("KTx", [P, XH, NM])
                Px = t9("Px", [P, 2, NM])
                PTx = t9("PTx", [P, 2, NM])
                dgx = t9("dgx", [P, 2, P])
                sx = t9("sx", [P, 4, 4])
                SKIP = 16 * NB * 4 + 16
                qm = t9("qm", [P, NB * SKIP])
                kx = t9("kx", [P, 2, 2, 512])
                vx = t9("vx", [P, NB, 2, 512])
                KTs = t9("KTs", [P, 2, XH, NM])
                Pm, PTm = t9("Pm", [P, NM]), t9("PTm", [P, NM])
                kx_here = [sem(f"kx_here{j}") for j in range(2)]
                vx_here, qm_zero, qm_ready = sem("vx_here"), sem("qm_zero"), sem("qm_ready")
                xk_mm, xk_out, xs_mm, xs_max, xp_exp, xd, xt_mm, xt_out, xv_mm, xo_out, chain9, x_shift = (
                    sem(f"x_{n}") for n in ("k_mm", "k_out", "s_mm", "max", "exp", "d", "t_mm", "t_out", "v_mm",
                                            "o_out", "chain", "shift"))
                sk_mm, sk_out, sq_mm, sm_ready, sp_ready, sp_n, st_mm, st_out, sv_mm = (
                    sem(f"xs_{n}") for n in ("k_mm", "k_out", "s_mm", "max", "exp", "norm", "t_mm", "t_out", "v_mm"))
                steps9 = [(h, qt) for h in range(XH) for qt in range(QT)]

                with nc.Block() as block:
                    @block.sync
                    def _(sp):
                        mem = I["cache_mem_kv"][0].rearrange("b (c p) v h d -> b p c v (h d)", p=P)
                        for b in range(NB):
                            sp.dma_start(vx[:, b, :, :], mem[b, :, :, 1, :]).then_inc(vx_here, 16)
                            if b >= 2:
                                sp.wait_ge(sk_mm, 2 * (b - 1))
                            sp.dma_start(kx[:, b % 2, :, :], mem[b, :, :, 0, :]).then_inc(kx_here[b % 2], 16)

                    @block.gpsimd
                    def _(pool):
                        pool.memset(qm[:, :], 0.0).then_inc(qm_zero, 1)

                    @block.tensor
                    def _(pe):
                        for i in range(2):
                            for h in (2 * i, 2 * i + 1):
                                for c in range(2):
                                    mm = pe.transpose(work[i][:, NM * (h % 2) + P * c:NM * (h % 2) + P * c + P],
                                                      memtok[:, c, P * h:P * h + P], ident)
                            mm.then_inc(xk_mm, 1)
                        pe.wait_ge(xk_out, 2)

                        def scores(n):
                            h, qt = steps9[n]
                            if n >= 4:
                                pe.wait_ge(xp_exp, n - 3)
                            pe.matmul(work[n % 4][:, 0:NM], qx[:, h, P * qt:P * qt + P], KTx[:, h, :],
                                      start=True, stop=True).then_inc(xs_mm, 1)

                        def values(n):
                            h, qt = steps9[n]
                            if qt == 0 and h >= 2:
                                pe.wait_ge(xo_out, h - 1)
                            pe.wait_ge(xt_out, n + 1)
                            for c in range(2):
                                mm = pe.matmul(gemm_big[h % 2][:, P * qt:P * qt + P],
                                               memtok[:, c, 512 + P * h:512 + P * h + P],
                                               PTx[:, n % 2, P * c:P * c + P], start=(c == 0), stop=(c == 1))
                            mm.then_inc(xv_mm, 1)

                        scores(0)
                        scores(1)
                        for n in range(len(steps9)):
                            if n + 2 < len(steps9):
                                scores(n + 2)
                            pe.wait_ge(xd, n + 1)
                            pe.wait_ge(xp_exp, n + 1)
                            if n >= 2:
                                pe.wait_ge(xt_out, n - 1)
                            for c in range(2):
                                mm = pe.matmul(gemm_small[n % 2][:, P * c:P * c + P], Px[:, n % 2, P * c:P * c + P],
                                               dgx[:, n % 2, :], start=True, stop=True)
                            mm.then_inc(xt_mm, 1)
                            if n:
                                values(n - 1)
                        values(len(steps9) - 1)
                        pe.wait_ge(xp_exp, len(steps9))
                        pe.wait_ge(qm_ready, 1)

                        def turn(b):
                            pe.wait_ge(kx_here[b % 2], 16 * (b // 2 + 1))
                            if b:
                                pe.wait_ge(sk_out, 2 * b)
                            for i in range(2):
                                for h in (2 * i, 2 * i + 1):
                                    for c in range(2):
                                        at = NM * (h % 2) + P * c
                                        mm = pe.transpose(work[i][:, at:at + P], kx[:, b % 2, c, P * h:P * h + P], ident)
                                mm.then_inc(sk_mm, 1)

                        turn(0)
                        for b in range(NB):
                            if b + 1 < NB:
                                turn(b + 1)
                            pe.wait_ge(sk_out, 2 * b + 2)
                            for h in range(XH):
                                at = P * (XH * b + h)
                                mm = pe.matmul(work[2][:, 0:NM], qm[:, at:at + P], KTs[:, b % 2, h, :],
                                               start=(b == 0 and h == 0), stop=(b == NB - 1 and h == XH - 1))
                            mm.then_inc(sq_mm, 1)
                        pe.wait_ge(sp_n, 1)
                        for c in range(2):
                            mm = pe.transpose(work[3][:, P * c:P * c + P], Pm[:, P * c:P * c + P], ident)
                        mm.then_inc(st_mm, 1)
                        pe.wait_ge(st_out, 1)
                        pe.wait_ge(vx_here, 16 * NB)
                        pe.wait_ge(xo_out, XH)
                        for b in range(NB):
                            for h in range(XH):
                                for c in range(2):
                                    at = P * c + 16 * b + ST * h
                                    mm = pe.matmul(gemm_big[0][:, TS * h + ST * b:TS * h + ST * b + ST],
                                                   vx[:, b, c, P * h:P * h + P], PTm[:, at:at + ST],
                                                   start=(c == 0), stop=(c == 1))
                        mm.then_inc(sv_mm, 1)

                    @block.scalar
                    def _(act):
                        for n, (h, qt) in enumerate(steps9):
                            act.wait_ge(xs_max, n + 1)
                            if n >= 2:
                                act.wait_ge(xt_mm, n - 1)
                            act.activation(Px[:, n % 2, :], work[n % 4][:, 0:NM], ACT.Exp, bias=sx[:, n % 4, 1:2],
                                           scale=XS, accum_out=sx[:, n % 4, 2:3]).then_inc(xp_exp, 1)
                            act.wait_ge(xt_mm, n + 1)
                            if n >= 2:
                                act.wait_ge(xv_mm, n - 1)
                            act.activation(PTx[:, n % 2, :], gemm_small[n % 2][:, 0:NM], ACT.Copy).then_inc(xt_out, 1)
                            if qt == 1 and h:
                                act.wait_ge(xv_mm, QT * h)
                                act.activation(ox[:, h - 1, 0:TP], gemm_big[(h - 1) % 2][:, :], ACT.Copy)\
                                    .then_inc(xo_out, 1)
                        act.wait_ge(xv_mm, len(steps9))
                        act.activation(ox[:, XH - 1, 0:TP], gemm_big[(XH - 1) % 2][:, :], ACT.Copy).then_inc(xo_out, 1)
                        for b in range(NB):
                            for i in range(2):
                                act.wait_ge(sk_mm, 2 * b + i + 1)
                                if b >= 2:
                                    act.wait_ge(sq_mm, b - 1)
                                act.activation(KTs[:, b % 2, 2 * i:2 * i + 2, :],
                                               work[i][:, :].rearrange("p (h m) -> p h m", h=2), ACT.Copy)\
                                    .then_inc(sk_out, 1)
                        act.wait_ge(sm_ready, 1)
                        act.activation(Pm[:, :], work[2][:, 0:NM], ACT.Exp, bias=sx[:, 0, 1:2], scale=XS,
                                       accum_out=sx[:, 0, 2:3]).then_inc(sp_ready, 1)

                    @block.vector
                    def _(dve):
                        c = Chain(dve, chain9)
                        for i in range(2):
                            dve.wait_ge(xk_mm, i + 1)
                            dve.tensor_copy(KTx[:, 2 * i:2 * i + 2, :], work[i][:, :].rearrange("p (h m) -> p h m", h=2))\
                                .then_inc(xk_out, 1)
                        dve.wait_ge(qm_zero, 1)
                        for h in range(XH):
                            ins = dve.tensor_copy(
                                qm[:, :].rearrange("p (b s) -> p b s", s=SKIP)[:, :, (P + ST) * h:(P + ST) * h + ST],
                                qx[:, h, TP:NT].rearrange("p (b t) -> p b t", b=NB))
                        ins.then_inc(qm_ready, 1)

                        def top(n):
                            dve.wait_ge(xs_mm, n + 1)
                            c.step(dve.tensor_reduce(sx[:, n % 4, 0:1], work[n % 4][:, 0:NM], AX, ALU.max))
                            dve.tensor_scalar(sx[:, n % 4, 1:2], sx[:, n % 4, 0:1], -XS, None, ALU.mult)\
                                .then_inc(xs_max, 1)

                        top(0)
                        for n in range(len(steps9)):
                            if n + 1 < len(steps9):
                                top(n + 1)
                            dve.wait_ge(xp_exp, n + 1)
                            c.step(dve.reciprocal(sx[:, n % 4, 3:4], sx[:, n % 4, 2:3]))
                            if n >= 2:
                                dve.wait_ge(xt_mm, n - 1)
                            dve.tensor_scalar(dgx[:, n % 2, :], ident, sx[:, n % 4, 3:4], None, ALU.mult)\
                                .then_inc(xd, 1)
                        dve.wait_ge(sq_mm, NB)
                        c.step(dve.tensor_reduce(sx[:, 0, 0:1], work[2][:, 0:NM], AX, ALU.max))
                        dve.tensor_scalar(sx[:, 0, 1:2], sx[:, 0, 0:1], -XS, None, ALU.mult).then_inc(sm_ready, 1)
                        dve.wait_ge(sp_ready, 1)
                        c.step(dve.reciprocal(sx[:, 0, 3:4], sx[:, 0, 2:3]))
                        dve.tensor_scalar(Pm[:, :], Pm[:, :], sx[:, 0, 3:4], None, ALU.mult).then_inc(sp_n, 1)
                        dve.wait_ge(st_mm, 1)
                        dve.tensor_copy(PTm[:, :], work[3][:, 0:NM]).then_inc(st_out, 1)
                        dve.wait_ge(sv_mm, 1)
                        dve.tensor_copy(ox[:, :, TP:NT], gemm_big[0][:, 0:P].rearrange("p (h t) -> p h t", h=XH))

            with nc.Block() as block:
                @block.sync
                def _(sp):
                    w = I["xa_wo"][0].rearrange("(k p) n -> p k n", p=P)
                    for n in range(8):
                        slot_free(sp, "xo", n // RING, n % RING)
                        sp.dma_start(ring[:, n % RING, 0:XH, :], w[:, :, P * n:P * n + P]).then_inc(w_loaded[n % RING], 16)

                @block.tensor
                def _(pe):
                    pe_gemm(pe, "xo", 8, XH, lambda k: ox[:, k, :])
                    norm_pe(pe, 3, nT)

                @block.scalar
                def _(act):
                    act.wait_ge(out_taken[1], stage["up"][0] // 2)
                    act.wait_ge(out_taken[0], stage["up"][0] // 2)
                    norm_act(act, 3, xT, nT)

                @block.vector
                def _(dve):
                    with dve.Fori(0, 2) as it:
                        for u in range(RING):
                            output_here(dve, "xo", it, u)
                            dve_add(dve, tile_of(xT, it, u), u % 2).then_inc(out_taken[u % 2], 1)
                    norm_dve(dve, 3, xT, V_FFN, nT)
            cross.close()

            with ExitStack() as c11:
                def t11(name, shape):
                    return c11.enter_context(nc.sbuf_tensor(name, shape, F32))

                NR, NQ = 4 + NE, QT + 1
                HT = t11("HT", [P, 2 * NE, NT])
                rw_ = t11("rw_", [P, KT, NR])
                rb = t11("rb", [P, NR])
                lgT = t11("lgT", [NR, NT])
                lg = t11("lg", [P, NQ, NR])
                a4 = t11("a4", [P, 8, NQ, 4])
                a1 = t11("a1", [P, 8, NQ])
                comb = t11("comb", [P, NQ, NE])
                combT = t11("combT", [NE, NT])
                ce = t11("ce", [NE, 2, NT])
                cb = t11("cb", [P, NT])
                sl = t11("sl", [P, 2, NT])
                hu = t11("hu", [P, NT])
                r_here, lt_mm, lt_out, l_mm, chain11, r_exp, r_sub, cm_ready, ct_mm, ct_out = (
                    sem(f"r_{n}") for n in ("here", "lt_mm", "lt_out", "l_mm", "chain", "exp", "sub", "comb",
                                            "ct_mm", "ct_out"))
                ce_ready, cb_mm, cb_out, silu_done, he_done, down_out = (
                    sem(f"e_{n}") for n in ("ce", "cb_mm", "cb_out", "silu", "h", "down_out"))

                with nc.Block() as block:
                    @block.sync
                    def _(sp):
                        sp.dma_start(rw_[:, :, 0:4], I["router_gw"][0].rearrange("(k p) n -> p k n", p=P))\
                            .then_inc(r_here, 16)
                        sp.dma_start(rw_[:, :, 4:NR], I["router_ew"][0].rearrange("(k p) n -> p k n", p=P))\
                            .then_inc(r_here, 16)
                        sp.dma_start(rb[:, 0:4], I["router_gb"].to_broadcast([P, 4])).then_inc(r_here, 16)
                        sp.dma_start(rb[:, 4:NR], I["router_eb"].to_broadcast([P, NE])).then_inc(r_here, 16)
                        up = [I[n][0].rearrange("e (k p) f -> e p k f", p=P) for n in ("exp_w_gate", "exp_w_up")]
                        with sp.Fori(0, NE) as e:
                            for u in range(RING):
                                slot_free(sp, "up", e, u)
                                sp.dma_start(ring[:, u, :, :],
                                             up[u % 2][bass.ds(e, 1), :, :, P * (u // 2):P * (u // 2) + P].rearrange(
                                                 "e p k f -> p (e k) f")).then_inc(w_loaded[u], 16)
                        down = I["exp_w_down"][0].rearrange("e f n -> (e f) n").rearrange(
                            "(s k p) n -> s p k n", s=RING, p=P)
                        with sp.Fori(0, KT) as n:
                            for u in range(RING):
                                slot_free(sp, "down", n, u)
                                sp.dma_start(ring[:, u, :, :], down[u, :, :, bass.ds(n * P, P)]).then_inc(w_loaded[u], 16)

                    @block.tensor
                    def _(pe):
                        pe.wait_ge(r_here, 64)
                        for i in range(2):
                            for k in range(KT):
                                mm = pe.matmul(work[i][0:NR, 0:HALF], rw_[:, k, :], nT[:, k, HALF * i:HALF * i + HALF],
                                               start=(k == 0), stop=(k == KT - 1))
                        mm.then_inc(lt_mm, 1)
                        pe.wait_ge(lt_out, 1)
                        for q in range(NQ):
                            n = P if q < QT else TS
                            mm = pe.transpose(work[2][0:n, NR * q:NR * q + NR], lgT[:, P * q:P * q + n], ident[0:NR, 0:NR])
                        mm.then_inc(l_mm, 1)
                        pe.wait_ge(cm_ready, 1)
                        for q in range(NQ):
                            n = P if q < QT else TS
                            bank_ = work[3][0:NE, P * q:P * q + n] if q < QT else work[2][0:NE, P:P + n]
                            mm = pe.transpose(bank_, comb[0:n, q, :], ident[0:n, 0:n])
                        mm.then_inc(ct_mm, 1)

                        def weights_over_partitions(e):
                            pe.wait_ge(ce_ready, e + 1)
                            pe.wait_ge(cb_out, e)
                            for i in range(2):
                                mm = pe.matmul(work[i][:, 0:HALF], const("ones", NE), ce[:, 0, HALF * i:HALF * i + HALF],
                                               start=True, stop=True)
                            mm.then_inc(cb_mm, 1)

                        pe_gemm(pe, "up", 4 * NE, KT, lambda k: nT[:, k, :], before=weights_over_partitions)
                        pe.wait_ge(he_done, 2 * NE)
                        for p in range(2):
                            pe.wait_ge(out_taken[p], stage["down"][0] // 2)
                        with pe.Fori(0, KT // 2) as it:
                            for j in range(2):
                                for u in range(RING):
                                    _, pieces, before = stage["down"]
                                    pe.wait_ge(w_loaded[u], it * 32 + (before + 16 * j + 16))
                                    if u == 0:
                                        pe.wait_ge(down_out, it * 2 + (j - 1) if j else it * 2)
                                    for k in range(KT):
                                        kk = KT * u + k
                                        for bank_, at in halves(j):
                                            mm = pe.matmul(bank_, ring[:, u, k, :], HT[:, kk, at:at + HALF],
                                                           start=(kk == 0), stop=(kk == 2 * NE - 1))
                                    mm.then_inc(w_done[u % 2], 1)

                    @block.scalar
                    def _(act):
                        act.wait_ge(r_sub, 1)
                        act.activation(a4[:, 1, :, :], a4[:, 1, :, :], ACT.Exp).then_inc(r_exp, 1)
                        act.wait_ge(r_sub, 2)
                        act.activation(a1[:, 4, :], a1[:, 4, :], ACT.Exp).then_inc(r_exp, 1)
                        with act.Fori(0, NE) as e:
                            act.wait_ge(cb_mm, e + 1)
                            act.wait_ge(he_done, e * 2)
                            for i in range(2):
                                ins = act.activation(cb[:, HALF * i:HALF * i + HALF], work[i][:, 0:HALF], ACT.Copy)
                            ins.then_inc(cb_out, 1)
                            for f in range(2):
                                output_here(act, "up", e, 2 * f)
                                act.wait_ge(he_done, e * 2)
                                for bank_, at in halves(0):
                                    ins = act.activation(sl[:, f, at:at + HALF], bank_, ACT.Silu)
                                ins.then_inc(out_taken[0], 1)

                    @block.vector
                    def _(dve):
                        c = Chain(dve, chain11)
                        dve.wait_ge(r_here, 64)
                        dve.wait_ge(lt_mm, 1)
                        c.step(dve.memset(lg[:, :, :], 0.0))
                        dve.tensor_copy(lgT[:, 0:HALF], work[0][0:NR, 0:HALF])
                        dve.tensor_copy(lgT[:, HALF:NT], work[1][0:NR, 0:HALF]).then_inc(lt_out, 1)
                        dve.wait_ge(l_mm, 1)
                        bias = rb[:, :].unsqueeze(1)
                        dve.tensor_tensor(lg[:, 0:QT, :], work[2][:, 0:NR * QT].rearrange("p (q n) -> p q n", n=NR),
                                          bias.to_broadcast([P, QT, NR]), ALU.add)
                        c.step(dve.tensor_tensor(lg[0:TS, QT, :], work[2][0:TS, NR * QT:NR * NQ], rb[0:TS, :], ALU.add))

                        def first_max(x, hot, top, seen):
                            c.step(dve.tensor_reduce(top, x, AX, ALU.max))
                            c.step(dve.tensor_tensor(hot, x, top.unsqueeze(2).to_broadcast([P, NQ, 4]), ALU.is_equal))
                            c.step(dve.tensor_copy(seen, hot[:, :, 0]))
                            for j in range(1, 4):
                                c.step(dve.tensor_tensor(a1[:, 7, :], hot[:, :, j], seen, ALU.mult))
                                c.step(dve.tensor_tensor(hot[:, :, j], hot[:, :, j], a1[:, 7, :], ALU.subtract))
                                c.step(dve.tensor_tensor(seen, seen, hot[:, :, j], ALU.max))

                        g_log, g_p, g_hot, le, tmp4, hot1, hot2, le2 = (a4[:, i, :, :] for i in range(8))
                        g_top, g_sum, g_w, m1, e2, m2, seen = (a1[:, i, :] for i in range(7))
                        c.step(dve.tensor_copy(g_log, lg[:, :, 0:4]))
                        c.step(dve.tensor_reduce(g_top, g_log, AX, ALU.max))
                        dve.tensor_tensor(g_p, g_log, g_top.unsqueeze(2).to_broadcast([P, NQ, 4]), ALU.subtract)\
                            .then_inc(r_sub, 1)
                        dve.wait_ge(r_exp, 1)
                        c.step(dve.tensor_reduce(g_sum, g_p, AX, ALU.add))
                        c.step(dve.reciprocal(g_sum, g_sum))
                        c.step(dve.tensor_tensor(g_p, g_p, g_sum.unsqueeze(2).to_broadcast([P, NQ, 4]), ALU.mult))
                        first_max(g_p, g_hot, g_w, seen)
                        for g in range(4):
                            mine = lg[:, :, 4 + 4 * g:8 + 4 * g]
                            on = g_hot[:, :, g:g + 1].to_broadcast([P, NQ, 4])
                            if g == 0:
                                c.step(dve.tensor_tensor(le, mine, on, ALU.mult))
                            else:
                                c.step(dve.tensor_tensor(tmp4, mine, on, ALU.mult))
                                c.step(dve.tensor_tensor(le, le, tmp4, ALU.add))
                        first_max(le, hot1, m1, seen)
                        c.step(dve.tensor_scalar(tmp4, hot1, -3e38, None, ALU.mult))
                        c.step(dve.tensor_tensor(le2, le, tmp4, ALU.add))
                        first_max(le2, hot2, m2, seen)
                        dve.tensor_tensor(e2, m2, m1, ALU.subtract).then_inc(r_sub, 1)
                        dve.wait_ge(r_exp, 2)
                        w1_, w2_ = g_sum, g_top
                        c.step(dve.tensor_scalar(w1_, e2, 1.0, None, ALU.add))
                        c.step(dve.reciprocal(w1_, w1_))
                        c.step(dve.tensor_tensor(w2_, w1_, e2, ALU.mult))
                        for w_, hot in ((w1_, hot1), (w2_, hot2)):
                            c.step(dve.tensor_tensor(w_, w_, g_w, ALU.mult))
                            c.step(dve.tensor_tensor(hot, hot, w_.unsqueeze(2).to_broadcast([P, NQ, 4]), ALU.mult))
                        c.step(dve.tensor_tensor(hot1, hot1, hot2, ALU.add))
                        for g in range(4):
                            ins = dve.tensor_tensor(comb[:, :, 4 * g:4 * g + 4], hot1,
                                                    g_hot[:, :, g:g + 1].to_broadcast([P, NQ, 4]), ALU.mult)
                        ins.then_inc(cm_ready, 1)
                        dve.wait_ge(ct_mm, 1)
                        dve.tensor_copy(combT[:, 0:TP], work[3][0:NE, :])
                        dve.tensor_copy(combT[:, TP:NT], work[2][0:NE, P:P + TS]).then_inc(ct_out, 1)
                        dve.wait_ge(ct_out, 1)
                        with dve.Fori(0, NE) as e:
                            dve.wait_ge(cb_mm, e)
                            dve.tensor_scalar(ce[:, 0, :], combT[:, :], ident[0:NE, bass.ds(e, 1)], None, ALU.mult)\
                                .then_inc(ce_ready, 1)
                            for f in range(2):
                                output_here(dve, "up", e, 2 * f + 1)
                                dve.wait_ge(cb_out, e + 1)
                                dve.wait_ge(he_done, e * 2 + f)
                                for bank_, at in halves(1):
                                    ins = dve.tensor_tensor(hu[:, at:at + HALF], bank_, cb[:, at:at + HALF], ALU.mult)
                                ins.then_inc(out_taken[1], 1)
                                dve.wait_ge(out_taken[1], e * 2 + (stage["up"][0] // 2 + f + 1))
                                dve.wait_ge(out_taken[0], e * 2 + (stage["up"][0] // 2 + f + 1))
                                dve.tensor_tensor(HT[:, bass.ds(e * 2 + f, 1), :].rearrange("p a n -> p (a n)"),
                                                  hu[:, :], sl[:, f, :], ALU.mult).then_inc(he_done, 1)
                        with dve.Fori(0, KT // 2) as it:
                            for j in range(2):
                                dve.wait_ge(w_done[1], it * 4 + (stage["down"][0] // 2 + 2 * j + 2))
                                dve_add(dve, xT[:, bass.ds(it * 2 + j, 1), :].rearrange("p a n -> p (a n)"), j)\
                                    .then_inc(down_out, 1)

            with ExitStack() as c12:
                yt = c12.enter_context(nc.sbuf_tensor("yt", [P, 2, D], F32))
                f_mm, f_out, y_stored = sem("f_mm"), sem("f_out"), [sem(f"y_stored{j}") for j in range(2)]
                with nc.Block() as block:
                    @block.tensor
                    def _(pe):
                        norm_pe(pe, 4, nT)
                        pe.wait_ge(norm_ready, 5 * KT)
                        for q in range(QT + 1):
                            rows, at = (P, P * q) if q < QT else (TS, TP)
                            for half in range(2):
                                n = 2 * q + half
                                if n >= 2:
                                    pe.wait_ge(f_out, n - 1)
                                for i in range(4):
                                    mm = pe.transpose(work[n % 2][0:rows, P * i:P * i + P],
                                                      nT[:, 4 * half + i, at:at + rows], ident)
                                mm.then_inc(f_mm, 1)

                    @block.scalar
                    def _(act):
                        norm_act(act, 4, xT, nT)

                    @block.vector
                    def _(dve):
                        norm_dve(dve, 4, xT, V_FIN, nT)
                        for n in range(2 * QT + 2):
                            q, half = n // 2, n % 2
                            rows = P if q < QT else TS
                            dve.wait_ge(f_mm, n + 1)
                            if q >= 2:
                                dve.wait_ge(y_stored[q % 2], 16 * (q // 2))
                            dve.tensor_copy(yt[0:rows, q % 2, 512 * half:512 * half + 512], work[n % 2][0:rows, :])\
                                .then_inc(f_out, 1)

                    @block.sync
                    def _(sp):
                        for q in range(QT + 1):
                            sp.wait_ge(f_out, 2 * q + 2)
                            if q < QT:
                                sp.dma_start(O["y_prompt"][0, P * q:P * q + P, :], yt[:, q % 2, :]).then_inc(y_stored[q % 2], 16)
                            else:
                                sp.dma_start(O["y_sample"].rearrange("b t n -> (b t) n"), yt[0:TS, q % 2, :])\
                                    .then_inc(y_stored[q % 2], 16)
                        sp.wait_ge(y_stored[0], 16 * 3)
                        sp.wait_ge(y_stored[1], 16 * 2)
                        sp.wait_ge(out_dma, stores[0])


_OUTS = [("y_prompt", (1, TP, D)), ("y_sample", (NB, ST, D)),
         ("kv_p", (1, 1, TP, 4, G, HD)), ("kv_s", (1, NB, ST, 4, G, HD)),
         ("win_p", (1, 1, WIN, 2, G, HD)), ("win_s", (1, NB, WIN, 2, G, HD)),
         ("C_p", (1, 1, MLH, HD, HD)), ("C_s", (1, NB, MLH, HD, HD)),
         ("n_p", (1, 1, MLH, HD)), ("n_s", (1, NB, MLH, HD)),
         ("m_p", (1, 1, MLH)), ("m_s", (1, NB, MLH)),
         ("h_p", (1, 1, 256)), ("h_s", (1, NB, 256)),
         ("conv_p", (1, 1, 3, 256)), ("conv_s", (1, NB, 3, 256)),
         ("mem_p", (1, 1, NM, 2, XH, XD))]


def kernel(**inputs):
    import concourse.bacc as _bacc
    from concourse.bass_utils import run_bass_kernel_spmd as _run

    nc = _bacc.Bacc("TRN2", target_bir_lowering=False, num_devices=1)
    arrays, ins = {}, {}
    for name, a in inputs.items():
        a = np.ascontiguousarray(a)
        arrays[f"in_{name}"] = a
        ins[name] = nc.dram_tensor(f"in_{name}", a.shape, mybir.dt.from_np(a.dtype), kind="ExternalInput").ap()
    consts = {}
    for name, a in zip(("const", "prompt", "past"), shape_constants()):
        a = np.ascontiguousarray(a)
        arrays[f"shape_{name}"] = a
        consts[name] = nc.dram_tensor(f"shape_{name}", a.shape, F32, kind="ExternalInput").ap()
    outs = {}
    for name, shape in _OUTS:
        outs[name] = nc.dram_tensor(f"out_{name}", shape, F32, kind="ExternalOutput").ap()
    build(nc, ins, outs, consts)
    r = _run(nc, [arrays], core_ids=[0])
    return tuple(r.results[0][f"out_{name}"] for name, _ in _OUTS)
```

```python
from contextlib import ExitStack

import numpy as np

import concourse.bass as bass
from concourse import mybir

F32 = mybir.dt.float32
I32 = mybir.dt.int32
F32R = mybir.dt.float32r
ALU = mybir.AluOpType
ACT = mybir.ActivationFunctionType
AX = mybir.AxisListType.X

P = 128
D = 1024
KT = D // P
TP = 512
NB, ST = 8, 4
TS = NB * ST
NT = TP + TS
QT = TP // P
HD = 64
MLH = 4
G, REP = 2, 4
PAGE, PAST = 128, 4096
NPB = PAST // PAGE
CT = PAST // 256
NCB = PAST // 32
PCB = TP // 32
NSB = PAST // 64
WIN = 512
XH, XD, NM = 4, 128, 256
NE, FF = 16, 256
HALF = NT // 2
EPS = 1e-6
NEG = -1e30
RING = 4

O_MLQ, O_I, O_F, O_LRU, O_NQ, O_KV, O_GATE = 0, 1024, 1028, 1032, 1544, 2056, 2824
T_Q, T_K, T_V, T_O, T_X, T_GL, T_NQ, T_KC, T_VC, T_KS, T_VS, T_KW, T_VW, T_IF, T_GT = \
    0, 2, 4, 6, 8, 10, 12, 16, 17, 18, 19, 20, 21, 22, 23
NPT = 24
V_MIX, V_XA, V_MEM, V_FFN, V_FIN, V_Y, V_CW, V_CB, V_BA, V_BX, V_LAM, V_PB, V_END = \
    0, 8, 16, 24, 32, 40, 48, 56, 58, 60, 62, 64, 66

CONST = {}
_at = 0
for _name, _n in (("ident", P), ("ones", P), ("headones", P), ("causal", P), ("blocked", P), ("eps", 1),
                  ("pair0", P), ("pair1", P), ("head0", P), ("head1", P), ("head2", P), ("head3", P),
                    ("sblocked", TS), ("inb", NB), ("grp", 32), ("bonus", 65),
                  ("bcmp", NCB), ("bwin", WIN), ("bnew", NB * TS), ("pcmp", QT * 8 * PCB), ("pvalid", QT * PCB),
                   ("vplace", 8)):
    CONST[_name] = (_at, _n)
    _at += _n
NCONST = _at


def shape_constants():
    c = np.zeros((P, NCONST), np.float32)

    def put(name, a):
        o, n = CONST[name]
        a = np.asarray(a, np.float32).reshape(len(a), n)
        c[:len(a), o:o + n] = a

    i = np.arange(P)
    put("ident", np.eye(P))
    put("ones", np.ones((P, P)))
    put("headones", i[:, None] // HD == i[None, :] // HD)
    put("causal", np.where(i[None, :] <= i[:, None], 0, NEG))
    put("blocked", np.where(i[:, None] <= i[None, :], 0, -NEG))
    put("eps", np.full((P, 1), EPS))
    for k in range(2):
        put(f"pair{k}", np.arange(MLH)[:, None] == 2 * k + i[None, :] // HD)
    for h in range(MLH):
        put(f"head{h}", (np.arange(MLH)[:, None] == h) & np.ones((1, P), bool))
    s = np.arange(TS)
    same = s[:, None] // ST == s[None, :] // ST
    put("sblocked", np.where(same & (s[:, None] <= s[None, :]), 0, -NEG))
    put("inb", s[:, None] // ST == np.arange(NB)[None, :])
    row_h, row_t = s // ST, s % ST
    put("grp", (row_h[:, None] // REP == row_h[None, :] // REP) & (row_t[:, None] == row_t[None, :]))
    bonus = np.zeros((32, 65))
    bonus[:, [0, 63, 64]] = 100.0
    put("bonus", bonus)
    slope = 2.0 ** -(row_h + 1.0)
    qpos = PAST + row_t
    put("bcmp", -slope[:, None] * (qpos[:, None] - (np.arange(NCB) * 32 + 31)[None, :]))
    kpos = PAST - WIN + np.arange(WIN)
    dist = qpos[:, None] - kpos[None, :]
    put("bwin", np.where(dist < WIN, -slope[:, None] * dist, NEG))
    new = np.empty((32, NB, TS))
    for b in range(NB):
        back = row_t[:, None] - (s % ST)[None, :]
        new[:, b] = np.where((s // ST == b)[None, :] & (back >= 0), -slope[:, None] * back, NEG)
    put("bnew", new)
    hs = 2.0 ** -(np.arange(8) + 1.0)
    q = np.arange(TP).reshape(QT, P).T
    dist = q[:, :, None] - (np.arange(PCB) * 32 + 31)[None, None, :]
    put("pcmp", np.where(dist >= 0, 0, NEG)[:, :, None, :] - hs[None, None, :, None] * dist[:, :, None, :])
    put("pvalid", dist >= 0)
    col = np.arange(8)
    put("vplace", (i[:, None] // 64 == col[None, :] % 2) & (i[:, None] // 16 % 4 == col[None, :] // 2))
    rel = np.arange(TP)[None, :] - (TP - P) - i[:, None]
    prompt = np.where(rel[:, None, :] <= 0, hs[None, :, None] * rel[:, None, :], NEG).astype(np.float32)
    past = (slope[:, None] * (np.arange(PAST)[None, :] - qpos[:, None])).astype(np.float32)
    return c, prompt, past


class Chain:

    def __init__(self, eng, sem, base=0):
        self.eng, self.sem, self.base, self.n = eng, sem, base, 0

    def step(self, ins):
        self.n += 1
        ins.then_inc(self.sem, 1)
        self.eng.wait_ge(self.sem, self.base + self.n)


class Semaphores:

    def __init__(self, nc):
        self.nc, self.part = nc, []

    def __call__(self, name):
        self.part.append(self.nc.alloc_semaphore(name=name))
        return self.part[-1]

    def keep(self):
        self.part = []

    def end_part(self):
        self.nc.clear_and_free_semaphores(self.part)
        self.part = []
        self.nc.all_engine_barrier()


def build(nc, I, O, K):
    with ExitStack() as ctx:
        sem = Semaphores(nc)

        def sb(name, shape, dt=F32):
            return ctx.enter_context(nc.sbuf_tensor(name, shape, dt))

        bank = [ctx.enter_context(nc.psum_tensor(f"bank{n}", [P, 512], F32)) for n in range(8)]
        gemm_big, gemm_small = bank[0:2], bank[2:4]
        work = bank[4:8]

        cst = sb("cst", [P, NCONST])
        vecT = sb("vecT", [P, V_END])
        xT = sb("xT", [P, KT, NT])
        ring = sb("ring", [P, RING, KT, P])
        yT = sb("yT", [P, KT, NT])
        memtok = sb("memtok", [P, 2, 2 * XH * XD])

        def const(name, rows=P):
            o, n = CONST[name]
            return cst[0:rows, o:o + n]

        ident = const("ident")

        w_loaded = [sem(f"w_loaded{u}") for u in range(RING)]
        w_high, w_split = sem("w_high"), [sem(f"w_split{p}") for p in range(2)]
        w_done = [sem(f"w_done{p}") for p in range(2)]
        out_taken = [sem(f"out_taken{p}") for p in range(2)]

        stage, first, dmas = {}, RING, 0
        for name, n, pieces in (("in", 24, 2), ("mem", 8, 1), ("out", 8, 3), ("xq", 4, 1), ("xo", 8, 1),
                                ("up0", 2 * NE, 1), ("down0", 16, 1), ("up1", 2 * NE, 1), ("down1", 16, 1)):
            stage[name] = (first, pieces, dmas)
            first += n
            dmas += 16 * pieces * n // RING

        def slot_free(sp, name, it, u):
            sp.wait_ge(w_done[u % 2], stage[name][0] // 2 + 2 * it + u // 2 - 1)

        def split(dve, x, high, low, high_sem, n):
            dve.tensor_copy(high, x).then_inc(high_sem, 1)
            dve.wait_ge(high_sem, n)
            return dve.tensor_tensor(low, x, high.bitcast(F32), ALU.subtract)

        def split_weights(dve, name, it, u, parts, kts=KT):
            at, pieces, before = stage[name]
            dve.wait_ge(w_done[u % 2], it * 2 + (at // 2 + u // 2))
            dve.wait_ge(w_loaded[u], 16 * pieces * it + before + 16 * pieces)
            high, low = (x[:, u % 2, 0:kts, :] for x in parts)
            split(dve, ring[:, u, 0:kts, :], high, low, w_high, it * RING + (at - RING + u + 1))\
                .then_inc(w_split[u % 2], 1)

        def split_and_take(eng, n_turns, split_, take):
            def turn(it, first_=False):
                for u in range(RING):
                    if not (first_ and u < 2):
                        take(it, u - 2)
                    split_(it, u)

            turn(0, True)
            if n_turns > 1:
                with eng.Fori(1, n_turns) as it:
                    turn(it)
            take(n_turns - 1, 2)
            take(n_turns - 1, 3)

        def halves(par, width=NT):
            if width <= TP:
                return [(gemm_big[par][:, 0:width], 0)]
            return [(gemm_big[par][:, 0:HALF], 0), (gemm_small[par][:, 0:HALF], HALF)]

        def product(pe, outs, w, x, start, stop):
            (w_hi, w_lo), (x_hi, x_lo) = w, x
            for m, (a, c) in enumerate(((w_lo, x_hi), (w_hi, x_lo), (w_hi, x_hi))):
                for out, at in outs:
                    mm = pe.matmul(out, a, c[:, at:at + out.shape[1]], start=start and m == 0, stop=stop and m == 2)
            return mm

        def pe_gemm(pe, name, n_tiles, kts, rhs, parts, width=NT, before=None):
            o2 = stage[name][0] // 2
            with pe.Fori(0, n_tiles // RING) as it:
                if before:
                    before(it)
                for u in range(RING):
                    par = u % 2
                    pe.wait_ge(w_split[par], it * 2 + (o2 + u // 2 + 1))
                    pe.wait_ge(out_taken[par], it * 2 + (o2 + u // 2))
                    for k in range(kts):
                        mm = product(pe, halves(par, width), [x[:, par, k, :] for x in parts], rhs(k),
                                     k == 0, k == kts - 1)
                    mm.then_inc(w_done[par], 1)

        def output_here(eng, name, it, u):
            eng.wait_ge(w_done[u % 2], it * 2 + stage[name][0] // 2 + u // 2 + 1)

        def act_copy(act, dst, par, n=NT):
            for bank_, at in halves(par, n):
                last = act.activation(dst[:, at:at + bank_.shape[1]], bank_, ACT.Copy)
            return last

        def dve_copy(dve, dst, par, n=NT):
            for bank_, at in halves(par, n):
                last = dve.tensor_copy(dst[:, at:at + bank_.shape[1]], bank_)
            return last

        def dve_add(dve, dst, par):
            for bank_, at in halves(par):
                last = dve.tensor_tensor(dst[:, at:at + HALF], bank_, dst[:, at:at + HALF], ALU.add)
            return last

        sq_ready, ss_ready = sem("sq_ready"), sem("ss_ready")
        std_ready, rstd_ready, norm_ready = sem("std_ready"), sem("rstd_ready"), sem("norm_ready")
        sums = work[2:4]
        spare = sb("spare", [1, 8])
        stdt = sb("stdt", [P, NT])

        def norm_act(act, k, x, out, width=NT):
            for t in range(KT):
                act.activation(out[:, t, 0:width], x[:, t, 0:width], ACT.Square).then_inc(sq_ready, 1)
            act.wait_ge(ss_ready, k + 1)
            if k:
                act.wait_ge(norm_ready, KT * k)
            w = min(width, HALF)
            if width > HALF:
                act.activation(stdt[:, HALF:NT], sums[1][:, 0:HALF], ACT.Sqrt, bias=const("eps"), scale=1.0 / D)
            act.activation(stdt[:, 0:w], sums[0][:, 0:w], ACT.Sqrt, bias=const("eps"),
                           scale=1.0 / D).then_inc(std_ready, 1)

        def norm_pe(pe, k, out, width=NT):
            w = min(width, HALF)
            if k:
                pe.wait_ge(std_ready, k)
            for t in range(KT):
                pe.wait_ge(sq_ready, KT * k + t + 1)
                ends = dict(start=(t == 0), stop=(t == KT - 1))
                if width > HALF:
                    pe.matmul(sums[1][:, 0:HALF], const("ones"), out[:, t, HALF:NT], **ends)
                mm = pe.matmul(sums[0][:, 0:w], const("ones"), out[:, t, 0:w], **ends)
            mm.then_inc(ss_ready, 1)

        def norm_dve(dve, k, x, gain, out, width=NT):
            dve.wait_ge(std_ready, k + 1)
            dve.reciprocal(stdt[:, 0:width], stdt[:, 0:width]).then_inc(rstd_ready, 1)
            dve.wait_ge(rstd_ready, k + 1)
            for t in range(KT):
                dve.scalar_tensor_tensor(out=out[:, t, 0:width], in0=x[:, t, 0:width],
                                         scalar=vecT[:, gain + t:gain + t + 1], in1=stdt[:, 0:width],
                                         op0=ALU.mult, op1=ALU.mult).then_inc(norm_ready, 1)

        x_high, x_split, x_cuts = sem("x_high"), sem("x_split"), [0]

        def split_x(dve, x, parts, tiles_, width=NT):
            for t in tiles_:
                x_cuts[0] += 1
                split(dve, x[:, t, 0:width], parts[0][:, t, 0:width], parts[1][:, t, 0:width], x_high, x_cuts[0])\
                    .then_inc(x_split, 1)

        const_here = sem("const_here")
        out_dma = sem("out_dma")
        stores = [0]

        def store(eng, dst, src, scattered=False):
            stores[0] += 16
            return eng.dma_start(dst, src, allow_slow_non_contiguous=scattered).then_inc(out_dma, 16)

        QB = sb("QB", [P, NB, 32])
        ksn, kwn = sb("ksn", [P, TS]), sb("kwn", [P, TS])
        vnew = sb("vnew", [TS, 2, P])
        gq = sb("gq", [32, NB, 3])
        hb = sb("hb", [P, 2])
        gate_dram = nc.dram_tensor("gate_dram", (TS, 24), F32).ap()

        sem.keep()

        mixed = ctx.enter_context(ExitStack())
        pT = mixed.enter_context(nc.sbuf_tensor("pT", [P, NPT, NT], F32))
        memkv = mixed.enter_context(nc.sbuf_tensor("memkv", [P, 2 * XH, NM], F32))
        TK, TV, TOKKV = 0, 2, 4
        TGATE = 10
        with ExitStack() as c1:
            hparts = [c1.enter_context(nc.sbuf_tensor(n, [P, KT, NT], F32R)) for n in ("h_high", "h_low")]
            hmparts = [c1.enter_context(nc.sbuf_tensor(n, [P, KT, NM], F32R)) for n in ("hm_high", "hm_low")]
            wparts = [c1.enter_context(nc.sbuf_tensor(n, [P, 2, KT, P], F32R)) for n in ("w1_high", "w1_low")]
            xtok = c1.enter_context(nc.sbuf_tensor("xtok", [P, 2, D], F32))
            mT = yT
            hT, hmT, vecs = pT[:, 0:KT, :], pT[:, KT:2 * KT, 0:NM], pT[0:V_END, 2 * KT, 0:P]
            vecs_here = sem("vecs_here")
            x_here = [sem(f"x_here{j}") for j in range(2)]
            turned, turned_out = sem("turned"), sem("turned_out")
            tiles = [(P, xT, P * q) for q in range(QT)] + [(TS, xT, TP)] + [(P, mT, 0), (P, mT, P)]

            block = nc.Block()
            with block:
                @block.sync
                def _(sp):
                    sp.dma_start(cst[:, :], K["const"]).then_inc(const_here, 16)
                    xs = [I["x_prompt"][0, P * q:P * q + P, :] for q in range(QT)]
                    xs += [I["x_sample"].rearrange("b t n -> (b t) n")]
                    xs += [I["mem_prompt"][0, P * q:P * q + P, :] for q in range(2)]
                    for n, src in enumerate(xs):
                        if n >= 2:
                            sp.wait_ge(turned, 2 * n - 2)
                        sp.dma_start(xtok[0:tiles[n][0], n % 2, :], src).then_inc(x_here[n % 2], 16)
                    w = I["w_in"][0].rearrange("(k p) n -> p k n", p=P)
                    for n in range(NPT):
                        u = n % RING
                        slot_free(sp, "in", n // RING, u)
                        if n < T_X:
                            cols = [(0, 64, O_MLQ + P * n), (64, 64, O_MLQ + P * n + 64)]
                        elif n < T_NQ:
                            cols = [(0, 64, O_LRU + P * (n - T_X)), (64, 64, O_LRU + P * (n - T_X) + 64)]
                        elif n < T_KC:
                            cols = [(64 * g, 64, O_NQ + 256 * g + 64 * (n - T_NQ)) for g in range(G)]
                        elif n < T_IF:
                            cols = [(0, 64, O_KV + P * (n - T_KC)), (64, 64, O_KV + P * (n - T_KC) + 64)]
                        elif n == T_IF:
                            cols = [(0, 4, O_I), (32, 4, O_F)]
                        else:
                            cols = [(0, 12, O_GATE), (12, 12, O_GATE + 12)]
                        for dst, m, src in cols:
                            sp.dma_start(ring[:, u, :, dst:dst + m], w[:, :, src:src + m]).then_inc(w_loaded[u], 16)
                    w = I["xa_wkv"][0].rearrange("(k p) n -> p k n", p=P)
                    for n in range(8):
                        slot_free(sp, "mem", n // RING, n % RING)
                        sp.dma_start(ring[:, n % RING, :, :], w[:, :, P * n:P * n + P]).then_inc(w_loaded[n % RING], 16)

                @block.gpsimd
                def _(pool):
                    for n, s_ in enumerate(w_done + w_split + out_taken):
                        pool.memset(spare[0:1, n:n + 1], 0.0).then_inc(s_, RING // 2)
                    rows = [(V_MIX, I["norm_mix"][0]), (V_XA, I["norm_xa"][0]), (V_MEM, I["norm_mem"][0]),
                            (V_FFN, I["norm_ffn"][0]), (V_FIN, I["final_norm"]), (V_CB, I["conv_b"][0]),
                            (V_BA, I["lru_ba"][0]), (V_BX, I["lru_bx"][0]), (V_LAM, I["lru_lambda"][0]),
                            (V_Y, I["mix_norm"][0, 0:512])]
                    for at, v in rows:
                        n = v.shape[0] // P
                        pool.dma_start(vecs[at:at + n, :], v.rearrange("(k p) -> k p", p=P)).then_inc(vecs_here, 16)
                    for g in range(G):
                        pool.dma_start(vecs[V_Y + 4:V_Y + 8, 64 * g:64 * g + 64],
                                       I["mix_norm"][0, 512 + 256 * g:768 + 256 * g]
                                       .rearrange("(r d) -> r d", r=REP)).then_inc(vecs_here, 16)
                    pool.dma_start(vecs[V_CW:V_CW + 8, :], I["conv_w"][0].rearrange("j (k p) -> (j k) p", p=P))\
                        .then_inc(vecs_here, 16)
                    pool.dma_start(vecs[V_PB:V_PB + 2, :], I["phi_b1"][0]).then_inc(vecs_here, 16)

                @block.tensor
                def _(pe):
                    pe.wait_ge(const_here, 16)
                    n = 0
                    for j, (rows, _, _) in enumerate(tiles):
                        pe.wait_ge(x_here[j % 2], 16 * (j // 2 + 1))
                        for half in range(2):
                            if n >= 2:
                                pe.wait_ge(turned_out, n - 1)
                            for i in range(4):
                                k = 4 * half + i
                                mm = pe.transpose(work[n % 2][:, P * i:P * i + rows],
                                                  xtok[0:rows, j % 2, P * k:P * k + P], ident[0:rows, 0:rows])
                            mm.then_inc(turned, 1)
                            n += 1
                    pe.wait_ge(vecs_here, 16 * 14)
                    pe.wait_ge(turned_out, n - 1)
                    pe.transpose(work[n % 2][:, 0:V_END], vecs, ident[0:V_END, 0:V_END]).then_inc(turned, 1)
                    norm_pe(pe, 0, hT)
                    norm_pe(pe, 1, hmT, NM)
                    pe.wait_ge(x_split, KT)
                    pe_gemm(pe, "in", NPT, KT, lambda k: [x[:, k, :] for x in hparts], wparts)
                    pe.wait_ge(x_split, 2 * KT)
                    pe_gemm(pe, "mem", 8, KT, lambda k: [x[:, k, :] for x in hmparts], wparts, NM)

                @block.scalar
                def _(act):
                    act.wait_ge(const_here, 16)
                    act.wait_ge(turned_out, 15)
                    norm_act(act, 0, xT, hT)
                    norm_act(act, 1, mT, hmT, NM)
                    with act.Fori(0, NPT // RING) as it:
                        for u in (0, 2):
                            output_here(act, "in", it, u)
                            act_copy(act, pT[:, bass.ds(it * RING + u, 1), :].rearrange("p a n -> p (a n)"), 0)\
                                .then_inc(out_taken[0], 1)
                    for n in range(0, 8, 2):
                        output_here(act, "mem", n // RING, n % RING)
                        act_copy(act, memkv[:, n, :], 0, NM).then_inc(out_taken[0], 1)

                @block.vector
                def _(dve):
                    n = 0
                    for rows, dst, at in tiles:
                        for half in range(2):
                            dve.wait_ge(turned, n + 1)
                            dve.tensor_copy(dst[:, 4 * half:4 * half + 4, at:at + rows],
                                            work[n % 2][:, :].rearrange("p (k c) -> p k c", k=4)[:, :, 0:rows])\
                                .then_inc(turned_out, 1)
                            n += 1
                    dve.wait_ge(turned, n + 1)
                    dve.tensor_copy(vecT[:, :], work[n % 2][:, 0:V_END]).then_inc(turned_out, 1)
                    dve.wait_ge(turned_out, n + 1)
                    norm_dve(dve, 0, xT, V_MIX, hT)
                    dve.wait_ge(norm_ready, KT)
                    split_x(dve, hT, hparts, range(KT))
                    norm_dve(dve, 1, mT, V_MEM, hmT, NM)
                    dve.wait_ge(norm_ready, 2 * KT)
                    split_x(dve, hmT, hmparts, range(KT), NM)

                    def take_in(it, n):
                        if n % 2:
                            output_here(dve, "in", it, n)
                            dve_copy(dve, pT[:, bass.ds(it * RING + n, 1), :].rearrange("p a n -> p (a n)"), 1)\
                                .then_inc(out_taken[1], 1)

                    split_and_take(dve, NPT // RING, lambda it, u: split_weights(dve, "in", it, u, wparts), take_in)

                    def take_mem(it, n):
                        if n % 2:
                            output_here(dve, "mem", it, n)
                            dve_copy(dve, memkv[:, bass.ds(it * RING + n, 1), :].rearrange("p a n -> p (a n)"), 1, NM)\
                                .then_inc(out_taken[1], 1)

                    split_and_take(dve, 2, lambda it, u: split_weights(dve, "mem", it, u, wparts), take_mem)


        tok = mixed.enter_context(nc.sbuf_tensor("tok", [P, QT, 11, P], F32))
        toks = mixed.enter_context(nc.sbuf_tensor("toks", [TS, 11, P], F32))
        gate_p = mixed.enter_context(nc.sbuf_tensor("gate_p", [P, QT, 24], F32))
        gate_s = mixed.enter_context(nc.sbuf_tensor("gate_s", [TS, 24], F32))
        lru_state = mixed.enter_context(nc.sbuf_tensor("lru_state", [32, 256], F32))
        lruT = mixed.enter_context(nc.sbuf_tensor("lruT", [P, 2, 32], F32))
        state_here, tok_turned, tok_taken = sem("state_here"), sem("tok_turned"), sem("tok_taken")
        tok_copied = [sem("tok_copied_act"), sem("tok_copied_dve")]
        to_turn = [T_K, T_K + 1, T_V, T_V + 1, T_KC, T_VC, T_KS, T_VS, T_KW, T_VW, T_GT]
        groups = []
        for q in range(QT + 1):
            at, rows = (P * q, P) if q < QT else (TP, TS)
            for j in range(0, len(to_turn), 4):
                part = to_turn[j:j + 4]
                dst = tok[:, q, j:j + len(part), :] if q < QT else toks[:, j:j + len(part), :]
                groups.append(([pT[:, t, at:at + rows] for t in part], rows, dst))
        for q in range(2):
            for j in range(0, 8, 4):
                groups.append(([memkv[:, j + i, P * q:P * q + P] for i in range(4)], P,
                               memtok[:, q, P * j:P * j + 512].rearrange("p (k c) -> p k c", k=4)))

        with nc.Block() as block:
            @block.sync
            def _(sp):
                sp.dma_start(lru_state[0:24, :], I["state_rglru_conv"][0].rearrange("b j w -> (b j) w"))\
                    .then_inc(state_here, 16)
                sp.dma_start(lru_state[24:32, :], I["state_rglru_h"][0]).then_inc(state_here, 16)
                store(sp, O["win_s"][0, :, 0:WIN - ST].rearrange("b t c g d -> b (t c g d)"),
                      I["state_nsa_win"][0, :, ST:WIN].rearrange("b t c g d -> b (t c g d)"))
                n = 0
                for q in range(QT + 1):
                    n += 3
                    sp.wait_ge(tok_copied[0], (n + 1) // 2)
                    sp.wait_ge(tok_copied[1], n // 2)
                    if q < QT:
                        rows = slice(P * q, P * q + P)
                        store(sp, O["kv_p"][0, 0, rows].rearrange("t c g d -> t (c g d)"),
                              tok[:, q, TOKKV:TOKKV + 4, :].rearrange("p c n -> p (c n)"))
                        store(sp, O["win_p"][0, 0, rows].rearrange("t c g d -> t (c g d)"),
                              tok[:, q, TOKKV + 4:TOKKV + 6, :].rearrange("p c n -> p (c n)"))
                    else:
                        store(sp, O["kv_s"][0].rearrange("b t c g d -> (b t) (c g d)"),
                              toks[:, TOKKV:TOKKV + 4, :].rearrange("p c n -> p (c n)"))
                        for b in range(NB):
                            store(sp, O["win_s"][0, b, WIN - ST:WIN].rearrange("t c g d -> t (c g d)"),
                                  toks[ST * b:ST * b + ST, TOKKV + 4:TOKKV + 6, :].rearrange("p c n -> p (c n)"))
                for q in range(2):
                    n += 2
                    sp.wait_ge(tok_copied[0], (n + 1) // 2)
                    sp.wait_ge(tok_copied[1], n // 2)
                    store(sp, O["mem_p"][0, 0, P * q:P * q + P].rearrange("t c h d -> t (c h d)"), memtok[:, q, :])

            @block.tensor
            def _(pe):
                for n, (srcs, rows, _) in enumerate(groups):
                    if n >= 4:
                        pe.wait_ge(tok_copied[n % 2], n // 2 - 1)
                    for i, src in enumerate(srcs):
                        mm = pe.transpose(work[n % 4][0:rows, P * i:P * i + P], src, ident)
                    mm.then_inc(tok_turned, 1)
                pe.wait_ge(state_here, 32)
                pe.wait_ge(tok_copied[0], len(groups) // 2 + len(groups) % 2 - 1)
                pe.wait_ge(tok_copied[1], len(groups) // 2)
                n = len(groups)
                for k in range(2):
                    mm = pe.transpose(work[n % 4][:, 32 * k:32 * k + 32], lru_state[:, P * k:P * k + P],
                                      ident[0:32, 0:32])
                mm.then_inc(tok_turned, 1)

            def copy_out(eng, par):
                for n, (srcs, rows, dst) in enumerate(groups):
                    if n % 2 == par:
                        eng.wait_ge(tok_turned, n + 1)
                        src = work[n % 4][0:rows, 0:P * len(srcs)].rearrange("p (k c) -> p k c", c=P)
                        ins = eng.activation(dst, src, ACT.Copy) if par == 0 else eng.tensor_copy(dst, src)
                        ins.then_inc(tok_copied[par], 1)

            @block.scalar
            def _(act):
                copy_out(act, 0)
                act.wait_ge(tok_copied[0], 8)
                act.wait_ge(tok_copied[1], 7)
                act.activation(gate_p[:, :, :], tok[:, :, TGATE, 0:24], ACT.Sigmoid)
                act.activation(gate_s[:, :], toks[:, TGATE, 0:24], ACT.Sigmoid)

            @block.vector
            def _(dve):
                copy_out(dve, 1)
                dve.wait_ge(tok_turned, len(groups) + 1)
                dve.tensor_copy(lruT[:, :, :],
                                work[len(groups) % 4][:, 0:64].rearrange("p (k c) -> p k c", k=2))

        with ExitStack() as c3:
            def t3(name, shape):
                return c3.enter_context(nc.sbuf_tensor(name, shape, F32))

            XP = TP + 3
            xpad = t3("xpad", [P, 2, XP])
            xsam = t3("xsam", [P, 2, NB, ST + 3])
            xc = t3("xc", [P, 2, NT])
            wab = t3("wab", [P, 2, 2, P])
            gr = t3("gr", [P, 2, NT])
            gi = t3("gi", [P, 2, NT])
            th = t3("th", [P, 2, NT])
            hseq = t3("hseq", [P, 2, NT])
            lam = t3("lam", [P, 8, 2])
            hl = t3("hl", [P, 2, 9])
            cl = t3("cl", [P, 2, 27])
            hlT = t3("hlT", [9, 2, P])
            clT = t3("clT", [27, 2, P])
            w_zero, w_here, chain, lru_mm = sem("lru_zero"), sem("lru_w"), sem("lru_chain"), sem("lru_mm")
            conv_done, gates_done, sp_done = sem("conv_done"), sem("gates_done"), sem("softplus_done")
            u_done, lru_act, last_done, last_turned, last_out = (
                sem("lru_u"), sem("lru_act"), sem("lru_last"), sem("lru_turned"), sem("lru_last_out"))
            lam_in = sem("lam_in")

            with nc.Block() as block:
                @block.sync
                def _(sp):
                    sp.wait_ge(w_zero, 1)
                    for j, name in enumerate(("lru_wa", "lru_wx")):
                        for k in range(4):
                            o = 64 * (k % 2)
                            sp.dma_start(wab[o:o + 64, j, k // 2, o:o + 64], I[name][0, k]).then_inc(w_here, 16)
                    sp.wait_ge(last_out, 2)
                    for k in range(2):
                        cols = slice(P * k, P * k + P)
                        store(sp, O["h_p"][0, :, cols], hlT[0:1, k, :])
                        store(sp, O["h_s"][0, :, cols], hlT[1:9, k, :])
                        store(sp, O["conv_p"][0, 0, :, cols], clT[0:3, k, :])
                        store(sp, O["conv_s"][0, :, :, cols].rearrange("b j w -> (b j) w"), clT[3:27, k, :])

                @block.gpsimd
                def _(pool):
                    pool.memset(wab[:, :, :, :], 0.0).then_inc(w_zero, 1)

                @block.tensor
                def _(pe):
                    pe.wait_ge(w_here, 16 * 8)
                    pe.wait_ge(conv_done, 1)
                    n = 0
                    for k in range(2):
                        for j in range(2):
                            if n >= 2:
                                pe.wait_ge(gates_done, n - 1)
                            pe.matmul(gemm_big[n % 2][:, :], wab[:, j, k, :], xc[:, k, 0:TP], start=True, stop=True)
                            pe.matmul(gemm_small[n % 2][:, 0:TS], wab[:, j, k, :], xc[:, k, TP:NT],
                                      start=True, stop=True).then_inc(lru_mm, 1)
                            n += 1
                    pe.wait_ge(last_done, 1)
                    for k in range(2):
                        pe.transpose(work[0][0:9, P * k:P * k + P], hl[:, k, :], ident)
                    for k in range(2):
                        mm = pe.transpose(work[1][0:27, P * k:P * k + P], cl[:, k, :], ident)
                    mm.then_inc(last_turned, 1)

                @block.scalar
                def _(act):
                    act.wait_ge(lam_in, 1)
                    act.activation(lam[:, 1, :], lam[:, 0, :], ACT.Exp).then_inc(sp_done, 1)
                    n = 0
                    for k in range(2):
                        for j, (dst, bias) in enumerate(((gr, V_BA), (gi, V_BX))):
                            act.wait_ge(lru_mm, n + 1)
                            act.activation(dst[:, k, 0:TP], gemm_big[n % 2][:, :], ACT.Sigmoid,
                                           bias=vecT[:, bias + k:bias + k + 1])
                            act.activation(dst[:, k, TP:NT], gemm_small[n % 2][:, 0:TS], ACT.Sigmoid,
                                           bias=vecT[:, bias + k:bias + k + 1]).then_inc(gates_done, 1)
                            n += 1
                    act.wait_ge(gates_done, 4)
                    act.wait_ge(sp_done, 2)
                    for k in range(2):
                        act.activation(th[:, k, :], gr[:, k, :], ACT.Tanh, scale=lam[:, 6, k:k + 1])
                    ins = act.activation(hseq[:, :, :], pT[:, T_GL:T_GL + 2, :], ACT.Gelu_apprx_tanh)
                    ins.then_inc(lru_act, 1)
                    for k in range(2):
                        ins = act.activation(gr[:, k, :], gr[:, k, :], ACT.Exp, scale=lam[:, 7, k:k + 1])
                    ins.then_inc(lru_act, 1)
                    act.wait_ge(u_done, 1)
                    act.activation(th[:, :, :], th[:, :, :], ACT.Sqrt).then_inc(lru_act, 1)

                @block.vector
                def _(dve):
                    c = Chain(dve, chain)
                    c.step(dve.tensor_scalar(lam[:, 2, :], vecT[:, V_LAM:V_LAM + 2], -1.0, None, ALU.mult))
                    dve.tensor_tensor(lam[:, 0, :], lam[:, 2, :], vecT[:, V_LAM:V_LAM + 2], ALU.min).then_inc(lam_in, 1)
                    c.step(dve.memset(xpad[:, :, 0:3], 0.0))
                    c.step(dve.tensor_copy(xpad[:, :, 3:XP], pT[:, T_X:T_X + 2, 0:TP]))
                    for k in range(2):
                        dve.tensor_copy(xsam[:, k, :, 0:3], lruT[:, k, 0:24].rearrange("p (b j) -> p b j", b=NB))
                        c.step(dve.tensor_copy(xsam[:, k, :, 3:7],
                                               pT[:, T_X + k, TP:NT].rearrange("p (b t) -> p b t", b=NB)))
                    for j in range(4):
                        for k in range(2):
                            tap = vecT[:, V_CW + 2 * j + k:V_CW + 2 * j + k + 1]
                            for dst, src in ((xc[:, k, 0:TP], xpad[:, k, j:j + TP]),
                                             (xc[:, k, TP:NT].rearrange("p (b t) -> p b t", b=NB),
                                              xsam[:, k, :, j:j + ST])):
                                if j == 0:
                                    ins = dve.tensor_scalar(dst, src, tap, vecT[:, V_CB + k:V_CB + k + 1],
                                                            ALU.mult, ALU.add)
                                else:
                                    ins = dve.scalar_tensor_tensor(out=dst, in0=src, scalar=tap, in1=dst,
                                                                   op0=ALU.mult, op1=ALU.add)
                        if j < 3:
                            c.step(ins)
                        else:
                            ins.then_inc(conv_done, 1)
                    dve.wait_ge(conv_done, 1)
                    y, s, s2, acc = lam[:, 1, :], lam[:, 3, :], lam[:, 4, :], lam[:, 5, :]
                    dve.wait_ge(sp_done, 1)
                    c.step(dve.tensor_scalar(s, y, 2.0, None, ALU.add))
                    c.step(dve.reciprocal(s, s))
                    c.step(dve.tensor_tensor(s, s, y, ALU.mult))
                    c.step(dve.tensor_tensor(s2, s, s, ALU.mult))
                    c.step(dve.tensor_scalar(acc, s2, 1.0 / 19, 1.0 / 17, ALU.mult, ALU.add))
                    for m in (15, 13, 11, 9, 7, 5, 3, 1):
                        c.step(dve.tensor_tensor(acc, acc, s2, ALU.mult))
                        c.step(dve.tensor_scalar(acc, acc, 1.0 / m, None, ALU.add))
                    c.step(dve.tensor_tensor(acc, acc, s, ALU.mult))
                    c.step(dve.tensor_scalar(s, lam[:, 2, :], 0.0, 0.5, ALU.max, ALU.mult))
                    c.step(dve.tensor_tensor(acc, acc, s, ALU.add))
                    dve.tensor_scalar(lam[:, 6, :], acc, 16.0, None, ALU.mult)
                    dve.tensor_scalar(lam[:, 7, :], acc, -16.0, None, ALU.mult).then_inc(sp_done, 1)
                    dve.wait_ge(lru_act, 1)
                    c.step(dve.tensor_tensor(gi[:, :, :], gi[:, :, :], xc[:, :, :], ALU.mult))
                    c.step(dve.tensor_scalar(xc[:, :, :], th[:, :, :], 1.0, None, ALU.add))
                    c.step(dve.reciprocal(xc[:, :, :], xc[:, :, :]))
                    dve.scalar_tensor_tensor(out=th[:, :, :], in0=th[:, :, :], scalar=2.0, in1=xc[:, :, :],
                                             op0=ALU.mult, op1=ALU.mult).then_inc(u_done, 1)
                    dve.wait_ge(lru_act, 3)
                    c.step(dve.tensor_tensor(gi[:, :, :], gi[:, :, :], th[:, :, :], ALU.mult))
                    h = xc
                    for k in range(2):
                        c.step(dve.tensor_tensor_scan(h[:, k, 0:TP], gr[:, k, 0:TP], gi[:, k, 0:TP], 0.0,
                                                      ALU.mult, ALU.add))
                    for k in range(2):
                        def step(x, t):
                            return x[:, k, TP:NT].rearrange("p (b t) -> p b t", t=ST)[:, :, t]
                        for t in range(ST):
                            prev = lruT[:, k, 24:32] if t == 0 else step(h, t - 1)
                            c.step(dve.tensor_tensor(step(h, t), step(gr, t), prev, ALU.mult))
                            c.step(dve.tensor_tensor(step(h, t), step(h, t), step(gi, t), ALU.add))
                    c.step(dve.tensor_copy(hl[:, :, 0:1], h[:, :, TP - 1:TP]))
                    for k in range(2):
                        c.step(dve.tensor_copy(hl[:, k, 1:9],
                                               h[:, k, TP:NT].rearrange("p (b t) -> p b t", t=ST)[:, :, ST - 1]))
                        c.step(dve.tensor_copy(cl[:, k, 3:27].rearrange("p (b j) -> p b j", b=NB),
                                               xsam[:, k, :, ST:ST + 3]))
                    dve.tensor_copy(cl[:, :, 0:3], xpad[:, :, TP:TP + 3]).then_inc(last_done, 1)
                    dve.tensor_tensor(yT[:, 2:4, :], h[:, :, :], hseq[:, :, :], ALU.mult)
                    dve.wait_ge(last_turned, 1)
                    dve.tensor_copy(hlT[:, :, :], work[0][0:9, 0:256].rearrange("p (k c) -> p k c", k=2))\
                        .then_inc(last_out, 1)
                    dve.tensor_copy(clT[:, :, :], work[1][0:27, 0:256].rearrange("p (k c) -> p k c", k=2))\
                        .then_inc(last_out, 1)

        with ExitStack() as c4:
            def t4(name, shape):
                return c4.enter_context(nc.sbuf_tensor(name, shape, F32))

            mlb = t4("mlb", [MLH, 2])
            m0 = t4("m0", [MLH, NB])
            lf, bsum, av, mx, wrow, emrow = (
                t4(n, [MLH, NT]) for n in ("lf", "bsum", "av", "mx", "wrow", "emrow"))
            mend = t4("mend", [MLH, 9])
            wcrow = t4("wcrow", [MLH, TS])
            decay = t4("decay", [MLH, NB])
            cols = t4("cols", [P, QT + 1, 2, MLH])
            sg = t4("sg", [P, 2, NT])
            wcb = t4("wcb", [P, 2, TS])
            qw = t4("qw", [HD, MLH, TS])
            nq = t4("nq", [HD, MLH, TS])
            n0 = t4("n0", [NB, 256])
            n0T = t4("n0T", [HD, MLH, NB])
            Cn = t4("Cn", [HD + 1, MLH, NB, HD])
            C0T = t4("C0T", [HD, MLH, NB, HD])
            Cp = t4("Cp", [HD + 1, MLH, HD])
            dg = t4("dg", [P, 2, P])
            idle = ring[:, :, :, :].rearrange("p u k c -> p (u k c)")
            E = idle[:, 0:2 * TP].rearrange("p (j t) -> p j t", j=2)
            W = idle[:, 2 * TP:4 * TP].rearrange("p (j t) -> p j t", j=2)
            vw = idle[:, 4 * TP:4 * TP + QT * MLH * (HD + 1)].rearrange("p (q h d) -> p q h d", q=QT, h=MLH)
            KM = idle[0:TS, 0:2 * TP].rearrange("p (j b d) -> p j b d", j=2, b=NB)
            dgs, Es, Ws = (t4(n, [TS, MLH, TS]) for n in ("dgs", "Es", "Ws"))
            vws = t4("vws", [TS, MLH, HD + 1])
            em = t4("em", [P, NT])
            dd = t4("dd", [P, NT])
            ax, ones4, fx = emrow, dd[0:MLH, :], em[0:MLH, :]
            db = t4("db", [HD + 1, MLH, NB])

            ml_in, ml_chain, ml_act, rows_ready = sem("ml_in"), sem("ml_chain"), sem("ml_act"), sem("ml_rows")
            cols_mm, cols_out = sem("ml_cols_mm"), sem("ml_cols_out")
            c0_mm, c0_out = sem("c0_turned"), sem("c0_out")
            mb_ready, dg_ready, e_ready, s_ready, w_ready, pv_done = (
                sem(f"ml_{n}") for n in ("mb", "dg", "e", "s", "w", "pv"))
            fin_mm, em_out, y_done = sem("ml_fin_mm"), sem("ml_em_out"), sem("ml_y")
            vw_ready, km_ready, cn_mm, cn_out, cp_mm, cp_out = (
                sem(f"ml_{n}") for n in ("vw", "km", "cn_mm", "cn_out", "cp_mm", "cp_out"))
            samp_mm, samp_e, samp_w, qw_ready = (sem(f"ml_{n}") for n in ("samp_mm", "samp_e", "samp_w", "qw"))
            steps = [(h, kt) for h in range(MLH) for kt in range(QT)]

            with nc.Block() as block:
                @block.sync
                def _(sp):
                    sp.dma_start(mlb[:, 0:1], I["ml_i_bias"].rearrange("a h -> h a"),
                                 allow_slow_non_contiguous=True).then_inc(ml_in, 16)
                    sp.dma_start(mlb[:, 1:2], I["ml_f_bias"].rearrange("a h -> h a"),
                                 allow_slow_non_contiguous=True).then_inc(ml_in, 16)
                    sp.dma_start(m0[:, :], I["state_mlstm_m"][0].rearrange("b h -> h b"),
                                 allow_slow_non_contiguous=True).then_inc(ml_in, 16)
                    sp.dma_start(n0[:, :], I["state_mlstm_n"][0].rearrange("b h d -> b (h d)")).then_inc(ml_in, 16)
                    for h in range(MLH):
                        sp.dma_start(Cn[0:HD, h, :, :], I["state_mlstm_C"][0, :, h].rearrange("b e d -> e b d"))\
                            .then_inc(ml_in, 16)
                        sp.dma_start(Cn[HD:HD + 1, h, :, :], I["state_mlstm_n"][0:1, :, h, :]).then_inc(ml_in, 16)
                    sp.wait_ge(rows_ready, 1)
                    store(sp, O["m_p"][0].rearrange("a h -> h a"), mend[:, 0:1], True)
                    store(sp, O["m_s"][0].rearrange("b h -> h b"), mend[:, 1:9], True)
                    sp.wait_ge(cp_out, 1)
                    store(sp, O["C_p"][0, 0].rearrange("h e d -> e h d"), Cp[0:HD, :, :])
                    store(sp, O["n_p"][0, 0:1], Cp[HD:HD + 1, :, :])
                    for h in range(MLH):
                        sp.wait_ge(cn_out, h + 1)
                        store(sp, O["C_s"][0, :, h].rearrange("b e d -> e b d"), Cn[0:HD, h, :, :])
                        store(sp, O["n_s"][0:1, :, h, :], Cn[HD:HD + 1, h, :, :])

                @block.tensor
                def _(pe):
                    pe.wait_ge(ml_in, 16 * 12)
                    for h in range(MLH):
                        if h >= 2:
                            pe.wait_ge(c0_out, h - 1)
                        for b in range(NB):
                            mm = pe.transpose(work[h % 2][0:HD, HD * b:HD * b + HD], Cn[0:HD, h, b, :],
                                              ident[0:HD, 0:HD])
                        mm.then_inc(c0_mm, 1)
                    for h in range(MLH):
                        mm = pe.transpose(work[2][0:HD, NB * h:NB * h + NB], n0[:, HD * h:HD * h + HD],
                                          ident[0:NB, 0:NB])
                    mm.then_inc(c0_mm, 1)
                    pe.wait_ge(rows_ready, 2)
                    for q in range(QT + 1):
                        at, n = (P * q, P) if q < QT else (TP, TS)
                        for j, row in enumerate((av, wrow)):
                            mm = pe.transpose(work[3][0:n, 8 * q + 4 * j:8 * q + 4 * j + 4], row[:, at:at + n],
                                              ident[0:MLH, 0:MLH])
                    mm.then_inc(cols_mm, 1)
                    pe.wait_ge(c0_out, 5)
                    for k in range(2):
                        pe.matmul(work[0][:, TS * k:TS * k + TS], const(f"pair{k}", MLH), wcrow[:, :],
                                  start=True, stop=True)
                    for h in range(MLH):
                        mm = pe.matmul(work[0][0:HD + 1, 64 + NB * h:64 + NB * h + NB],
                                       const(f"head{h}", MLH)[:, 0:HD + 1], decay[:, :], start=True, stop=True)
                    mm.then_inc(cols_mm, 1)
                    for h in range(MLH):
                        k, o = h // 2, HD * (h % 2)
                        s_bank = (work[1], gemm_big[0])[h % 2]
                        pe.matmul(s_bank[0:TS, TS * k:TS * k + TS], pT[o:o + HD, T_K + k, TP:NT],
                                  pT[o:o + HD, T_Q + k, TP:NT], start=True, stop=True)
                    for h in range(MLH):
                        mm = pe.matmul(work[2][0:TS, TS * h:TS * h + TS], const(f"head{h}", MLH)[:, 0:TS],
                                       mx[:, TP:NT], start=True, stop=True)
                    mm.then_inc(samp_mm, 1)
                    pe.wait_ge(cols_out, 2)

                    def scores(n):
                        h, kt = steps[n]
                        k, o = h // 2, HD * (h % 2)
                        if kt == 0:
                            if h:
                                pe.wait_ge(e_ready, QT * h)
                            pe.matmul(work[0][:, 0:TP], const(f"head{h}", MLH), mx[:, 0:TP],
                                      start=True, stop=True).then_inc(mb_ready, 1)
                        if n == 0:
                            pe.wait_ge(samp_w, 1)
                        if n >= 2:
                            pe.wait_ge(w_ready, n - 1)
                        pe.matmul(work[1 + n % 2][:, 0:TP - P * kt], pT[o:o + HD, T_K + k, P * kt:P * kt + P],
                                  pT[o:o + HD, T_Q + k, P * kt:TP], start=True, stop=True).then_inc(s_ready, 1)

                    scores(0)
                    for n, (h, kt) in enumerate(steps):
                        k, o = h // 2, HD * (h % 2)
                        if n + 1 < len(steps):
                            scores(n + 1)
                        if kt == 0 and o == 0 and k:
                            pe.wait_ge(y_done, k)
                        pe.wait_ge(w_ready, n + 1)
                        w = W[:, n % 2, 0:TP - P * kt]
                        ends = dict(start=(kt == 0), stop=(kt == QT - 1))
                        pe.matmul(gemm_big[0][o:o + HD, P * kt:TP], tok[:, kt, TV + k, o:o + HD], w, **ends)
                        pe.matmul(gemm_big[1][o:o + HD, P * kt:TP], const("ones")[:, 0:HD], w, **ends)\
                            .then_inc(pv_done, 1)
                        if kt == QT - 1:
                            num, den = gemm_small[0][o:o + HD, 0:TS], gemm_small[1][o:o + HD, 0:TS]
                            if n == QT - 1:
                                pe.wait_ge(qw_ready, 1)
                            pe.matmul(num, toks[:, TV + k, o:o + HD], Ws[:, h, :], start=True, stop=False)
                            for b in range(NB):
                                pe.matmul(num[:, ST * b:ST * b + ST], C0T[:, h, b, :],
                                          qw[:, h, ST * b:ST * b + ST], start=False, stop=(b == NB - 1))
                            pe.matmul(den, const("ones", TS)[:, 0:HD], Ws[:, h, :], start=True, stop=False)
                            pe.matmul(den, const("ones", HD)[:, 0:HD], nq[:, h, :], start=False, stop=True)
                            if o:
                                if k:
                                    pe.wait_ge(em_out, 1)
                                pe.matmul(work[3][:, :], const(f"pair{k}", MLH), emrow[:, 0:TP],
                                          start=True, stop=True).then_inc(fin_mm, 1)
                                pe.wait_ge(e_ready, n + 1)
                                pe.wait_ge(em_out, k) if k else None
                                pe.wait_ge(dg_ready, n + 1)
                                pe.matmul(gemm_small[0][:, 64:64 + TS], const(f"pair{k}", MLH), emrow[:, TP:NT],
                                          start=True, stop=True).then_inc(fin_mm, 1)
                    pe.wait_ge(vw_ready, 1)
                    pe.wait_ge(em_out, 2)
                    for h in range(MLH):
                        k, o = h // 2, HD * (h % 2)
                        for kt in range(QT):
                            mm = pe.matmul(work[3][0:HD + 1, HD * h:HD * h + HD], vw[:, kt, h, :],
                                           tok[:, kt, TK + k, o:o + HD], start=(kt == 0), stop=(kt == QT - 1))
                    mm.then_inc(cp_mm, 1)
                    pe.wait_ge(w_ready, len(steps))
                    for h in range(MLH):
                        pe.wait_ge(km_ready, h + 1)
                        if h >= 2:
                            pe.wait_ge(cn_out, h - 1)
                        pe.matmul(work[1 + h % 2][0:HD + 1, :], vws[:, h, :],
                                  KM[:, h % 2, :, :].rearrange("s b d -> s (b d)"),
                                  start=True, stop=True).then_inc(cn_mm, 1)

                @block.scalar
                def _(act):
                    one = const("ones")[:, 0:1]
                    act.activation(sg[:, :, :], pT[:, T_O:T_O + 2, :], ACT.Sigmoid)
                    act.wait_ge(ml_chain, 2)
                    act.activation(lf[:, :], ax[:, :], ACT.Exp, scale=-1.0).then_inc(ml_act, 1)
                    act.wait_ge(ml_act, 1)
                    act.activation(lf[:, :], lf[:, :], ACT.Ln, bias=one[0:MLH]).then_inc(ml_act, 1)
                    act.wait_ge(ml_in, 16 * 12)
                    for h in range(MLH):
                        act.wait_ge(c0_mm, h + 1)
                        act.activation(C0T[:, h, :, :], work[h % 2][0:HD, :].rearrange("p (b e) -> p b e", b=NB),
                                       ACT.Copy).then_inc(c0_out, 1)
                    act.wait_ge(c0_mm, 5)
                    act.activation(n0T[:, :, :], work[2][0:HD, 0:NB * MLH].rearrange("p (h b) -> p h b", h=MLH),
                                   ACT.Copy).then_inc(c0_out, 1)
                    act.wait_ge(rows_ready, 1)
                    act.activation(wrow[:, :], wrow[:, :], ACT.Exp)
                    act.activation(emrow[:, :], emrow[:, :], ACT.Exp, scale=-1.0)
                    act.activation(wcrow[:, :], wcrow[:, :], ACT.Exp)
                    act.activation(decay[:, :], decay[:, :], ACT.Exp).then_inc(rows_ready, 1)
                    act.wait_ge(cols_mm, 1)
                    act.activation(cols[:, 0:QT, :, :],
                                   work[3][:, 0:32].rearrange("p (q j h) -> p q j h", q=QT, j=2), ACT.Copy)
                    act.activation(cols[0:TS, QT, :, :], work[3][0:TS, 32:40].rearrange("p (j h) -> p j h", j=2),
                                   ACT.Copy).then_inc(cols_out, 1)
                    act.wait_ge(cols_mm, 2)
                    act.activation(wcb[:, :, :], work[0][:, 0:64].rearrange("p (k t) -> p k t", k=2), ACT.Copy)
                    act.activation(db[:, :, :], work[0][0:HD + 1, 64:64 + NB * MLH]
                                   .rearrange("p (h b) -> p h b", h=MLH), ACT.Copy).then_inc(cols_out, 1)
                    act.wait_ge(samp_e, 1)
                    for h in range(MLH):
                        ins = act.activation(Es[:, h, :], dgs[:, h, :], ACT.Exp, scale=-1.0,
                                             bias=cols[0:TS, QT, 0, h:h + 1])
                    ins.then_inc(samp_e, 1)
                    for n, (h, kt) in enumerate(steps):
                        act.wait_ge(dg_ready, n + 1)
                        if n >= 2:
                            act.wait_ge(w_ready, n - 1)
                        a = cols[:, kt, 0, h:h + 1]
                        ins = act.activation(E[:, n % 2, 0:P], dg[:, n % 2, :], ACT.Exp, bias=a, scale=-1.0)
                        if kt < QT - 1:
                            ins = act.activation(E[:, n % 2, P:TP - P * kt], work[0][:, P * kt + P:TP], ACT.Exp,
                                                 bias=a, scale=-1.0)
                        ins.then_inc(e_ready, 1)
                        if kt == QT - 1 and h % 2:
                            k = h // 2
                            act.wait_ge(fin_mm, 2 * k + 2)
                            if k:
                                act.wait_ge(y_done, k)
                            act.activation(em[:, 0:TP], work[3][:, :], ACT.Copy)
                            act.activation(em[:, TP:NT], gemm_small[0][:, 64:64 + TS], ACT.Copy).then_inc(em_out, 1)

                @block.vector
                def _(dve):
                    c = Chain(dve, ml_chain)
                    def steps_of(x):
                        return x[:, TP:NT].rearrange("p (b t) -> p b t", b=NB)

                    dve.wait_ge(ml_in, 16 * 12)
                    c.step(dve.tensor_scalar(fx[:, :], pT[32:36, T_IF, :], mlb[:, 1:2], None, ALU.add))
                    c.step(dve.scalar_tensor_tensor(out=ax[:, :], in0=fx[:, :], scalar=-1.0, in1=fx[:, :],
                                                    op0=ALU.mult, op1=ALU.max))
                    c.step(dve.memset(ones4[:, :], 1.0))
                    dve.wait_ge(ml_act, 2)
                    c.step(dve.scalar_tensor_tensor(out=lf[:, :], in0=fx[:, :], scalar=0.0, in1=lf[:, :],
                                                    op0=ALU.min, op1=ALU.subtract))
                    c.step(dve.tensor_tensor_scan(bsum[:, 0:TP], ones4[:, 0:TP], lf[:, 0:TP], 0.0,
                                                  ALU.mult, ALU.add))
                    bs, ls, as_, ms = steps_of(bsum), steps_of(lf), steps_of(av), steps_of(mx)
                    c.step(dve.tensor_copy(bs[:, :, 0], ls[:, :, 0]))
                    for t in range(1, ST):
                        c.step(dve.tensor_tensor(bs[:, :, t], bs[:, :, t - 1], ls[:, :, t], ALU.add))
                    c.step(dve.scalar_tensor_tensor(out=av[:, :], in0=pT[0:MLH, T_IF, :], scalar=mlb[:, 0:1],
                                                    in1=bsum[:, :], op0=ALU.add, op1=ALU.subtract))
                    c.step(dve.tensor_tensor_scan(mx[:, 0:TP], av[:, 0:TP], av[:, 0:TP], 0.0, ALU.max, ALU.max))
                    for t in range(ST):
                        c.step(dve.tensor_tensor(ms[:, :, t], as_[:, :, t], m0[:, :] if t == 0 else ms[:, :, t - 1],
                                                 ALU.max))
                    dve.tensor_scalar(wrow[:, 0:TP], av[:, 0:TP], mx[:, TP - 1:TP], None, ALU.subtract)
                    for t in range(ST):
                        dve.tensor_tensor(steps_of(wrow)[:, :, t], as_[:, :, t], ms[:, :, ST - 1], ALU.subtract)
                        dve.tensor_tensor(wcrow[:, :].rearrange("p (b t) -> p b t", b=NB)[:, :, t], m0[:, :],
                                          ms[:, :, t], ALU.subtract)
                    dve.tensor_tensor(decay[:, :], m0[:, :], ms[:, :, ST - 1], ALU.subtract)
                    c.step(dve.tensor_tensor(emrow[:, :], bsum[:, :], mx[:, :], ALU.add))
                    dve.tensor_copy(mend[:, 0:1], emrow[:, TP - 1:TP])
                    dve.tensor_copy(mend[:, 1:9], steps_of(emrow)[:, :, ST - 1]).then_inc(rows_ready, 1)
                    dve.wait_ge(cols_out, 2)
                    for h in range(MLH):
                        k, o = h // 2, HD * (h % 2)
                        ins = dve.tensor_tensor(qw[:, h, :], pT[o:o + HD, T_Q + k, TP:NT], wcb[o:o + HD, k, :],
                                                ALU.mult)
                    c.step(ins)
                    dve.wait_ge(c0_out, 5)
                    for h in range(MLH):
                        ins = dve.tensor_tensor(nq[:, h, :].rearrange("p (b t) -> p b t", b=NB),
                                                qw[:, h, :].rearrange("p (b t) -> p b t", b=NB),
                                                n0T[:, h, :].unsqueeze(2).to_broadcast([HD, NB, ST]), ALU.mult)
                    ins.then_inc(qw_ready, 1)
                    dve.wait_ge(samp_mm, 1)
                    for h in range(MLH):
                        ins = dve.tensor_tensor(dgs[:, h, :], work[2][0:TS, TS * h:TS * h + TS],
                                                const("sblocked", TS), ALU.add)
                    ins.then_inc(samp_e, 1)
                    dve.wait_ge(samp_e, 2)
                    for h in range(MLH):
                        ins = dve.scalar_tensor_tensor(
                            out=Ws[:, h, :], in0=(work[1], gemm_big[0])[h % 2][0:TS, TS * (h // 2):TS * (h // 2) + TS],
                            scalar=HD ** -0.5, in1=Es[:, h, :], op0=ALU.mult, op1=ALU.mult)
                    ins.then_inc(samp_w, 1)

                    def finish(k):
                        dve.wait_ge(em_out, k + 1)
                        dve.wait_ge(pv_done, 2 * QT * (k + 1))
                        for cols_, big, small in ((slice(0, TP), gemm_big[1], None), (slice(TP, NT), None, gemm_small[1])):
                            den = big[:, :] if big is not None else small[:, 0:TS]
                            c.step(dve.scalar_tensor_tensor(out=dd[:, cols_], in0=den, scalar=-1.0, in1=em[:, cols_],
                                                            op0=ALU.mult, op1=ALU.max))
                            c.step(dve.tensor_tensor(dd[:, cols_], den, dd[:, cols_], ALU.max))
                        c.step(dve.reciprocal(dd[:, :], dd[:, :]))
                        c.step(dve.tensor_tensor(dd[:, :], dd[:, :], sg[:, k, :], ALU.mult))
                        dve.tensor_tensor(yT[:, k, 0:TP], gemm_big[0][:, :], dd[:, 0:TP], ALU.mult)
                        dve.tensor_tensor(yT[:, k, TP:NT], gemm_small[0][:, 0:TS], dd[:, TP:NT], ALU.mult)\
                            .then_inc(y_done, 1)

                    for n, (h, kt) in enumerate(steps):
                        dve.wait_ge(mb_ready, h + 1)
                        if n >= 2:
                            dve.wait_ge(e_ready, n - 1)
                        dve.tensor_tensor(dg[:, n % 2, :], work[0][:, P * kt:P * kt + P], const("blocked"), ALU.add)\
                            .then_inc(dg_ready, 1)
                        dve.wait_ge(e_ready, n + 1)
                        dve.wait_ge(s_ready, n + 1)
                        if n >= 2:
                            dve.wait_ge(pv_done, n - 1)
                        w = TP - P * kt
                        dve.scalar_tensor_tensor(out=W[:, n % 2, 0:w], in0=work[1 + n % 2][:, 0:w],
                                                 scalar=HD ** -0.5, in1=E[:, n % 2, 0:w],
                                                 op0=ALU.mult, op1=ALU.mult).then_inc(w_ready, 1)
                        if kt == QT - 1 and h % 2:
                            finish(h // 2)
                    for h in range(MLH):
                        k, o = h // 2, HD * (h % 2)
                        for kt in range(QT):
                            dve.tensor_scalar(vw[:, kt, h, 0:HD], tok[:, kt, TV + k, o:o + HD],
                                              cols[:, kt, 1, h:h + 1], None, ALU.mult)
                        dve.tensor_scalar(vws[:, h, 0:HD], toks[:, TV + k, o:o + HD], cols[0:TS, QT, 1, h:h + 1],
                                          None, ALU.mult)
                    dve.tensor_copy(vw[:, :, :, HD], cols[:, 0:QT, 1, :])
                    dve.tensor_copy(vws[:, :, HD], cols[0:TS, QT, 1, :]).then_inc(vw_ready, 1)
                    for h in range(MLH):
                        k, o = h // 2, HD * (h % 2)
                        if h >= 2:
                            dve.wait_ge(cn_mm, h - 1)
                        dve.tensor_tensor(KM[:, h % 2, :, :],
                                          toks[:, TK + k, o:o + HD].unsqueeze(1).to_broadcast([TS, NB, HD]),
                                          const("inb", TS).unsqueeze(2).to_broadcast([TS, NB, HD]), ALU.mult)\
                            .then_inc(km_ready, 1)
                        c.step(dve.tensor_tensor(Cn[:, h, :, :], Cn[:, h, :, :],
                                                 db[:, h, :].unsqueeze(2).to_broadcast([HD + 1, NB, HD]), ALU.mult))
                        dve.wait_ge(cn_mm, h + 1)
                        dve.scalar_tensor_tensor(out=Cn[:, h, :, :],
                                                 in0=work[1 + h % 2][0:HD + 1, :].rearrange("p (b d) -> p b d", b=NB),
                                                 scalar=HD ** -0.5, in1=Cn[:, h, :, :], op0=ALU.mult, op1=ALU.add)\
                            .then_inc(cn_out, 1)
                    dve.wait_ge(cp_mm, 1)
                    dve.tensor_scalar(Cp[:, :, :], work[3][0:HD + 1, 0:256].rearrange("p (h d) -> p h d", h=MLH),
                                      HD ** -0.5, None, ALU.mult).then_inc(cp_out, 1)
        sem.end_part()

        def turn_cmp(pe, raw, dst):
            for j in range(4):
                mm = pe.transpose(dst[:, P * j:P * j + P], raw[:, j, :, :].rearrange("p a d -> p (a d)"), ident)
            return mm

        def hidden(pe, w1, ZT, nblk, dst):
            for kv in range(2):
                z = ZT[:, 2 * kv:2 * kv + 2, :].rearrange("p g (n c) -> p g n c", c=16)
                for c in range(16):
                    mm = pe.matmul(dst[:, 2 * nblk * kv:2 * nblk * (kv + 1)], w1[:, kv, c, :],
                                   z[:, :, :, c], start=(c == 0), stop=(c == 15))
            return mm

        def load_phi(sp, w1, w2, sem_):
            sp.dma_start(w1[:, :, :, :], I["phi_w1"][0].rearrange("v (c p) h -> p v c h", p=P)).then_inc(sem_, 16)
            sp.dma_start(w2[:, 0, 0:HD], I["phi_w2"][0, 0]).then_inc(sem_, 16)
            sp.dma_start(w2[:, 1, HD:P], I["phi_w2"][0, 0]).then_inc(sem_, 16)
            sp.dma_start(w2[:, 2, 0:HD], I["phi_w2"][0, 1]).then_inc(sem_, 16)

        kcp = mixed.enter_context(nc.sbuf_tensor("kcp", [P, PCB], F32))
        vexp = mixed.enter_context(nc.sbuf_tensor("vexp", [P, REP, G, HD], F32))
        with ExitStack() as c5:
            def t5(name, shape):
                return c5.enter_context(nc.sbuf_tensor(name, shape, F32))

            w1 = t5("w1p", [P, 2, 16, P])
            w2 = t5("w2p", [P, 3, P])
            raw = t5("rawp", [P, 2, 4, 2, HD])
            ZT = t5("ZTp", [P, 4, 2 * P])
            pos = t5("pos", [32, P])
            posT = t5("posT", [P, 32])
            hid = t5("hid", [P, 2, G, PCB])
            hrep = t5("hrep", [P, G, REP, PCB])
            vrep = t5("vrep", [P, HD])
            gate_dma, qb_zero, scaled = sem("gate_dma"), sem("QB_zero"), sem("q_scaled")
            phi_here, w2_zero, raw_here = sem("phi_here"), sem("w2_zero"), sem("rawp_here")
            z_mm, z_out, pos_mm, hb_ready, h_mm, h_ready, hrep_ready, kv_mm, vrep_ready = (
                sem(f"pcmp_{n}") for n in ("z_mm", "z_out", "pos_mm", "hb", "h_mm", "h", "hrep", "kv_mm", "vrep"))

            with nc.Block() as block:
                @block.sync
                def _(sp):
                    sp.wait_ge(out_dma, stores[0])
                    for j in range(2):
                        for a in range(2):
                            sp.dma_start(raw[:, j, :, a, :],
                                         O["kv_p"][0, 0, 256 * j + a:256 * j + 256:2, 0:2].rearrange(
                                             "p c g d -> p (c g) d")).then_inc(raw_here, 16)
                    sp.dma_start(pos[:, :], I["cmp_pos"][0].rearrange("v (c a) d -> (v c) (a d)", a=2))\
                        .then_inc(raw_here, 16)
                    sp.wait_ge(w2_zero, 1)
                    load_phi(sp, w1, w2, phi_here)

                    sp.dma_start(gate_dram, gate_s[:, :]).then_inc(gate_dma, 16)
                    sp.wait_ge(gate_dma, 16)
                    for h in range(8):
                        for br in range(3):
                            sp.dma_start(gq[ST * h:ST * h + ST, :, br],
                                         gate_dram.rearrange("(b t) c -> c t b", b=NB)[8 * br + h],
                                         allow_slow_non_contiguous=True).then_inc(gate_dma, 16)
                    sp.wait_ge(gate_dma, 16 * 25)

                @block.gpsimd
                def _(pool):
                    pool.memset(QB[:, :, :], 0.0).then_inc(qb_zero, 1)
                    pool.memset(w2[:, :, :], 0.0).then_inc(w2_zero, 1)

                @block.tensor
                def _(pe):
                    pe.wait_ge(raw_here, 80)
                    for j in range(2):
                        turn_cmp(pe, raw[:, j, :, :, :], work[j]).then_inc(z_mm, 1)
                    pe.transpose(work[2][:, 0:32], pos[:, :], ident[0:32, 0:32]).then_inc(z_mm, 1)
                    pe.wait_ge(phi_here, 64)
                    pe.wait_ge(z_out, 3)
                    for kv in range(2):
                        for c in range(16):
                            mm = pe.matmul(work[3][:, kv:kv + 1], w1[:, kv, c, :], posT[:, 16 * kv + c:16 * kv + c + 1],
                                           start=(c == 0), stop=(c == 15))
                    mm.then_inc(pos_mm, 1)
                    hidden(pe, w1, ZT, PCB, work[0]).then_inc(h_mm, 1)
                    pe.wait_ge(h_ready, 1)
                    for g in range(G):
                        mm = pe.matmul(work[1][:, 0:PCB], w2[:, g, :], hid[:, 0, g, :], start=(g == 0), stop=(g == 1))
                    mm.then_inc(kv_mm, 1)
                    pe.wait_ge(hrep_ready, 1)
                    for g in range(G):
                        mm = pe.matmul(work[2][HD * g:HD * g + HD, 0:HD], hrep[:, g, :, :].rearrange("p r n -> p (r n)"),
                                       w2[:, 2, 0:HD], start=True, stop=True)
                    mm.then_inc(kv_mm, 1)

                @block.scalar
                def _(act):
                    act.wait_ge(h_mm, 1)
                    act.wait_ge(hb_ready, 1)
                    for kv in range(2):
                        ins = act.activation(hid[:, kv, :, :].rearrange("p g n -> p (g n)"),
                                             work[0][:, 2 * PCB * kv:2 * PCB * (kv + 1)], ACT.Gelu_apprx_tanh,
                                             bias=hb[:, kv:kv + 1])
                    ins.then_inc(h_ready, 1)

                @block.vector
                def _(dve):
                    for j in range(2):
                        dve.wait_ge(z_mm, j + 1)
                        dve.tensor_copy(ZT[:, :, P * j:P * j + P], work[j][:, :].rearrange("p (k c) -> p k c", k=4))\
                            .then_inc(z_out, 1)
                    dve.wait_ge(z_mm, 3)
                    dve.tensor_copy(posT[:, :], work[2][:, 0:32]).then_inc(z_out, 1)
                    dve.tensor_scalar(pT[:, T_NQ:T_NQ + 4, :], pT[:, T_NQ:T_NQ + 4, :], HD ** -0.5, None, ALU.mult)\
                        .then_inc(scaled, 1)
                    dve.wait_ge(qb_zero, 1)
                    dve.wait_ge(scaled, 1)
                    for g in range(G):
                        rows = slice(HD * g, HD * g + HD)
                        for r in range(REP):
                            at = 16 * g + ST * r
                            dve.tensor_copy(QB[rows, :, at:at + ST],
                                            pT[rows, T_NQ + r, TP:NT].rearrange("p (b t) -> p b t", b=NB))
                    dve.tensor_copy(ksn[:, :], pT[:, T_KS, TP:NT])
                    dve.tensor_copy(kwn[:, :], pT[:, T_KW, TP:NT])
                    dve.tensor_copy(vnew[:, 0, :], toks[:, TOKKV + 3, :])
                    dve.tensor_copy(vnew[:, 1, :], toks[:, TOKKV + 5, :])
                    dve.wait_ge(pos_mm, 1)
                    dve.tensor_tensor(hb[:, :], work[3][:, 0:2], vecT[:, V_PB:V_PB + 2], ALU.add).then_inc(hb_ready, 1)
                    dve.wait_ge(h_ready, 1)
                    dve.tensor_copy(hrep[:, :, :, :], hid[:, 1, :, :].unsqueeze(2).to_broadcast([P, G, REP, PCB]))\
                        .then_inc(hrep_ready, 1)
                    dve.wait_ge(kv_mm, 1)
                    dve.tensor_copy(kcp[:, :], work[1][:, 0:PCB])
                    dve.wait_ge(kv_mm, 2)
                    dve.tensor_copy(vrep[:, :], work[2][:, 0:HD]).then_inc(vrep_ready, 1)
                    dve.wait_ge(vrep_ready, 1)
                    dve.tensor_tensor(vexp[:, :, :, :],
                                      vrep[:, :].unsqueeze(1).to_broadcast([P, 8, HD]).rearrange(
                                          "p (r g) d -> p r g d", r=REP),
                                      const("vplace").rearrange("p (r g) -> p r g", r=REP).unsqueeze(3)
                                      .to_broadcast([P, REP, G, HD]), ALU.mult)

        with ExitStack() as c6:
            def t6(name, shape):
                return c6.enter_context(nc.sbuf_tensor(name, shape, F32))

            tab = t6("tab", [P, 8, TP])
            qz = ring[:, :, :, :].rearrange("p u k c -> p (u k c)").rearrange("p (g r t) -> p g r t", g=G, r=REP)
            qz_zero, qz_ready = sem("qz_zero"), sem("qz_ready")
            sc = t6("sc", [P, QT, G, REP, PCB])
            mxc, smc = t6("mxc", [P, QT * 8]), t6("smc", [P, QT * 8])
            pcT = t6("pcT", [P, TP])
            Pb = t6("Pb", [P, 4, TP])
            PT = t6("PT", [P, 2, TP])
            dgm = t6("dgm", [P, 2, P])
            stat = t6("stat", [P, 4, 4])
            tab_here, cs_mm, nchain, c_exp, pc_mm, pc_out = (
                sem(f"nsa_{n}") for n in ("tab", "cs_mm", "chain", "c_exp", "pc_mm", "pc_out"))
            s_mm, s_max, p_exp, d_ready, pt_mm, pt_out, pv_mm, y_out, pc_ready = (
                sem(f"nsa_{n}") for n in ("s_mm", "s_max", "p_exp", "d", "pt_mm", "pt_out", "pv", "y", "pc"))
            steps6 = [(r, br, qt, g) for r in range(REP) for br in range(2) for qt in range(QT) for g in range(G)]
            PER_R = 2 * QT * G

            with nc.Block() as block:
                @block.sync
                def _(sp):
                    sp.dma_start(tab[:, :, :], K["prompt"]).then_inc(tab_here, 16)

                @block.gpsimd
                def _(pool):
                    pool.memset(qz[HD:P, 0, :, :], 0.0)
                    pool.memset(qz[0:HD, 1, :, :], 0.0).then_inc(qz_zero, 1)

                @block.tensor
                def _(pe):
                    pe.wait_ge(qz_zero, 1)
                    pe.wait_ge(qz_ready, 1)
                    for qt in range(QT):
                        for r in range(REP):
                            for g in range(G):
                                at = PCB * (REP * qt + r)
                                mm = pe.matmul(work[g][:, at:at + PCB],
                                               qz[:, g, r, P * qt:P * qt + P], kcp[:, :], start=True, stop=True)
                                if (qt, r) == (QT - 1, REP - 1):
                                    mm.then_inc(cs_mm, 1)
                    pe.wait_ge(pc_ready, 1)
                    for qt in range(QT):
                        mm = pe.transpose(work[2][:, P * qt:P * qt + P],
                                          sc[:, qt, :, :, :].rearrange("p g r n -> p (g r n)"), ident)
                    mm.then_inc(pc_mm, 1)
                    pe.wait_ge(pc_out, 1)

                    def scores(n):
                        r, br, qt, g = steps6[n]
                        if n >= 4:
                            pe.wait_ge(s_max, n - 3)
                        pe.matmul(work[n % 4][:, 0:P * qt + P], qz[:, g, r, P * qt:P * qt + P],
                                  pT[:, (T_KS, T_KW)[br], 0:P * qt + P],
                                  start=True, stop=True).then_inc(s_mm, 1)

                    def values(n):
                        r, br, qt, g = steps6[n]
                        y = gemm_big[r % 2]
                        if n % PER_R == 0:
                            if r >= 2:
                                pe.wait_ge(y_out, r - 1)
                            pe.matmul(y[:, :], vexp[:, r, :, :].rearrange("p g d -> p (g d)"), pcT[:, :],
                                      start=True, stop=False, skip_group_check=True)
                        pe.wait_ge(pt_out, n + 1)
                        for kt in range(qt + 1):
                            mm = pe.matmul(y[HD * g:HD * g + HD, P * qt:P * qt + P],
                                           tok[:, kt, TOKKV + 3 + 2 * br, HD * g:HD * g + HD],
                                           PT[:, n % 2, P * kt:P * kt + P], start=False,
                                           stop=(n % PER_R == PER_R - 1 and kt == qt), skip_group_check=True)
                        mm.then_inc(pv_mm, 1)

                    scores(0)
                    scores(1)
                    for n, (r, br, qt, g) in enumerate(steps6):
                        if n + 2 < len(steps6):
                            scores(n + 2)
                        pe.wait_ge(d_ready, n + 1)
                        pe.wait_ge(p_exp, n + 1)
                        if n >= 2:
                            pe.wait_ge(pt_out, n - 1)
                        for kt in range(qt + 1):
                            mm = pe.matmul(gemm_small[n % 2][:, P * kt:P * kt + P], Pb[:, n % 4, P * kt:P * kt + P],
                                           dgm[:, n % 2, :], start=True, stop=True)
                        mm.then_inc(pt_mm, 1)
                        if n:
                            values(n - 1)
                    values(len(steps6) - 1)

                @block.scalar
                def _(act):
                    act.wait_ge(c_exp, 1)
                    act.activation(sc[:, :, :, :, :], sc[:, :, :, :, :], ACT.Exp).then_inc(c_exp, 1)
                    for n, (r, br, qt, g) in enumerate(steps6):
                        act.wait_ge(s_max, n + 1)
                        L = P * qt + P
                        act.activation(Pb[:, n % 4, 0:L], Pb[:, n % 4, 0:L], ACT.Exp, bias=stat[:, n % 4, 1:2],
                                       accum_out=stat[:, n % 4, 2:3]).then_inc(p_exp, 1)
                        act.wait_ge(pt_mm, n + 1)
                        if n >= 2:
                            act.wait_ge(pv_mm, n - 1)
                        act.activation(PT[:, n % 2, 0:L], gemm_small[n % 2][:, 0:L], ACT.Copy).then_inc(pt_out, 1)
                        if n % PER_R == 0 and n:
                            act.wait_ge(pv_mm, n)
                            act.activation(yT[:, 4 + r - 1, 0:TP], gemm_big[(r - 1) % 2][:, :], ACT.Copy)\
                                .then_inc(y_out, 1)
                    act.wait_ge(pv_mm, len(steps6))
                    act.activation(yT[:, 7, 0:TP], gemm_big[1][:, :], ACT.Copy).then_inc(y_out, 1)

                @block.vector
                def _(dve):
                    c = Chain(dve, nchain)
                    for g in range(G):
                        rows = slice(HD * g, HD * g + HD)
                        ins = dve.tensor_copy(qz[rows, g, :, :], pT[rows, T_NQ:T_NQ + 4, 0:TP])
                    ins.then_inc(qz_ready, 1)
                    dve.wait_ge(cs_mm, 2)
                    tabc = const("pcmp").rearrange("p (q g r n) -> p q g r n", q=QT, g=G, r=REP)
                    for g in range(G):
                        ins = dve.tensor_tensor(sc[:, :, g, :, :],
                                                work[g][:, 0:256].rearrange("p (q r n) -> p q r n", q=QT, r=REP),
                                                tabc[:, :, g, :, :], ALU.add)
                    c.step(ins)
                    flat = sc[:, :, :, :, :].rearrange("p q g r n -> p (q g r) n")
                    c.step(dve.tensor_reduce(mxc[:, :], flat, AX, ALU.max))
                    dve.tensor_tensor(flat, flat, mxc[:, :].unsqueeze(2).to_broadcast([P, QT * 8, PCB]),
                                      ALU.subtract).then_inc(c_exp, 1)
                    dve.wait_ge(c_exp, 2)
                    c.step(dve.tensor_reduce(smc[:, :], flat, AX, ALU.add))
                    c.step(dve.reciprocal(smc[:, :], smc[:, :]))
                    c.step(dve.tensor_tensor(smc[:, :].rearrange("p (q h) -> p q h", q=QT),
                                             smc[:, :].rearrange("p (q h) -> p q h", q=QT), gate_p[:, :, 0:8], ALU.mult))
                    c.step(dve.tensor_tensor(flat, flat, smc[:, :].unsqueeze(2).to_broadcast([P, QT * 8, PCB]),
                                             ALU.mult))
                    valid = const("pvalid").rearrange("p (q n) -> p q n", q=QT)
                    for qt in range(QT):
                        ins = dve.tensor_tensor(sc[:, qt, :, :, :].rearrange("p g r n -> p (g r) n"),
                                                sc[:, qt, :, :, :].rearrange("p g r n -> p (g r) n"),
                                                valid[:, qt, :].unsqueeze(1).to_broadcast([P, 8, PCB]), ALU.mult)
                    ins.then_inc(pc_ready, 1)
                    dve.wait_ge(pc_mm, 1)
                    dve.tensor_copy(pcT[:, :], work[2][:, :]).then_inc(pc_out, 1)
                    dve.wait_ge(tab_here, 16)

                    def top(n):
                        r, br, qt, g = steps6[n]
                        L = P * qt + P
                        dve.wait_ge(s_mm, n + 1)
                        if n >= 4:
                            dve.wait_ge(pt_mm, n - 3)
                        c.step(dve.tensor_tensor_reduce(Pb[:, n % 4, 0:L], work[n % 4][:, 0:L],
                                                        tab[:, REP * g + r, TP - L:TP], 1.0, -3e38, ALU.add, ALU.max,
                                                        stat[:, n % 4, 0:1]))
                        dve.tensor_scalar(stat[:, n % 4, 1:2], stat[:, n % 4, 0:1], -1.0, None, ALU.mult)\
                            .then_inc(s_max, 1)

                    top(0)
                    for n, (r, br, qt, g) in enumerate(steps6):
                        if n + 1 < len(steps6):
                            top(n + 1)
                        dve.wait_ge(p_exp, n + 1)
                        c.step(dve.reciprocal(stat[:, n % 4, 3:4], stat[:, n % 4, 2:3]))
                        if n >= 2:
                            dve.wait_ge(pt_mm, n - 1)
                        h = 8 * (br + 1) + REP * g + r
                        dve.tensor_scalar(dgm[:, n % 2, :], ident, stat[:, n % 4, 3:4], gate_p[:, qt, h:h + 1],
                                          ALU.mult, ALU.mult).then_inc(d_ready, 1)

        mixed.close()

        with ExitStack() as c7:
            def t7(name, shape, dt=F32):
                return c7.enter_context(nc.sbuf_tensor(name, shape, dt))

            R = 32
            w1 = t7("w1s", [P, 2, 16, P])
            w2 = t7("w2s", [P, 3, P])
            both = t7("both", [2 * R, PAST])
            ss, past = both[0:R, :], both[R:2 * R, :]
            sw = t7("sw", [R, WIN])
            sn = t7("sn", [R, 2, TS])
            rawc = t7("rawc", [P, CT // 2, 2, 2, P])
            kv = t7("kv", [P, CT, 2, 2, P])
            rw = t7("rw", [P, 4, 2, P])
            ZT = t7("ZTs", [P, 4, CT * P])
            hid = t7("hids", [P, 2, G, NCB])
            kc = t7("kcs", [P, NCB])
            vc = t7("vcs", [NCB, P])
            Qb = t7("Qb", [P, R])
            KTb = t7("KTb", [P, 2, 512])
            PTs = t7("PTs", [P, 2, 512])
            pn = t7("pn", [R, NCB])
            sel = t7("sel", [R, 4, 65])
            top8 = t7("top8", [R, 2, 8])
            bnb = stdt[0:R, NB * NPB:NB * NPB + TS + 1]
            st = t7("st", [R, 16])
            Os = t7("Os", [R, P])
            rawc2 = ring[:, :, :, :].rearrange("p u k n -> p (u k n)").rearrange("p (j a c n) -> p j a c n", a=2, c=2, n=P)
            pages = stdt[0:1, 0:NB * NPB].bitcast(I32)

            pg_here, c7_const, s_w2z, s_w2 = sem("pages_here"), sem("past_here"), sem("w2s_zero"), sem("phis_here")
            rawc_here = [sem(f"rawc_here{j}") for j in range(CT)]
            kv_here = [sem(f"kv_here{j}") for j in range(CT // 2)]
            rw_here = sem("rw_here")
            z_mm, h_mm, h_ready, kc_mm, kc_out = (sem(f"s_{n}") for n in ("z_mm", "h_mm", "h", "kc_mm", "kc_out"))
            z_out = [sem(f"s_z_out{n}") for n in ("a", "v")]
            qb_ready, cs_mm, pn_exp, pn_sub, pn_ready, imp_mm = (
                sem(f"s_{n}") for n in ("qb", "cs_mm", "pn_exp", "pn_sub", "pn", "imp_mm"))
            kt_mm, kt_out, sl_mm, sl_out, new_mm, new_out = (
                sem(f"s_{n}") for n in ("kt_mm", "kt_out", "sl_mm", "sl_out", "new_mm", "new_out"))
            m_ready, e_ready, pt_mm, pt_out, o_mm, o_ready, ot_mm, y_put, chain7 = (
                sem(f"s_{n}") for n in ("m", "e", "pt_mm", "pt_out", "o_mm", "o", "ot_mm", "y", "chain"))
            NKT = CT // 2 + 1
            NPT_ = 10
            CH = 31

            def settled(dve):
                dve.memset(bnb[:, TS:TS + 1], 0.0)

            def settled_pe(pe, n=0, sem_=None):
                ins = pe.transpose(work[3][:, 384:512], ident, ident)
                if n:
                    ins.then_inc(sem_, n)

            def raw_slot(j):
                return rawc[:, j, :, :, :] if j < CT // 2 else rawc2[:, j - CT // 2, :, :, :]

            COPIER = [0, 0, 0, 0, 1, 1, 1, 1] + [0, 1] * 4

            def copied(eng, b, j):
                who = COPIER[j]
                eng.wait_ge(z_out[who], b * COPIER.count(who) + (COPIER[:j].count(who) + 1))

            def copy_z(copy, eng, b, tiles, who):
                for j in tiles:
                    if COPIER[j] != who:
                        continue
                    eng.wait_ge(z_mm, b * CT + (j + 1))
                    for g in range(G):
                        for a in range(2):
                            ins = copy(ZT[HD * a:HD * a + HD, g::2, P * j:P * j + P],
                                       work[j % 2][HD * g:HD * g + HD, 256 * a:256 * a + 256].rearrange(
                                           "p (c n) -> p c n", c=2))
                    ins.then_inc(z_out[who], 1)

            with nc.Block() as block:
                @block.sync
                def _(sp):
                    sp.dma_start(pages[:, :], I["page_table"].rearrange("b n -> (b n)").rearrange("(a n) -> a n", a=1))\
                        .then_inc(pg_here, 16)
                    sp.dma_start(past[:, :], K["past"]).then_inc(c7_const, 16)
                    sp.wait_ge(s_w2z, 1)
                    load_phi(sp, w1, w2, s_w2)
                    sp.wait_ge(pg_here, 16)
                    cache = I["cache_nsa_kv"][0].rearrange("n (p a) c g d -> n p a c (g d)", a=2)

                    def page_numbers(b, j):
                        _, page = nc.values_load_multi_w_load_instructions(
                            pages[0:1, bass.ds(b * NPB + 2 * j, 8)], engines=[mybir.EngineType.SP],
                            min_val=0, max_val=319)
                        return page

                    def page_half(dst, page, half, kinds):
                        return sp.dma_start(dst[64 * half:64 * half + 64, :, :, :].rearrange("p a c n -> p a (c n)"),
                                            cache[bass.ds(page, 1), :, :, kinds, :].rearrange(
                                                "n p a c m -> p (n a) (c m)"))

                    def load_raw(b, tiles, turned):
                        for j in tiles:
                            if j % 4 == 0:
                                page = page_numbers(b, j)
                            if turned is not None:
                                sp.wait_ge(z_mm, turned + (j + 1))
                            for half in range(2):
                                page_half(raw_slot(j), page[2 * (j % 4) + half], half, slice(0, 2)).then_inc(rawc_here[j], 16)

                    def load_kv(b):
                        sp.wait_ge(o_mm, b * NPT_ + 2)
                        sp.dma_start(rw[:, :, :, :], I["state_nsa_win"][0, bass.ds(b, 1)].rearrange(
                            "b (c p) v g d -> p (b c) v (g d)", p=P)).then_inc(rw_here, 16)
                        for j in range(CT):
                            if j % 4 == 0:
                                page = page_numbers(b, j)
                            sp.wait_ge(o_mm, b * NPT_ + (3 + j // 2))
                            for half in range(2):
                                page_half(kv[:, j, :, :, :], page[2 * (j % 4) + half], half, slice(2, 4)).then_inc(kv_here[j // 2], 16)

                    early, late = range(CT // 2), range(CT // 2, CT)
                    load_raw(0, range(CT), None)
                    load_raw(1, early, 0)
                    with sp.Fori(0, NB - 2) as b:
                        load_kv(b)
                        load_raw(b + 1, late, b * CT)
                        load_raw(b + 2, early, b * CT + CT)
                    load_kv(NB - 2)
                    load_raw(NB - 1, late, (NB - 2) * CT)
                    load_kv(NB - 1)

                @block.gpsimd
                def _(pool):
                    pool.memset(w2[:, :, :], 0.0).then_inc(s_w2z, 1)

                @block.tensor
                def _(pe):
                    pe.wait_ge(s_w2, 64)

                    def turn_raw(b):
                        for j in range(CT):
                            pe.wait_ge(rawc_here[j], b * 32 + 32)
                            if j >= 2:
                                copied(pe, b, j - 2)
                            for i in range(4):
                                mm = pe.transpose(work[j % 2][:, P * i:P * i + P], raw_slot(j)[:, i // 2, i % 2, :], ident)
                            mm.then_inc(z_mm, 1)

                    settled_pe(pe, NPT_, o_mm)
                    turn_raw(0)

                    def batch(b, more):
                        for who in range(2):
                            pe.wait_ge(z_out[who], b * (CT // 2) + CT // 2)
                        hidden(pe, w1, ZT, NCB, work[2]).then_inc(h_mm, 1)
                        pe.wait_ge(qb_ready, b + 1)

                        def keys(n):
                            if n < CT // 2:
                                pe.wait_ge(kv_here[n], b * 64 + 64)
                            else:
                                pe.wait_ge(rw_here, b * 16 + 16)
                            if n >= 2:
                                pe.wait_ge(kt_out, b * NKT + (n - 1))
                            for i in range(4):
                                src = kv[:, 2 * n + i // 2, i % 2, 0, :] if n < CT // 2 else rw[:, i, 0, :]
                                mm = pe.transpose(gemm_small[n % 2][:, P * i:P * i + P], src, ident)
                            mm.then_inc(kt_mm, 1)

                        def scores(n):
                            pe.wait_ge(kt_out, b * NKT + (n + 1))
                            if n >= 2:
                                pe.wait_ge(sl_out, b * NKT + (n - 1))
                            pe.matmul(gemm_big[n % 2][0:R, :], Qb[:, :], KTb[:, n % 2, :],
                                      start=True, stop=True).then_inc(sl_mm, 1)

                        keys(0)
                        keys(1)
                        pe.wait_ge(h_ready, b + 1)
                        for g in range(G):
                            pe.matmul(work[3][:, 0:NCB], w2[:, g, :], hid[:, 0, g, :], start=(g == 0), stop=(g == 1))
                        for g in range(G):
                            mm = pe.matmul(work[3][:, P + HD * g:P + HD * g + HD], hid[:, 1, g, :], w2[:, 2, 0:HD],
                                           start=True, stop=True)
                        mm.then_inc(kc_mm, 1)
                        scores(0)
                        pe.wait_ge(kc_out, b + 1)
                        pe.matmul(work[2][0:R, 0:NCB], Qb[:, :], kc[:, :], start=True, stop=True).then_inc(cs_mm, 1)
                        for n in range(1, NKT):
                            if n + 1 < NKT:
                                keys(n + 1)
                            if n == 4:
                                pe.wait_ge(pn_ready, b + 1)
                            scores(n)
                            if n == 4:
                                pe.matmul(work[2][0:R, P:2 * P], const("grp", R), pn[:, :],
                                          start=True, stop=True).then_inc(imp_mm, 1)
                        pe.wait_ge(sl_out, b * NKT + (NKT - 1))
                        for i, new in enumerate((ksn, kwn)):
                            mm = pe.matmul(gemm_big[1][0:R, P * i:P * i + TS], Qb[:, :], new[:, :],
                                           start=True, stop=True)
                        mm.then_inc(new_mm, 1)
                        if more:
                            turn_raw(b + 1)

                        groups7 = [[(pn[:, :], vc[:, :], 0, P)] +
                                   [(sn[:, i, :], vnew[:, i, :], 1 + i, TS) for i in range(2)]]
                        groups7 += [[(sw[:, P * i:P * i + P], rw[:, i, 1, :], 2, P) for i in range(4)]]
                        flat = [(ss[:, 256 * j + a:256 * j + 256:2], kv[:, j, a, 1, :], 1, P)
                                for j in range(CT) for a in range(2)]
                        groups7 += [flat[4 * i:4 * i + 4] for i in range(8)]
                        o_bank = [work[3][0:R, 0:P], gemm_small[0][0:R, 0:P], gemm_small[1][0:R, 0:P]]
                        opened = set()

                        def turn(n):
                            for i, (src, _, _, m) in enumerate(groups7[n]):
                                mm = pe.transpose(work[n % 2][0:m, P * i:P * i + R], src, ident[0:R, 0:R])
                            mm.then_inc(pt_mm, 1)

                        def values(n):
                            pe.wait_ge(pt_out, b * NPT_ + (n + 1))
                            for i, (_, val, br, m) in enumerate(groups7[n]):
                                last = (n, i) in ((0, 0), (1, 3), (9, 3))
                                mm = pe.matmul(o_bank[br], PTs[0:m, n % 2, P * i:P * i + R], val,
                                               start=(br not in opened), stop=last)
                                opened.add(br)
                            mm.then_inc(o_mm, 1)

                        if more:
                            copied(pe, b + 1, CT - 2)
                            copied(pe, b + 1, CT - 1)
                        pe.wait_ge(e_ready, b * 2 + 1)
                        settled_pe(pe)
                        turn(0)
                        for n in range(1, NPT_):
                            turn(n)
                            if n == 1:
                                pe.wait_ge(e_ready, b * 2 + 2)
                            values(n - 1)
                        values(NPT_ - 1)
                        pe.wait_ge(o_ready, b + 1)
                        settled_pe(pe)
                        pe.transpose(work[3][:, 256:256 + R], Os[:, :], ident[0:R, 0:R]).then_inc(ot_mm, 1)

                    with pe.Fori(0, NB - 1) as b:
                        batch(b, True)
                    batch(NB - 1, False)

                @block.scalar
                def _(act):
                    def copy(dst, src):
                        return act.activation(dst, src, ACT.Copy)

                    copy_z(copy, act, 0, range(CT), 0)

                    def batch(b, more):
                        act.wait_ge(h_mm, b + 1)
                        for kv_ in range(2):
                            ins = act.activation(hid[:, kv_, :, :].rearrange("p g n -> p (g n)"),
                                                 work[2][:, 256 * kv_:256 * kv_ + 256], ACT.Gelu_apprx_tanh,
                                                 bias=hb[:, kv_:kv_ + 1])
                        ins.then_inc(h_ready, 1)
                        act.wait_ge(kc_mm, b + 1)
                        act.activation(kc[:, :], work[3][:, 0:NCB], ACT.Copy)
                        act.activation(vc[:, :], work[3][:, P:2 * P], ACT.Copy).then_inc(kc_out, 1)
                        def keys_out(n):
                            act.wait_ge(kt_mm, b * NKT + (n + 1))
                            if n >= 2:
                                act.wait_ge(sl_mm, b * NKT + (n - 1))
                            if n < CT // 2:
                                dst = KTb[:, n % 2, :].rearrange("q (j p a) -> q j a p", j=2, a=2)
                                src = gemm_small[n % 2][:, :].rearrange("q (j a p) -> q j a p", j=2, a=2)
                            else:
                                dst, src = KTb[:, n % 2, :], gemm_small[n % 2][:, :]
                            act.activation(dst, src, ACT.Copy).then_inc(kt_out, 1)

                        keys_out(0)
                        keys_out(1)
                        act.wait_ge(pn_sub, b + 1)
                        act.activation(pn[:, :], pn[:, :], ACT.Exp, bias=st[:, 1:2], accum_out=st[:, 2:3])\
                            .then_inc(pn_exp, 1)
                        for n in range(2, NKT):
                            keys_out(n)
                        if more:
                            copy_z(copy, act, b + 1, range(4), 0)
                        act.wait_ge(m_ready, b * 2 + 1)
                        act.activation(sw[:, :], sw[:, :], ACT.Exp, bias=st[:, 7:8], accum_out=st[:, 8:9])
                        act.activation(sn[:, 1, :], sn[:, 1, :], ACT.Exp, bias=st[:, 7:8], accum_out=st[:, 9:10])
                        act.wait_ge(m_ready, b * 2 + 2)
                        act.activation(sn[:, 0, :], sn[:, 0, :], ACT.Exp, bias=st[:, 4:5], accum_out=st[:, 6:7])\
                            .then_inc(e_ready, 1)
                        act.activation(ss[:, :], ss[:, :], ACT.Exp, bias=st[:, 4:5], accum_out=st[:, 5:6])\
                            .then_inc(e_ready, 1)
                        if more:
                            copy_z(copy, act, b + 1, range(4, CT), 0)

                    with act.Fori(0, NB - 1) as b:
                        batch(b, True)
                    batch(NB - 1, False)

                @block.vector
                def _(dve):
                    copy_z(dve.tensor_copy, dve, 0, range(CT), 1)

                    def batch(b, more):
                        c = Chain(dve, chain7, b * CH)
                        dve.tensor_copy(Qb[:, :], QB[:, bass.ds(b, 1), :].rearrange("p a q -> p (a q)"))\
                            .then_inc(qb_ready, 1)
                        dve.wait_ge(cs_mm, b + 1)
                        settled(dve)
                        c.step(dve.tensor_tensor_reduce(pn[:, :], work[2][0:R, 0:NCB], const("bcmp", R), 1.0, -3e38,
                                                        ALU.add, ALU.max, st[:, 0:1]))
                        dve.tensor_scalar(st[:, 1:2], st[:, 0:1], -1.0, None, ALU.mult).then_inc(pn_sub, 1)

                        def scores_out(n):
                            dve.wait_ge(sl_mm, b * NKT + (n + 1))
                            if n < CT // 2:
                                dst, table = ss[:, 512 * n:512 * n + 512], past[:, 512 * n:512 * n + 512]
                            else:
                                dst, table = sw[:, :], const("bwin", R)
                            dve.tensor_tensor(dst, gemm_big[n % 2][0:R, :], table, ALU.add).then_inc(sl_out, 1)

                        dve.wait_ge(c7_const, 16)
                        scores_out(0)
                        dve.wait_ge(pn_exp, b + 1)
                        c.step(dve.reciprocal(st[:, 3:4], st[:, 2:3]))
                        dve.tensor_scalar(pn[:, :], pn[:, :], st[:, 3:4], None, ALU.mult).then_inc(pn_ready, 1)
                        for n in range(1, 5):
                            scores_out(n)
                        dve.wait_ge(imp_mm, b + 1)
                        two = work[2][0:R, P:2 * P].rearrange("p (n a) -> p n a", a=2)
                        c.step(dve.tensor_copy(sel[:, 3, 0:64], two[:, :, 1]))
                        c.step(dve.tensor_tensor(sel[:, 0, 0:64], two[:, :, 0], sel[:, 3, 0:64], ALU.add))
                        c.step(dve.memset(sel[:, 0, 64:65], 0.0))
                        c.step(dve.tensor_tensor(sel[:, 0, :], sel[:, 0, :], const("bonus", R), ALU.add))
                        for i in range(2):
                            settled(dve)
                            c.step(dve.max(top8[:, i, :], sel[:, i, :]))
                            settled(dve)
                            c.step(dve.match_replace(sel[:, i + 1, :], top8[:, i, :], sel[:, i, :], -3e38))
                        c.step(dve.tensor_scalar(sel[:, 3, :], sel[:, 2, :], -1e38, NEG, ALU.is_gt, ALU.mult))
                        for n in range(5, NKT):
                            scores_out(n)
                        c.step(dve.tensor_copy(bnb[:, 0:TS], cst[0:R, bass.ds(b * TS + CONST["bnew"][0], TS)]))
                        dve.wait_ge(new_mm, b + 1)
                        settled(dve)
                        for i in range(2):
                            ins = dve.tensor_tensor_reduce(
                                sn[:, i, :], gemm_big[1][0:R, P * i:P * i + TS],
                                bnb[:, 0:TS], 1.0, -3e38, ALU.add, ALU.max,
                                st[:, 10 + i:11 + i])
                        c.step(ins)
                        c.step(dve.tensor_reduce(st[:, 12:13], sw[:, :], AX, ALU.max))
                        c.step(dve.tensor_tensor(st[:, 12:13], st[:, 12:13], st[:, 11:12], ALU.max))
                        dve.tensor_scalar(st[:, 7:8], st[:, 12:13], -1.0, None, ALU.mult).then_inc(m_ready, 1)
                        settled(dve)
                        c.step(dve.tensor_tensor_reduce(
                            ss[:, :].rearrange("p (n k) -> p n k", k=64), ss[:, :].rearrange("p (n k) -> p n k", k=64),
                            sel[:, 3, 0:64].unsqueeze(2).to_broadcast([R, 64, 64]), 1.0, -3e38, ALU.add, ALU.max,
                            st[:, 13:14]))
                        c.step(dve.tensor_tensor(st[:, 13:14], st[:, 13:14], st[:, 10:11], ALU.max))
                        dve.tensor_scalar(st[:, 4:5], st[:, 13:14], -1.0, None, ALU.mult).then_inc(m_ready, 1)
                        if more:
                            copy_z(dve.tensor_copy, dve, b + 1, range(CT), 1)
                        for n in range(NPT_):
                            dve.wait_ge(pt_mm, b * NPT_ + (n + 1))
                            k, m = (3, TS) if n == 0 else (4, P)
                            src = work[n % 2][:, :].rearrange("p (k c) -> p k c", k=4)
                            dst = PTs[:, n % 2, :].rearrange("p (k c) -> p k c", k=4)
                            if n == 0:
                                dve.tensor_copy(dst[:, 0, 0:R], src[:, 0, 0:R])
                                dve.tensor_copy(dst[0:TS, 1:3, 0:R], src[0:TS, 1:3, 0:R]).then_inc(pt_out, 1)
                            else:
                                dve.tensor_copy(dst[:, :, 0:R], src[:, :, 0:R]).then_inc(pt_out, 1)
                        c.step(dve.tensor_tensor(st[:, 5:6], st[:, 5:6], st[:, 6:7], ALU.add))
                        c.step(dve.tensor_tensor(st[:, 8:9], st[:, 8:9], st[:, 9:10], ALU.add))
                        dve.reciprocal(st[:, 5:6], st[:, 5:6])
                        c.step(dve.reciprocal(st[:, 8:9], st[:, 8:9]))
                        gates = gq[:, bass.ds(b, 1), :].rearrange("p a c -> p (a c)")
                        c.step(dve.tensor_copy(st[:, 13:16], gates))
                        dve.tensor_tensor(st[:, 5:6], st[:, 5:6], st[:, 14:15], ALU.mult)
                        c.step(dve.tensor_tensor(st[:, 8:9], st[:, 8:9], st[:, 15:16], ALU.mult))
                        dve.wait_ge(o_mm, b * NPT_ + 2 * NPT_)
                        c.step(dve.tensor_scalar(Os[:, :], work[3][0:R, 0:P], st[:, 13:14], None, ALU.mult))
                        c.step(dve.scalar_tensor_tensor(out=Os[:, :], in0=gemm_small[0][0:R, 0:P], scalar=st[:, 5:6],
                                                        in1=Os[:, :], op0=ALU.mult, op1=ALU.add))
                        dve.scalar_tensor_tensor(out=Os[:, :], in0=gemm_small[1][0:R, 0:P], scalar=st[:, 8:9],
                                                 in1=Os[:, :], op0=ALU.mult, op1=ALU.add).then_inc(o_ready, 1)
                        dve.wait_ge(ot_mm, b + 1)
                        for g in range(G):
                            rows = slice(HD * g, HD * g + HD)
                            dve.tensor_copy(
                                yT[rows, 4:8, bass.ds(b * ST + TP, ST)],
                                work[3][rows, 256 + 16 * g:272 + 16 * g].rearrange("p (r t) -> p r t", r=REP))
                        assert c.n <= CH
                        while c.n < CH:
                            c.step(dve.tensor_copy(st[:, 0:1], st[:, 1:2]))

                    with dve.Fori(0, NB - 1) as b:
                        batch(b, True)
                    batch(NB - 1, False)
        sem.end_part()

        def tile_of(x, it, u):
            return x[:, bass.ds(it * RING + u, 1), :].rearrange("p a n -> p (a n)")

        with ExitStack() as c8:
            nparts = [c8.enter_context(nc.sbuf_tensor(n, [P, KT, NT], F32R)) for n in ("n_high", "n_low")]
            wparts = [c8.enter_context(nc.sbuf_tensor(n, [P, 2, KT, P], F32R)) for n in ("w8_high", "w8_low")]
            cross = c8.enter_context(ExitStack())
            nT = cross.enter_context(nc.sbuf_tensor("nT", [P, KT, NT], F32))
            qx = cross.enter_context(nc.sbuf_tensor("qx", [P, XH, NT], F32))
            ox = cross.enter_context(nc.sbuf_tensor("ox", [P, XH, NT], F32))
            hstd = cross.enter_context(nc.sbuf_tensor("hstd", [P, 2, NT], F32))
            hsq, hss, hsd, hinv, y_norm = (sem(f"head_{n}") for n in ("sq", "sum", "std", "inv", "norm"))

            with nc.Block() as block:
                @block.sync
                def _(sp):
                    w = I["w_out"][0]
                    for n in range(8):
                        u, cols_ = n % RING, slice(P * n, P * n + P)
                        slot_free(sp, "out", n // RING, u)
                        sp.dma_start(ring[:, u, 0:4, :], w[0:512, cols_].rearrange("(k p) n -> p k n", p=P))\
                            .then_inc(w_loaded[u], 16)
                        for g in range(G):
                            sp.dma_start(ring[HD * g:HD * g + HD, u, 4:8, :],
                                         w[512 + 256 * g:768 + 256 * g, cols_].rearrange("(r d) n -> d r n", r=REP))\
                                .then_inc(w_loaded[u], 16)
                    w = I["xa_wq"][0].rearrange("(k p) n -> p k n", p=P)
                    for n in range(4):
                        slot_free(sp, "xq", 0, n)
                        sp.dma_start(ring[:, n, :, :], w[:, :, P * n:P * n + P]).then_inc(w_loaded[n], 16)

                @block.tensor
                def _(pe):
                    for k in range(KT):
                        pe.wait_ge(hsq, k + 1)
                        if k >= 2:
                            pe.wait_ge(hsd, k - 1)
                        for i in range(2):
                            mm = pe.matmul(work[2 * (k % 2) + i][:, 0:HALF], const("headones"),
                                           nT[:, k, HALF * i:HALF * i + HALF], start=True, stop=True)
                        mm.then_inc(hss, 1)
                    pe.wait_ge(x_split, 3 * KT)
                    pe_gemm(pe, "out", 8, KT, lambda k: [x[:, k, :] for x in nparts], wparts)
                    norm_pe(pe, 2, yT)
                    pe.wait_ge(x_split, 4 * KT)
                    pe_gemm(pe, "xq", 4, KT, lambda k: [x[:, k, :] for x in nparts], wparts)

                @block.scalar
                def _(act):
                    for k in range(KT):
                        act.activation(nT[:, k, :], yT[:, k, :], ACT.Square).then_inc(hsq, 1)
                    for k in range(KT):
                        act.wait_ge(hss, k + 1)
                        if k >= 2:
                            act.wait_ge(y_norm, k - 1)
                        for i in range(2):
                            ins = act.activation(hstd[:, k % 2, HALF * i:HALF * i + HALF],
                                                 work[2 * (k % 2) + i][:, 0:HALF], ACT.Sqrt,
                                                 bias=const("eps"), scale=1.0 / HD)
                        ins.then_inc(hsd, 1)
                    act.wait_ge(out_taken[1], stage["xq"][0] // 2)
                    act.wait_ge(out_taken[0], stage["xq"][0] // 2)
                    norm_act(act, 2, xT, yT)
                    for n in (0, 2):
                        output_here(act, "xq", 0, n)
                        act_copy(act, qx[:, n, :], 0).then_inc(out_taken[0], 1)

                @block.vector
                def _(dve):
                    for k in range(KT):
                        dve.wait_ge(hsd, k + 1)
                        dve.reciprocal(hstd[:, k % 2, :], hstd[:, k % 2, :]).then_inc(hinv, 1)
                        dve.wait_ge(hinv, k + 1)
                        dve.scalar_tensor_tensor(out=nT[:, k, :], in0=yT[:, k, :], scalar=vecT[:, V_Y + k:V_Y + k + 1],
                                                 in1=hstd[:, k % 2, :], op0=ALU.mult, op1=ALU.mult).then_inc(y_norm, 1)
                    dve.wait_ge(y_norm, KT)
                    split_x(dve, nT, nparts, range(KT))

                    def take_out(it, n):
                        output_here(dve, "out", it, n)
                        dve_add(dve, tile_of(xT, it, n), n % 2).then_inc(out_taken[n % 2], 1)

                    split_and_take(dve, 2, lambda it, u: split_weights(dve, "out", it, u, wparts), take_out)
                    norm_dve(dve, 2, xT, V_XA, yT)
                    dve.wait_ge(norm_ready, 3 * KT)
                    split_x(dve, yT, nparts, range(KT))

                    def take_xq(it, n):
                        if n % 2:
                            output_here(dve, "xq", it, n)
                            dve_copy(dve, qx[:, n, :], 1).then_inc(out_taken[1], 1)

                    split_and_take(dve, 1, lambda it, u: split_weights(dve, "xq", it, u, wparts), take_xq)

            with ExitStack() as c9:
                def t9(name, shape):
                    return c9.enter_context(nc.sbuf_tensor(name, shape, F32))

                XS = XD ** -0.5
                KTx = t9("KTx", [P, XH, NM])
                Px = t9("Px", [P, 2, NM])
                PTx = t9("PTx", [P, 2, NM])
                dgx = t9("dgx", [P, 2, P])
                sx = t9("sx", [P, 4, 4])
                SKIP = 16 * NB * 4 + 16
                qm = t9("qm", [P, NB * SKIP])
                idle = nT[:, :, :].rearrange("p k n -> p (k n)")
                kx = idle[:, 0:2048].rearrange("p (b c n) -> p b c n", b=2, c=2)
                KTs = idle[:, 2048:4096].rearrange("p (b h m) -> p b h m", b=2, h=XH)
                vx2 = t9("vx", [P, NB // 2, 2, 512])
                vx1 = ring[:, :, :, :].rearrange("p b k n -> p b (k n)").rearrange("p b (c n) -> p b c n", c=2)
                Pm, PTm = t9("Pm", [P, NM]), t9("PTm", [P, NM])

                def vx(b, c, cols_):
                    return vx1[:, b, c, cols_] if b < NB // 2 else vx2[:, b - NB // 2, c, cols_]

                kx_here = [sem(f"kx_here{j}") for j in range(2)]
                vx_here, qm_zero, qm_ready = sem("vx_here"), sem("qm_zero"), sem("qm_ready")
                xk_mm, xk_out, xs_mm, xs_max, xp_exp, xd, xt_mm, xt_out, xv_mm, xo_out, chain9, x_shift = (
                    sem(f"x_{n}") for n in ("k_mm", "k_out", "s_mm", "max", "exp", "d", "t_mm", "t_out", "v_mm",
                                            "o_out", "chain", "shift"))
                sk_mm, sk_out, sq_mm, sm_ready, sp_ready, sp_n, st_mm, st_out, sv_mm = (
                    sem(f"xs_{n}") for n in ("k_mm", "k_out", "s_mm", "max", "exp", "norm", "t_mm", "t_out", "v_mm"))
                steps9 = [(h, qt) for h in range(XH) for qt in range(QT)]

                with nc.Block() as block:
                    @block.sync
                    def _(sp):
                        mem = I["cache_mem_kv"][0].rearrange("b (c p) v h d -> b p c v (h d)", p=P)
                        for b in range(NB):
                            sp.dma_start(vx(b, slice(0, 2), slice(0, 512)), mem[b, :, :, 1, :]).then_inc(vx_here, 16)
                            if b >= 2:
                                sp.wait_ge(sk_mm, 2 * (b - 1))
                            sp.dma_start(kx[:, b % 2, :, :], mem[b, :, :, 0, :]).then_inc(kx_here[b % 2], 16)

                    @block.gpsimd
                    def _(pool):
                        pool.memset(qm[:, :], 0.0).then_inc(qm_zero, 1)

                    @block.tensor
                    def _(pe):
                        for i in range(2):
                            for h in (2 * i, 2 * i + 1):
                                for c in range(2):
                                    mm = pe.transpose(work[i][:, NM * (h % 2) + P * c:NM * (h % 2) + P * c + P],
                                                      memtok[:, c, P * h:P * h + P], ident)
                            mm.then_inc(xk_mm, 1)
                        pe.wait_ge(xk_out, 2)

                        def scores(n):
                            h, qt = steps9[n]
                            if n >= 4:
                                pe.wait_ge(xp_exp, n - 3)
                            pe.matmul(work[n % 4][:, 0:NM], qx[:, h, P * qt:P * qt + P], KTx[:, h, :],
                                      start=True, stop=True).then_inc(xs_mm, 1)

                        def values(n):
                            h, qt = steps9[n]
                            if qt == 0 and h >= 2:
                                pe.wait_ge(xo_out, h - 1)
                            pe.wait_ge(xt_out, n + 1)
                            for c in range(2):
                                mm = pe.matmul(gemm_big[h % 2][:, P * qt:P * qt + P],
                                               memtok[:, c, 512 + P * h:512 + P * h + P],
                                               PTx[:, n % 2, P * c:P * c + P], start=(c == 0), stop=(c == 1))
                            mm.then_inc(xv_mm, 1)

                        scores(0)
                        scores(1)
                        for n in range(len(steps9)):
                            if n + 2 < len(steps9):
                                scores(n + 2)
                            pe.wait_ge(xd, n + 1)
                            pe.wait_ge(xp_exp, n + 1)
                            if n >= 2:
                                pe.wait_ge(xt_out, n - 1)
                            for c in range(2):
                                mm = pe.matmul(gemm_small[n % 2][:, P * c:P * c + P], Px[:, n % 2, P * c:P * c + P],
                                               dgx[:, n % 2, :], start=True, stop=True)
                            mm.then_inc(xt_mm, 1)
                            if n:
                                values(n - 1)
                        values(len(steps9) - 1)
                        pe.wait_ge(xp_exp, len(steps9))
                        pe.wait_ge(qm_ready, 1)

                        def turn(b):
                            pe.wait_ge(kx_here[b % 2], 16 * (b // 2 + 1))
                            if b:
                                pe.wait_ge(sk_out, 2 * b)
                            for i in range(2):
                                for h in (2 * i, 2 * i + 1):
                                    for c in range(2):
                                        at = NM * (h % 2) + P * c
                                        mm = pe.transpose(work[i][:, at:at + P], kx[:, b % 2, c, P * h:P * h + P], ident)
                                mm.then_inc(sk_mm, 1)

                        turn(0)
                        for b in range(NB):
                            if b + 1 < NB:
                                turn(b + 1)
                            pe.wait_ge(sk_out, 2 * b + 2)
                            for h in range(XH):
                                at = P * (XH * b + h)
                                mm = pe.matmul(work[2][:, 0:NM], qm[:, at:at + P], KTs[:, b % 2, h, :],
                                               start=(b == 0 and h == 0), stop=(b == NB - 1 and h == XH - 1))
                            mm.then_inc(sq_mm, 1)
                        pe.wait_ge(sp_n, 1)
                        for c in range(2):
                            mm = pe.transpose(work[3][:, P * c:P * c + P], Pm[:, P * c:P * c + P], ident)
                        mm.then_inc(st_mm, 1)
                        pe.wait_ge(st_out, 1)
                        pe.wait_ge(vx_here, 16 * NB)
                        pe.wait_ge(xo_out, XH)
                        for b in range(NB):
                            for h in range(XH):
                                for c in range(2):
                                    at = P * c + 16 * b + ST * h
                                    mm = pe.matmul(gemm_big[0][:, TS * h + ST * b:TS * h + ST * b + ST],
                                                   vx(b, c, slice(P * h, P * h + P)), PTm[:, at:at + ST],
                                                   start=(c == 0), stop=(c == 1))
                        mm.then_inc(sv_mm, 1)

                    @block.scalar
                    def _(act):
                        for n, (h, qt) in enumerate(steps9):
                            act.wait_ge(xs_max, n + 1)
                            if n >= 2:
                                act.wait_ge(xt_mm, n - 1)
                            act.activation(Px[:, n % 2, :], work[n % 4][:, 0:NM], ACT.Exp, bias=sx[:, n % 4, 1:2],
                                           scale=XS, accum_out=sx[:, n % 4, 2:3]).then_inc(xp_exp, 1)
                            act.wait_ge(xt_mm, n + 1)
                            if n >= 2:
                                act.wait_ge(xv_mm, n - 1)
                            act.activation(PTx[:, n % 2, :], gemm_small[n % 2][:, 0:NM], ACT.Copy).then_inc(xt_out, 1)
                            if qt == 1 and h:
                                act.wait_ge(xv_mm, QT * h)
                                act.activation(ox[:, h - 1, 0:TP], gemm_big[(h - 1) % 2][:, :], ACT.Copy)\
                                    .then_inc(xo_out, 1)
                        act.wait_ge(xv_mm, len(steps9))
                        act.activation(ox[:, XH - 1, 0:TP], gemm_big[(XH - 1) % 2][:, :], ACT.Copy).then_inc(xo_out, 1)
                        for b in range(NB):
                            for i in range(2):
                                act.wait_ge(sk_mm, 2 * b + i + 1)
                                if b >= 2:
                                    act.wait_ge(sq_mm, b - 1)
                                act.activation(KTs[:, b % 2, 2 * i:2 * i + 2, :],
                                               work[i][:, :].rearrange("p (h m) -> p h m", h=2), ACT.Copy)\
                                    .then_inc(sk_out, 1)
                        act.wait_ge(sm_ready, 1)
                        act.activation(Pm[:, :], work[2][:, 0:NM], ACT.Exp, bias=sx[:, 0, 1:2], scale=XS,
                                       accum_out=sx[:, 0, 2:3]).then_inc(sp_ready, 1)

                    @block.vector
                    def _(dve):
                        c = Chain(dve, chain9)
                        for i in range(2):
                            dve.wait_ge(xk_mm, i + 1)
                            dve.tensor_copy(KTx[:, 2 * i:2 * i + 2, :], work[i][:, :].rearrange("p (h m) -> p h m", h=2))\
                                .then_inc(xk_out, 1)
                        dve.wait_ge(qm_zero, 1)
                        for h in range(XH):
                            ins = dve.tensor_copy(
                                qm[:, :].rearrange("p (b s) -> p b s", s=SKIP)[:, :, (P + ST) * h:(P + ST) * h + ST],
                                qx[:, h, TP:NT].rearrange("p (b t) -> p b t", b=NB))
                        ins.then_inc(qm_ready, 1)

                        def top(n):
                            dve.wait_ge(xs_mm, n + 1)
                            c.step(dve.tensor_reduce(sx[:, n % 4, 0:1], work[n % 4][:, 0:NM], AX, ALU.max))
                            dve.tensor_scalar(sx[:, n % 4, 1:2], sx[:, n % 4, 0:1], -XS, None, ALU.mult)\
                                .then_inc(xs_max, 1)

                        top(0)
                        for n in range(len(steps9)):
                            if n + 1 < len(steps9):
                                top(n + 1)
                            dve.wait_ge(xp_exp, n + 1)
                            c.step(dve.reciprocal(sx[:, n % 4, 3:4], sx[:, n % 4, 2:3]))
                            if n >= 2:
                                dve.wait_ge(xt_mm, n - 1)
                            dve.tensor_scalar(dgx[:, n % 2, :], ident, sx[:, n % 4, 3:4], None, ALU.mult)\
                                .then_inc(xd, 1)
                        dve.wait_ge(sq_mm, NB)
                        c.step(dve.tensor_reduce(sx[:, 0, 0:1], work[2][:, 0:NM], AX, ALU.max))
                        dve.tensor_scalar(sx[:, 0, 1:2], sx[:, 0, 0:1], -XS, None, ALU.mult).then_inc(sm_ready, 1)
                        dve.wait_ge(sp_ready, 1)
                        c.step(dve.reciprocal(sx[:, 0, 3:4], sx[:, 0, 2:3]))
                        dve.tensor_scalar(Pm[:, :], Pm[:, :], sx[:, 0, 3:4], None, ALU.mult).then_inc(sp_n, 1)
                        dve.wait_ge(st_mm, 1)
                        dve.tensor_copy(PTm[:, :], work[3][:, 0:NM]).then_inc(st_out, 1)
                        dve.wait_ge(sv_mm, 1)
                        dve.tensor_copy(ox[:, :, TP:NT], gemm_big[0][:, 0:P].rearrange("p (h t) -> p h t", h=XH))

            with nc.Block() as block:
                @block.sync
                def _(sp):
                    w = I["xa_wo"][0].rearrange("(k p) n -> p k n", p=P)
                    for n in range(8):
                        slot_free(sp, "xo", n // RING, n % RING)
                        sp.dma_start(ring[:, n % RING, 0:XH, :], w[:, :, P * n:P * n + P]).then_inc(w_loaded[n % RING], 16)

                @block.tensor
                def _(pe):
                    pe.wait_ge(x_split, 4 * KT + XH)
                    pe_gemm(pe, "xo", 8, XH, lambda k: [x[:, k, :] for x in nparts], wparts)
                    norm_pe(pe, 3, nT)

                @block.scalar
                def _(act):
                    act.wait_ge(out_taken[1], stage["up0"][0] // 2)
                    act.wait_ge(out_taken[0], stage["up0"][0] // 2)
                    norm_act(act, 3, xT, nT)

                @block.vector
                def _(dve):
                    split_x(dve, ox, nparts, range(XH))

                    def take_xo(it, n):
                        output_here(dve, "xo", it, n)
                        dve_add(dve, tile_of(xT, it, n), n % 2).then_inc(out_taken[n % 2], 1)

                    split_and_take(dve, 2, lambda it, u: split_weights(dve, "xo", it, u, wparts, XH), take_xo)
                    norm_dve(dve, 3, xT, V_FFN, nT)
                    dve.wait_ge(norm_ready, 4 * KT)
                    split_x(dve, nT, nparts, range(KT))
            cross.close()

            with ExitStack() as c11:
                def t11(name, shape):
                    return c11.enter_context(nc.sbuf_tensor(name, shape, F32))

                NR, NQ = 4 + NE, QT + 1
                PARTS = 2
                EP = NE // PARTS
                Hparts = [c11.enter_context(nc.sbuf_tensor(n, [P, 2 * EP, NT], F32R)) for n in ("H_high", "H_low")]
                rw_ = t11("rw_", [P, KT, NR])
                rparts = [c11.enter_context(nc.sbuf_tensor(n, [P, KT, NR], F32R)) for n in ("r_high", "r_low")]
                rb = t11("rb", [P, NR])
                lgT, combT, ce = yT[0:NR, 4, :], yT[0:NE, 5, :], yT[0:NE, 6, :]
                sl, hu, cb, hid = yT[:, 0:2, :], yT[:, 2, :], yT[:, 3, :], yT[:, 7, :]
                lg = t11("lg", [P, NQ, NR])
                a4 = t11("a4", [P, 8, NQ, 4])
                a1 = t11("a1", [P, 8, NQ])
                comb = t11("comb", [P, NQ, NE])
                r_here, lt_mm, lt_out, l_mm, chain11, r_exp, r_sub, cm_ready, ct_mm, ct_out = (
                    sem(f"r_{n}") for n in ("here", "lt_mm", "lt_out", "l_mm", "chain", "exp", "sub", "comb",
                                            "ct_mm", "ct_out"))
                ce_ready, cb_mm, cb_out, hu_used, h_high, he_done = (
                    sem(f"e_{n}") for n in ("ce", "cb_mm", "cb_out", "hu", "h_high", "h"))
                rw_split = sem("rw_split")

                with nc.Block() as block:
                    @block.sync
                    def _(sp):
                        sp.dma_start(rw_[:, :, 0:4], I["router_gw"][0].rearrange("(k p) n -> p k n", p=P))\
                            .then_inc(r_here, 16)
                        sp.dma_start(rw_[:, :, 4:NR], I["router_ew"][0].rearrange("(k p) n -> p k n", p=P))\
                            .then_inc(r_here, 16)
                        sp.dma_start(rb[:, 0:4], I["router_gb"].to_broadcast([P, 4])).then_inc(r_here, 16)
                        sp.dma_start(rb[:, 4:NR], I["router_eb"].to_broadcast([P, NE])).then_inc(r_here, 16)
                        up = [I[n][0].rearrange("e (k p) f -> e p k f", p=P) for n in ("exp_w_gate", "exp_w_up")]
                        down = I["exp_w_down"][0].rearrange("e f n -> (e f) n").rearrange("(s k p) n -> s p k n", k=KT, p=P)
                        for part in range(PARTS):
                            with sp.Fori(0, EP) as e:
                                for u in range(RING):
                                    slot_free(sp, f"up{part}", e, u)
                                    sp.dma_start(ring[:, u, :, :],
                                                 up[u % 2][bass.ds(e + EP * part, 1), :, :,
                                                           P * (u // 2):P * (u // 2) + P].rearrange(
                                                               "e p k f -> p (e k) f")).then_inc(w_loaded[u], 16)
                            with sp.Fori(0, KT // 2) as it:
                                for u in range(RING):
                                    slot_free(sp, f"down{part}", it, u)
                                    sp.dma_start(ring[:, u, :, :],
                                                 down[2 * part + u % 2, :, :, bass.ds((it * 2 + u // 2) * P, P)])\
                                        .then_inc(w_loaded[u], 16)

                    @block.tensor
                    def _(pe):
                        pe.wait_ge(rw_split, 1)
                        for k in range(KT):
                            mm = product(pe, [(work[i][0:NR, 0:HALF], HALF * i) for i in range(2)],
                                         [x[:, k, :] for x in rparts], [x[:, k, :] for x in nparts], k == 0, k == KT - 1)
                        mm.then_inc(lt_mm, 1)
                        pe.wait_ge(lt_out, 1)
                        for q in range(NQ):
                            n = P if q < QT else TS
                            mm = pe.transpose(work[2][0:n, NR * q:NR * q + NR], lgT[:, P * q:P * q + n], ident[0:NR, 0:NR])
                        mm.then_inc(l_mm, 1)
                        pe.wait_ge(cm_ready, 1)
                        for q in range(NQ):
                            n = P if q < QT else TS
                            bank_ = work[3][0:NE, P * q:P * q + n] if q < QT else work[2][0:NE, P:P + n]
                            mm = pe.transpose(bank_, comb[0:n, q, :], ident[0:n, 0:n])
                        mm.then_inc(ct_mm, 1)

                        for part in range(PARTS):
                            def weights_over_partitions(e):
                                pe.wait_ge(ce_ready, e + (EP * part + 1))
                                pe.wait_ge(cb_out, e + (EP * part + 1))
                                for i in range(2):
                                    mm = pe.matmul(work[i][:, 0:HALF], const("ones", NE),
                                                   ce[:, HALF * i:HALF * i + HALF], start=True, stop=True)
                                mm.then_inc(cb_mm, 1)

                            pe_gemm(pe, f"up{part}", 4 * EP, KT, lambda k: [x[:, k, :] for x in nparts], wparts,
                                    before=weights_over_partitions)
                            pe.wait_ge(he_done, 2 + 2 * EP * (part + 1))
                            o2 = stage[f"down{part}"][0] // 2
                            with pe.Fori(0, KT // 2) as it:
                                for u in range(RING):
                                    pe.wait_ge(w_split[u % 2], it * 2 + (o2 + u // 2 + 1))
                                    if u % 2 == 0:
                                        pe.wait_ge(out_taken[u // 2], it * 2 + o2)
                                    for k in range(KT):
                                        kk = KT * (u % 2) + k
                                        mm = product(pe, halves(u // 2), [x[:, u % 2, k, :] for x in wparts],
                                                     [x[:, kk, :] for x in Hparts], kk == 0, kk == 2 * EP - 1)
                                    mm.then_inc(w_done[u % 2], 1)

                    @block.scalar
                    def _(act):
                        act.wait_ge(r_sub, 1)
                        act.activation(a4[:, 1, :, :], a4[:, 1, :, :], ACT.Exp).then_inc(r_exp, 1)
                        act.wait_ge(r_sub, 2)
                        act.activation(a1[:, 4, :], a1[:, 4, :], ACT.Exp).then_inc(r_exp, 1)
                        for part in range(PARTS):
                            with act.Fori(0, EP) as e:
                                act.wait_ge(cb_mm, e + (EP * part + 1))
                                act.wait_ge(he_done, e * 2 + (2 * EP * part + 2))
                                for i in range(2):
                                    ins = act.activation(cb[:, HALF * i:HALF * i + HALF], work[i][:, 0:HALF], ACT.Copy)
                                ins.then_inc(cb_out, 1)
                                for f in range(2):
                                    output_here(act, f"up{part}", e, 2 * f)
                                    for bank_, at in halves(0):
                                        ins = act.activation(sl[:, f, at:at + HALF], bank_, ACT.Silu)
                                    ins.then_inc(out_taken[0], 1)

                    @block.vector
                    def _(dve):
                        c = Chain(dve, chain11)
                        dve.wait_ge(r_here, 64)
                        c.step(dve.tensor_copy(rparts[0][:, :, :], rw_[:, :, :]))
                        dve.tensor_tensor(rparts[1][:, :, :], rw_[:, :, :], rparts[0][:, :, :].bitcast(F32), ALU.subtract)\
                            .then_inc(rw_split, 1)
                        dve.wait_ge(lt_mm, 1)
                        c.step(dve.memset(lg[:, :, :], 0.0))
                        dve.tensor_copy(lgT[:, 0:HALF], work[0][0:NR, 0:HALF])
                        dve.tensor_copy(lgT[:, HALF:NT], work[1][0:NR, 0:HALF]).then_inc(lt_out, 1)
                        dve.wait_ge(l_mm, 1)
                        bias = rb[:, :].unsqueeze(1)
                        dve.tensor_tensor(lg[:, 0:QT, :], work[2][:, 0:NR * QT].rearrange("p (q n) -> p q n", n=NR),
                                          bias.to_broadcast([P, QT, NR]), ALU.add)
                        c.step(dve.tensor_tensor(lg[0:TS, QT, :], work[2][0:TS, NR * QT:NR * NQ], rb[0:TS, :], ALU.add))

                        def first_max(x, hot, top, seen):
                            c.step(dve.tensor_reduce(top, x, AX, ALU.max))
                            c.step(dve.tensor_tensor(hot, x, top.unsqueeze(2).to_broadcast([P, NQ, 4]), ALU.is_equal))
                            c.step(dve.tensor_copy(seen, hot[:, :, 0]))
                            for j in range(1, 4):
                                c.step(dve.tensor_tensor(a1[:, 7, :], hot[:, :, j], seen, ALU.mult))
                                c.step(dve.tensor_tensor(hot[:, :, j], hot[:, :, j], a1[:, 7, :], ALU.subtract))
                                c.step(dve.tensor_tensor(seen, seen, hot[:, :, j], ALU.max))

                        g_log, g_p, g_hot, le, tmp4, hot1, hot2, le2 = (a4[:, i, :, :] for i in range(8))
                        g_top, g_sum, g_w, m1, e2, m2, seen = (a1[:, i, :] for i in range(7))
                        c.step(dve.tensor_copy(g_log, lg[:, :, 0:4]))
                        c.step(dve.tensor_reduce(g_top, g_log, AX, ALU.max))
                        dve.tensor_tensor(g_p, g_log, g_top.unsqueeze(2).to_broadcast([P, NQ, 4]), ALU.subtract)\
                            .then_inc(r_sub, 1)
                        dve.wait_ge(r_exp, 1)
                        c.step(dve.tensor_reduce(g_sum, g_p, AX, ALU.add))
                        c.step(dve.reciprocal(g_sum, g_sum))
                        c.step(dve.tensor_tensor(g_p, g_p, g_sum.unsqueeze(2).to_broadcast([P, NQ, 4]), ALU.mult))
                        first_max(g_p, g_hot, g_w, seen)
                        for g in range(4):
                            mine = lg[:, :, 4 + 4 * g:8 + 4 * g]
                            on = g_hot[:, :, g:g + 1].to_broadcast([P, NQ, 4])
                            if g == 0:
                                c.step(dve.tensor_tensor(le, mine, on, ALU.mult))
                            else:
                                c.step(dve.tensor_tensor(tmp4, mine, on, ALU.mult))
                                c.step(dve.tensor_tensor(le, le, tmp4, ALU.add))
                        first_max(le, hot1, m1, seen)
                        c.step(dve.tensor_scalar(tmp4, hot1, -3e38, None, ALU.mult))
                        c.step(dve.tensor_tensor(le2, le, tmp4, ALU.add))
                        first_max(le2, hot2, m2, seen)
                        dve.tensor_tensor(e2, m2, m1, ALU.subtract).then_inc(r_sub, 1)
                        dve.wait_ge(r_exp, 2)
                        w1_, w2_ = g_sum, g_top
                        c.step(dve.tensor_scalar(w1_, e2, 1.0, None, ALU.add))
                        c.step(dve.reciprocal(w1_, w1_))
                        c.step(dve.tensor_tensor(w2_, w1_, e2, ALU.mult))
                        for w_, hot in ((w1_, hot1), (w2_, hot2)):
                            c.step(dve.tensor_tensor(w_, w_, g_w, ALU.mult))
                            c.step(dve.tensor_tensor(hot, hot, w_.unsqueeze(2).to_broadcast([P, NQ, 4]), ALU.mult))
                        c.step(dve.tensor_tensor(hot1, hot1, hot2, ALU.add))
                        for g in range(4):
                            ins = dve.tensor_tensor(comb[:, :, 4 * g:4 * g + 4], hot1,
                                                    g_hot[:, :, g:g + 1].to_broadcast([P, NQ, 4]), ALU.mult)
                        ins.then_inc(cm_ready, 1)
                        dve.wait_ge(ct_mm, 1)
                        dve.tensor_copy(combT[:, 0:TP], work[3][0:NE, :])
                        dve.tensor_copy(combT[:, TP:NT], work[2][0:NE, P:P + TS]).then_inc(ct_out, 1)
                        dve.wait_ge(ct_out, 1)
                        dve.memset(spare[0:1, 6:7], 0.0).then_inc(he_done, 2)
                        dve.memset(spare[0:1, 7:8], 0.0).then_inc(cb_out, 1)
                        for part in range(PARTS):
                            up_, o2 = f"up{part}", stage[f"up{part}"][0] // 2

                            def spread(e):
                                dve.tensor_scalar(ce[:, :], combT[:, :], ident[0:NE, bass.ds(e + EP * part, 1)], None,
                                                  ALU.mult).then_inc(ce_ready, 1)

                            def split_up(e, u):
                                split_weights(dve, up_, e, u, wparts)
                                if u == 3:
                                    dve.wait_ge(cb_mm, e + (EP * part + 1))
                                    spread(e + 1)

                            def take_up(e, n):
                                if n % 2 == 0:
                                    return
                                f = n // 2
                                dve.wait_ge(cb_out, e + (EP * part + 2 + (f < 0) * -1))
                                output_here(dve, up_, e, n)
                                for bank_, at in halves(1):
                                    ins = dve.tensor_tensor(hu[:, at:at + HALF], bank_, cb[:, at:at + HALF], ALU.mult)
                                ins.then_inc(out_taken[1], 1)
                                dve.wait_ge(out_taken[1], e * 2 + (o2 + f + 1))
                                dve.wait_ge(out_taken[0], e * 2 + (o2 + f + 1))
                                high, low = (x[:, bass.ds(e * 2 + f, 1), :].rearrange("p a n -> p (a n)") for x in Hparts)
                                dve.tensor_tensor(hid[:, :], hu[:, :], sl[:, f % 2, :], ALU.mult).then_inc(hu_used, 1)
                                dve.wait_ge(hu_used, e * 2 + (2 * EP * part + f + 1))
                                split(dve, hid[:, :], high, low, h_high, e * 2 + (2 * EP * part + f + 1))\
                                    .then_inc(he_done, 1)

                            def take_down(it, n):
                                if n % 2 == 0:
                                    return
                                output_here(dve, f"down{part}", it, n)
                                pair = n // 2 % 2
                                dve_add(dve, xT[:, bass.ds(it * 2 + n // 2, 1), :].rearrange("p a n -> p (a n)"), pair)\
                                    .then_inc(out_taken[pair], 2)

                            if part == 0:
                                spread(0)
                            split_and_take(dve, EP, split_up, take_up)
                            split_and_take(dve, KT // 2,
                                           lambda it, u: split_weights(dve, f"down{part}", it, u, wparts), take_down)

            with ExitStack() as c12:
                yt = c12.enter_context(nc.sbuf_tensor("yt", [P, 2, D], F32))
                f_mm, f_out, y_stored = sem("f_mm"), sem("f_out"), [sem(f"y_stored{j}") for j in range(2)]
                with nc.Block() as block:
                    @block.tensor
                    def _(pe):
                        norm_pe(pe, 4, yT)
                        pe.wait_ge(norm_ready, 5 * KT)
                        for q in range(QT + 1):
                            rows, at = (P, P * q) if q < QT else (TS, TP)
                            for half in range(2):
                                n = 2 * q + half
                                if n >= 2:
                                    pe.wait_ge(f_out, n - 1)
                                for i in range(4):
                                    mm = pe.transpose(work[n % 2][0:rows, P * i:P * i + P],
                                                      yT[:, 4 * half + i, at:at + rows], ident)
                                mm.then_inc(f_mm, 1)

                    @block.scalar
                    def _(act):
                        norm_act(act, 4, xT, yT)

                    @block.vector
                    def _(dve):
                        norm_dve(dve, 4, xT, V_FIN, yT)
                        for n in range(2 * QT + 2):
                            q, half = n // 2, n % 2
                            rows = P if q < QT else TS
                            dve.wait_ge(f_mm, n + 1)
                            if q >= 2:
                                dve.wait_ge(y_stored[q % 2], 16 * (q // 2))
                            dve.tensor_copy(yt[0:rows, q % 2, 512 * half:512 * half + 512], work[n % 2][0:rows, :])\
                                .then_inc(f_out, 1)

                    @block.sync
                    def _(sp):
                        for q in range(QT + 1):
                            sp.wait_ge(f_out, 2 * q + 2)
                            if q < QT:
                                sp.dma_start(O["y_prompt"][0, P * q:P * q + P, :], yt[:, q % 2, :]).then_inc(y_stored[q % 2], 16)
                            else:
                                sp.dma_start(O["y_sample"].rearrange("b t n -> (b t) n"), yt[0:TS, q % 2, :])\
                                    .then_inc(y_stored[q % 2], 16)
                        sp.wait_ge(y_stored[0], 16 * 3)
                        sp.wait_ge(y_stored[1], 16 * 2)
                        sp.wait_ge(out_dma, stores[0])


_OUTS = [("y_prompt", (1, TP, D)), ("y_sample", (NB, ST, D)),
         ("kv_p", (1, 1, TP, 4, G, HD)), ("kv_s", (1, NB, ST, 4, G, HD)),
         ("win_p", (1, 1, WIN, 2, G, HD)), ("win_s", (1, NB, WIN, 2, G, HD)),
         ("C_p", (1, 1, MLH, HD, HD)), ("C_s", (1, NB, MLH, HD, HD)),
         ("n_p", (1, 1, MLH, HD)), ("n_s", (1, NB, MLH, HD)),
         ("m_p", (1, 1, MLH)), ("m_s", (1, NB, MLH)),
         ("h_p", (1, 1, 256)), ("h_s", (1, NB, 256)),
         ("conv_p", (1, 1, 3, 256)), ("conv_s", (1, NB, 3, 256)),
         ("mem_p", (1, 1, NM, 2, XH, XD))]


def kernel(**inputs):
    import concourse.bacc as _bacc
    from concourse.bass_utils import run_bass_kernel_spmd as _run

    nc = _bacc.Bacc("TRN2", target_bir_lowering=False, num_devices=1)
    arrays, ins = {}, {}
    for name, a in inputs.items():
        a = np.ascontiguousarray(a)
        arrays[f"in_{name}"] = a
        ins[name] = nc.dram_tensor(f"in_{name}", a.shape, mybir.dt.from_np(a.dtype), kind="ExternalInput").ap()
    consts = {}
    for name, a in zip(("const", "prompt", "past"), shape_constants()):
        a = np.ascontiguousarray(a)
        arrays[f"shape_{name}"] = a
        consts[name] = nc.dram_tensor(f"shape_{name}", a.shape, F32, kind="ExternalInput").ap()
    outs = {}
    for name, shape in _OUTS:
        outs[name] = nc.dram_tensor(f"out_{name}", shape, F32, kind="ExternalOutput").ap()
    build(nc, ins, outs, consts)
    r = _run(nc, [arrays], core_ids=[0])
    return tuple(r.results[0][f"out_{name}"] for name, _ in _OUTS)
```

```python
from contextlib import ExitStack

import numpy as np

import concourse.bass as bass
from concourse import mybir

F32 = mybir.dt.float32
I32 = mybir.dt.int32
F32R = mybir.dt.float32r
ALU = mybir.AluOpType
ACT = mybir.ActivationFunctionType
AX = mybir.AxisListType.X

P = 128
D = 1024
KT = D // P
TP = 512
NB, ST = 8, 4
TS = NB * ST
NT = TP + TS
QT = TP // P
HD = 64
MLH = 4
G, REP = 2, 4
PAGE, PAST = 128, 4096
NPB = PAST // PAGE
CT = PAST // 256
NCB = PAST // 32
PCB = TP // 32
WIN = 512
XH, XD, NM = 4, 128, 256
NE, FF = 16, 256
HALF = NT // 2
EPS = 1e-6
NEG = -1e30
RING = 4

O_MLQ, O_I, O_F, O_LRU, O_NQ, O_KV, O_GATE = 0, 1024, 1028, 1032, 1544, 2056, 2824
T_Q, T_K, T_V, T_O, T_X, T_GL, T_NQ, T_KC, T_VC, T_KS, T_VS, T_KW, T_VW, T_IF, T_GT = \
    0, 2, 4, 6, 8, 10, 12, 16, 17, 18, 19, 20, 21, 22, 23
NPT = 24
V_MIX, V_XA, V_MEM, V_FFN, V_FIN, V_Y, V_CW, V_CB, V_BA, V_BX, V_LAM, V_PB, V_END = \
    0, 8, 16, 24, 32, 40, 48, 56, 58, 60, 62, 64, 66

CONST = {}
_at = 0
for _name, _n in (("ident", P), ("ones", P), ("headones", P), ("causal", P), ("blocked", P), ("eps", 1),
                  ("pair0", P), ("pair1", P), ("head0", P), ("head1", P), ("head2", P), ("head3", P),
                    ("sblocked", TS), ("inb", NB), ("grp", 32), ("bonus", 65),
                  ("bcmp", NCB), ("bwin", WIN), ("bnew", NB * TS), ("pcmp", QT * 8 * PCB), ("pvalid", QT * PCB),
                   ("vplace", 8)):
    CONST[_name] = (_at, _n)
    _at += _n
NCONST = _at


def shape_constants():
    c = np.zeros((P, NCONST), np.float32)

    def put(name, a):
        o, n = CONST[name]
        a = np.asarray(a, np.float32).reshape(len(a), n)
        c[:len(a), o:o + n] = a

    i = np.arange(P)
    put("ident", np.eye(P))
    put("ones", np.ones((P, P)))
    put("headones", i[:, None] // HD == i[None, :] // HD)
    put("causal", np.where(i[None, :] <= i[:, None], 0, NEG))
    put("blocked", np.where(i[:, None] <= i[None, :], 0, -NEG))
    put("eps", np.full((P, 1), EPS))
    for k in range(2):
        put(f"pair{k}", np.arange(MLH)[:, None] == 2 * k + i[None, :] // HD)
    for h in range(MLH):
        put(f"head{h}", (np.arange(MLH)[:, None] == h) & np.ones((1, P), bool))
    s = np.arange(TS)
    same = s[:, None] // ST == s[None, :] // ST
    put("sblocked", np.where(same & (s[:, None] <= s[None, :]), 0, -NEG))
    put("inb", s[:, None] // ST == np.arange(NB)[None, :])
    row_h, row_t = s // ST, s % ST
    put("grp", (row_h[:, None] // REP == row_h[None, :] // REP) & (row_t[:, None] == row_t[None, :]))
    bonus = np.zeros((32, 65))
    bonus[:, [0, 63, 64]] = 100.0
    put("bonus", bonus)
    slope = 2.0 ** -(row_h + 1.0)
    qpos = PAST + row_t
    put("bcmp", -slope[:, None] * (qpos[:, None] - (np.arange(NCB) * 32 + 31)[None, :]))
    kpos = PAST - WIN + np.arange(WIN)
    dist = qpos[:, None] - kpos[None, :]
    put("bwin", np.where(dist < WIN, -slope[:, None] * dist, NEG))
    new = np.empty((32, NB, TS))
    for b in range(NB):
        back = row_t[:, None] - (s % ST)[None, :]
        new[:, b] = np.where((s // ST == b)[None, :] & (back >= 0), -slope[:, None] * back, NEG)
    put("bnew", new)
    hs = 2.0 ** -(np.arange(8) + 1.0)
    q = np.arange(TP).reshape(QT, P).T
    dist = q[:, :, None] - (np.arange(PCB) * 32 + 31)[None, None, :]
    put("pcmp", np.where(dist >= 0, 0, NEG)[:, :, None, :] - hs[None, None, :, None] * dist[:, :, None, :])
    put("pvalid", dist >= 0)
    col = np.arange(8)
    put("vplace", (i[:, None] // 64 == col[None, :] % 2) & (i[:, None] // 16 % 4 == col[None, :] // 2))
    rel = np.arange(TP)[None, :] - (TP - P) - i[:, None]
    prompt = np.where(rel[:, None, :] <= 0, hs[None, :, None] * rel[:, None, :], NEG).astype(np.float32)
    past = (slope[:, None] * (np.arange(PAST)[None, :] - qpos[:, None])).astype(np.float32)
    heads = np.zeros((P, KT * 16 + D), np.float32)
    for k in range(KT):
        heads[i, 16 * k + 2 * k + i // HD] = 1
    heads[np.arange(D) // HD, KT * 16 + np.arange(D)] = 1
    return c, prompt, past, heads


class Chain:

    def __init__(self, eng, sem, base=0):
        self.eng, self.sem, self.base, self.n = eng, sem, base, 0

    def step(self, ins):
        self.n += 1
        ins.then_inc(self.sem, 1)
        self.eng.wait_ge(self.sem, self.base + self.n)


class Semaphores:

    def __init__(self, nc):
        self.nc, self.part = nc, []

    def __call__(self, name):
        self.part.append(self.nc.alloc_semaphore(name=name))
        return self.part[-1]

    def keep(self):
        self.part = []

    def end_part(self):
        self.nc.clear_and_free_semaphores(self.part)
        self.part = []
        self.nc.all_engine_barrier()


def build(nc, I, O, K):
    with ExitStack() as ctx:
        sem = Semaphores(nc)

        def sb(name, shape, dt=F32):
            return ctx.enter_context(nc.sbuf_tensor(name, shape, dt))

        bank = [ctx.enter_context(nc.psum_tensor(f"bank{n}", [P, 512], F32)) for n in range(8)]
        gemm_big, gemm_small = bank[0:2], bank[2:4]
        work = bank[4:8]

        cst = sb("cst", [P, NCONST])
        vecT = sb("vecT", [P, V_END])
        xT = sb("xT", [P, KT, NT])
        ring = sb("ring", [P, RING, KT, P])
        yT = sb("yT", [P, KT, NT])
        memtok = sb("memtok", [P, 2, 2 * XH * XD])

        def const(name, rows=P):
            o, n = CONST[name]
            return cst[0:rows, o:o + n]

        ident = const("ident")

        w_loaded = [sem(f"w_loaded{u}") for u in range(RING)]
        w_high, w_split = sem("w_high"), [sem(f"w_split{p}") for p in range(2)]
        w_done = [sem(f"w_done{p}") for p in range(2)]
        out_taken = [sem(f"out_taken{p}") for p in range(2)]

        stage, first, dmas = {}, RING, 0
        for name, n, pieces in (("in", 24, 2), ("mem", 8, 1), ("out", 8, 3), ("xq", 4, 1), ("xo", 8, 1),
                                ("up0", 2 * NE, 1), ("down0", 16, 1), ("up1", 2 * NE, 1), ("down1", 16, 1)):
            stage[name] = (first, pieces, dmas)
            first += n
            dmas += 16 * pieces * n // RING

        def slot_free(sp, name, it, u):
            sp.wait_ge(w_done[u % 2], stage[name][0] // 2 + 2 * it + u // 2 - 1)

        def split(dve, x, high, low, high_sem, n):
            dve.tensor_copy(high, x).then_inc(high_sem, 1)
            dve.wait_ge(high_sem, n)
            return dve.tensor_tensor(low, x, high.bitcast(F32), ALU.subtract)

        def split_weights(dve, name, it, u, parts, kts=KT):
            at, pieces, before = stage[name]
            dve.wait_ge(w_done[u % 2], it * 2 + (at // 2 + u // 2))
            dve.wait_ge(w_loaded[u], 16 * pieces * it + before + 16 * pieces)
            high, low = (x[:, u % 2, 0:kts, :] for x in parts)
            split(dve, ring[:, u, 0:kts, :], high, low, w_high, it * RING + (at - RING + u + 1))\
                .then_inc(w_split[u % 2], 1)

        def split_first(split_):
            split_(0, 0)
            split_(0, 1)

        def split_and_take(eng, n_turns, split_, take):
            for u in (2, 3):
                take(0, u - 2)
                split_(0, u)
            if n_turns > 1:
                with eng.Fori(1, n_turns) as it:
                    for u in range(RING):
                        take(it, u - 2)
                        split_(it, u)
            take(n_turns - 1, 2)
            take(n_turns - 1, 3)

        def halves(par, width=NT):
            if width <= TP:
                return [(gemm_big[par][:, 0:width], 0)]
            return [(gemm_big[par][:, 0:HALF], 0), (gemm_small[par][:, 0:HALF], HALF)]

        def product(pe, outs, w, x, start, stop):
            (w_hi, w_lo), (x_hi, x_lo) = w, x
            for m, (a, c) in enumerate(((w_lo, x_hi), (w_hi, x_lo), (w_hi, x_hi))):
                for out, at in outs:
                    mm = pe.matmul(out, a, c[:, at:at + out.shape[1]], start=start and m == 0, stop=stop and m == 2)
            return mm

        def pe_gemm(pe, name, n_tiles, kts, rhs, parts, x_before, width=NT, between=None):
            o2 = stage[name][0] // 2
            with pe.Fori(0, n_tiles // RING) as it:
                for u in range(RING):
                    par = u % 2
                    if between and u == 1:
                        between(it)
                    pe.wait_ge(w_split[par], it * 2 + (o2 + u // 2 + 1))
                    pe.wait_ge(out_taken[par], it * 2 + (o2 + u // 2))
                    for k in range(kts):
                        pe.wait_ge(x_split, x_before + k + 1)
                        mm = product(pe, halves(par, width), [x[:, par, k, :] for x in parts], rhs(k),
                                     k == 0, k == kts - 1)
                    mm.then_inc(w_done[par], 1)

        def output_here(eng, name, it, u):
            eng.wait_ge(w_done[u % 2], it * 2 + stage[name][0] // 2 + u // 2 + 1)

        def act_copy(act, dst, par, n=NT):
            for bank_, at in halves(par, n):
                last = act.activation(dst[:, at:at + bank_.shape[1]], bank_, ACT.Copy)
            return last

        def dve_copy(dve, dst, par, n=NT):
            for bank_, at in halves(par, n):
                last = dve.tensor_copy(dst[:, at:at + bank_.shape[1]], bank_)
            return last

        def dve_add(dve, dst, par):
            for bank_, at in halves(par):
                last = dve.tensor_tensor(dst[:, at:at + HALF], bank_, dst[:, at:at + HALF], ALU.add)
            return last

        sq_ready, ss_ready = sem("sq_ready"), sem("ss_ready")
        std_ready, rstd_ready, norm_ready = sem("std_ready"), sem("rstd_ready"), sem("norm_ready")
        sums = work[2:4]
        spare = sb("spare", [1, 8])
        stdt = sb("stdt", [P, NT])

        def norm_act(act, k, x, out, width=NT, after=None):
            for t in range(KT):
                if after:
                    act.wait_ge(out_taken[t % 2], stage[after][0] // 2 + t // 2 + 1)
                act.activation(out[:, t, 0:width], x[:, t, 0:width], ACT.Square).then_inc(sq_ready, 1)
            act.wait_ge(ss_ready, k + 1)
            if k:
                act.wait_ge(norm_ready, KT * k)
            w = min(width, HALF)
            if width > HALF:
                act.activation(stdt[:, HALF:NT], sums[1][:, 0:HALF], ACT.Sqrt, bias=const("eps"), scale=1.0 / D)
            act.activation(stdt[:, 0:w], sums[0][:, 0:w], ACT.Sqrt, bias=const("eps"),
                           scale=1.0 / D).then_inc(std_ready, 1)

        def norm_pe(pe, k, out, width=NT):
            w = min(width, HALF)
            if k:
                pe.wait_ge(std_ready, k)
            for t in range(KT):
                pe.wait_ge(sq_ready, KT * k + t + 1)
                ends = dict(start=(t == 0), stop=(t == KT - 1))
                if width > HALF:
                    pe.matmul(sums[1][:, 0:HALF], const("ones"), out[:, t, HALF:NT], **ends)
                mm = pe.matmul(sums[0][:, 0:w], const("ones"), out[:, t, 0:w], **ends)
            mm.then_inc(ss_ready, 1)

        def norm_dve(dve, k, x, gain, out, width=NT):
            dve.wait_ge(std_ready, k + 1)
            dve.reciprocal(stdt[:, 0:width], stdt[:, 0:width]).then_inc(rstd_ready, 1)
            dve.wait_ge(rstd_ready, k + 1)
            for t in range(KT):
                dve.scalar_tensor_tensor(out=out[:, t, 0:width], in0=x[:, t, 0:width],
                                         scalar=vecT[:, gain + t:gain + t + 1], in1=stdt[:, 0:width],
                                         op0=ALU.mult, op1=ALU.mult).then_inc(norm_ready, 1)

        x_high, x_split, x_cuts = sem("x_high"), sem("x_split"), [0]

        def split_x(dve, x, parts, tiles_, width=NT):
            for t in tiles_:
                x_cuts[0] += 1
                split(dve, x[:, t, 0:width], parts[0][:, t, 0:width], parts[1][:, t, 0:width], x_high, x_cuts[0])\
                    .then_inc(x_split, 1)

        def norm_split(dve, k, x, gain, out, parts, width=NT):
            before = x_cuts[0]
            dve.wait_ge(std_ready, k + 1)
            dve.reciprocal(stdt[:, 0:width], stdt[:, 0:width]).then_inc(rstd_ready, 1)
            dve.wait_ge(rstd_ready, k + 1)
            for t in range(KT + 2):
                if t < KT:
                    dve.scalar_tensor_tensor(out=out[:, t, 0:width], in0=x[:, t, 0:width],
                                             scalar=vecT[:, gain + t:gain + t + 1], in1=stdt[:, 0:width],
                                             op0=ALU.mult, op1=ALU.mult).then_inc(norm_ready, 1)
                if 1 <= t <= KT:
                    dve.wait_ge(norm_ready, KT * k + t)
                    dve.tensor_copy(parts[0][:, t - 1, 0:width], out[:, t - 1, 0:width]).then_inc(x_high, 1)
                if t >= 2:
                    dve.wait_ge(x_high, before + t - 1)
                    dve.tensor_tensor(parts[1][:, t - 2, 0:width], out[:, t - 2, 0:width],
                                      parts[0][:, t - 2, 0:width].bitcast(F32), ALU.subtract).then_inc(x_split, 1)
            x_cuts[0] += KT

        const_here = sem("const_here")
        out_dma = sem("out_dma")
        stores = [0]

        def store(eng, dst, src, scattered=False):
            stores[0] += 16
            return eng.dma_start(dst, src, allow_slow_non_contiguous=scattered).then_inc(out_dma, 16)

        QB = sb("QB", [P, NB, 32])
        ksn, kwn = sb("ksn", [P, TS]), sb("kwn", [P, TS])
        vnew = sb("vnew", [TS, 2, P])
        gq = sb("gq", [32, NB, 3])
        hb = sb("hb", [P, 2])
        gate_dram = nc.dram_tensor("gate_dram", (TS, 24), F32).ap()

        sem.keep()

        mixed = ctx.enter_context(ExitStack())
        pT = mixed.enter_context(nc.sbuf_tensor("pT", [P, NPT, NT], F32))
        memkv = mixed.enter_context(nc.sbuf_tensor("memkv", [P, 2 * XH, NM], F32))
        TK, TV, TOKKV = 0, 2, 4
        TGATE = 10
        with ExitStack() as c1:
            hparts = [c1.enter_context(nc.sbuf_tensor(n, [P, KT, NT], F32R)) for n in ("h_high", "h_low")]
            hmparts = [c1.enter_context(nc.sbuf_tensor(n, [P, KT, NM], F32R)) for n in ("hm_high", "hm_low")]
            wparts = [c1.enter_context(nc.sbuf_tensor(n, [P, 2, KT, P], F32R)) for n in ("w1_high", "w1_low")]
            xtok = c1.enter_context(nc.sbuf_tensor("xtok", [P, 2, D], F32))
            mT = yT
            hT, hmT, vecs = pT[:, 0:KT, :], pT[:, KT:2 * KT, 0:NM], pT[0:V_END, 2 * KT, 0:P]
            vecs_here, rest_here = sem("vecs_here"), sem("rest_here")
            x_here = [sem(f"x_here{j}") for j in range(2)]
            turned, turned_out = sem("turned"), sem("turned_out")
            tiles = [(P, xT, P * q) for q in range(QT)] + [(TS, xT, TP)] + [(P, mT, 0), (P, mT, P)]

            block = nc.Block()
            with block:
                @block.sync
                def _(sp):
                    sp.dma_start(cst[:, 0:P], K["const"][:, 0:P]).then_inc(const_here, 16)
                    xs = [I["x_prompt"][0, P * q:P * q + P, :] for q in range(QT)]
                    xs += [I["x_sample"].rearrange("b t n -> (b t) n")]
                    xs += [I["mem_prompt"][0, P * q:P * q + P, :] for q in range(2)]
                    for n, src in enumerate(xs):
                        if n >= 2:
                            sp.wait_ge(turned, 2 * n - 2)
                        sp.dma_start(xtok[0:tiles[n][0], n % 2, :], src).then_inc(x_here[n % 2], 16)
                        if n == 1:
                            sp.dma_start(cst[:, P:NCONST], K["const"][:, P:NCONST]).then_inc(rest_here, 16)
                    w = I["w_in"][0].rearrange("(k p) n -> p k n", p=P)
                    for n in range(NPT):
                        u = n % RING
                        slot_free(sp, "in", n // RING, u)
                        if n < T_X:
                            cols = [(0, 64, O_MLQ + P * n), (64, 64, O_MLQ + P * n + 64)]
                        elif n < T_NQ:
                            cols = [(0, 64, O_LRU + P * (n - T_X)), (64, 64, O_LRU + P * (n - T_X) + 64)]
                        elif n < T_KC:
                            cols = [(64 * g, 64, O_NQ + 256 * g + 64 * (n - T_NQ)) for g in range(G)]
                        elif n < T_IF:
                            cols = [(0, 64, O_KV + P * (n - T_KC)), (64, 64, O_KV + P * (n - T_KC) + 64)]
                        elif n == T_IF:
                            cols = [(0, 4, O_I), (32, 4, O_F)]
                        else:
                            cols = [(0, 12, O_GATE), (12, 12, O_GATE + 12)]
                        for dst, m, src in cols:
                            sp.dma_start(ring[:, u, :, dst:dst + m], w[:, :, src:src + m]).then_inc(w_loaded[u], 16)
                    w = I["xa_wkv"][0].rearrange("(k p) n -> p k n", p=P)
                    for n in range(8):
                        slot_free(sp, "mem", n // RING, n % RING)
                        sp.dma_start(ring[:, n % RING, :, :], w[:, :, P * n:P * n + P]).then_inc(w_loaded[n % RING], 16)

                @block.gpsimd
                def _(pool):
                    for n, s_ in enumerate(w_done + w_split + out_taken):
                        pool.memset(spare[0:1, n:n + 1], 0.0).then_inc(s_, RING // 2)
                    rows = [(V_MIX, I["norm_mix"][0]), (V_XA, I["norm_xa"][0]), (V_MEM, I["norm_mem"][0]),
                            (V_FFN, I["norm_ffn"][0]), (V_FIN, I["final_norm"]), (V_CB, I["conv_b"][0]),
                            (V_BA, I["lru_ba"][0]), (V_BX, I["lru_bx"][0]), (V_LAM, I["lru_lambda"][0]),
                            (V_Y, I["mix_norm"][0, 0:512])]
                    for at, v in rows:
                        n = v.shape[0] // P
                        pool.dma_start(vecs[at:at + n, :], v.rearrange("(k p) -> k p", p=P)).then_inc(vecs_here, 16)
                    for g in range(G):
                        pool.dma_start(vecs[V_Y + 4:V_Y + 8, 64 * g:64 * g + 64],
                                       I["mix_norm"][0, 512 + 256 * g:768 + 256 * g]
                                       .rearrange("(r d) -> r d", r=REP)).then_inc(vecs_here, 16)
                    pool.dma_start(vecs[V_CW:V_CW + 8, :], I["conv_w"][0].rearrange("j (k p) -> (j k) p", p=P))\
                        .then_inc(vecs_here, 16)
                    pool.dma_start(vecs[V_PB:V_PB + 2, :], I["phi_b1"][0]).then_inc(vecs_here, 16)

                @block.tensor
                def _(pe):
                    pe.wait_ge(const_here, 16)
                    n = 0
                    for j, (rows, _, _) in enumerate(tiles):
                        pe.wait_ge(x_here[j % 2], 16 * (j // 2 + 1))
                        for half in range(2):
                            if n >= 2:
                                pe.wait_ge(turned_out, n - 1)
                            for i in range(4):
                                k = 4 * half + i
                                mm = pe.transpose(work[n % 2][:, P * i:P * i + rows],
                                                  xtok[0:rows, j % 2, P * k:P * k + P], ident[0:rows, 0:rows])
                            mm.then_inc(turned, 1)
                            n += 1
                    pe.wait_ge(vecs_here, 16 * 14)
                    pe.wait_ge(turned_out, n - 1)
                    pe.transpose(work[n % 2][:, 0:V_END], vecs, ident[0:V_END, 0:V_END]).then_inc(turned, 1)
                    pe.wait_ge(rest_here, 16)
                    norm_pe(pe, 0, hT)
                    norm_pe(pe, 1, hmT, NM)
                    pe_gemm(pe, "in", NPT, KT, lambda k: [x[:, k, :] for x in hparts], wparts, 0)
                    pe_gemm(pe, "mem", 8, KT, lambda k: [x[:, k, :] for x in hmparts], wparts, KT, NM)

                @block.scalar
                def _(act):
                    act.wait_ge(rest_here, 16)
                    act.wait_ge(turned_out, 15)
                    norm_act(act, 0, xT, hT)
                    norm_act(act, 1, mT, hmT, NM)
                    with act.Fori(0, NPT // RING) as it:
                        for u in (0, 2):
                            output_here(act, "in", it, u)
                            act_copy(act, pT[:, bass.ds(it * RING + u, 1), :].rearrange("p a n -> p (a n)"), 0)\
                                .then_inc(out_taken[0], 1)
                    for n in range(0, 8, 2):
                        output_here(act, "mem", n // RING, n % RING)
                        act_copy(act, memkv[:, n, :], 0, NM).then_inc(out_taken[0], 1)

                @block.vector
                def _(dve):
                    n = 0
                    for rows, dst, at in tiles:
                        for half in range(2):
                            dve.wait_ge(turned, n + 1)
                            dve.tensor_copy(dst[:, 4 * half:4 * half + 4, at:at + rows],
                                            work[n % 2][:, :].rearrange("p (k c) -> p k c", k=4)[:, :, 0:rows])\
                                .then_inc(turned_out, 1)
                            n += 1
                    dve.wait_ge(turned, n + 1)
                    dve.tensor_copy(vecT[:, :], work[n % 2][:, 0:V_END]).then_inc(turned_out, 1)
                    dve.wait_ge(turned_out, n + 1)
                    def split_in(it, u):
                        split_weights(dve, "in", it, u, wparts)

                    split_first(split_in)
                    norm_split(dve, 0, xT, V_MIX, hT, hparts)
                    norm_split(dve, 1, mT, V_MEM, hmT, hmparts, NM)

                    def take_in(it, n):
                        if n % 2:
                            output_here(dve, "in", it, n)
                            dve_copy(dve, pT[:, bass.ds(it * RING + n, 1), :].rearrange("p a n -> p (a n)"), 1)\
                                .then_inc(out_taken[1], 1)

                    split_and_take(dve, NPT // RING, split_in, take_in)

                    def split_mem(it, u):
                        split_weights(dve, "mem", it, u, wparts)

                    def take_mem(it, n):
                        if n % 2:
                            output_here(dve, "mem", it, n)
                            dve_copy(dve, memkv[:, bass.ds(it * RING + n, 1), :].rearrange("p a n -> p (a n)"), 1, NM)\
                                .then_inc(out_taken[1], 1)

                    split_first(split_mem)
                    split_and_take(dve, 2, split_mem, take_mem)


        tok = mixed.enter_context(nc.sbuf_tensor("tok", [P, QT, 11, P], F32))
        toks = mixed.enter_context(nc.sbuf_tensor("toks", [TS, 11, P], F32))
        gate_p = mixed.enter_context(nc.sbuf_tensor("gate_p", [P, QT, 24], F32))
        gate_s = mixed.enter_context(nc.sbuf_tensor("gate_s", [TS, 24], F32))
        lru_state = mixed.enter_context(nc.sbuf_tensor("lru_state", [32, 256], F32))
        lruT = mixed.enter_context(nc.sbuf_tensor("lruT", [P, 2, 32], F32))
        state_here, tok_turned = sem("state_here"), sem("tok_turned")
        tok_copied = [sem("tok_copied_act"), sem("tok_copied_dve")]
        to_turn = [T_K, T_K + 1, T_V, T_V + 1, T_KC, T_VC, T_KS, T_VS, T_KW, T_VW, T_GT]
        groups = []
        for q in range(QT + 1):
            at, rows = (P * q, P) if q < QT else (TP, TS)
            for j in range(0, len(to_turn), 4):
                part = to_turn[j:j + 4]
                dst = tok[:, q, j:j + len(part), :] if q < QT else toks[:, j:j + len(part), :]
                groups.append(([pT[:, t, at:at + rows] for t in part], rows, dst))
        for q in range(2):
            for j in range(0, 8, 4):
                groups.append(([memkv[:, j + i, P * q:P * q + P] for i in range(4)], P,
                               memtok[:, q, P * j:P * j + 512].rearrange("p (k c) -> p k c", k=4)))

        with nc.Block() as block:
            @block.sync
            def _(sp):
                sp.dma_start(lru_state[0:24, :], I["state_rglru_conv"][0].rearrange("b j w -> (b j) w"))\
                    .then_inc(state_here, 16)
                sp.dma_start(lru_state[24:32, :], I["state_rglru_h"][0]).then_inc(state_here, 16)
                store(sp, O["win_s"][0, :, 0:WIN - ST].rearrange("b t c g d -> b (t c g d)"),
                      I["state_nsa_win"][0, :, ST:WIN].rearrange("b t c g d -> b (t c g d)"))
                n = 0
                for q in range(QT + 1):
                    n += 3
                    sp.wait_ge(tok_copied[0], (n + 1) // 2)
                    sp.wait_ge(tok_copied[1], n // 2)
                    if q < QT:
                        rows = slice(P * q, P * q + P)
                        store(sp, O["kv_p"][0, 0, rows].rearrange("t c g d -> t (c g d)"),
                              tok[:, q, TOKKV:TOKKV + 4, :].rearrange("p c n -> p (c n)"))
                        store(sp, O["win_p"][0, 0, rows].rearrange("t c g d -> t (c g d)"),
                              tok[:, q, TOKKV + 4:TOKKV + 6, :].rearrange("p c n -> p (c n)"))
                    else:
                        store(sp, O["kv_s"][0].rearrange("b t c g d -> (b t) (c g d)"),
                              toks[:, TOKKV:TOKKV + 4, :].rearrange("p c n -> p (c n)"))
                        for b in range(NB):
                            store(sp, O["win_s"][0, b, WIN - ST:WIN].rearrange("t c g d -> t (c g d)"),
                                  toks[ST * b:ST * b + ST, TOKKV + 4:TOKKV + 6, :].rearrange("p c n -> p (c n)"))
                for q in range(2):
                    n += 2
                    sp.wait_ge(tok_copied[0], (n + 1) // 2)
                    sp.wait_ge(tok_copied[1], n // 2)
                    store(sp, O["mem_p"][0, 0, P * q:P * q + P].rearrange("t c h d -> t (c h d)"), memtok[:, q, :])

            @block.tensor
            def _(pe):
                for n, (srcs, rows, _) in enumerate(groups):
                    if n >= 4:
                        pe.wait_ge(tok_copied[n % 2], n // 2 - 1)
                    for i, src in enumerate(srcs):
                        mm = pe.transpose(work[n % 4][0:rows, P * i:P * i + P], src, ident)
                    mm.then_inc(tok_turned, 1)
                pe.wait_ge(state_here, 32)
                pe.wait_ge(tok_copied[0], len(groups) // 2 + len(groups) % 2 - 1)
                pe.wait_ge(tok_copied[1], len(groups) // 2)
                n = len(groups)
                for k in range(2):
                    mm = pe.transpose(work[n % 4][:, 32 * k:32 * k + 32], lru_state[:, P * k:P * k + P],
                                      ident[0:32, 0:32])
                mm.then_inc(tok_turned, 1)

            def copy_out(eng, par):
                for n, (srcs, rows, dst) in enumerate(groups):
                    if n % 2 == par:
                        eng.wait_ge(tok_turned, n + 1)
                        src = work[n % 4][0:rows, 0:P * len(srcs)].rearrange("p (k c) -> p k c", c=P)
                        ins = eng.activation(dst, src, ACT.Copy) if par == 0 else eng.tensor_copy(dst, src)
                        ins.then_inc(tok_copied[par], 1)

            @block.scalar
            def _(act):
                copy_out(act, 0)
                act.wait_ge(tok_copied[0], 8)
                act.wait_ge(tok_copied[1], 7)
                act.activation(gate_p[:, :, :], tok[:, :, TGATE, 0:24], ACT.Sigmoid)
                act.activation(gate_s[:, :], toks[:, TGATE, 0:24], ACT.Sigmoid)

            @block.vector
            def _(dve):
                copy_out(dve, 1)
                dve.wait_ge(tok_turned, len(groups) + 1)
                dve.tensor_copy(lruT[:, :, :],
                                work[len(groups) % 4][:, 0:64].rearrange("p (k c) -> p k c", k=2))

        with ExitStack() as c3:
            def t3(name, shape):
                return c3.enter_context(nc.sbuf_tensor(name, shape, F32))

            XP = TP + 3
            xpad = t3("xpad", [P, 2, XP])
            xsam = t3("xsam", [P, 2, NB, ST + 3])
            xc = t3("xc", [P, 2, NT])
            wab = t3("wab", [P, 2, 2, P])
            gr = t3("gr", [P, 2, NT])
            gi = t3("gi", [P, 2, NT])
            th = t3("th", [P, 2, NT])
            hseq = t3("hseq", [P, 2, NT])
            lam = t3("lam", [P, 8, 2])
            hl = t3("hl", [P, 2, 9])
            cl = t3("cl", [P, 2, 27])
            hlT = t3("hlT", [9, 2, P])
            clT = t3("clT", [27, 2, P])
            w_zero, w_here, chain, lru_mm = sem("lru_zero"), sem("lru_w"), sem("lru_chain"), sem("lru_mm")
            conv_done, gates_done, sp_done = sem("conv_done"), sem("gates_done"), sem("softplus_done")
            lru_act, last_done, last_turned, last_out = (
                sem("lru_act"), sem("lru_last"), sem("lru_turned"), sem("lru_last_out"))
            lam_in = sem("lam_in")

            with nc.Block() as block:
                @block.sync
                def _(sp):
                    sp.wait_ge(w_zero, 1)
                    for j, name in enumerate(("lru_wa", "lru_wx")):
                        for k in range(4):
                            o = 64 * (k % 2)
                            sp.dma_start(wab[o:o + 64, j, k // 2, o:o + 64], I[name][0, k]).then_inc(w_here, 16)
                    sp.wait_ge(last_out, 2)
                    for k in range(2):
                        cols = slice(P * k, P * k + P)
                        store(sp, O["h_p"][0, :, cols], hlT[0:1, k, :])
                        store(sp, O["h_s"][0, :, cols], hlT[1:9, k, :])
                        store(sp, O["conv_p"][0, 0, :, cols], clT[0:3, k, :])
                        store(sp, O["conv_s"][0, :, :, cols].rearrange("b j w -> (b j) w"), clT[3:27, k, :])

                @block.gpsimd
                def _(pool):
                    pool.memset(wab[:, :, :, :], 0.0).then_inc(w_zero, 1)

                @block.tensor
                def _(pe):
                    pe.wait_ge(w_here, 16 * 8)
                    pe.wait_ge(conv_done, 1)
                    n = 0
                    for k in range(2):
                        for j in range(2):
                            if n >= 2:
                                pe.wait_ge(gates_done, n - 1)
                            pe.matmul(gemm_big[n % 2][:, :], wab[:, j, k, :], xc[:, k, 0:TP], start=True, stop=True)
                            pe.matmul(gemm_small[n % 2][:, 0:TS], wab[:, j, k, :], xc[:, k, TP:NT],
                                      start=True, stop=True).then_inc(lru_mm, 1)
                            n += 1
                    pe.wait_ge(last_done, 1)
                    for k in range(2):
                        pe.transpose(work[0][0:9, P * k:P * k + P], hl[:, k, :], ident)
                    for k in range(2):
                        mm = pe.transpose(work[1][0:27, P * k:P * k + P], cl[:, k, :], ident)
                    mm.then_inc(last_turned, 1)

                @block.scalar
                def _(act):
                    act.wait_ge(lam_in, 1)
                    act.activation(lam[:, 1, :], lam[:, 0, :], ACT.Exp).then_inc(sp_done, 1)
                    n = 0
                    for k in range(2):
                        for j, (dst, bias) in enumerate(((gr, V_BA), (gi, V_BX))):
                            act.wait_ge(lru_mm, n + 1)
                            act.activation(dst[:, k, 0:TP], gemm_big[n % 2][:, :], ACT.Sigmoid,
                                           bias=vecT[:, bias + k:bias + k + 1])
                            act.activation(dst[:, k, TP:NT], gemm_small[n % 2][:, 0:TS], ACT.Sigmoid,
                                           bias=vecT[:, bias + k:bias + k + 1]).then_inc(gates_done, 1)
                            n += 1
                    act.wait_ge(gates_done, 4)
                    act.wait_ge(sp_done, 2)
                    for k in range(2):
                        ins = act.activation(th[:, k, :], gr[:, k, :], ACT.Tanh, scale=lam[:, 6, k:k + 1])
                    ins.then_inc(lru_act, 1)
                    for k in range(2):
                        ins = act.activation(gr[:, k, :], gr[:, k, :], ACT.Exp, scale=lam[:, 7, k:k + 1])
                    ins.then_inc(lru_act, 1)
                    act.wait_ge(lru_act, 1)
                    act.activation(th[:, :, :], th[:, :, :], ACT.Sqrt).then_inc(lru_act, 1)
                    act.activation(hseq[:, :, :], pT[:, T_GL:T_GL + 2, :], ACT.Gelu_apprx_tanh).then_inc(lru_act, 1)

                @block.vector
                def _(dve):
                    c = Chain(dve, chain)
                    c.step(dve.tensor_scalar(lam[:, 2, :], vecT[:, V_LAM:V_LAM + 2], -1.0, None, ALU.mult))
                    dve.tensor_tensor(lam[:, 0, :], lam[:, 2, :], vecT[:, V_LAM:V_LAM + 2], ALU.min).then_inc(lam_in, 1)
                    c.step(dve.memset(xpad[:, :, 0:3], 0.0))
                    c.step(dve.tensor_copy(xpad[:, :, 3:XP], pT[:, T_X:T_X + 2, 0:TP]))
                    for k in range(2):
                        dve.tensor_copy(xsam[:, k, :, 0:3], lruT[:, k, 0:24].rearrange("p (b j) -> p b j", b=NB))
                        c.step(dve.tensor_copy(xsam[:, k, :, 3:7],
                                               pT[:, T_X + k, TP:NT].rearrange("p (b t) -> p b t", b=NB)))
                    for j in range(4):
                        for k in range(2):
                            tap = vecT[:, V_CW + 2 * j + k:V_CW + 2 * j + k + 1]
                            for dst, src in ((xc[:, k, 0:TP], xpad[:, k, j:j + TP]),
                                             (xc[:, k, TP:NT].rearrange("p (b t) -> p b t", b=NB),
                                              xsam[:, k, :, j:j + ST])):
                                if j == 0:
                                    ins = dve.tensor_scalar(dst, src, tap, vecT[:, V_CB + k:V_CB + k + 1],
                                                            ALU.mult, ALU.add)
                                else:
                                    ins = dve.scalar_tensor_tensor(out=dst, in0=src, scalar=tap, in1=dst,
                                                                   op0=ALU.mult, op1=ALU.add)
                        if j < 3:
                            c.step(ins)
                        else:
                            ins.then_inc(conv_done, 1)
                    dve.wait_ge(conv_done, 1)
                    y, s, s2, acc = lam[:, 1, :], lam[:, 3, :], lam[:, 4, :], lam[:, 5, :]
                    dve.wait_ge(sp_done, 1)
                    c.step(dve.tensor_scalar(s, y, 2.0, None, ALU.add))
                    c.step(dve.reciprocal(s, s))
                    c.step(dve.tensor_tensor(s, s, y, ALU.mult))
                    c.step(dve.tensor_tensor(s2, s, s, ALU.mult))
                    c.step(dve.tensor_scalar(acc, s2, 1.0 / 19, 1.0 / 17, ALU.mult, ALU.add))
                    for m in (15, 13, 11, 9, 7, 5, 3, 1):
                        c.step(dve.tensor_tensor(acc, acc, s2, ALU.mult))
                        c.step(dve.tensor_scalar(acc, acc, 1.0 / m, None, ALU.add))
                    c.step(dve.tensor_tensor(acc, acc, s, ALU.mult))
                    c.step(dve.tensor_scalar(s, lam[:, 2, :], 0.0, 0.5, ALU.max, ALU.mult))
                    c.step(dve.tensor_tensor(acc, acc, s, ALU.add))
                    dve.tensor_scalar(lam[:, 6, :], acc, 8.0, None, ALU.mult)
                    dve.tensor_scalar(lam[:, 7, :], acc, -16.0, None, ALU.mult).then_inc(sp_done, 1)
                    dve.wait_ge(gates_done, 4)
                    c.step(dve.tensor_tensor(gi[:, :, :], gi[:, :, :], xc[:, :, :], ALU.mult))
                    dve.wait_ge(lru_act, 2)
                    c.step(dve.scalar_tensor_tensor(out=gi[:, :, :], in0=gr[:, :, :], scalar=1.0, in1=gi[:, :, :],
                                                    op0=ALU.add, op1=ALU.mult))
                    dve.wait_ge(lru_act, 3)
                    c.step(dve.tensor_tensor(gi[:, :, :], gi[:, :, :], th[:, :, :], ALU.mult))
                    h = xc
                    for k in range(2):
                        c.step(dve.tensor_tensor_scan(h[:, k, 0:TP], gr[:, k, 0:TP], gi[:, k, 0:TP], 0.0,
                                                      ALU.mult, ALU.add))
                    for k in range(2):
                        def step(x, t):
                            return x[:, k, TP:NT].rearrange("p (b t) -> p b t", t=ST)[:, :, t]
                        for t in range(ST):
                            prev = lruT[:, k, 24:32] if t == 0 else step(h, t - 1)
                            c.step(dve.tensor_tensor(step(h, t), step(gr, t), prev, ALU.mult))
                            c.step(dve.tensor_tensor(step(h, t), step(h, t), step(gi, t), ALU.add))
                    c.step(dve.tensor_copy(hl[:, :, 0:1], h[:, :, TP - 1:TP]))
                    for k in range(2):
                        c.step(dve.tensor_copy(hl[:, k, 1:9],
                                               h[:, k, TP:NT].rearrange("p (b t) -> p b t", t=ST)[:, :, ST - 1]))
                        c.step(dve.tensor_copy(cl[:, k, 3:27].rearrange("p (b j) -> p b j", b=NB),
                                               xsam[:, k, :, ST:ST + 3]))
                    dve.tensor_copy(cl[:, :, 0:3], xpad[:, :, TP:TP + 3]).then_inc(last_done, 1)
                    dve.wait_ge(lru_act, 4)
                    dve.tensor_tensor(yT[:, 2:4, :], h[:, :, :], hseq[:, :, :], ALU.mult)
                    dve.wait_ge(last_turned, 1)
                    dve.tensor_copy(hlT[:, :, :], work[0][0:9, 0:256].rearrange("p (k c) -> p k c", k=2))\
                        .then_inc(last_out, 1)
                    dve.tensor_copy(clT[:, :, :], work[1][0:27, 0:256].rearrange("p (k c) -> p k c", k=2))\
                        .then_inc(last_out, 1)

        def load_phi1(sp, dst, kv, sem_):
            sp.dma_start(dst[:, :, :], I["phi_w1"][0, kv].rearrange("(c p) h -> p c h", p=P)).then_inc(sem_, 16)

        with ExitStack() as c4:
            def t4(name, shape):
                return c4.enter_context(nc.sbuf_tensor(name, shape, F32))

            mlb = t4("mlb", [MLH, 2])
            m0 = t4("m0", [MLH, NB])
            lf, bsum, av, mx, wrow, emrow = (
                t4(n, [MLH, NT]) for n in ("lf", "bsum", "av", "mx", "wrow", "emrow"))
            mend = t4("mend", [MLH, 9])
            wcrow = t4("wcrow", [MLH, TS])
            decay = t4("decay", [MLH, NB])
            cols = t4("cols", [P, QT + 1, 2, MLH])
            sg = t4("sg", [P, 2, NT])
            wcb = t4("wcb", [P, 2, TS])
            qw = t4("qw", [HD, MLH, TS])
            nq = t4("nq", [HD, MLH, TS])
            n0 = t4("n0", [NB, 256])
            n0T = t4("n0T", [HD, MLH, NB])
            Cn = t4("Cn", [HD + 1, MLH, NB, HD])
            C0T = t4("C0T", [HD, MLH, NB, HD])
            Cp = t4("Cp", [HD + 1, MLH, HD])
            dg = t4("dg", [P, QT, P])
            idle = ring[:, :, :, :].rearrange("p u k c -> p (u k c)")
            E = idle[:, 0:2 * TP].rearrange("p (j t) -> p j t", j=2)
            W = idle[:, 2 * TP:4 * TP].rearrange("p (j t) -> p j t", j=2)
            vw = idle[:, 4 * TP:4 * TP + QT * MLH * (HD + 1)].rearrange("p (q h d) -> p q h d", q=QT, h=MLH)
            KM = idle[0:TS, 0:2 * TP].rearrange("p (j b d) -> p j b d", j=2, b=NB)
            dgs, Es, Ws = (t4(n, [TS, MLH, TS]) for n in ("dgs", "Es", "Ws"))
            vws = t4("vws", [TS, MLH, HD + 1])
            em = t4("em", [P, NT])
            dd = stdt
            ax, ones4, fx = emrow, dd[0:MLH, :], em[0:MLH, :]
            db = t4("db", [HD + 1, MLH, NB])

            ml_in, ml_chain, ml_act, rows_ready = sem("ml_in"), sem("ml_chain"), sem("ml_act"), sem("ml_rows")
            cols_mm, cols_out = sem("ml_cols_mm"), sem("ml_cols_out")
            c0_mm, c0_out = sem("c0_turned"), sem("c0_out")
            mb_ready, dg_ready, e_ready, s_ready, w_ready, pv_done = (
                sem(f"ml_{n}") for n in ("mb", "dg", "e", "s", "w", "pv"))
            fin_mm, em_out, y_done = sem("ml_fin_mm"), sem("ml_em_out"), sem("ml_y")
            vw_ready, km_ready, cn_mm, cn_out, cp_mm, cp_out = (
                sem(f"ml_{n}") for n in ("vw", "km", "cn_mm", "cn_out", "cp_mm", "cp_out"))
            cn_scaled = sem("ml_cn_scaled")
            samp_mm, samp_e, samp_w, qw_ready = (sem(f"ml_{n}") for n in ("samp_mm", "samp_e", "samp_w", "qw"))
            steps = [(h, kt) for h in range(MLH) for kt in range(QT)]

            raw = yT[:, 4:6, :].rearrange("p k n -> p (k n)")[:, 0:1024].rearrange("p (j k a d) -> p j k a d", j=2, k=4, a=2)
            pos = yT[0:32, 6, 0:P]
            phi1k = memkv[:, :, :].rearrange("p k n -> p (k n)").rearrange("p (c h) -> p c h", h=P)
            raw_here, gate_dma, phi1_here = sem("rawp_here"), sem("gate_dma"), sem("phi1_here")

            with nc.Block() as block:
                @block.sync
                def _(sp):
                    sp.dma_start(mlb[:, 0:1], I["ml_i_bias"].rearrange("a h -> h a"),
                                 allow_slow_non_contiguous=True).then_inc(ml_in, 16)
                    sp.dma_start(mlb[:, 1:2], I["ml_f_bias"].rearrange("a h -> h a"),
                                 allow_slow_non_contiguous=True).then_inc(ml_in, 16)
                    sp.dma_start(m0[:, :], I["state_mlstm_m"][0].rearrange("b h -> h b"),
                                 allow_slow_non_contiguous=True).then_inc(ml_in, 16)
                    sp.dma_start(n0[:, :], I["state_mlstm_n"][0].rearrange("b h d -> b (h d)")).then_inc(ml_in, 16)
                    for h in range(MLH):
                        sp.dma_start(Cn[0:HD, h, :, :], I["state_mlstm_C"][0, :, h].rearrange("b e d -> e b d"))\
                            .then_inc(ml_in, 16)
                        sp.dma_start(Cn[HD:HD + 1, h, :, :], I["state_mlstm_n"][0:1, :, h, :]).then_inc(ml_in, 16)
                    sp.wait_ge(out_dma, stores[0])
                    for j in range(2):
                        for a in range(2):
                            sp.dma_start(raw[:, j, :, a, :],
                                         O["kv_p"][0, 0, 256 * j + a:256 * j + 256:2, 0:2].rearrange(
                                             "p c g d -> p (c g) d")).then_inc(raw_here, 16)
                    sp.dma_start(pos[:, :], I["cmp_pos"][0].rearrange("v (c a) d -> (v c) (a d)", a=2))\
                        .then_inc(raw_here, 16)
                    load_phi1(sp, phi1k, 0, phi1_here)
                    sp.dma_start(gate_dram, gate_s[:, :]).then_inc(gate_dma, 16)
                    sp.wait_ge(gate_dma, 16)
                    for h in range(8):
                        for br in range(3):
                            sp.dma_start(gq[ST * h:ST * h + ST, :, br],
                                         gate_dram.rearrange("(b t) c -> c t b", b=NB)[8 * br + h],
                                         allow_slow_non_contiguous=True).then_inc(gate_dma, 16)
                    sp.wait_ge(gate_dma, 16 * 25)
                    sp.wait_ge(raw_here, 80)
                    sp.wait_ge(phi1_here, 16)

                    sp.wait_ge(rows_ready, 1)
                    store(sp, O["m_p"][0].rearrange("a h -> h a"), mend[:, 0:1], True)
                    store(sp, O["m_s"][0].rearrange("b h -> h b"), mend[:, 1:9], True)
                    sp.wait_ge(cp_out, 1)
                    store(sp, O["C_p"][0, 0].rearrange("h e d -> e h d"), Cp[0:HD, :, :])
                    store(sp, O["n_p"][0, 0:1], Cp[HD:HD + 1, :, :])
                    for h in range(MLH):
                        sp.wait_ge(cn_out, h + 1)
                        store(sp, O["C_s"][0, :, h].rearrange("b e d -> e b d"), Cn[0:HD, h, :, :])
                        store(sp, O["n_s"][0:1, :, h, :], Cn[HD:HD + 1, h, :, :])
                    sp.wait_ge(out_dma, stores[0])

                @block.tensor
                def _(pe):
                    pe.wait_ge(ml_in, 16 * 12)
                    for h in range(MLH):
                        if h >= 2:
                            pe.wait_ge(c0_out, h - 1)
                        for b in range(NB):
                            mm = pe.transpose(work[h % 2][0:HD, HD * b:HD * b + HD], Cn[0:HD, h, b, :],
                                              ident[0:HD, 0:HD])
                        mm.then_inc(c0_mm, 1)
                    for h in range(MLH):
                        mm = pe.transpose(work[2][0:HD, NB * h:NB * h + NB], n0[:, HD * h:HD * h + HD],
                                          ident[0:NB, 0:NB])
                    mm.then_inc(c0_mm, 1)
                    pe.wait_ge(rows_ready, 2)
                    for q in range(QT + 1):
                        at, n = (P * q, P) if q < QT else (TP, TS)
                        for j, row in enumerate((av, wrow)):
                            mm = pe.transpose(work[3][0:n, 8 * q + 4 * j:8 * q + 4 * j + 4], row[:, at:at + n],
                                              ident[0:MLH, 0:MLH])
                    mm.then_inc(cols_mm, 1)
                    pe.wait_ge(c0_out, 5)
                    for k in range(2):
                        pe.matmul(work[0][:, TS * k:TS * k + TS], const(f"pair{k}", MLH), wcrow[:, :],
                                  start=True, stop=True)
                    for h in range(MLH):
                        mm = pe.matmul(work[0][0:HD + 1, 64 + NB * h:64 + NB * h + NB],
                                       const(f"head{h}", MLH)[:, 0:HD + 1], decay[:, :], start=True, stop=True)
                    mm.then_inc(cols_mm, 1)
                    for h in range(MLH):
                        k, o = h // 2, HD * (h % 2)
                        s_bank = (work[1], gemm_big[0])[h % 2]
                        pe.matmul(s_bank[0:TS, TS * k:TS * k + TS], pT[o:o + HD, T_K + k, TP:NT],
                                  pT[o:o + HD, T_Q + k, TP:NT], start=True, stop=True)
                    for h in range(MLH):
                        mm = pe.matmul(work[2][0:TS, TS * h:TS * h + TS], const(f"head{h}", MLH)[:, 0:TS],
                                       mx[:, TP:NT], start=True, stop=True)
                    mm.then_inc(samp_mm, 1)
                    pe.wait_ge(cols_out, 2)

                    def scores(n):
                        h, kt = steps[n]
                        k, o = h // 2, HD * (h % 2)
                        if kt == 0:
                            if h:
                                pe.wait_ge(e_ready, QT * h)
                            pe.matmul(work[0][:, 0:TP], const(f"head{h}", MLH), mx[:, 0:TP],
                                      start=True, stop=True).then_inc(mb_ready, 1)
                        if n == 0:
                            pe.wait_ge(samp_w, 1)
                        if n >= 2:
                            pe.wait_ge(w_ready, n - 1)
                        pe.matmul(work[1 + n % 2][:, 0:TP - P * kt], pT[o:o + HD, T_K + k, P * kt:P * kt + P],
                                  pT[o:o + HD, T_Q + k, P * kt:TP], start=True, stop=True).then_inc(s_ready, 1)

                    scores(0)
                    for n, (h, kt) in enumerate(steps):
                        k, o = h // 2, HD * (h % 2)
                        if n + 1 < len(steps):
                            scores(n + 1)
                        if kt == 0 and o == 0 and k:
                            pe.wait_ge(y_done, k)
                        pe.wait_ge(w_ready, n + 1)
                        w = W[:, n % 2, 0:TP - P * kt]
                        ends = dict(start=(kt == 0), stop=(kt == QT - 1))
                        pe.matmul(gemm_big[0][o:o + HD, P * kt:TP], tok[:, kt, TV + k, o:o + HD], w, **ends)
                        pe.matmul(gemm_big[1][o:o + HD, P * kt:TP], const("ones")[:, 0:HD], w, **ends)\
                            .then_inc(pv_done, 1)
                        if kt == QT - 1:
                            num, den = gemm_small[0][o:o + HD, 0:TS], gemm_small[1][o:o + HD, 0:TS]
                            if n == QT - 1:
                                pe.wait_ge(qw_ready, 1)
                            pe.matmul(num, toks[:, TV + k, o:o + HD], Ws[:, h, :], start=True, stop=False)
                            for b in range(NB):
                                pe.matmul(num[:, ST * b:ST * b + ST], C0T[:, h, b, :],
                                          qw[:, h, ST * b:ST * b + ST], start=False, stop=(b == NB - 1))
                            pe.matmul(den, const("ones", TS)[:, 0:HD], Ws[:, h, :], start=True, stop=False)
                            pe.matmul(den, const("ones", HD)[:, 0:HD], nq[:, h, :], start=False, stop=True)
                            if o:
                                if k:
                                    pe.wait_ge(em_out, 1)
                                pe.matmul(work[3][:, :], const(f"pair{k}", MLH), emrow[:, 0:TP],
                                          start=True, stop=True).then_inc(fin_mm, 1)
                                pe.wait_ge(e_ready, n + 1)
                                pe.wait_ge(em_out, k) if k else None
                                pe.wait_ge(dg_ready, h + 1)
                                pe.matmul(gemm_small[0][:, 64:64 + TS], const(f"pair{k}", MLH), emrow[:, TP:NT],
                                          start=True, stop=True).then_inc(fin_mm, 1)
                    pe.wait_ge(vw_ready, 1)
                    pe.wait_ge(em_out, 2)
                    for h in range(MLH):
                        k, o = h // 2, HD * (h % 2)
                        for kt in range(QT):
                            mm = pe.matmul(work[3][0:HD + 1, HD * h:HD * h + HD], vw[:, kt, h, :],
                                           tok[:, kt, TK + k, o:o + HD], start=(kt == 0), stop=(kt == QT - 1))
                    mm.then_inc(cp_mm, 1)
                    pe.wait_ge(w_ready, len(steps))
                    for h in range(MLH):
                        pe.wait_ge(km_ready, h + 1)
                        if h >= 2:
                            pe.wait_ge(cn_out, h - 1)
                        pe.matmul(work[1 + h % 2][0:HD + 1, :], vws[:, h, :],
                                  KM[:, h % 2, :, :].rearrange("s b d -> s (b d)"),
                                  start=True, stop=True).then_inc(cn_mm, 1)

                @block.scalar
                def _(act):
                    one = const("ones")[:, 0:1]
                    act.activation(sg[:, :, :], pT[:, T_O:T_O + 2, :], ACT.Sigmoid)
                    act.wait_ge(ml_chain, 2)
                    act.activation(lf[:, :], ax[:, :], ACT.Exp, scale=-1.0).then_inc(ml_act, 1)
                    act.wait_ge(ml_act, 1)
                    act.activation(lf[:, :], lf[:, :], ACT.Ln, bias=one[0:MLH]).then_inc(ml_act, 1)
                    act.wait_ge(ml_in, 16 * 12)
                    for h in range(MLH):
                        act.wait_ge(c0_mm, h + 1)
                        act.activation(C0T[:, h, :, :], work[h % 2][0:HD, :].rearrange("p (b e) -> p b e", b=NB),
                                       ACT.Copy).then_inc(c0_out, 1)
                    act.wait_ge(c0_mm, 5)
                    act.activation(n0T[:, :, :], work[2][0:HD, 0:NB * MLH].rearrange("p (h b) -> p h b", h=MLH),
                                   ACT.Copy).then_inc(c0_out, 1)
                    act.wait_ge(rows_ready, 1)
                    act.activation(wrow[:, :], wrow[:, :], ACT.Exp)
                    act.activation(emrow[:, :], emrow[:, :], ACT.Exp, scale=-1.0)
                    act.activation(wcrow[:, :], wcrow[:, :], ACT.Exp)
                    act.activation(decay[:, :], decay[:, :], ACT.Exp).then_inc(rows_ready, 1)
                    act.wait_ge(cols_mm, 1)
                    act.activation(cols[:, 0:QT, :, :],
                                   work[3][:, 0:32].rearrange("p (q j h) -> p q j h", q=QT, j=2), ACT.Copy)
                    act.activation(cols[0:TS, QT, :, :], work[3][0:TS, 32:40].rearrange("p (j h) -> p j h", j=2),
                                   ACT.Copy).then_inc(cols_out, 1)
                    act.wait_ge(cols_mm, 2)
                    act.activation(wcb[:, :, :], work[0][:, 0:64].rearrange("p (k t) -> p k t", k=2), ACT.Copy)
                    act.activation(db[:, :, :], work[0][0:HD + 1, 64:64 + NB * MLH]
                                   .rearrange("p (h b) -> p h b", h=MLH), ACT.Copy).then_inc(cols_out, 1)
                    act.wait_ge(samp_e, 1)
                    for h in range(MLH):
                        ins = act.activation(Es[:, h, :], dgs[:, h, :], ACT.Exp, scale=-1.0,
                                             bias=cols[0:TS, QT, 0, h:h + 1])
                    ins.then_inc(samp_e, 1)
                    for n, (h, kt) in enumerate(steps):
                        act.wait_ge(dg_ready, h + 1)
                        if n >= 2:
                            act.wait_ge(w_ready, n - 1)
                        a = cols[:, kt, 0, h:h + 1]
                        ins = act.activation(E[:, n % 2, 0:P], dg[:, kt, :], ACT.Exp, bias=a, scale=-1.0)
                        if kt < QT - 1:
                            ins = act.activation(E[:, n % 2, P:TP - P * kt], work[0][:, P * kt + P:TP], ACT.Exp,
                                                 bias=a, scale=-1.0)
                        ins.then_inc(e_ready, 1)
                        if kt == QT - 1 and h % 2:
                            k = h // 2
                            act.wait_ge(fin_mm, 2 * k + 2)
                            if k:
                                act.wait_ge(y_done, k)
                            act.activation(em[:, 0:TP], work[3][:, :], ACT.Copy)
                            act.activation(em[:, TP:NT], gemm_small[0][:, 64:64 + TS], ACT.Copy).then_inc(em_out, 1)

                @block.vector
                def _(dve):
                    c = Chain(dve, ml_chain)
                    def steps_of(x):
                        return x[:, TP:NT].rearrange("p (b t) -> p b t", b=NB)

                    dve.wait_ge(ml_in, 16 * 12)
                    c.step(dve.tensor_scalar(fx[:, :], pT[32:36, T_IF, :], mlb[:, 1:2], None, ALU.add))
                    c.step(dve.scalar_tensor_tensor(out=ax[:, :], in0=fx[:, :], scalar=-1.0, in1=fx[:, :],
                                                    op0=ALU.mult, op1=ALU.max))
                    c.step(dve.memset(ones4[:, :], 1.0))
                    dve.wait_ge(ml_act, 2)
                    c.step(dve.scalar_tensor_tensor(out=lf[:, :], in0=fx[:, :], scalar=0.0, in1=lf[:, :],
                                                    op0=ALU.min, op1=ALU.subtract))
                    c.step(dve.tensor_tensor_scan(bsum[:, 0:TP], ones4[:, 0:TP], lf[:, 0:TP], 0.0,
                                                  ALU.mult, ALU.add))
                    bs, ls, as_, ms = steps_of(bsum), steps_of(lf), steps_of(av), steps_of(mx)
                    c.step(dve.tensor_copy(bs[:, :, 0], ls[:, :, 0]))
                    for t in range(1, ST):
                        c.step(dve.tensor_tensor(bs[:, :, t], bs[:, :, t - 1], ls[:, :, t], ALU.add))
                    c.step(dve.scalar_tensor_tensor(out=av[:, :], in0=pT[0:MLH, T_IF, :], scalar=mlb[:, 0:1],
                                                    in1=bsum[:, :], op0=ALU.add, op1=ALU.subtract))
                    c.step(dve.tensor_tensor_scan(mx[:, 0:TP], av[:, 0:TP], av[:, 0:TP], 0.0, ALU.max, ALU.max))
                    for t in range(ST):
                        c.step(dve.tensor_tensor(ms[:, :, t], as_[:, :, t], m0[:, :] if t == 0 else ms[:, :, t - 1],
                                                 ALU.max))
                    dve.tensor_scalar(wrow[:, 0:TP], av[:, 0:TP], mx[:, TP - 1:TP], None, ALU.subtract)
                    for t in range(ST):
                        dve.tensor_tensor(steps_of(wrow)[:, :, t], as_[:, :, t], ms[:, :, ST - 1], ALU.subtract)
                        dve.tensor_tensor(wcrow[:, :].rearrange("p (b t) -> p b t", b=NB)[:, :, t], m0[:, :],
                                          ms[:, :, t], ALU.subtract)
                    dve.tensor_tensor(decay[:, :], m0[:, :], ms[:, :, ST - 1], ALU.subtract)
                    c.step(dve.tensor_tensor(emrow[:, :], bsum[:, :], mx[:, :], ALU.add))
                    dve.tensor_copy(mend[:, 0:1], emrow[:, TP - 1:TP])
                    dve.tensor_copy(mend[:, 1:9], steps_of(emrow)[:, :, ST - 1]).then_inc(rows_ready, 1)
                    dve.wait_ge(cols_out, 2)
                    for h in range(MLH):
                        k, o = h // 2, HD * (h % 2)
                        ins = dve.tensor_tensor(qw[:, h, :], pT[o:o + HD, T_Q + k, TP:NT], wcb[o:o + HD, k, :],
                                                ALU.mult)
                    c.step(ins)
                    dve.wait_ge(c0_out, 5)
                    for h in range(MLH):
                        ins = dve.tensor_tensor(nq[:, h, :].rearrange("p (b t) -> p b t", b=NB),
                                                qw[:, h, :].rearrange("p (b t) -> p b t", b=NB),
                                                n0T[:, h, :].unsqueeze(2).to_broadcast([HD, NB, ST]), ALU.mult)
                    ins.then_inc(qw_ready, 1)
                    dve.wait_ge(samp_mm, 1)
                    for h in range(MLH):
                        ins = dve.tensor_tensor(dgs[:, h, :], work[2][0:TS, TS * h:TS * h + TS],
                                                const("sblocked", TS), ALU.add)
                    ins.then_inc(samp_e, 1)
                    dve.wait_ge(samp_e, 2)
                    for h in range(MLH):
                        ins = dve.scalar_tensor_tensor(
                            out=Ws[:, h, :], in0=(work[1], gemm_big[0])[h % 2][0:TS, TS * (h // 2):TS * (h // 2) + TS],
                            scalar=HD ** -0.5, in1=Es[:, h, :], op0=ALU.mult, op1=ALU.mult)
                    ins.then_inc(samp_w, 1)

                    def finish(k):
                        dve.wait_ge(em_out, k + 1)
                        dve.wait_ge(pv_done, 2 * QT * (k + 1))
                        for cols_, big, small in ((slice(0, TP), gemm_big[1], None), (slice(TP, NT), None, gemm_small[1])):
                            den = big[:, :] if big is not None else small[:, 0:TS]
                            c.step(dve.scalar_tensor_tensor(out=dd[:, cols_], in0=den, scalar=-1.0, in1=em[:, cols_],
                                                            op0=ALU.mult, op1=ALU.max))
                            c.step(dve.tensor_tensor(dd[:, cols_], den, dd[:, cols_], ALU.max))
                        c.step(dve.reciprocal(dd[:, :], dd[:, :]))
                        c.step(dve.tensor_tensor(dd[:, :], dd[:, :], sg[:, k, :], ALU.mult))
                        dve.tensor_tensor(yT[:, k, 0:TP], gemm_big[0][:, :], dd[:, 0:TP], ALU.mult)
                        dve.tensor_tensor(yT[:, k, TP:NT], gemm_small[0][:, 0:TS], dd[:, TP:NT], ALU.mult)\
                            .then_inc(y_done, 1)

                    for n, (h, kt) in enumerate(steps):
                        if kt == 0:
                            dve.wait_ge(mb_ready, h + 1)
                            dve.tensor_tensor(dg[:, :, :], work[0][:, :].rearrange("p (q t) -> p q t", q=QT),
                                              const("blocked").unsqueeze(1).to_broadcast([P, QT, P]), ALU.add)\
                                .then_inc(dg_ready, 1)
                        dve.wait_ge(e_ready, n + 1)
                        dve.wait_ge(s_ready, n + 1)
                        if n >= 2:
                            dve.wait_ge(pv_done, n - 1)
                        w = TP - P * kt
                        dve.scalar_tensor_tensor(out=W[:, n % 2, 0:w], in0=work[1 + n % 2][:, 0:w],
                                                 scalar=HD ** -0.5, in1=E[:, n % 2, 0:w],
                                                 op0=ALU.mult, op1=ALU.mult).then_inc(w_ready, 1)
                        k, o = h // 2, HD * (h % 2)
                        dve.tensor_scalar(vw[:, kt, h, 0:HD], tok[:, kt, TV + k, o:o + HD],
                                          cols[:, kt, 1, h:h + 1], None, ALU.mult)
                        if kt == 1:
                            dve.tensor_tensor(Cn[:, h, :, :], Cn[:, h, :, :],
                                              db[:, h, :].unsqueeze(2).to_broadcast([HD + 1, NB, HD]), ALU.mult)\
                                .then_inc(cn_scaled, 1)
                        if kt == 2:
                            dve.tensor_scalar(vws[:, h, 0:HD], toks[:, TV + k, o:o + HD], cols[0:TS, QT, 1, h:h + 1],
                                              None, ALU.mult)
                        if n == len(steps) - 1:
                            dve.tensor_copy(vw[:, :, :, HD], cols[:, 0:QT, 1, :])
                            dve.tensor_copy(vws[:, :, HD], cols[0:TS, QT, 1, :]).then_inc(vw_ready, 1)
                        if kt == QT - 1 and h % 2:
                            finish(h // 2)
                    def spread_keys(h):
                        k, o = h // 2, HD * (h % 2)
                        dve.tensor_tensor(KM[:, h % 2, :, :],
                                          toks[:, TK + k, o:o + HD].unsqueeze(1).to_broadcast([TS, NB, HD]),
                                          const("inb", TS).unsqueeze(2).to_broadcast([TS, NB, HD]), ALU.mult)\
                            .then_inc(km_ready, 1)

                    spread_keys(0)
                    spread_keys(1)
                    dve.wait_ge(cn_scaled, MLH)
                    for h in range(MLH):
                        dve.wait_ge(cn_mm, h + 1)
                        if h + 2 < MLH:
                            spread_keys(h + 2)
                        dve.scalar_tensor_tensor(out=Cn[:, h, :, :],
                                                 in0=work[1 + h % 2][0:HD + 1, :].rearrange("p (b d) -> p b d", b=NB),
                                                 scalar=HD ** -0.5, in1=Cn[:, h, :, :], op0=ALU.mult, op1=ALU.add)\
                            .then_inc(cn_out, 1)
                    dve.wait_ge(cp_mm, 1)
                    dve.tensor_scalar(Cp[:, :, :], work[3][0:HD + 1, 0:256].rearrange("p (h d) -> p h d", h=MLH),
                                      HD ** -0.5, None, ALU.mult).then_inc(cp_out, 1)
        sem.end_part()

        def turn_cmp(pe, raw, dst):
            for j in range(4):
                mm = pe.transpose(dst[:, P * j:P * j + P], raw[:, j, :, :].rearrange("p a d -> p (a d)"), ident)
            return mm

        def hidden(pe, w1, ZT, nblk, dst):
            for kv in range(2):
                z = ZT[:, 2 * kv:2 * kv + 2, :].rearrange("p g (n c) -> p g n c", c=16)
                for c in range(16):
                    mm = pe.matmul(dst[:, 2 * nblk * kv:2 * nblk * (kv + 1)], w1[kv][:, c, :],
                                   z[:, :, :, c], start=(c == 0), stop=(c == 15))
            return mm

        def load_phi(sp, w1, w2, sem_):
            for kv in range(2):
                if w1[kv] is not None:
                    load_phi1(sp, w1[kv], kv, sem_)
            sp.dma_start(w2[:, 0, 0:HD], I["phi_w2"][0, 0]).then_inc(sem_, 16)
            sp.dma_start(w2[:, 1, HD:P], I["phi_w2"][0, 0]).then_inc(sem_, 16)
            sp.dma_start(w2[:, 2, 0:HD], I["phi_w2"][0, 1]).then_inc(sem_, 16)

        kcp = mixed.enter_context(nc.sbuf_tensor("kcp", [P, PCB], F32))
        vexp = mixed.enter_context(nc.sbuf_tensor("vexp", [P, REP, G, HD], F32))
        tab = mixed.enter_context(nc.sbuf_tensor("tab", [P, 8, TP], F32))
        tab_here, pg_here = sem("tab_here"), sem("pages_here")
        pages = stdt[0:1, 0:NB * NPB].bitcast(I32)
        with ExitStack() as c5:
            def t5(name, shape):
                return c5.enter_context(nc.sbuf_tensor(name, shape, F32))

            w1 = (phi1k, t5("w1p", [P, 16, P]))
            w2 = t5("w2p", [P, 3, P])
            NCOL = G * PCB + 1
            ZT = t5("ZTp", [P, 2, 16, NCOL])
            hid = t5("hid", [P, 2, G, PCB])
            hrep = t5("hrep", [P, G, REP, PCB])
            vrep = t5("vrep", [P, HD])
            qb_zero, scaled = sem("QB_zero"), sem("q_scaled")
            phi_here, w2_zero = sem("phi_here"), sem("w2_zero")
            z_mm, z_out, hb_ready, h_mm, h_ready, hrep_ready, kv_mm, vrep_ready = (
                sem(f"pcmp_{n}") for n in ("z_mm", "z_out", "hb", "h_mm", "h", "hrep", "kv_mm", "vrep"))

            with nc.Block() as block:
                @block.sync
                def _(sp):
                    sp.wait_ge(w2_zero, 1)
                    load_phi(sp, (None, w1[1]), w2, phi_here)
                    sp.dma_start(tab[:, :, :], K["prompt"]).then_inc(tab_here, 16)
                    sp.dma_start(pages[:, :], I["page_table"].rearrange("b n -> (b n)").rearrange("(a n) -> a n", a=1))\
                        .then_inc(pg_here, 16)

                @block.gpsimd
                def _(pool):
                    pool.memset(QB[:, :, :], 0.0).then_inc(qb_zero, 1)
                    pool.memset(w2[:, :, :], 0.0).then_inc(w2_zero, 1)

                @block.tensor
                def _(pe):
                    for j in range(2):
                        turn_cmp(pe, raw[:, j, :, :, :], work[j]).then_inc(z_mm, 1)
                    pe.transpose(work[2][:, 0:32], pos[:, :], ident[0:32, 0:32]).then_inc(z_mm, 1)
                    pe.wait_ge(phi_here, 64)
                    pe.wait_ge(z_out, 3)
                    for kv in range(2):
                        for c in range(16):
                            mm = pe.matmul(work[3][:, NCOL * kv:NCOL * kv + NCOL], w1[kv][:, c, :], ZT[:, kv, c, :],
                                           start=(c == 0), stop=(c == 15))
                    mm.then_inc(h_mm, 1)
                    pe.wait_ge(h_ready, 1)
                    for g in range(G):
                        mm = pe.matmul(work[1][:, 0:PCB], w2[:, g, :], hid[:, 0, g, :], start=(g == 0), stop=(g == 1))
                    mm.then_inc(kv_mm, 1)
                    pe.wait_ge(hrep_ready, 1)
                    for g in range(G):
                        mm = pe.matmul(work[2][HD * g:HD * g + HD, 0:HD], hrep[:, g, :, :].rearrange("p r n -> p (r n)"),
                                       w2[:, 2, 0:HD], start=True, stop=True)
                    mm.then_inc(kv_mm, 1)

                @block.scalar
                def _(act):
                    act.wait_ge(h_mm, 1)
                    act.wait_ge(hb_ready, 1)
                    for kv in range(2):
                        ins = act.activation(hid[:, kv, :, :].rearrange("p g n -> p (g n)"),
                                             work[3][:, NCOL * kv:NCOL * kv + 2 * PCB], ACT.Gelu_apprx_tanh,
                                             bias=hb[:, kv:kv + 1])
                    ins.then_inc(h_ready, 1)

                @block.vector
                def _(dve):
                    for j in range(2):
                        dve.wait_ge(z_mm, j + 1)
                        for kv in range(2):
                            for g in range(G):
                                at = PCB * g + 8 * j
                                ins = dve.tensor_copy(
                                    ZT[:, kv, :, at:at + 8],
                                    work[j][:, P * (2 * kv + g):P * (2 * kv + g) + P].rearrange("p (n c) -> p c n", c=16))
                        ins.then_inc(z_out, 1)
                    dve.wait_ge(z_mm, 3)
                    dve.tensor_copy(ZT[:, :, :, 2 * PCB], work[2][:, 0:32].rearrange("p (v c) -> p v c", v=2))\
                        .then_inc(z_out, 1)
                    dve.tensor_scalar(pT[:, T_NQ:T_NQ + 4, :], pT[:, T_NQ:T_NQ + 4, :], HD ** -0.5, None, ALU.mult)\
                        .then_inc(scaled, 1)
                    dve.wait_ge(qb_zero, 1)
                    dve.wait_ge(scaled, 1)
                    for g in range(G):
                        rows = slice(HD * g, HD * g + HD)
                        for r in range(REP):
                            at = 16 * g + ST * r
                            dve.tensor_copy(QB[rows, :, at:at + ST],
                                            pT[rows, T_NQ + r, TP:NT].rearrange("p (b t) -> p b t", b=NB))
                    dve.tensor_copy(ksn[:, :], pT[:, T_KS, TP:NT])
                    dve.tensor_copy(kwn[:, :], pT[:, T_KW, TP:NT])
                    dve.tensor_copy(vnew[:, 0, :], toks[:, TOKKV + 3, :])
                    dve.tensor_copy(vnew[:, 1, :], toks[:, TOKKV + 5, :])
                    dve.wait_ge(h_mm, 1)
                    dve.tensor_tensor(hb[:, :], work[3][:, 2 * PCB:2 * NCOL:NCOL], vecT[:, V_PB:V_PB + 2], ALU.add).then_inc(hb_ready, 1)
                    dve.wait_ge(h_ready, 1)
                    dve.tensor_copy(hrep[:, :, :, :], hid[:, 1, :, :].unsqueeze(2).to_broadcast([P, G, REP, PCB]))\
                        .then_inc(hrep_ready, 1)
                    dve.wait_ge(kv_mm, 1)
                    dve.tensor_copy(kcp[:, :], work[1][:, 0:PCB])
                    dve.wait_ge(kv_mm, 2)
                    dve.tensor_copy(vrep[:, :], work[2][:, 0:HD]).then_inc(vrep_ready, 1)
                    dve.wait_ge(vrep_ready, 1)
                    dve.tensor_tensor(vexp[:, :, :, :],
                                      vrep[:, :].unsqueeze(1).to_broadcast([P, 8, HD]).rearrange(
                                          "p (r g) d -> p r g d", r=REP),
                                      const("vplace").rearrange("p (r g) -> p r g", r=REP).unsqueeze(3)
                                      .to_broadcast([P, REP, G, HD]), ALU.mult)

        with ExitStack() as c6:
            def t6(name, shape):
                return c6.enter_context(nc.sbuf_tensor(name, shape, F32))

            qz = ring[:, :, :, :].rearrange("p u k c -> p (u k c)").rearrange("p (g r t) -> p g r t", g=G, r=REP)
            qz_zero, qz_ready = sem("qz_zero"), sem("qz_ready")
            sc = t6("sc", [P, QT, G, REP, PCB])
            mxc, smc = t6("mxc", [P, QT * 8]), t6("smc", [P, QT * 8])
            pcT = t6("pcT", [P, TP])
            Pb = t6("Pb", [P, 4, TP])
            PT = t6("PT", [P, 2, TP])
            stat = t6("stat", [P, 4, 4])
            cs_mm, nchain, c_exp, pc_mm, pc_out = (
                sem(f"nsa_{n}") for n in ("cs_mm", "chain", "c_exp", "pc_mm", "pc_out"))
            s_mm, s_max, p_exp, d_ready, pt_mm, pt_out, pv_mm, y_out, pc_ready = (
                sem(f"nsa_{n}") for n in ("s_mm", "s_max", "p_exp", "d", "pt_mm", "pt_out", "pv", "y", "pc"))
            steps6 = [(r, br, qt, g) for r in range(REP) for br in range(2) for qt in range(QT) for g in range(G)]
            PER_R = 2 * QT * G

            with nc.Block() as block:
                @block.gpsimd
                def _(pool):
                    pool.memset(qz[HD:P, 0, :, :], 0.0)
                    pool.memset(qz[0:HD, 1, :, :], 0.0).then_inc(qz_zero, 1)

                @block.tensor
                def _(pe):
                    pe.wait_ge(qz_zero, 1)
                    pe.wait_ge(qz_ready, 1)
                    for qt in range(QT):
                        for r in range(REP):
                            for g in range(G):
                                at = PCB * (REP * qt + r)
                                mm = pe.matmul(work[g][:, at:at + PCB],
                                               qz[:, g, r, P * qt:P * qt + P], kcp[:, :], start=True, stop=True)
                                if (qt, r) == (QT - 1, REP - 1):
                                    mm.then_inc(cs_mm, 1)
                    pe.wait_ge(pc_ready, 1)
                    for qt in range(QT):
                        mm = pe.transpose(work[2][:, P * qt:P * qt + P],
                                          sc[:, qt, :, :, :].rearrange("p g r n -> p (g r n)"), ident)
                    mm.then_inc(pc_mm, 1)
                    pe.wait_ge(pc_out, 1)

                    def scores(n):
                        r, br, qt, g = steps6[n]
                        if n >= 4:
                            pe.wait_ge(s_max, n - 3)
                        pe.matmul(work[n % 4][:, 0:P * qt + P], qz[:, g, r, P * qt:P * qt + P],
                                  pT[:, (T_KS, T_KW)[br], 0:P * qt + P],
                                  start=True, stop=True).then_inc(s_mm, 1)

                    def values(n):
                        r, br, qt, g = steps6[n]
                        y = gemm_big[r % 2]
                        if n % PER_R == 0:
                            if r >= 2:
                                pe.wait_ge(y_out, r - 1)
                            pe.matmul(y[:, :], vexp[:, r, :, :].rearrange("p g d -> p (g d)"), pcT[:, :],
                                      start=True, stop=False, skip_group_check=True)
                        pe.wait_ge(pt_out, n + 1)
                        for kt in range(qt + 1):
                            mm = pe.matmul(y[HD * g:HD * g + HD, P * qt:P * qt + P],
                                           tok[:, kt, TOKKV + 3 + 2 * br, HD * g:HD * g + HD],
                                           PT[:, n % 2, P * kt:P * kt + P], start=False,
                                           stop=(n % PER_R == PER_R - 1 and kt == qt), skip_group_check=True)
                        mm.then_inc(pv_mm, 1)

                    scores(0)
                    scores(1)
                    scores(2)
                    for n, (r, br, qt, g) in enumerate(steps6):
                        if n + 3 < len(steps6):
                            scores(n + 3)
                        pe.wait_ge(d_ready, n + 1)
                        pe.wait_ge(p_exp, n + 1)
                        if n >= 2:
                            pe.wait_ge(pt_out, n - 1)
                        for kt in range(qt + 1):
                            mm = pe.transpose(gemm_small[n % 2][:, P * kt:P * kt + P], Pb[:, n % 4, P * kt:P * kt + P],
                                              ident)
                        mm.then_inc(pt_mm, 1)
                        if n:
                            values(n - 1)
                    values(len(steps6) - 1)

                @block.scalar
                def _(act):
                    act.wait_ge(c_exp, 1)
                    act.activation(sc[:, :, :, :, :], sc[:, :, :, :, :], ACT.Exp).then_inc(c_exp, 1)

                    def weights(n):
                        act.wait_ge(s_max, n + 1)
                        L = P * steps6[n][2] + P
                        act.activation(Pb[:, n % 4, 0:L], Pb[:, n % 4, 0:L], ACT.Exp, bias=stat[:, n % 4, 1:2],
                                       accum_out=stat[:, n % 4, 2:3]).then_inc(p_exp, 1)

                    weights(0)
                    for n, (r, br, qt, g) in enumerate(steps6):
                        if n + 1 < len(steps6):
                            weights(n + 1)
                        L = P * qt + P
                        act.wait_ge(pt_mm, n + 1)
                        if n >= 2:
                            act.wait_ge(pv_mm, n - 1)
                        act.activation(PT[:, n % 2, 0:L], gemm_small[n % 2][:, 0:L], ACT.Copy).then_inc(pt_out, 1)
                        if n % PER_R == 0 and n:
                            act.wait_ge(pv_mm, n)
                            act.activation(yT[:, 4 + r - 1, 0:TP], gemm_big[(r - 1) % 2][:, :], ACT.Copy)\
                                .then_inc(y_out, 1)
                    act.wait_ge(pv_mm, len(steps6))
                    act.activation(yT[:, 7, 0:TP], gemm_big[1][:, :], ACT.Copy).then_inc(y_out, 1)

                @block.vector
                def _(dve):
                    c = Chain(dve, nchain)
                    for g in range(G):
                        rows = slice(HD * g, HD * g + HD)
                        ins = dve.tensor_copy(qz[rows, g, :, :], pT[rows, T_NQ:T_NQ + 4, 0:TP])
                    ins.then_inc(qz_ready, 1)
                    dve.wait_ge(cs_mm, 2)
                    tabc = const("pcmp").rearrange("p (q g r n) -> p q g r n", q=QT, g=G, r=REP)
                    for g in range(G):
                        ins = dve.tensor_tensor(sc[:, :, g, :, :],
                                                work[g][:, 0:256].rearrange("p (q r n) -> p q r n", q=QT, r=REP),
                                                tabc[:, :, g, :, :], ALU.add)
                    c.step(ins)
                    flat = sc[:, :, :, :, :].rearrange("p q g r n -> p (q g r) n")
                    c.step(dve.tensor_reduce(mxc[:, :], flat, AX, ALU.max))
                    dve.tensor_tensor(flat, flat, mxc[:, :].unsqueeze(2).to_broadcast([P, QT * 8, PCB]),
                                      ALU.subtract).then_inc(c_exp, 1)
                    dve.wait_ge(c_exp, 2)
                    c.step(dve.tensor_reduce(smc[:, :], flat, AX, ALU.add))
                    c.step(dve.reciprocal(smc[:, :], smc[:, :]))
                    c.step(dve.tensor_tensor(smc[:, :].rearrange("p (q h) -> p q h", q=QT),
                                             smc[:, :].rearrange("p (q h) -> p q h", q=QT), gate_p[:, :, 0:8], ALU.mult))
                    c.step(dve.tensor_tensor(flat, flat, smc[:, :].unsqueeze(2).to_broadcast([P, QT * 8, PCB]),
                                             ALU.mult))
                    valid = const("pvalid").rearrange("p (q n) -> p q n", q=QT)
                    for qt in range(QT):
                        ins = dve.tensor_tensor(sc[:, qt, :, :, :].rearrange("p g r n -> p (g r) n"),
                                                sc[:, qt, :, :, :].rearrange("p g r n -> p (g r) n"),
                                                valid[:, qt, :].unsqueeze(1).to_broadcast([P, 8, PCB]), ALU.mult)
                    ins.then_inc(pc_ready, 1)
                    dve.wait_ge(pc_mm, 1)
                    dve.tensor_copy(pcT[:, :], work[2][:, :]).then_inc(pc_out, 1)
                    dve.wait_ge(tab_here, 16)

                    def top(n):
                        r, br, qt, g = steps6[n]
                        L = P * qt + P
                        dve.wait_ge(s_mm, n + 1)
                        if n >= 4:
                            dve.wait_ge(pt_mm, n - 3)
                        c.step(dve.tensor_tensor_reduce(Pb[:, n % 4, 0:L], work[n % 4][:, 0:L],
                                                        tab[:, REP * g + r, TP - L:TP], 1.0, -3e38, ALU.add, ALU.max,
                                                        stat[:, n % 4, 0:1]))
                        dve.tensor_scalar(stat[:, n % 4, 1:2], stat[:, n % 4, 0:1], -1.0, None, ALU.mult)\
                            .then_inc(s_max, 1)

                    top(0)
                    top(1)
                    for n, (r, br, qt, g) in enumerate(steps6):
                        dve.wait_ge(p_exp, n + 1)
                        c.step(dve.reciprocal(stat[:, n % 4, 3:4], stat[:, n % 4, 2:3]))
                        h = 8 * (br + 1) + REP * g + r
                        dve.tensor_scalar(Pb[:, n % 4, 0:P * qt + P], Pb[:, n % 4, 0:P * qt + P], stat[:, n % 4, 3:4],
                                          gate_p[:, qt, h:h + 1], ALU.mult, ALU.mult).then_inc(d_ready, 1)
                        if n + 2 < len(steps6):
                            top(n + 2)

        mixed.close()

        with ExitStack() as c7:
            def t7(name, shape, dt=F32):
                return c7.enter_context(nc.sbuf_tensor(name, shape, dt))

            R = 32
            w1 = [t7(f"w1s{kv}", [P, 16, P]) for kv in range(2)]
            w2 = t7("w2s", [P, 3, P])
            both = t7("both", [2 * R, PAST])
            ss, past = both[0:R, :], both[R:2 * R, :]
            sw = t7("sw", [R, WIN])
            sn = t7("sn", [R, 2, TS])
            rawc = t7("rawc", [P, CT // 2, 2, 2, P])
            kv = t7("kv", [P, CT, 2, 2, P])
            rw = t7("rw", [P, 4, 2, P])
            ZT = t7("ZTs", [P, 4, CT * P])
            hid = t7("hids", [P, 2, G, NCB])
            kc = t7("kcs", [P, NCB])
            vc = t7("vcs", [NCB, P])
            Qb = t7("Qb", [P, R])
            KTb = t7("KTb", [P, 2, 512])
            PTs = t7("PTs", [P, 2, 512])
            pn = t7("pn", [R, NCB])
            sel = t7("sel", [R, 4, 65])
            top8 = t7("top8", [R, 2, 8])
            bnb = stdt[0:R, NB * NPB:NB * NPB + TS + 1]
            st = t7("st", [R, 18])
            Os = t7("Os", [R, P])
            rawc2 = ring[:, :, :, :].rearrange("p u k n -> p (u k n)").rearrange("p (j a c n) -> p j a c n", a=2, c=2, n=P)

            c7_const, s_w2z, s_w2 = sem("past_here"), sem("w2s_zero"), sem("phis_here")
            rawc_here = [sem(f"rawc_here{j}") for j in range(CT)]
            raw0_here = [sem(f"raw0_here{j}") for j in range(CT // 2)]
            kv_here = [sem(f"kv_here{j}") for j in range(CT // 2)]
            rw_here = sem("rw_here")
            z_mm, h_mm, h_ready, kc_mm, kc_out = (sem(f"s_{n}") for n in ("z_mm", "h_mm", "h", "kc_mm", "kc_out"))
            z_out = [sem(f"s_z_out{n}") for n in ("a", "v")]
            qb_ready, cs_mm, pn_exp, pn_sub, pn_ready, imp_mm = (
                sem(f"s_{n}") for n in ("qb", "cs_mm", "pn_exp", "pn_sub", "pn", "imp_mm"))
            kt_mm, kt_out, sl_mm, sl_out = (
                sem(f"s_{n}") for n in ("kt_mm", "kt_out", "sl_mm", "sl_out"))
            m_ready, e_ready, pt_mm, pt_out, o_mm, o_ready, ot_mm, chain7 = (
                sem(f"s_{n}") for n in ("m", "e", "pt_mm", "pt_out", "o_mm", "o", "ot_mm", "chain"))
            NKT = CT // 2 + 1
            NPT_ = 10
            CH = 33

            def settled(dve):
                dve.memset(bnb[:, TS:TS + 1], 0.0)

            def settled_pe(pe, n=0, sem_=None):
                ins = pe.transpose(work[3][:, 384:512], ident, ident)
                if n:
                    ins.then_inc(sem_, n)

            cache = I["cache_nsa_kv"][0].rearrange("n (p a) c g d -> n p a c (g d)", a=2)

            def page_numbers(eng_type, b, j):
                _, page = nc.values_load_multi_w_load_instructions(
                    pages[0:1, bass.ds(b * NPB + 2 * j, 16)], engines=[eng_type],
                    min_val=0,
                    max_val=I["cache_nsa_kv"].shape[1] - 1)
                return page

            def page_half(eng, dst, page, half, kinds):
                return eng.dma_start(dst[64 * half:64 * half + 64, :, :, :].rearrange("p a c n -> p a (c n)"),
                                    cache[bass.ds(page, 1), :, :, kinds, :].rearrange(
                                        "n p a c m -> p (n a) (c m)"))

            def raw_slot(j):
                return rawc[:, j, :, :, :] if j < CT // 2 else rawc2[:, j - CT // 2, :, :, :]

            def load_raw(eng, kind, here, b, tiles, turned):
                for j in tiles:
                    if j % 8 == 0:
                        page = page_numbers(kind, b, j)
                    if turned is not None:
                        eng.wait_ge(z_mm, turned + (j + 1))
                        eng.wait_ge(pg_here, 16)
                    for half in range(2):
                        page_half(eng, raw_slot(j), page[2 * (j % 8) + half], half, slice(0, 2)).then_inc(here(j), 16)

            early, late = range(CT // 2), range(CT // 2, CT)
            SP, POOL = mybir.EngineType.SP, mybir.EngineType.Pool

            COPIER = [0] * 13 + [1] * 3

            def copied(eng, b, j):
                who = COPIER[j]
                eng.wait_ge(z_out[who], b * COPIER.count(who) + (COPIER[:j].count(who) + 1))

            def copy_z(copy, eng, b, tiles, who):
                for j in tiles:
                    if COPIER[j] != who:
                        continue
                    eng.wait_ge(z_mm, b * CT + (j + 1))
                    for g in range(G):
                        for a in range(2):
                            ins = copy(ZT[HD * a:HD * a + HD, g::2, P * j:P * j + P],
                                       work[j % 2][HD * g:HD * g + HD, 256 * a:256 * a + 256].rearrange(
                                           "p (c n) -> p c n", c=2))
                    ins.then_inc(z_out[who], 1)

            with nc.Block() as block:
                @block.sync
                def _(sp):
                    sp.dma_start(past[:, :], K["past"]).then_inc(c7_const, 16)
                    sp.wait_ge(s_w2z, 1)
                    load_phi(sp, w1, w2, s_w2)
                    sp.wait_ge(pg_here, 16)
                    def load_kv(b):
                        sp.wait_ge(o_mm, b * NPT_ + 2)
                        sp.dma_start(rw[:, :, :, :], I["state_nsa_win"][0, bass.ds(b, 1)].rearrange(
                            "b (c p) v g d -> p (b c) v (g d)", p=P)).then_inc(rw_here, 16)
                        for j in range(CT):
                            if j % 8 == 0:
                                page = page_numbers(SP, b, j)
                            sp.wait_ge(o_mm, b * NPT_ + (3 + j // 2))
                            for half in range(2):
                                page_half(sp, kv[:, j, :, :, :], page[2 * (j % 8) + half], half, slice(2, 4)).then_inc(kv_here[j // 2], 16)

                    load_raw(sp, SP, lambda j: raw0_here[j - CT // 2], 0, late, None)
                    with sp.Fori(0, NB) as b:
                        load_kv(b)

                @block.gpsimd
                def _(pool):
                    pool.memset(w2[:, :, :], 0.0).then_inc(s_w2z, 1)
                    pool.wait_ge(pg_here, 16)

                    load_raw(pool, POOL, lambda j: rawc_here[j], 0, early, None)
                    load_raw(pool, POOL, lambda j: rawc_here[j], 1, early, 0)
                    with pool.Fori(0, NB - 2) as b:
                        load_raw(pool, POOL, lambda j: rawc_here[j], b + 1, late, b * CT)
                        load_raw(pool, POOL, lambda j: rawc_here[j], b + 2, early, b * CT + CT)
                    load_raw(pool, POOL, lambda j: rawc_here[j], NB - 1, late, (NB - 2) * CT)

                @block.tensor
                def _(pe):
                    pe.wait_ge(s_w2, 80)

                    def turn_raw(b, tiles, first=False):
                        for j in tiles:
                            if j in early:
                                pe.wait_ge(rawc_here[j], b * 32 + 32)
                            elif first:
                                pe.wait_ge(raw0_here[j - CT // 2], 32)
                            else:
                                pe.wait_ge(rawc_here[j], b * 32)
                            if j >= 2:
                                copied(pe, b, j - 2)
                            for i in range(4):
                                mm = pe.transpose(work[j % 2][:, P * i:P * i + P], raw_slot(j)[:, i // 2, i % 2, :], ident)
                            mm.then_inc(z_mm, 1)

                    settled_pe(pe, NPT_, o_mm)
                    turn_raw(0, range(CT), True)

                    def batch(b, more):
                        for who in range(2):
                            pe.wait_ge(z_out[who], b * COPIER.count(who) + COPIER.count(who))
                        hidden(pe, w1, ZT, NCB, work[2]).then_inc(h_mm, 1)
                        pe.wait_ge(qb_ready, b + 1)

                        def keys(n):
                            if n < CT // 2:
                                pe.wait_ge(kv_here[n], b * 64 + 64)
                            else:
                                pe.wait_ge(rw_here, b * 16 + 16)
                            if n >= 2:
                                pe.wait_ge(kt_out, b * NKT + (n - 1))
                            for i in range(4):
                                src = kv[:, 2 * n + i // 2, i % 2, 0, :] if n < CT // 2 else rw[:, i, 0, :]
                                mm = pe.transpose(gemm_small[n % 2][:, P * i:P * i + P], src, ident)
                            mm.then_inc(kt_mm, 1)

                        def scores(n):
                            pe.wait_ge(kt_out, b * NKT + (n + 1))
                            if n >= 2:
                                pe.wait_ge(sl_out, b * NKT + (n - 1))
                            pe.matmul(gemm_big[n % 2][0:R, :], Qb[:, :], KTb[:, n % 2, :],
                                      start=True, stop=True).then_inc(sl_mm, 1)

                        keys(0)
                        keys(1)
                        pe.wait_ge(h_ready, b + 1)
                        for g in range(G):
                            pe.matmul(work[3][:, 0:NCB], w2[:, g, :], hid[:, 0, g, :], start=(g == 0), stop=(g == 1))
                        for g in range(G):
                            mm = pe.matmul(work[3][:, P + HD * g:P + HD * g + HD], hid[:, 1, g, :], w2[:, 2, 0:HD],
                                           start=True, stop=True)
                        mm.then_inc(kc_mm, 1)
                        scores(0)
                        pe.wait_ge(kc_out, b + 1)
                        pe.matmul(work[2][0:R, 0:NCB], Qb[:, :], kc[:, :], start=True, stop=True)
                        for i, new in enumerate((ksn, kwn)):
                            mm = pe.matmul(work[2][0:R, P * (2 + i):P * (2 + i) + TS], Qb[:, :], new[:, :],
                                           start=True, stop=True)
                        mm.then_inc(cs_mm, 1)
                        for n in range(1, NKT):
                            if n + 1 < NKT:
                                keys(n + 1)
                            if n == 4:
                                pe.wait_ge(pn_ready, b + 1)
                            scores(n)
                            if n == 4:
                                pe.matmul(work[2][0:R, P:2 * P], const("grp", R), pn[:, :],
                                          start=True, stop=True).then_inc(imp_mm, 1)
                            if more:
                                turn_raw(b + 1, [n - 1])
                        if more:
                            turn_raw(b + 1, range(NKT - 1, CT))

                        groups7 = [[(pn[:, :], vc[:, :], 0, P)] +
                                   [(sn[:, i, :], vnew[:, i, :], 1 + i, TS) for i in range(2)]]
                        groups7 += [[(sw[:, P * i:P * i + P], rw[:, i, 1, :], 2, P) for i in range(4)]]
                        flat = [(ss[:, 256 * j + a:256 * j + 256:2], kv[:, j, a, 1, :], 1, P)
                                for j in range(CT) for a in range(2)]
                        groups7 += [flat[4 * i:4 * i + 4] for i in range(8)]
                        o_bank = [work[3][0:R, 0:P], gemm_small[0][0:R, 0:P], gemm_small[1][0:R, 0:P]]
                        opened = set()

                        def turn(n):
                            for i, (src, _, _, m) in enumerate(groups7[n]):
                                mm = pe.transpose(work[n % 2][0:m, P * i:P * i + R], src, ident[0:R, 0:R])
                            mm.then_inc(pt_mm, 1)

                        def values(n):
                            pe.wait_ge(pt_out, b * NPT_ + (n + 1))
                            for i, (_, val, br, m) in enumerate(groups7[n]):
                                last = (n, i) in ((0, 0), (1, 3), (9, 3))
                                mm = pe.matmul(o_bank[br], PTs[0:m, n % 2, P * i:P * i + R], val,
                                               start=(br not in opened), stop=last)
                                opened.add(br)
                            mm.then_inc(o_mm, 1)

                        if more:
                            copied(pe, b + 1, CT - 2)
                            copied(pe, b + 1, CT - 1)
                        pe.wait_ge(e_ready, b * 2 + 1)
                        settled_pe(pe)
                        turn(0)
                        for n in range(1, NPT_):
                            turn(n)
                            if n == 1:
                                pe.wait_ge(e_ready, b * 2 + 2)
                            values(n - 1)
                        values(NPT_ - 1)
                        pe.wait_ge(o_ready, b + 1)
                        settled_pe(pe)
                        pe.transpose(work[3][:, 256:256 + R], Os[:, :], ident[0:R, 0:R]).then_inc(ot_mm, 1)

                    with pe.Fori(0, NB - 1) as b:
                        batch(b, True)
                    batch(NB - 1, False)

                @block.scalar
                def _(act):
                    def copy(dst, src):
                        return act.activation(dst, src, ACT.Copy)

                    copy_z(copy, act, 0, range(CT), 0)

                    def batch(b, more):
                        act.wait_ge(h_mm, b + 1)
                        for kv_ in range(2):
                            ins = act.activation(hid[:, kv_, :, :].rearrange("p g n -> p (g n)"),
                                                 work[2][:, 256 * kv_:256 * kv_ + 256], ACT.Gelu_apprx_tanh,
                                                 bias=hb[:, kv_:kv_ + 1])
                        ins.then_inc(h_ready, 1)
                        act.wait_ge(kc_mm, b + 1)
                        act.activation(kc[:, :], work[3][:, 0:NCB], ACT.Copy)
                        act.activation(vc[:, :], work[3][:, P:2 * P], ACT.Copy).then_inc(kc_out, 1)
                        def keys_out(n):
                            act.wait_ge(kt_mm, b * NKT + (n + 1))
                            if n >= 2:
                                act.wait_ge(sl_mm, b * NKT + (n - 1))
                            if n < CT // 2:
                                dst = KTb[:, n % 2, :].rearrange("q (j p a) -> q j a p", j=2, a=2)
                                src = gemm_small[n % 2][:, :].rearrange("q (j a p) -> q j a p", j=2, a=2)
                            else:
                                dst, src = KTb[:, n % 2, :], gemm_small[n % 2][:, :]
                            act.activation(dst, src, ACT.Copy).then_inc(kt_out, 1)

                        keys_out(0)
                        keys_out(1)
                        act.wait_ge(pn_sub, b + 1)
                        act.activation(pn[:, :], pn[:, :], ACT.Exp, bias=st[:, 1:2], accum_out=st[:, 2:3])\
                            .then_inc(pn_exp, 1)
                        for n in range(2, NKT):
                            keys_out(n)
                            if more:
                                copy_z(copy, act, b + 1, [n - 2], 0)
                        if more:
                            copy_z(copy, act, b + 1, range(NKT - 2, 13), 0)
                        act.wait_ge(m_ready, b * 2 + 1)
                        act.activation(sw[:, :], sw[:, :], ACT.Exp, bias=st[:, 7:8], accum_out=st[:, 8:9])
                        act.activation(sn[:, 1, :], sn[:, 1, :], ACT.Exp, bias=st[:, 7:8], accum_out=st[:, 9:10])
                        act.wait_ge(m_ready, b * 2 + 2)
                        act.activation(sn[:, 0, :], sn[:, 0, :], ACT.Exp, bias=st[:, 4:5], accum_out=st[:, 6:7])\
                            .then_inc(e_ready, 1)
                        act.activation(ss[:, :], ss[:, :], ACT.Exp, bias=st[:, 4:5], accum_out=st[:, 5:6])\
                            .then_inc(e_ready, 1)
                        if more:
                            copy_z(copy, act, b + 1, range(13, CT), 0)

                    with act.Fori(0, NB - 1) as b:
                        batch(b, True)
                    batch(NB - 1, False)

                @block.vector
                def _(dve):
                    copy_z(dve.tensor_copy, dve, 0, range(CT), 1)

                    def batch(b, more):
                        c = Chain(dve, chain7, b * CH)
                        dve.tensor_copy(Qb[:, :], QB[:, bass.ds(b, 1), :].rearrange("p a q -> p (a q)"))\
                            .then_inc(qb_ready, 1)
                        dve.wait_ge(cs_mm, b + 1)
                        settled(dve)
                        c.step(dve.tensor_tensor_reduce(pn[:, :], work[2][0:R, 0:NCB], const("bcmp", R), 1.0, -3e38,
                                                        ALU.add, ALU.max, st[:, 0:1]))
                        dve.tensor_scalar(st[:, 1:2], st[:, 0:1], -1.0, None, ALU.mult).then_inc(pn_sub, 1)
                        c.step(dve.tensor_copy(bnb[:, 0:TS], cst[0:R, bass.ds(b * TS + CONST["bnew"][0], TS)]))
                        settled(dve)
                        for i in range(2):
                            ins = dve.tensor_tensor_reduce(
                                sn[:, i, :], work[2][0:R, P * (2 + i):P * (2 + i) + TS],
                                bnb[:, 0:TS], 1.0, -3e38, ALU.add, ALU.max,
                                st[:, 10 + i:11 + i])
                        c.step(ins)

                        def raw_out(n):
                            if more:
                                copy_z(dve.tensor_copy, dve, b + 1, [n - 1], 1)

                        def masked(half):
                            part = ss[:, 2048 * half:2048 * half + 2048].rearrange("p (n k) -> p n k", k=64)
                            settled(dve)
                            c.step(dve.tensor_tensor_reduce(
                                part, part, sel[:, 3, 32 * half:32 * half + 32].unsqueeze(2).to_broadcast([R, 32, 64]),
                                1.0, -3e38, ALU.add, ALU.max, st[:, 16 + half:17 + half]))

                        def scores_out(n):
                            dve.wait_ge(sl_mm, b * NKT + (n + 1))
                            if n < CT // 2:
                                dst, table = ss[:, 512 * n:512 * n + 512], past[:, 512 * n:512 * n + 512]
                            else:
                                dst, table = sw[:, :], const("bwin", R)
                            dve.tensor_tensor(dst, gemm_big[n % 2][0:R, :], table, ALU.add).then_inc(sl_out, 1)

                        dve.wait_ge(c7_const, 16)
                        scores_out(0)
                        dve.wait_ge(pn_exp, b + 1)
                        c.step(dve.reciprocal(st[:, 3:4], st[:, 2:3]))
                        dve.tensor_scalar(pn[:, :], pn[:, :], st[:, 3:4], None, ALU.mult).then_inc(pn_ready, 1)
                        for n in range(1, 5):
                            scores_out(n)
                            raw_out(n)
                        dve.wait_ge(imp_mm, b + 1)
                        two = work[2][0:R, P:2 * P].rearrange("p (n a) -> p n a", a=2)
                        c.step(dve.tensor_copy(sel[:, 3, 0:64], two[:, :, 1]))
                        c.step(dve.tensor_tensor(sel[:, 0, 0:64], two[:, :, 0], sel[:, 3, 0:64], ALU.add))
                        c.step(dve.memset(sel[:, 0, 64:65], 0.0))
                        c.step(dve.tensor_tensor(sel[:, 0, :], sel[:, 0, :], const("bonus", R), ALU.add))
                        for i in range(2):
                            settled(dve)
                            c.step(dve.max(top8[:, i, :], sel[:, i, :]))
                            settled(dve)
                            c.step(dve.match_replace(sel[:, i + 1, :], top8[:, i, :], sel[:, i, :], -3e38))
                        c.step(dve.tensor_scalar(sel[:, 3, :], sel[:, 2, :], -1e38, NEG, ALU.is_gt, ALU.mult))
                        for n in range(5, NKT):
                            scores_out(n)
                            raw_out(n)
                            if n == 6:
                                masked(0)
                        dve.wait_ge(sl_out, b * NKT + NKT)
                        c.step(dve.tensor_reduce(st[:, 12:13], sw[:, :], AX, ALU.max))
                        c.step(dve.tensor_tensor(st[:, 12:13], st[:, 12:13], st[:, 11:12], ALU.max))
                        dve.tensor_scalar(st[:, 7:8], st[:, 12:13], -1.0, None, ALU.mult).then_inc(m_ready, 1)
                        masked(1)
                        c.step(dve.tensor_tensor(st[:, 13:14], st[:, 16:17], st[:, 17:18], ALU.max))
                        c.step(dve.tensor_tensor(st[:, 13:14], st[:, 13:14], st[:, 10:11], ALU.max))
                        dve.tensor_scalar(st[:, 4:5], st[:, 13:14], -1.0, None, ALU.mult).then_inc(m_ready, 1)
                        if more:
                            copy_z(dve.tensor_copy, dve, b + 1, range(NKT - 1, CT), 1)
                        for n in range(NPT_):
                            dve.wait_ge(pt_mm, b * NPT_ + (n + 1))
                            k, m = (3, TS) if n == 0 else (4, P)
                            src = work[n % 2][:, :].rearrange("p (k c) -> p k c", k=4)
                            dst = PTs[:, n % 2, :].rearrange("p (k c) -> p k c", k=4)
                            if n == 0:
                                dve.tensor_copy(dst[:, 0, 0:R], src[:, 0, 0:R])
                                dve.tensor_copy(dst[0:TS, 1:3, 0:R], src[0:TS, 1:3, 0:R]).then_inc(pt_out, 1)
                            else:
                                dve.tensor_copy(dst[:, :, 0:R], src[:, :, 0:R]).then_inc(pt_out, 1)
                        c.step(dve.tensor_tensor(st[:, 5:6], st[:, 5:6], st[:, 6:7], ALU.add))
                        c.step(dve.tensor_tensor(st[:, 8:9], st[:, 8:9], st[:, 9:10], ALU.add))
                        dve.reciprocal(st[:, 5:6], st[:, 5:6])
                        c.step(dve.reciprocal(st[:, 8:9], st[:, 8:9]))
                        gates = gq[:, bass.ds(b, 1), :].rearrange("p a c -> p (a c)")
                        c.step(dve.tensor_copy(st[:, 13:16], gates))
                        dve.tensor_tensor(st[:, 5:6], st[:, 5:6], st[:, 14:15], ALU.mult)
                        c.step(dve.tensor_tensor(st[:, 8:9], st[:, 8:9], st[:, 15:16], ALU.mult))
                        dve.wait_ge(o_mm, b * NPT_ + 2 * NPT_)
                        c.step(dve.tensor_scalar(Os[:, :], work[3][0:R, 0:P], st[:, 13:14], None, ALU.mult))
                        c.step(dve.scalar_tensor_tensor(out=Os[:, :], in0=gemm_small[0][0:R, 0:P], scalar=st[:, 5:6],
                                                        in1=Os[:, :], op0=ALU.mult, op1=ALU.add))
                        dve.scalar_tensor_tensor(out=Os[:, :], in0=gemm_small[1][0:R, 0:P], scalar=st[:, 8:9],
                                                 in1=Os[:, :], op0=ALU.mult, op1=ALU.add).then_inc(o_ready, 1)
                        dve.wait_ge(ot_mm, b + 1)
                        for g in range(G):
                            rows = slice(HD * g, HD * g + HD)
                            dve.tensor_copy(
                                yT[rows, 4:8, bass.ds(b * ST + TP, ST)],
                                work[3][rows, 256 + 16 * g:272 + 16 * g].rearrange("p (r t) -> p r t", r=REP))
                        assert c.n <= CH
                        while c.n < CH:
                            c.step(dve.tensor_copy(st[:, 0:1], st[:, 1:2]))

                    with dve.Fori(0, NB - 1) as b:
                        batch(b, True)
                    batch(NB - 1, False)
        sem.end_part()

        def tile_of(x, it, u):
            return x[:, bass.ds(it * RING + u, 1), :].rearrange("p a n -> p (a n)")

        with ExitStack() as c8:
            nparts = [c8.enter_context(nc.sbuf_tensor(n, [P, KT, NT], F32R)) for n in ("n_high", "n_low")]
            wparts = [c8.enter_context(nc.sbuf_tensor(n, [P, 2, KT, P], F32R)) for n in ("w8_high", "w8_low")]
            NR, NQ = 4 + NE, QT + 1
            rw_ = c8.enter_context(nc.sbuf_tensor("rw_", [P, KT, NR], F32))
            rb = c8.enter_context(nc.sbuf_tensor("rb", [P, NR], F32))
            rparts = [c8.enter_context(nc.sbuf_tensor(n, [P, KT, NR], F32R)) for n in ("r_high", "r_low")]
            r_here, rw_high, rw_split, lt_mm = sem("r_here"), sem("rw_high"), sem("rw_split"), sem("lt_mm")
            up = [I[n][0].rearrange("e (k p) f -> e p k f", p=P) for n in ("exp_w_gate", "exp_w_up")]
            EP = NE // 2

            def load_up(sp, part, e, u):
                slot_free(sp, f"up{part}", e, u)
                sp.dma_start(ring[:, u, :, :],
                             up[u % 2][bass.ds(e + EP * part, 1), :, :, P * (u // 2):P * (u // 2) + P].rearrange(
                                 "e p k f -> p (e k) f")).then_inc(w_loaded[u], 16)

            cross = c8.enter_context(ExitStack())
            nT = cross.enter_context(nc.sbuf_tensor("nT", [P, KT, NT], F32))
            qx = cross.enter_context(nc.sbuf_tensor("qx", [P, XH, NT], F32))
            ox = cross.enter_context(nc.sbuf_tensor("ox", [P, XH, NT], F32))
            heads = cross.enter_context(nc.sbuf_tensor("heads", [P, KT * 16 + D], F32))
            hstd = stdt[0:16, :]
            heads_here = sem("heads_here")
            hsq, hss, hsd, hinv, hspread, y_norm = (
                sem(f"head_{n}") for n in ("sq", "sum", "std", "inv", "spread", "norm"))

            with nc.Block() as block:
                @block.sync
                def _(sp):
                    sp.dma_start(heads[:, :], K["heads"]).then_inc(heads_here, 16)
                    w = I["w_out"][0]
                    for n in range(8):
                        u, cols_ = n % RING, slice(P * n, P * n + P)
                        slot_free(sp, "out", n // RING, u)
                        sp.dma_start(ring[:, u, 0:4, :], w[0:512, cols_].rearrange("(k p) n -> p k n", p=P))\
                            .then_inc(w_loaded[u], 16)
                        for g in range(G):
                            sp.dma_start(ring[HD * g:HD * g + HD, u, 4:8, :],
                                         w[512 + 256 * g:768 + 256 * g, cols_].rearrange("(r d) n -> d r n", r=REP))\
                                .then_inc(w_loaded[u], 16)
                    w = I["xa_wq"][0].rearrange("(k p) n -> p k n", p=P)
                    for n in range(4):
                        slot_free(sp, "xq", 0, n)
                        sp.dma_start(ring[:, n, :, :], w[:, :, P * n:P * n + P]).then_inc(w_loaded[n], 16)

                @block.tensor
                def _(pe):
                    pe.wait_ge(heads_here, 16)
                    for k in range(KT):
                        pe.wait_ge(hsq, k + 1)
                        for i in range(2):
                            mm = pe.matmul(work[i][0:16, 0:HALF], heads[:, 16 * k:16 * k + 16],
                                           nT[:, k, HALF * i:HALF * i + HALF], start=(k == 0), stop=(k == KT - 1))
                    mm.then_inc(hss, 1)
                    pe.wait_ge(hinv, 1)
                    for k in range(KT):
                        if k >= 2:
                            pe.wait_ge(y_norm, k - 1)
                        for i in range(2):
                            mm = pe.matmul(work[2 * (k % 2) + i][:, 0:HALF],
                                           heads[0:16, KT * 16 + P * k:KT * 16 + P * k + P],
                                           hstd[:, HALF * i:HALF * i + HALF], start=True, stop=True)
                        mm.then_inc(hspread, 1)
                    pe_gemm(pe, "out", 8, KT, lambda k: [x[:, k, :] for x in nparts], wparts, 2 * KT)
                    norm_pe(pe, 2, yT)
                    pe_gemm(pe, "xq", 4, KT, lambda k: [x[:, k, :] for x in nparts], wparts, 3 * KT)

                @block.scalar
                def _(act):
                    for k in range(KT):
                        act.activation(nT[:, k, :], yT[:, k, :], ACT.Square).then_inc(hsq, 1)
                    act.wait_ge(hss, 1)
                    for i in range(2):
                        ins = act.activation(hstd[:, HALF * i:HALF * i + HALF], work[i][0:16, 0:HALF], ACT.Sqrt,
                                             bias=const("eps", 16), scale=1.0 / HD)
                    ins.then_inc(hsd, 1)
                    norm_act(act, 2, xT, yT, after="out")
                    for n in (0, 2):
                        output_here(act, "xq", 0, n)
                        act_copy(act, qx[:, n, :], 0).then_inc(out_taken[0], 1)

                @block.vector
                def _(dve):
                    def split_out(it, u):
                        split_weights(dve, "out", it, u, wparts)

                    split_first(split_out)
                    dve.wait_ge(hsd, 1)
                    dve.reciprocal(hstd[:, :], hstd[:, :]).then_inc(hinv, 1)
                    before = x_cuts[0]
                    for k in range(KT + 2):
                        if k < KT:
                            dve.wait_ge(hspread, k + 1)
                            for i in range(2):
                                half = slice(HALF * i, HALF * i + HALF)
                                ins = dve.scalar_tensor_tensor(out=nT[:, k, half], in0=yT[:, k, half],
                                                               scalar=vecT[:, V_Y + k:V_Y + k + 1],
                                                               in1=work[2 * (k % 2) + i][:, 0:HALF],
                                                               op0=ALU.mult, op1=ALU.mult)
                            ins.then_inc(y_norm, 1)
                        if 1 <= k <= KT:
                            dve.wait_ge(y_norm, k)
                            dve.tensor_copy(nparts[0][:, k - 1, :], nT[:, k - 1, :]).then_inc(x_high, 1)
                        if k >= 2:
                            dve.wait_ge(x_high, before + k - 1)
                            dve.tensor_tensor(nparts[1][:, k - 2, :], nT[:, k - 2, :],
                                              nparts[0][:, k - 2, :].bitcast(F32), ALU.subtract).then_inc(x_split, 1)
                    x_cuts[0] += KT

                    def take_out(it, n):
                        output_here(dve, "out", it, n)
                        dve_add(dve, tile_of(xT, it, n), n % 2).then_inc(out_taken[n % 2], 1)

                    split_and_take(dve, 2, split_out, take_out)

                    def split_xq(it, u):
                        split_weights(dve, "xq", it, u, wparts)

                    split_first(split_xq)
                    norm_split(dve, 2, xT, V_XA, yT, nparts)

                    def take_xq(it, n):
                        if n % 2:
                            output_here(dve, "xq", it, n)
                            dve_copy(dve, qx[:, n, :], 1).then_inc(out_taken[1], 1)

                    split_and_take(dve, 1, split_xq, take_xq)

            with ExitStack() as c9:
                def t9(name, shape):
                    return c9.enter_context(nc.sbuf_tensor(name, shape, F32))

                XS = XD ** -0.5
                KTx = t9("KTx", [P, XH, NM])
                Px = t9("Px", [P, 2, NM])
                PTx = t9("PTx", [P, 2, NM])
                sx = t9("sx", [P, 4, 4])
                SKIP = 16 * NB * 4 + 16
                qm = t9("qm", [P, NB * SKIP])
                idle = nT[:, :, :].rearrange("p k n -> p (k n)")
                kx = idle[:, 0:2048].rearrange("p (b c n) -> p b c n", b=2, c=2)
                KTs = idle[:, 2048:4096].rearrange("p (b h m) -> p b h m", b=2, h=XH)
                vx2 = t9("vx", [P, NB // 2, 2, 512])
                vx1 = ring[:, :, :, :].rearrange("p b k n -> p b (k n)").rearrange("p b (c n) -> p b c n", c=2)
                Pm, PTm = t9("Pm", [P, NM]), t9("PTm", [P, NM])

                def vx(b, c, cols_):
                    return vx1[:, b, c, cols_] if b < NB // 2 else vx2[:, b - NB // 2, c, cols_]

                kx_here = [sem(f"kx_here{j}") for j in range(2)]
                vx_here, qm_zero, qm_ready = sem("vx_here"), sem("qm_zero"), sem("qm_ready")
                xk_mm, xk_out, xs_mm, xs_max, xp_exp, xd, xt_mm, xt_out, xv_mm, xo_out, chain9 = (
                    sem(f"x_{n}") for n in ("k_mm", "k_out", "s_mm", "max", "exp", "d", "t_mm", "t_out", "v_mm",
                                            "o_out", "chain"))
                sk_mm, sk_out, sq_mm, sm_ready, sp_ready, sp_n, st_mm, st_out, sv_mm = (
                    sem(f"xs_{n}") for n in ("k_mm", "k_out", "s_mm", "max", "exp", "norm", "t_mm", "t_out", "v_mm"))
                steps9 = [(h, qt) for h in range(XH) for qt in range(QT)]

                with nc.Block() as block:
                    @block.sync
                    def _(sp):
                        mem = I["cache_mem_kv"][0].rearrange("b (c p) v h d -> b p c v (h d)", p=P)
                        for b in range(NB):
                            sp.dma_start(vx(b, slice(0, 2), slice(0, 512)), mem[b, :, :, 1, :]).then_inc(vx_here, 16)
                            if b >= 2:
                                sp.wait_ge(sk_mm, 2 * (b - 1))
                            sp.dma_start(kx[:, b % 2, :, :], mem[b, :, :, 0, :]).then_inc(kx_here[b % 2], 16)

                    @block.gpsimd
                    def _(pool):
                        pool.memset(qm[:, :], 0.0).then_inc(qm_zero, 1)

                    @block.tensor
                    def _(pe):
                        for i in range(2):
                            for h in (2 * i, 2 * i + 1):
                                for c in range(2):
                                    mm = pe.transpose(work[i][:, NM * (h % 2) + P * c:NM * (h % 2) + P * c + P],
                                                      memtok[:, c, P * h:P * h + P], ident)
                            mm.then_inc(xk_mm, 1)
                        pe.wait_ge(xk_out, 2)

                        def scores(n):
                            h, qt = steps9[n]
                            if n >= 4:
                                pe.wait_ge(xp_exp, n - 3)
                            pe.matmul(work[n % 4][:, 0:NM], qx[:, h, P * qt:P * qt + P], KTx[:, h, :],
                                      start=True, stop=True).then_inc(xs_mm, 1)

                        def values(n):
                            h, qt = steps9[n]
                            if qt == 0 and h >= 2:
                                pe.wait_ge(xo_out, h - 1)
                            pe.wait_ge(xt_out, n + 1)
                            for c in range(2):
                                mm = pe.matmul(gemm_big[h % 2][:, P * qt:P * qt + P],
                                               memtok[:, c, 512 + P * h:512 + P * h + P],
                                               PTx[:, n % 2, P * c:P * c + P], start=(c == 0), stop=(c == 1))
                            mm.then_inc(xv_mm, 1)

                        scores(0)
                        scores(1)
                        scores(2)
                        for n in range(len(steps9)):
                            if n + 3 < len(steps9):
                                scores(n + 3)
                            pe.wait_ge(xd, n + 1)
                            pe.wait_ge(xp_exp, n + 1)
                            if n >= 2:
                                pe.wait_ge(xt_out, n - 1)
                            for c in range(2):
                                mm = pe.transpose(gemm_small[n % 2][:, P * c:P * c + P], Px[:, n % 2, P * c:P * c + P],
                                                  ident)
                            mm.then_inc(xt_mm, 1)
                            if n:
                                values(n - 1)
                        values(len(steps9) - 1)
                        pe.wait_ge(xp_exp, len(steps9))
                        pe.wait_ge(qm_ready, 1)

                        def turn(b):
                            pe.wait_ge(kx_here[b % 2], 16 * (b // 2 + 1))
                            if b:
                                pe.wait_ge(sk_out, 2 * b)
                            for i in range(2):
                                for h in (2 * i, 2 * i + 1):
                                    for c in range(2):
                                        at = NM * (h % 2) + P * c
                                        mm = pe.transpose(work[i][:, at:at + P], kx[:, b % 2, c, P * h:P * h + P], ident)
                                mm.then_inc(sk_mm, 1)

                        turn(0)
                        for b in range(NB):
                            if b + 1 < NB:
                                turn(b + 1)
                            pe.wait_ge(sk_out, 2 * b + 2)
                            for h in range(XH):
                                at = P * (XH * b + h)
                                mm = pe.matmul(work[2][:, 0:NM], qm[:, at:at + P], KTs[:, b % 2, h, :],
                                               start=(b == 0 and h == 0), stop=(b == NB - 1 and h == XH - 1))
                            mm.then_inc(sq_mm, 1)
                        pe.wait_ge(sp_n, 1)
                        for c in range(2):
                            mm = pe.transpose(work[3][:, P * c:P * c + P], Pm[:, P * c:P * c + P], ident)
                        mm.then_inc(st_mm, 1)
                        pe.wait_ge(st_out, 1)
                        pe.wait_ge(vx_here, 16 * NB)
                        pe.wait_ge(xo_out, XH)
                        for b in range(NB):
                            for h in range(XH):
                                for c in range(2):
                                    at = P * c + 16 * b + ST * h
                                    mm = pe.matmul(gemm_big[0][:, TS * h + ST * b:TS * h + ST * b + ST],
                                                   vx(b, c, slice(P * h, P * h + P)), PTm[:, at:at + ST],
                                                   start=(c == 0), stop=(c == 1))
                        mm.then_inc(sv_mm, 1)

                    @block.scalar
                    def _(act):
                        def weights(n):
                            act.wait_ge(xs_max, n + 1)
                            if n >= 2:
                                act.wait_ge(xt_mm, n - 1)
                            act.activation(Px[:, n % 2, :], work[n % 4][:, 0:NM], ACT.Exp, bias=sx[:, n % 4, 1:2],
                                           scale=XS, accum_out=sx[:, n % 4, 2:3]).then_inc(xp_exp, 1)

                        weights(0)
                        for n, (h, qt) in enumerate(steps9):
                            if n + 1 < len(steps9):
                                weights(n + 1)
                            act.wait_ge(xt_mm, n + 1)
                            if n >= 2:
                                act.wait_ge(xv_mm, n - 1)
                            act.activation(PTx[:, n % 2, :], gemm_small[n % 2][:, 0:NM], ACT.Copy).then_inc(xt_out, 1)
                            if qt == 1 and h:
                                act.wait_ge(xv_mm, QT * h)
                                act.activation(ox[:, h - 1, 0:TP], gemm_big[(h - 1) % 2][:, :], ACT.Copy)\
                                    .then_inc(xo_out, 1)
                        act.wait_ge(xv_mm, len(steps9))
                        act.activation(ox[:, XH - 1, 0:TP], gemm_big[(XH - 1) % 2][:, :], ACT.Copy).then_inc(xo_out, 1)
                        for b in range(NB):
                            for i in range(2):
                                act.wait_ge(sk_mm, 2 * b + i + 1)
                                if b >= 2:
                                    act.wait_ge(sq_mm, b - 1)
                                act.activation(KTs[:, b % 2, 2 * i:2 * i + 2, :],
                                               work[i][:, :].rearrange("p (h m) -> p h m", h=2), ACT.Copy)\
                                    .then_inc(sk_out, 1)
                        act.wait_ge(sm_ready, 1)
                        act.activation(Pm[:, :], work[2][:, 0:NM], ACT.Exp, bias=sx[:, 0, 1:2], scale=XS,
                                       accum_out=sx[:, 0, 2:3]).then_inc(sp_ready, 1)

                    @block.vector
                    def _(dve):
                        c = Chain(dve, chain9)
                        for i in range(2):
                            dve.wait_ge(xk_mm, i + 1)
                            dve.tensor_copy(KTx[:, 2 * i:2 * i + 2, :], work[i][:, :].rearrange("p (h m) -> p h m", h=2))\
                                .then_inc(xk_out, 1)
                        dve.wait_ge(qm_zero, 1)
                        for h in range(XH):
                            ins = dve.tensor_copy(
                                qm[:, :].rearrange("p (b s) -> p b s", s=SKIP)[:, :, (P + ST) * h:(P + ST) * h + ST],
                                qx[:, h, TP:NT].rearrange("p (b t) -> p b t", b=NB))
                        ins.then_inc(qm_ready, 1)

                        def top(n):
                            dve.wait_ge(xs_mm, n + 1)
                            c.step(dve.tensor_reduce(sx[:, n % 4, 0:1], work[n % 4][:, 0:NM], AX, ALU.max))
                            dve.tensor_scalar(sx[:, n % 4, 1:2], sx[:, n % 4, 0:1], -XS, None, ALU.mult)\
                                .then_inc(xs_max, 1)

                        top(0)
                        top(1)
                        for n in range(len(steps9)):
                            dve.wait_ge(xp_exp, n + 1)
                            c.step(dve.reciprocal(sx[:, n % 4, 3:4], sx[:, n % 4, 2:3]))
                            dve.tensor_scalar(Px[:, n % 2, :], Px[:, n % 2, :], sx[:, n % 4, 3:4], None, ALU.mult)\
                                .then_inc(xd, 1)
                            if n + 2 < len(steps9):
                                top(n + 2)
                        dve.wait_ge(sq_mm, NB)
                        c.step(dve.tensor_reduce(sx[:, 0, 0:1], work[2][:, 0:NM], AX, ALU.max))
                        dve.tensor_scalar(sx[:, 0, 1:2], sx[:, 0, 0:1], -XS, None, ALU.mult).then_inc(sm_ready, 1)
                        dve.wait_ge(sp_ready, 1)
                        c.step(dve.reciprocal(sx[:, 0, 3:4], sx[:, 0, 2:3]))
                        dve.tensor_scalar(Pm[:, :], Pm[:, :], sx[:, 0, 3:4], None, ALU.mult).then_inc(sp_n, 1)
                        dve.wait_ge(st_mm, 1)
                        dve.tensor_copy(PTm[:, :], work[3][:, 0:NM]).then_inc(st_out, 1)
                        dve.wait_ge(sv_mm, 1)
                        dve.tensor_copy(ox[:, :, TP:NT], gemm_big[0][:, 0:P].rearrange("p (h t) -> p h t", h=XH))

            with nc.Block() as block:
                @block.sync
                def _(sp):
                    w = I["xa_wo"][0].rearrange("(k p) n -> p k n", p=P)
                    for n in range(8):
                        slot_free(sp, "xo", n // RING, n % RING)
                        sp.dma_start(ring[:, n % RING, 0:XH, :], w[:, :, P * n:P * n + P]).then_inc(w_loaded[n % RING], 16)
                    sp.dma_start(rw_[:, :, 0:4], I["router_gw"][0].rearrange("(k p) n -> p k n", p=P))\
                        .then_inc(r_here, 16)
                    sp.dma_start(rw_[:, :, 4:NR], I["router_ew"][0].rearrange("(k p) n -> p k n", p=P))\
                        .then_inc(r_here, 16)
                    sp.dma_start(rb[:, 0:4], I["router_gb"].to_broadcast([P, 4])).then_inc(r_here, 16)
                    sp.dma_start(rb[:, 4:NR], I["router_eb"].to_broadcast([P, NE])).then_inc(r_here, 16)
                    for u in range(RING):
                        load_up(sp, 0, 0, u)

                @block.tensor
                def _(pe):
                    pe_gemm(pe, "xo", 8, XH, lambda k: [x[:, k, :] for x in nparts], wparts, 4 * KT)
                    norm_pe(pe, 3, nT)
                    pe.wait_ge(rw_split, 1)
                    pe.wait_ge(std_ready, 4)
                    for k in range(KT):
                        pe.wait_ge(x_split, 4 * KT + XH + k + 1)
                        mm = product(pe, [(work[i][0:NR, 0:HALF], HALF * i) for i in range(2)],
                                     [x[:, k, :] for x in rparts], [x[:, k, :] for x in nparts], k == 0, k == KT - 1)
                    mm.then_inc(lt_mm, 1)

                @block.scalar
                def _(act):
                    norm_act(act, 3, xT, nT, after="xo")

                @block.vector
                def _(dve):
                    def split_xo(it, u):
                        split_weights(dve, "xo", it, u, wparts, XH)

                    split_x(dve, ox, nparts, range(XH))
                    split_first(split_xo)

                    def take_xo(it, n):
                        output_here(dve, "xo", it, n)
                        dve_add(dve, tile_of(xT, it, n), n % 2).then_inc(out_taken[n % 2], 1)

                    split_and_take(dve, 2, split_xo, take_xo)
                    for u in range(2):
                        split_weights(dve, "up0", 0, u, wparts)
                    dve.wait_ge(r_here, 64)
                    split(dve, rw_[:, :, :], rparts[0][:, :, :], rparts[1][:, :, :], rw_high, 1).then_inc(rw_split, 1)
                    norm_split(dve, 3, xT, V_FFN, nT, nparts)
            cross.close()

            with ExitStack() as c11:
                def t11(name, shape):
                    return c11.enter_context(nc.sbuf_tensor(name, shape, F32))

                PARTS = NE // EP
                Hparts = [c11.enter_context(nc.sbuf_tensor(n, [P, 2 * EP, NT], F32R)) for n in ("H_high", "H_low")]
                lgT, combT, ce = yT[0:NR, 4, :], yT[0:NE, 5, :], yT[0:NE, 6, :]
                sl, hu, cb, hid = yT[:, 0:2, :], yT[:, 2, :], yT[:, 3, :], yT[:, 7, :]
                lg = t11("lg", [P, NQ, NR])
                a4 = t11("a4", [P, 8, NQ, 4])
                a1 = t11("a1", [P, 8, NQ])
                comb = t11("comb", [P, NQ, NE])
                lt_out, l_mm, chain11, r_exp, r_sub, cm_ready, ct_mm, ct_out = (
                    sem(f"r_{n}") for n in ("lt_out", "l_mm", "chain", "exp", "sub", "comb",
                                            "ct_mm", "ct_out"))
                ce_ready, cb_mm, cb_out, hu_used, h_high, he_done = (
                    sem(f"e_{n}") for n in ("ce", "cb_mm", "cb_out", "hu", "h_high", "h"))

                with nc.Block() as block:
                    @block.sync
                    def _(sp):
                        down = I["exp_w_down"][0].rearrange("e f n -> (e f) n").rearrange("(s k p) n -> s p k n", k=KT, p=P)
                        for part in range(PARTS):
                            with sp.Fori(1 - part, EP) as e:
                                for u in range(RING):
                                    load_up(sp, part, e, u)
                            with sp.Fori(0, KT // 2) as it:
                                for u in range(RING):
                                    slot_free(sp, f"down{part}", it, u)
                                    sp.dma_start(ring[:, u, :, :],
                                                 down[2 * part + u % 2, :, :, bass.ds((it * 2 + u // 2) * P, P)])\
                                        .then_inc(w_loaded[u], 16)

                    @block.tensor
                    def _(pe):
                        pe.wait_ge(lt_out, 1)
                        for q in range(NQ):
                            n = P if q < QT else TS
                            mm = pe.transpose(work[2][0:n, NR * q:NR * q + NR], lgT[:, P * q:P * q + n], ident[0:NR, 0:NR])
                        mm.then_inc(l_mm, 1)
                        pe.wait_ge(cm_ready, 1)
                        for q in range(NQ):
                            n = P if q < QT else TS
                            bank_ = work[3][0:NE, P * q:P * q + n] if q < QT else work[2][0:NE, P:P + n]
                            mm = pe.transpose(bank_, comb[0:n, q, :], ident[0:n, 0:n])
                        mm.then_inc(ct_mm, 1)

                        for part in range(PARTS):
                            def weights_over_partitions(e):
                                pe.wait_ge(ce_ready, e + (EP * part + 1))
                                pe.wait_ge(cb_out, e + (EP * part + 1))
                                for i in range(2):
                                    mm = pe.matmul(work[i][:, 0:HALF], const("ones", NE),
                                                   ce[:, HALF * i:HALF * i + HALF], start=True, stop=True)
                                mm.then_inc(cb_mm, 1)

                            pe_gemm(pe, f"up{part}", 4 * EP, KT, lambda k: [x[:, k, :] for x in nparts], wparts,
                                    4 * KT + XH, between=weights_over_partitions)
                            pe.wait_ge(he_done, 2 + 2 * EP * (part + 1))
                            o2 = stage[f"down{part}"][0] // 2
                            with pe.Fori(0, KT // 2) as it:
                                for u in range(RING):
                                    pe.wait_ge(w_split[u % 2], it * 2 + (o2 + u // 2 + 1))
                                    if u % 2 == 0:
                                        pe.wait_ge(out_taken[u // 2], it * 2 + o2)
                                    for k in range(KT):
                                        kk = KT * (u % 2) + k
                                        mm = product(pe, halves(u // 2), [x[:, u % 2, k, :] for x in wparts],
                                                     [x[:, kk, :] for x in Hparts], kk == 0, kk == 2 * EP - 1)
                                    mm.then_inc(w_done[u % 2], 1)

                    @block.scalar
                    def _(act):
                        act.wait_ge(r_sub, 1)
                        act.activation(a4[:, 1, :, :], a4[:, 1, :, :], ACT.Exp).then_inc(r_exp, 1)
                        act.wait_ge(r_sub, 2)
                        act.activation(a1[:, 4, :], a1[:, 4, :], ACT.Exp).then_inc(r_exp, 1)
                        for part in range(PARTS):
                            with act.Fori(0, EP) as e:
                                for f in range(2):
                                    if f == 0:
                                        act.wait_ge(he_done, e * 2 + (2 * EP * part + 2))
                                    else:
                                        act.wait_ge(cb_mm, e + (EP * part + 1))
                                        for i in range(2):
                                            ins = act.activation(cb[:, HALF * i:HALF * i + HALF],
                                                                 work[i][:, 0:HALF], ACT.Copy)
                                        ins.then_inc(cb_out, 1)
                                    output_here(act, f"up{part}", e, 2 * f)
                                    for bank_, at in halves(0):
                                        ins = act.activation(sl[:, f, at:at + HALF], bank_, ACT.Silu)
                                    ins.then_inc(out_taken[0], 1)

                    @block.vector
                    def _(dve):
                        c = Chain(dve, chain11)
                        dve.wait_ge(lt_mm, 1)
                        c.step(dve.memset(lg[:, :, :], 0.0))
                        dve.tensor_copy(lgT[:, 0:HALF], work[0][0:NR, 0:HALF])
                        dve.tensor_copy(lgT[:, HALF:NT], work[1][0:NR, 0:HALF]).then_inc(lt_out, 1)
                        dve.wait_ge(l_mm, 1)
                        bias = rb[:, :].unsqueeze(1)
                        dve.tensor_tensor(lg[:, 0:QT, :], work[2][:, 0:NR * QT].rearrange("p (q n) -> p q n", n=NR),
                                          bias.to_broadcast([P, QT, NR]), ALU.add)
                        c.step(dve.tensor_tensor(lg[0:TS, QT, :], work[2][0:TS, NR * QT:NR * NQ], rb[0:TS, :], ALU.add))

                        def first_max(x, hot, top, seen):
                            c.step(dve.tensor_reduce(top, x, AX, ALU.max))
                            c.step(dve.tensor_tensor(hot, x, top.unsqueeze(2).to_broadcast([P, NQ, 4]), ALU.is_equal))
                            c.step(dve.tensor_copy(seen, hot[:, :, 0]))
                            for j in range(1, 4):
                                c.step(dve.tensor_tensor(a1[:, 7, :], hot[:, :, j], seen, ALU.mult))
                                c.step(dve.tensor_tensor(hot[:, :, j], hot[:, :, j], a1[:, 7, :], ALU.subtract))
                                c.step(dve.tensor_tensor(seen, seen, hot[:, :, j], ALU.max))

                        g_log, g_p, g_hot, le, tmp4, hot1, hot2, le2 = (a4[:, i, :, :] for i in range(8))
                        g_top, g_sum, g_w, m1, e2, m2, seen = (a1[:, i, :] for i in range(7))
                        c.step(dve.tensor_copy(g_log, lg[:, :, 0:4]))
                        c.step(dve.tensor_reduce(g_top, g_log, AX, ALU.max))
                        dve.tensor_tensor(g_p, g_log, g_top.unsqueeze(2).to_broadcast([P, NQ, 4]), ALU.subtract)\
                            .then_inc(r_sub, 1)
                        dve.wait_ge(r_exp, 1)
                        c.step(dve.tensor_reduce(g_sum, g_p, AX, ALU.add))
                        c.step(dve.reciprocal(g_sum, g_sum))
                        c.step(dve.tensor_tensor(g_p, g_p, g_sum.unsqueeze(2).to_broadcast([P, NQ, 4]), ALU.mult))
                        first_max(g_p, g_hot, g_w, seen)
                        for g in range(4):
                            mine = lg[:, :, 4 + 4 * g:8 + 4 * g]
                            on = g_hot[:, :, g:g + 1].to_broadcast([P, NQ, 4])
                            if g == 0:
                                c.step(dve.tensor_tensor(le, mine, on, ALU.mult))
                            else:
                                c.step(dve.tensor_tensor(tmp4, mine, on, ALU.mult))
                                c.step(dve.tensor_tensor(le, le, tmp4, ALU.add))
                        first_max(le, hot1, m1, seen)
                        c.step(dve.tensor_scalar(tmp4, hot1, -3e38, None, ALU.mult))
                        c.step(dve.tensor_tensor(le2, le, tmp4, ALU.add))
                        first_max(le2, hot2, m2, seen)
                        dve.tensor_tensor(e2, m2, m1, ALU.subtract).then_inc(r_sub, 1)
                        dve.wait_ge(r_exp, 2)
                        w1_, w2_ = g_sum, g_top
                        c.step(dve.tensor_scalar(w1_, e2, 1.0, None, ALU.add))
                        c.step(dve.reciprocal(w1_, w1_))
                        c.step(dve.tensor_tensor(w2_, w1_, e2, ALU.mult))
                        for w_, hot in ((w1_, hot1), (w2_, hot2)):
                            c.step(dve.tensor_tensor(w_, w_, g_w, ALU.mult))
                            c.step(dve.tensor_tensor(hot, hot, w_.unsqueeze(2).to_broadcast([P, NQ, 4]), ALU.mult))
                        c.step(dve.tensor_tensor(hot1, hot1, hot2, ALU.add))
                        for g in range(4):
                            ins = dve.tensor_tensor(comb[:, :, 4 * g:4 * g + 4], hot1,
                                                    g_hot[:, :, g:g + 1].to_broadcast([P, NQ, 4]), ALU.mult)
                        ins.then_inc(cm_ready, 1)
                        dve.wait_ge(ct_mm, 1)
                        dve.tensor_copy(combT[:, 0:TP], work[3][0:NE, :])
                        dve.tensor_copy(combT[:, TP:NT], work[2][0:NE, P:P + TS]).then_inc(ct_out, 1)
                        dve.wait_ge(ct_out, 1)
                        dve.memset(spare[0:1, 6:7], 0.0).then_inc(he_done, 2)
                        dve.memset(spare[0:1, 7:8], 0.0).then_inc(cb_out, 1)
                        for part in range(PARTS):
                            up_, o2 = f"up{part}", stage[f"up{part}"][0] // 2

                            def spread(e):
                                dve.tensor_scalar(ce[:, :], combT[:, :], ident[0:NE, bass.ds(e + EP * part, 1)], None,
                                                  ALU.mult).then_inc(ce_ready, 1)

                            def split_up(e, u):
                                split_weights(dve, up_, e, u, wparts)

                            def spread_next(e):
                                dve.wait_ge(cb_mm, e + (EP * part + 1))
                                spread(e + 1)

                            def take_up(e, n):
                                if n % 2 == 0:
                                    return
                                f = n // 2
                                dve.wait_ge(cb_out, e + (EP * part + 2 + (f < 0) * -1))
                                output_here(dve, up_, e, n)
                                for bank_, at in halves(1):
                                    ins = dve.tensor_tensor(hu[:, at:at + HALF], bank_, cb[:, at:at + HALF], ALU.mult)
                                ins.then_inc(out_taken[1], 1)
                                dve.wait_ge(out_taken[1], e * 2 + (o2 + f + 1))
                                dve.wait_ge(out_taken[0], e * 2 + (o2 + f + 1))
                                high, low = (x[:, bass.ds(e * 2 + f, 1), :].rearrange("p a n -> p (a n)") for x in Hparts)
                                dve.tensor_tensor(hid[:, :], hu[:, :], sl[:, f % 2, :], ALU.mult).then_inc(hu_used, 1)
                                dve.wait_ge(hu_used, e * 2 + (2 * EP * part + f + 1))
                                split(dve, hid[:, :], high, low, h_high, e * 2 + (2 * EP * part + f + 1))\
                                    .then_inc(he_done, 1)
                                if f == 0:
                                    spread_next(e)

                            def take_down(it, n):
                                if n % 2 == 0:
                                    return
                                output_here(dve, f"down{part}", it, n)
                                pair = n // 2 % 2
                                dve_add(dve, xT[:, bass.ds(it * 2 + n // 2, 1), :].rearrange("p a n -> p (a n)"), pair)\
                                    .then_inc(out_taken[pair], 2)

                            def split_down(it, u):
                                split_weights(dve, f"down{part}", it, u, wparts)

                            if part == 0:
                                spread(0)
                            else:
                                split_first(split_up)
                            split_and_take(dve, EP, split_up, take_up)
                            split_first(split_down)
                            split_and_take(dve, KT // 2, split_down, take_down)

            with ExitStack() as c12:
                yt = c12.enter_context(nc.sbuf_tensor("yt", [P, 2, D], F32))
                f_mm, f_out, y_stored = sem("f_mm"), sem("f_out"), [sem(f"y_stored{j}") for j in range(2)]
                with nc.Block() as block:
                    @block.tensor
                    def _(pe):
                        norm_pe(pe, 4, yT)
                        pe.wait_ge(norm_ready, 5 * KT)
                        for q in range(QT + 1):
                            rows, at = (P, P * q) if q < QT else (TS, TP)
                            for half in range(2):
                                n = 2 * q + half
                                if n >= 2:
                                    pe.wait_ge(f_out, n - 1)
                                for i in range(4):
                                    mm = pe.transpose(work[n % 2][0:rows, P * i:P * i + P],
                                                      yT[:, 4 * half + i, at:at + rows], ident)
                                mm.then_inc(f_mm, 1)

                    @block.scalar
                    def _(act):
                        norm_act(act, 4, xT, yT)

                    @block.vector
                    def _(dve):
                        norm_dve(dve, 4, xT, V_FIN, yT)
                        for n in range(2 * QT + 2):
                            q, half = n // 2, n % 2
                            rows = P if q < QT else TS
                            dve.wait_ge(f_mm, n + 1)
                            if q >= 2:
                                dve.wait_ge(y_stored[q % 2], 16 * (q // 2))
                            dve.tensor_copy(yt[0:rows, q % 2, 512 * half:512 * half + 512], work[n % 2][0:rows, :])\
                                .then_inc(f_out, 1)

                    @block.sync
                    def _(sp):
                        for q in range(QT + 1):
                            sp.wait_ge(f_out, 2 * q + 2)
                            if q < QT:
                                sp.dma_start(O["y_prompt"][0, P * q:P * q + P, :], yt[:, q % 2, :]).then_inc(y_stored[q % 2], 16)
                            else:
                                sp.dma_start(O["y_sample"].rearrange("b t n -> (b t) n"), yt[0:TS, q % 2, :])\
                                    .then_inc(y_stored[q % 2], 16)
                        sp.wait_ge(y_stored[0], 16 * 3)
                        sp.wait_ge(y_stored[1], 16 * 2)
                        sp.wait_ge(out_dma, stores[0])


_OUTS = [("y_prompt", (1, TP, D)), ("y_sample", (NB, ST, D)),
         ("kv_p", (1, 1, TP, 4, G, HD)), ("kv_s", (1, NB, ST, 4, G, HD)),
         ("win_p", (1, 1, WIN, 2, G, HD)), ("win_s", (1, NB, WIN, 2, G, HD)),
         ("C_p", (1, 1, MLH, HD, HD)), ("C_s", (1, NB, MLH, HD, HD)),
         ("n_p", (1, 1, MLH, HD)), ("n_s", (1, NB, MLH, HD)),
         ("m_p", (1, 1, MLH)), ("m_s", (1, NB, MLH)),
         ("h_p", (1, 1, 256)), ("h_s", (1, NB, 256)),
         ("conv_p", (1, 1, 3, 256)), ("conv_s", (1, NB, 3, 256)),
         ("mem_p", (1, 1, NM, 2, XH, XD))]


def kernel(**inputs):
    import concourse.bacc as _bacc
    from concourse.bass_utils import run_bass_kernel_spmd as _run

    nc = _bacc.Bacc("TRN2", target_bir_lowering=False, num_devices=1)
    arrays, ins = {}, {}
    for name, a in inputs.items():
        a = np.ascontiguousarray(a)
        arrays[f"in_{name}"] = a
        ins[name] = nc.dram_tensor(f"in_{name}", a.shape, mybir.dt.from_np(a.dtype), kind="ExternalInput").ap()
    consts = {}
    for name, a in zip(("const", "prompt", "past", "heads"), shape_constants()):
        a = np.ascontiguousarray(a)
        arrays[f"shape_{name}"] = a
        consts[name] = nc.dram_tensor(f"shape_{name}", a.shape, F32, kind="ExternalInput").ap()
    outs = {}
    for name, shape in _OUTS:
        outs[name] = nc.dram_tensor(f"out_{name}", shape, F32, kind="ExternalOutput").ap()
    build(nc, ins, outs, consts)
    r = _run(nc, [arrays], core_ids=[0])
    return tuple(r.results[0][f"out_{name}"] for name, _ in _OUTS)
```
